# Optimizing a Trainium2 kernel written in Bass

```python
import jax, jax.numpy as jnp
from jax import lax
import numpy as np

D_MODEL = 1024
BATCH = 1
SEQ = 1024
DEPTH = 1
DEC_BATCH = 1
DEC_SEQ = 512
PAST_LEN = 128

RWKV_HEAD = 64
RWKV_WIDTH = D_MODEL // 2
RWKV_HEADS = RWKV_WIDTH // RWKV_HEAD
DECAY_LORA = 64
ICLR_LORA = 64
GATE_LORA = 128
GN_EPS = 64e-5
MLA_HEADS = 8
QK_NOPE = 64
QK_ROPE = 32
V_HEAD = 64
Q_LORA = 768
KV_LORA = 256
ROPE_THETA = 10000.0
Q_BLOCK = 128
N_GROUPS = 4
EXPERTS_PER_GROUP = 8
N_EXPERTS = N_GROUPS * EXPERTS_PER_GROUP
TOP_K = 2
D_EXPERT = 256
MOE_BLOCK = 128
N_BRANCHES = 2
EPS = 1e-6

RWKV_COLS = 3 * RWKV_WIDTH + 2 * DECAY_LORA + 2 * ICLR_LORA + GATE_LORA
MLA_COLS = Q_LORA + KV_LORA + QK_ROPE
GATE_COLS = N_BRANCHES * D_MODEL
IN_COLS = RWKV_COLS + MLA_COLS + GATE_COLS
RWKV_SPLITS = (RWKV_WIDTH, 2 * RWKV_WIDTH, 3 * RWKV_WIDTH,
               3 * RWKV_WIDTH + DECAY_LORA, 3 * RWKV_WIDTH + 2 * DECAY_LORA,
               3 * RWKV_WIDTH + 2 * DECAY_LORA + ICLR_LORA,
               3 * RWKV_WIDTH + 2 * DECAY_LORA + 2 * ICLR_LORA)

kernel_name = 'hybrid_rwkv7_mla_hmoe_encoder'

def rms_norm(x, gain):
    xf = x.astype(jnp.float32)
    y = xf * lax.rsqrt(jnp.mean(xf * xf, axis=-1, keepdims=True) + EPS)
    return (y * gain.astype(jnp.float32)).astype(x.dtype)

def centred_shift(p, mu_prev, mu_next):
    prev = jnp.pad(p, ((0, 0), (1, 0), (0, 0)))[:, :-1]
    nxt = jnp.pad(p, ((0, 0), (0, 1), (0, 0)))[:, 1:]
    return p + mu_prev * (prev - p) + mu_next * (nxt - p)

def wkv7_scan(r, w, k, v, kk, a, reverse):
    B, S, H, N = r.shape

    def step(state, inp):
        r_t, w_t, k_t, v_t, kk_t, a_t = inp
        sa = jnp.einsum('bhvk,bhk->bhv', state, -kk_t)
        state = (state * w_t[:, :, None, :] + sa[..., None] * (kk_t * a_t)[:, :, None, :]
                 + v_t[..., None] * k_t[:, :, None, :])
        return state, jnp.einsum('bhvk,bhk->bhv', state, r_t)

    xs = tuple(jnp.moveaxis(t, 1, 0) for t in (r, w, k, v, kk, a))
    _, ys = lax.scan(step, jnp.zeros((B, H, N, N), jnp.float32), xs, reverse=reverse)
    return jnp.moveaxis(ys, 0, 1)

def rwkv7_mixer(p, shift_mu, decay_w0, decay_up, iclr_a0, iclr_up, gate_up, k_k, k_a, r_k, gn_w, gn_b, w_o_rwkv):
    B, S, _ = p.shape
    p = centred_shift(p.astype(jnp.float32), shift_mu[0], shift_mu[1])
    r, k, v, wd_f, wd_b, ad_f, ad_b, gd = jnp.split(p, RWKV_SPLITS, axis=-1)
    hs = (B, S, RWKV_HEADS, RWKV_HEAD)
    kk = (k * k_k).reshape(hs)
    kk = kk / jnp.maximum(jnp.sqrt(jnp.sum(kk * kk, axis=-1, keepdims=True)), 1e-12)
    r_h, v_h = r.reshape(hs), v.reshape(hs)
    ys = []
    for d, (wd, ad) in enumerate(((wd_f, ad_f), (wd_b, ad_b))):
        w_log = -jax.nn.softplus(-(decay_w0[d] + jnp.tanh(wd) @ decay_up[d])) - 0.5
        decay = jnp.exp(-jnp.exp(w_log))
        a = jax.nn.sigmoid(iclr_a0[d] + ad @ iclr_up[d])
        k_d = k * (1.0 + (a - 1.0) * k_a)
        ys.append(wkv7_scan(r_h, decay.reshape(hs), k_d.reshape(hs), v_h, kk, a.reshape(hs), reverse=(d == 1)))
    y = ys[0] + ys[1]
    mu = jnp.mean(y, axis=-1, keepdims=True)
    var = jnp.mean(jnp.square(y - mu), axis=-1, keepdims=True)
    y = ((y - mu) * lax.rsqrt(var + GN_EPS)).reshape(B, S, RWKV_WIDTH) * gn_w + gn_b
    bonus = jnp.sum(r_h * k.reshape(hs) * r_k, axis=-1, keepdims=True) * v_h
    g = jax.nn.sigmoid(gd) @ gate_up
    out = (y + bonus.reshape(B, S, RWKV_WIDTH)) * g
    return out.astype(w_o_rwkv.dtype) @ w_o_rwkv

def rope_tables(S):
    inv = 1.0 / (ROPE_THETA ** (jnp.arange(0, QK_ROPE, 2, dtype=jnp.float32) / QK_ROPE))
    ang = jnp.arange(S, dtype=jnp.float32)[:, None] * inv[None, :]
    return jnp.cos(ang), jnp.sin(ang)

def apply_rope(x, cos, sin):
    xf = x.astype(jnp.float32)
    x1, x2 = xf[..., :QK_ROPE // 2], xf[..., QK_ROPE // 2:]
    return jnp.concatenate([x1 * cos - x2 * sin, x1 * sin + x2 * cos], axis=-1).astype(x.dtype)

def mla_mixer(p, q_a_norm, w_uq, kv_a_norm, w_uk, w_uv, q_nope_norm, q_rope_norm, k_nope_norm, k_rope_norm, w_o_mla):
    B, S, _ = p.shape
    c_q, c_kv, k_pe = jnp.split(p, [Q_LORA, Q_LORA + KV_LORA], axis=-1)
    q = (rms_norm(c_q, q_a_norm) @ w_uq).reshape(B, S, MLA_HEADS, QK_NOPE + QK_ROPE)
    q_nope, q_pe = jnp.split(q, [QK_NOPE], axis=-1)
    c_kv = rms_norm(c_kv, kv_a_norm)
    k_nope = (c_kv @ w_uk).reshape(B, S, MLA_HEADS, QK_NOPE)
    v = (c_kv @ w_uv).reshape(B, S, MLA_HEADS, V_HEAD)
    cos, sin = rope_tables(S)
    q_nope = rms_norm(q_nope, q_nope_norm)
    k_nope = rms_norm(k_nope, k_nope_norm)
    q_pe = apply_rope(rms_norm(q_pe, q_rope_norm), cos[:, None, :], sin[:, None, :])
    k_pe = apply_rope(rms_norm(k_pe, k_rope_norm), cos, sin)
    scale = (QK_NOPE + QK_ROPE) ** -0.5
    n_blk = S // Q_BLOCK

    def to_blocks(t):
        return jnp.moveaxis(t.reshape(B, n_blk, Q_BLOCK, *t.shape[2:]), 1, 0)

    def attend(blk):
        qn, qr = blk
        s = (jnp.einsum('bqhd,bkhd->bhqk', qn, k_nope, preferred_element_type=jnp.float32)
             + jnp.einsum('bqhr,bkr->bhqk', qr, k_pe, preferred_element_type=jnp.float32)) * scale
        pr = jax.nn.softmax(s, axis=-1).astype(v.dtype)
        return jnp.einsum('bhqk,bkhd->bqhd', pr, v)

    o = lax.map(attend, (to_blocks(q_nope), to_blocks(q_pe)))
    o = jnp.moveaxis(o, 0, 1).reshape(B, S, MLA_HEADS * V_HEAD)
    return o @ w_o_mla

def hier_moe(h, w_rg, b_rg, w_re, b_re, w13, w2):
    B, S, D = h.shape
    N = B * S
    xt = h.reshape(N, D)
    g_prob = jax.nn.softmax((xt @ w_rg).astype(jnp.float32) + b_rg.astype(jnp.float32), axis=-1)
    grp = jnp.argmax(g_prob, axis=-1).astype(jnp.int32)
    p_grp = jnp.max(g_prob, axis=-1)
    e_logits = ((xt @ w_re).astype(jnp.float32) + b_re.astype(jnp.float32)).reshape(N, N_GROUPS, EXPERTS_PER_GROUP)
    e_in = jnp.take_along_axis(e_logits, grp[:, None, None], axis=1)[:, 0]
    top_p, top_i = lax.top_k(jax.nn.softmax(e_in, axis=-1), TOP_K)
    top_p = top_p / jnp.sum(top_p, axis=-1, keepdims=True)
    weight = (p_grp[:, None] * top_p).reshape(-1)
    expert = (grp[:, None] * EXPERTS_PER_GROUP + top_i.astype(jnp.int32)).reshape(-1)
    token = jnp.repeat(jnp.arange(N, dtype=jnp.int32), TOP_K)
    A = N * TOP_K
    order = jnp.argsort(expert)
    e_sorted = expert[order]
    counts = jnp.bincount(expert, length=N_EXPERTS)
    padded = (counts + MOE_BLOCK - 1) // MOE_BLOCK * MOE_BLOCK
    pad_end = jnp.cumsum(padded)
    pad_start = pad_end - padded
    start = jnp.cumsum(counts) - counts
    dest = pad_start[e_sorted] + jnp.arange(A, dtype=jnp.int32) - start[e_sorted]
    P = A + N_EXPERTS * MOE_BLOCK
    n_blk = P // MOE_BLOCK
    buf_tok = jnp.full((P,), N, jnp.int32).at[dest].set(token[order])
    buf_w = jnp.zeros((P,), jnp.float32).at[dest].set(weight[order])
    blk_e = jnp.minimum(jnp.searchsorted(pad_end, jnp.arange(n_blk, dtype=jnp.int32) * MOE_BLOCK, side='right'),
                        N_EXPERTS - 1)
    x_pad = jnp.concatenate([xt, jnp.zeros((1, D), xt.dtype)], axis=0)
    xb = x_pad[buf_tok].reshape(n_blk, MOE_BLOCK, D)

    def expert_block(args):
        xblk, e = args
        gt, up = jnp.split(xblk @ w13[e], 2, axis=-1)
        return (jax.nn.silu(gt) * up) @ w2[e]

    yb = lax.map(expert_block, (xb, blk_e)).reshape(P, D)
    out = jax.ops.segment_sum(yb.astype(jnp.float32) * buf_w[:, None], buf_tok, num_segments=N + 1)[:N]
    return out.astype(h.dtype).reshape(B, S, D)

def encoder_layer(x, c, w_ada, b_ada, norm1, w_in, shift_mu, decay_w0, decay_up, iclr_a0, iclr_up, gate_up,
                  k_k, k_a, r_k, gn_w, gn_b, w_o_rwkv, q_a_norm, w_uq, kv_a_norm, w_uk, w_uv,
                  q_nope_norm, q_rope_norm, k_nope_norm, k_rope_norm, w_o_mla, b_merge, w_out,
                  norm2, w_rg, b_rg, w_re, b_re, w13, w2):
    mod = (jax.nn.silu(c) @ w_ada + b_ada)[:, None, :]
    shift1, scale1, gate1, shift2, scale2, gate2 = jnp.split(mod, 6, axis=-1)
    h = rms_norm(x, norm1) * (1 + scale1) + shift1
    p = h @ w_in
    p_rwkv, p_mla, p_gate = jnp.split(p, [RWKV_COLS, RWKV_COLS + MLA_COLS], axis=-1)
    y_a = rwkv7_mixer(p_rwkv, shift_mu, decay_w0, decay_up, iclr_a0, iclr_up, gate_up, k_k, k_a, r_k,
                      gn_w, gn_b, w_o_rwkv).astype(x.dtype)
    y_b = mla_mixer(p_mla, q_a_norm, w_uq, kv_a_norm, w_uk, w_uv, q_nope_norm, q_rope_norm,
                    k_nope_norm, k_rope_norm, w_o_mla).astype(x.dtype)
    gates = jax.nn.sigmoid((p_gate + b_merge).astype(jnp.float32)).astype(x.dtype)
    g_a, g_b = jnp.split(gates, N_BRANCHES, axis=-1)
    x = x + gate1 * ((g_a * y_a + g_b * y_b) @ w_out)
    h2 = rms_norm(x, norm2) * (1 + scale2) + shift2
    x = x + gate2 * hier_moe(h2, w_rg, b_rg, w_re, b_re, w13, w2)
    return x

def setup_inputs(seed: int = 0) -> dict:
    key = jax.random.key(seed)
    ks = iter(list(jax.random.split(key, 64)))

    def nrm(shape, std):
        return std * jax.random.normal(next(ks), shape, jnp.float32)

    def gain(shape):
        return 1.0 + 0.05 * jax.random.normal(next(ks), shape, jnp.float32)

    L, D, C = DEPTH, D_MODEL, RWKV_WIDTH
    return {
        'x_prompt': nrm((BATCH, SEQ, D), 1.0),
        'x_sample': nrm((DEC_BATCH, DEC_SEQ, D), 1.0),
        'c_prompt': nrm((BATCH, D), 1.0),
        'c_sample': nrm((DEC_BATCH, D), 1.0),
        'w_ada': nrm((L, D, 6 * D), 0.5 * D ** -0.5),
        'b_ada': nrm((L, 6 * D), 0.02),
        'norm1': gain((L, D)),
        'w_in': nrm((L, D, IN_COLS), D ** -0.5),
        'shift_mu': 0.5 * jax.random.uniform(next(ks), (L, 2, RWKV_COLS), jnp.float32),
        'decay_w0': jax.random.uniform(next(ks), (L, 2, C), jnp.float32, minval=-6.0, maxval=0.0),
        'decay_up': nrm((L, 2, DECAY_LORA, C), 0.1),
        'iclr_a0': nrm((L, 2, C), 0.5),
        'iclr_up': nrm((L, 2, ICLR_LORA, C), 0.5 * ICLR_LORA ** -0.5),
        'gate_up': nrm((L, GATE_LORA, C), GATE_LORA ** -0.5),
        'k_k': 0.85 + 0.05 * jax.random.normal(next(ks), (L, C), jnp.float32),
        'k_a': gain((L, C)),
        'r_k': nrm((L, RWKV_HEADS, RWKV_HEAD), 0.1),
        'gn_w': gain((L, C)),
        'gn_b': nrm((L, C), 0.02),
        'w_o_rwkv': nrm((L, C, D), C ** -0.5),
        'q_a_norm': gain((L, Q_LORA)),
        'w_uq': nrm((L, Q_LORA, MLA_HEADS * (QK_NOPE + QK_ROPE)), Q_LORA ** -0.5),
        'kv_a_norm': gain((L, KV_LORA)),
        'w_uk': nrm((L, KV_LORA, MLA_HEADS * QK_NOPE), KV_LORA ** -0.5),
        'w_uv': nrm((L, KV_LORA, MLA_HEADS * V_HEAD), KV_LORA ** -0.5),
        'q_nope_norm': gain((L, QK_NOPE)),
        'q_rope_norm': gain((L, QK_ROPE)),
        'k_nope_norm': gain((L, QK_NOPE)),
        'k_rope_norm': gain((L, QK_ROPE)),
        'w_o_mla': nrm((L, MLA_HEADS * V_HEAD, D), (MLA_HEADS * V_HEAD) ** -0.5),
        'b_merge': nrm((L, GATE_COLS), 0.1),
        'w_out': nrm((L, D, D), D ** -0.5),
        'norm2': gain((L, D)),
        'w_rg': nrm((L, D, N_GROUPS), D ** -0.5),
        'b_rg': nrm((L, N_GROUPS), 0.01),
        'w_re': nrm((L, D, N_EXPERTS), D ** -0.5),
        'b_re': nrm((L, N_EXPERTS), 0.01),
        'w13': nrm((L, N_EXPERTS, D, 2 * D_EXPERT), D ** -0.5),
        'w2': nrm((L, N_EXPERTS, D_EXPERT, D), D_EXPERT ** -0.5),
    }

def reference(x_prompt, x_sample, c_prompt, c_sample, w_ada, b_ada, norm1, w_in, shift_mu, decay_w0, decay_up,
              iclr_a0, iclr_up, gate_up, k_k, k_a, r_k, gn_w, gn_b, w_o_rwkv, q_a_norm, w_uq, kv_a_norm,
              w_uk, w_uv, q_nope_norm, q_rope_norm, k_nope_norm, k_rope_norm, w_o_mla, b_merge, w_out,
              norm2, w_rg, b_rg, w_re, b_re, w13, w2):
    weights = (w_ada, b_ada, norm1, w_in, shift_mu, decay_w0, decay_up, iclr_a0, iclr_up, gate_up,
               k_k, k_a, r_k, gn_w, gn_b, w_o_rwkv, q_a_norm, w_uq, kv_a_norm, w_uk, w_uv,
               q_nope_norm, q_rope_norm, k_nope_norm, k_rope_norm, w_o_mla, b_merge, w_out,
               norm2, w_rg, b_rg, w_re, b_re, w13, w2)

    def trunk(x, c):
        for l in range(DEPTH):
            x = encoder_layer(x, c, *[w[l] for w in weights])
        return x

    y_prompt = trunk(x_prompt, c_prompt)
    y_sample = trunk(x_sample, c_sample)
    return (y_prompt, y_sample)


_drawn_inputs = setup_inputs


def setup_inputs(seed=0):
    import zlib

    import numpy as np

    out = dict(_drawn_inputs(seed))
    spreads = {}
    factors = {'b_ada': 2.95,
     'norm1': 4.56,
     'decay_up': 5.385,
     'iclr_a0': 2.911,
     'iclr_up': 3.381,
     'k_k': 30.0,
     'k_a': 16.643,
     'gn_w': 35.454,
     'gn_b': 64.0,
     'q_a_norm': 8.0,
     'w_uq': 3.671,
     'kv_a_norm': 8.0,
     'w_uk': 4.263,
     'q_nope_norm': 8.0,
     'q_rope_norm': 8.0,
     'k_nope_norm': 8.0,
     'k_rope_norm': 8.0,
     'b_merge': 7.406,
     'b_rg': 62.928,
     'b_re': 64.0,
     'norm2': 8.0}
    for name, (base, spread) in spreads.items():
        noise = np.random.default_rng([zlib.crc32(name.encode()), seed]).standard_normal(out[name].shape)
        drawn = base * np.exp(spread * noise) if base else spread * noise
        out[name] = __import__('jax').numpy.asarray(drawn.astype(out[name].dtype))
    for name, factor in factors.items():
        out[name] = (out[name] * factor).astype(out[name].dtype)
    return out
```

```python
from contextlib import ExitStack

import numpy as np

import concourse.bass as bass
from concourse import mybir

ALU = mybir.AluOpType
ACT = mybir.ActivationFunctionType
AX = mybir.AxisListType
F32 = mybir.dt.float32
I32 = mybir.dt.int32
U32 = mybir.dt.uint32

P = 128
D = 1024
DF = D // P
SEQS = (1024, 512)
TOK = sum(SEQS)
TT = TOK // P
NB = 512
NT = TOK // NB
EPS = 1e-6

COLS = {}
_n = 0
for _name, _w in (("b_ada", 48), ("norm1", 8), ("mu_prev", 24), ("mu_next", 24), ("b_merge", 16),
                  ("w0", 8), ("a0", 8), ("k_k", 4), ("k_a", 4), ("r_k", 4), ("gn_w", 4), ("gn_b", 4),
                  ("qa_norm", 6), ("kva_norm", 2), ("q_gain", 1), ("k_gain", 1)):
    COLS[_name] = (_n, _w)
    _n += _w
NCOLS = _n

SHIFT1, SCALE1, GATE1, SHIFT2, SCALE2, GATE2 = range(6)
N_SHIFTED = 24
N_GATES = 16


class Chain:

    def __init__(self, eng, sem, base=0, i=None, per=0):
        self.eng, self.sem, self.base, self.i, self.per, self.n = eng, sem, base, i, per, 0

    def value(self):
        v = self.base + self.n
        return v if self.i is None else self.i * self.per + v

    def __call__(self, ins):
        self.n += 1
        ins.then_inc(self.sem, 1)
        self.eng.wait_ge(self.sem, self.value())

    def end(self):
        assert self.i is None or self.n == self.per, (self.n, self.per)


def alone(eng, sem):
    eng.sem_inc(sem, 1)


class Scope:

    def __init__(self, nc, ctx):
        self.nc, self.ctx, self.sems = nc, ctx, []
        ctx.callback(self.clear)

    def clear(self):
        if self.sems:
            self.nc.clear_and_free_semaphores(self.sems)
            self.nc.all_engine_barrier()

    def sb(self, name, shape, dt=F32):
        return self.ctx.enter_context(self.nc.sbuf_tensor(name, shape, dt))

    def ps(self, name, shape, dt=F32):
        return self.ctx.enter_context(self.nc.psum_tensor(name, shape, dt))

    def sem(self, name):
        self.sems.append(self.nc.alloc_semaphore(name))
        return self.sems[-1]


def col(consts, name, k=0, n=None):
    first, width = COLS[name]
    return consts["cols"][:, first + k:first + (width if n is None else k + n)]


def load_constants(nc, dram, consts):
    with ExitStack() as ctx:
        s = Scope(nc, ctx)
        loaded = s.sem("constants_loaded")
        block = ctx.enter_context(nc.Block())

        @block.sync
        def _(sp):
            sp.dma_start(consts["cols"][:], dram["cols"][:, :]).then_inc(loaded, 16)
            sp.dma_start(consts["ident"][:], dram["ident"][:, :]).then_inc(loaded, 16)
            sp.dma_start(consts["ones"][:], dram["ones"][:, :]).then_inc(loaded, 16)
            sp.wait_ge(loaded, 48)


def modulation(nc, dram, consts):
    mod = consts["mod"]
    with ExitStack() as ctx:
        s = Scope(nc, ctx)
        c_rows = s.sb("c_rows", [2 * DF, P])
        c_col = s.sb("c_col", [P, 2 * DF])
        c_tanh = s.sb("c_tanh", [P, 2 * DF])
        c_silu = s.sb("c_silu", [P, 2 * DF])
        w = s.sb("w_ada_tile", [P, 2, DF, 512])
        rows = s.sb("mod_rows_sb", [96, P])
        ps_c = s.ps("ps_c", [P, 512])
        ps_mod = s.ps("ps_mod", [P, 2, 512])
        c_loaded = s.sem("c_loaded")
        w_loaded = [s.sem(f"w_ada_loaded{b}") for b in range(2)]
        c_turned = s.sem("c_turned")
        tanh_done = s.sem("tanh_done")
        silu_done = s.sem("silu_done")
        ps_full = [s.sem(f"mod_ps_full{b}") for b in range(2)]
        ps_free = [s.sem(f"mod_ps_free{b}") for b in range(2)]
        dve_own = s.sem("mod_dve_own")
        rows_turned = s.sem("rows_turned")
        rows_ready = s.sem("rows_ready")
        stored = s.sem("mod_stored")
        block = ctx.enter_context(nc.Block())

        @block.sync
        def _(sp):
            sp.dma_start(c_rows[:], dram["c"][:, :]).then_inc(c_loaded, 16)
            with sp.Fori(0, 6) as j:
                for b in range(2):
                    sp.wait_ge(ps_full[b], j)
                    sp.dma_start(w[:, b], dram["w_ada"][bass.ds(j, 1), b].rearrange("a p k m -> p (a k) m")).then_inc(w_loaded[b], 16)
            sp.wait_ge(rows_ready, 1)
            sp.dma_start(dram["mod_rows"][:, :], rows[:]).then_inc(stored, 16)
            sp.wait_ge(stored, 16)

        @block.tensor
        def _(pe):
            pe.wait_ge(c_loaded, 16)
            nc.tensor.transpose(ps_c[:, 0:2 * DF], c_rows[:], consts["ident"][0:2 * DF, 0:2 * DF]).then_inc(c_turned, 1)
            pe.wait_ge(silu_done, 2)
            with pe.Fori(0, 6) as j:
                for b in range(2):
                    pe.wait_ge(w_loaded[b], 16 * j + 16)
                    pe.wait_ge(ps_free[b], j)
                    for m in range(4):
                        for k in range(DF):
                            mm = nc.tensor.matmul(ps_mod[:, b, 2 * m:2 * m + 2], w[:, b, k, P * m:P * m + P],
                                                  c_silu[:, k::DF], start=(k == 0), stop=(k == DF - 1))
                    mm.then_inc(ps_full[b], 1)
            pe.wait_ge(dve_own, 1)
            nc.tensor.transpose(ps_c[0:96, 0:P], mod[:].rearrange("p j s f -> p (j s f)"), consts["ident"][:]).then_inc(rows_turned, 1)

        @block.scalar
        def _(act):
            act.wait_ge(c_turned, 1)
            nc.scalar.activation(c_tanh[:], ps_c[:, 0:2 * DF], ACT.Tanh, scale=0.5).then_inc(tanh_done, 1)
            act.wait_ge(rows_turned, 1)
            nc.scalar.copy(rows[:], ps_c[0:96, 0:P]).then_inc(rows_ready, 1)

        @block.vector
        def _(dve):
            dve.wait_ge(tanh_done, 1)
            nc.vector.tensor_scalar(c_col[:], ps_c[:, 0:2 * DF], 0.5, None, ALU.mult).then_inc(silu_done, 1)
            dve.wait_ge(silu_done, 1)
            nc.vector.scalar_tensor_tensor(out=c_silu[:], in0=c_tanh[:], scalar=1.0, in1=c_col[:],
                                           op0=ALU.add, op1=ALU.mult).then_inc(silu_done, 1)
            with dve.Fori(0, 6) as j:
                for b in range(2):
                    dve.wait_ge(ps_full[b], j + 1)
                    first = COLS["b_ada"][0] + 4 * b
                    for q in range(2):
                        out = mod[:, bass.ds(j, 1), q, 4 * b:4 * b + 4].rearrange("p a f -> p (a f)")
                        bias = consts["cols"][:, bass.ds(j * 8 + first, 4)]
                        ins = nc.vector.tensor_tensor(out, ps_mod[:, b, q:8:2], bias, ALU.add)
                    ins.then_inc(ps_free[b], 1)
            dve.wait_ge(ps_free[1], 6)
            for n, part in enumerate((SCALE1, SCALE2)):
                ins = nc.vector.tensor_scalar(mod[:, part], mod[:, part], 1.0, None, ALU.add)
            ins.then_inc(dve_own, 1)
            dve.wait_ge(dve_own, 1)
            for q in range(2):
                ins = nc.vector.tensor_tensor(consts["scale1"][:, q], mod[:, SCALE1, q], col(consts, "norm1"), ALU.mult)
            ins.then_inc(dve_own, 1)
            dve.wait_ge(dve_own, 2)


def norm_and_turn(nc, dram, consts, h_t):
    with ExitStack() as ctx:
        s = Scope(nc, ctx)
        x = s.sb("x_tile", [P, 2, D])
        sq = s.sb("x_square", [P, 2, D])
        ss = s.sb("x_ss", [P, 2, 2])
        xn = s.sb("x_normed", [P, 2, D])
        ps = s.ps("ps_turn", [P, 2, 2, 512])
        loaded = [s.sem(f"x_loaded{b}") for b in range(2)]
        summed = [s.sem(f"x_summed{b}") for b in range(2)]
        normed = [s.sem(f"x_normed{b}") for b in range(2)]
        turned = [s.sem(f"x_turned{b}") for b in range(2)]
        act_out = [s.sem(f"h_act{b}") for b in range(2)]
        dve_out = [s.sem(f"h_dve{b}") for b in range(2)]
        own = s.sem("norm_own")
        unread = s.sem("norm_unread")
        rms_in = [s.sem(f"rms_in{b}") for b in range(2)]
        rms_ready = [s.sem(f"rms_ready{b}") for b in range(2)]
        block = ctx.enter_context(nc.Block())
        runs = ((0, 0, SEQS[0] // P), (1, SEQS[0] // P, SEQS[1] // P))

        @block.sync
        def _(sp):
            with sp.Fori(0, TT // 2) as i:
                for b in range(2):
                    sp.wait_ge(normed[b], i)
                    sp.dma_start(x[:, b], dram["x"][bass.ds(i * 2 * P + b * P, P), :]).then_inc(loaded[b], 16)

        @block.scalar
        def _(act):
            for q, t0, n in runs:
                with act.Fori(t0 // 2, (t0 + n) // 2) as i:
                    for b in range(2):
                        act.wait_ge(loaded[b], 16 * i + 16)
                        nc.scalar.activation(sq[:, b], x[:, b], ACT.Square, accum_out=ss[:, b, 0:1]).then_inc(summed[b], 1)
                    for b in range(2):
                        act.wait_ge(rms_in[b], i + 1)
                        nc.scalar.activation(ss[:, b, 1:2], ss[:, b, 0:1], ACT.Sqrt).then_inc(rms_ready[b], 1)
                    for b in range(2):
                        act.wait_ge(turned[b], i + 1)
                        alone(act, unread)
                        for f in range(4):
                            ins = nc.scalar.activation(h_t[:, f, bass.ds(i * 2 * P + b * P, P)], ps[:, b, 0, P * f:P * f + P],
                                                       ACT.Identity, bias=consts["mod"][:, SHIFT1, q, f:f + 1],
                                                       scale=consts["scale1"][:, q, f:f + 1])
                        ins.then_inc(act_out[b], 1)

        @block.vector
        def _(dve):
            for q, t0, n in runs:
                with dve.Fori(t0 // 2, (t0 + n) // 2) as i:
                    step = Chain(dve, own, 0, i, 2)
                    for b in range(2):
                        dve.wait_ge(summed[b], i + 1)
                        nc.vector.tensor_scalar(ss[:, b, 0:1], ss[:, b, 0:1], 1.0 / D, EPS, ALU.mult, ALU.add).then_inc(rms_in[b], 1)
                    for b in range(2):
                        dve.wait_ge(rms_ready[b], i + 1)
                        step(nc.vector.reciprocal(ss[:, b, 1:2], ss[:, b, 1:2]))
                        dve.wait_ge(turned[b], i)
                        nc.vector.tensor_scalar(xn[:, b], x[:, b], ss[:, b, 1:2], None, ALU.mult).then_inc(normed[b], 1)
                    step.end()
                    for b in range(2):
                        dve.wait_ge(turned[b], i + 1)
                        for f in range(4, 8):
                            ins = nc.vector.tensor_scalar(h_t[:, f, bass.ds(i * 2 * P + b * P, P)], ps[:, b, 1, P * (f - 4):P * (f - 3)],
                                                          consts["scale1"][:, q, f:f + 1], consts["mod"][:, SHIFT1, q, f:f + 1],
                                                          ALU.mult, ALU.add)
                        ins.then_inc(dve_out[b], 1)

        @block.tensor
        def _(pe):
            with pe.Fori(0, TT // 2) as i:
                for b in range(2):
                    pe.wait_ge(normed[b], i + 1)
                    pe.wait_ge(act_out[b], i)
                    pe.wait_ge(dve_out[b], i)
                    for f in range(DF):
                        mm = nc.tensor.transpose(ps[:, b, f // 4, P * (f % 4):P * (f % 4) + P], xn[:, b, P * f:P * f + P], consts["ident"][:])
                    mm.then_inc(turned[b], 1)


def project_in(nc, dram, consts, h_t):
    L, R = SEQS
    W = TOK + 1
    starts = (1, 513, L + 2)
    with ExitStack() as ctx:
        s = Scope(nc, ctx)
        w = s.sb("w_in_tile", [P, 2, DF, P])
        row = s.sb("p_row", [P, 2, TOK + 3])
        mix = s.sb("p_mixed", [P, 2, W])
        mu_c = s.sb("mu_centre", [P, N_SHIFTED])
        ps = s.ps("ps_in", [P, 2, NT, NB])
        w_loaded = [s.sem(f"w_in_loaded{b}") for b in range(2)]
        full = [[s.sem(f"in_full{b}{n}") for n in range(NT)] for b in range(2)]
        copied = [[s.sem(f"in_copied{b}{n}") for n in range(NT)] for b in range(2)]
        mixed = [s.sem(f"in_mixed{b}") for b in range(2)]
        stored = [s.sem(f"in_stored{b}") for b in range(2)]
        ready = s.sem("in_ready")
        bias_now = s.sb("bias_now", [P, 2])
        bias_ready = s.sem("bias_ready")
        own = s.sem("in_own")
        unread = s.sem("in_unread")
        block = ctx.enter_context(nc.Block())
        HS, HG = N_SHIFTED // 2, N_GATES // 2

        @block.sync
        def _(sp):
            with sp.Fori(0, HS + HG) as i:
                for b in range(2):
                    sp.wait_ge(full[b][NT - 1], i)
                    sp.dma_start(w[:, b], dram["w_in"][bass.ds(2 * i + b, 1)].rearrange("a p k m -> p (a k) m")).then_inc(w_loaded[b], 16)

        @block.tensor
        def _(pe):
            with pe.Fori(0, HS + HG) as i:
                for b in range(2):
                    pe.wait_ge(w_loaded[b], 16 * i + 16)
                    for n in range(NT):
                        pe.wait_ge(copied[b][n], i)
                        for k in range(DF):
                            mm = nc.tensor.matmul(ps[:, b, n], w[:, b, k], h_t[:, k, NB * n:NB * n + NB],
                                                  start=(k == 0), stop=(k == DF - 1))
                        mm.then_inc(full[b][n], 1)

        @block.scalar
        def _(act):
            act.wait_ge(ready, 1)
            with act.Fori(0, HS) as i:
                for b in range(2):
                    act.wait_ge(mixed[b], i)
                    for n in range(NT):
                        act.wait_ge(full[b][n], i + 1)
                        nc.scalar.copy(row[:, b, starts[n]:starts[n] + NB], ps[:, b, n]).then_inc(copied[b][n], 1)
                    act.wait_ge(mixed[b], i + 1)
                    act.dma_start(dram["p_t"][bass.ds(2 * i + b, 1), :, 0:L].rearrange("a p t -> (a p) t"), mix[:, b, 0:L]).then_inc(stored[b], 16)
                    act.dma_start(dram["p_t"][bass.ds(2 * i + b, 1), :, L:TOK].rearrange("a p t -> (a p) t"), mix[:, b, L + 1:W]).then_inc(stored[b], 16)
            with act.Fori(HS, HS + HG) as i:
                for b in range(2):
                    act.wait_ge(mixed[b], i)
                    alone(act, unread)
                    nc.scalar.copy(bias_now[:, b:b + 1], consts["half_merge"][:, bass.ds(2 * i + (b - N_SHIFTED), 1)]).then_inc(bias_ready, 1)
                    act.wait_ge(bias_ready, 2 * i + (b + 1 - 2 * HS))
                    for n in range(NT):
                        act.wait_ge(full[b][n], i + 1)
                        nc.scalar.activation(row[:, b, NB * n:NB * n + NB], ps[:, b, n], ACT.Tanh, bias=bias_now[:, b:b + 1], scale=0.5).then_inc(copied[b][n], 1)
                    act.wait_ge(mixed[b], i + 1)
                    act.dma_start(dram["gates"][bass.ds(2 * i + (b - N_SHIFTED), 1)].rearrange("a p t -> (a p) t"), mix[:, b, 0:TOK]).then_inc(stored[b], 16)
            for b in range(2):
                act.wait_ge(stored[b], 16 * (2 * HS + HG))

        @block.vector
        def _(dve):
            prev, nxt = COLS["mu_prev"][0], COLS["mu_next"][0]
            start = Chain(dve, own)
            start(nc.vector.tensor_tensor(mu_c[:], col(consts, "mu_prev"), col(consts, "mu_next"), ALU.add))
            start(nc.vector.tensor_scalar(mu_c[:], mu_c[:], -1.0, 1.0, ALU.mult, ALU.add))
            start(nc.vector.tensor_scalar(consts["half_merge"][:], col(consts, "b_merge"), 0.5, None, ALU.mult))
            start(nc.vector.memset(row[:], 0.0))
            start(nc.vector.memset(mix[:], 0.0))
            dve.sem_inc(ready, 1)
            with dve.Fori(0, HS) as i:
                step = Chain(dve, own, start.n, i, 4)
                for b in range(2):
                    c = 2 * i + b
                    for n in range(NT):
                        dve.wait_ge(copied[b][n], i + 1)
                    dve.wait_ge(stored[b], 32 * i)
                    step(nc.vector.tensor_scalar(mix[:, b], row[:, b, 1:1 + W], mu_c[:, bass.ds(c, 1)], None, ALU.mult))
                    step(nc.vector.scalar_tensor_tensor(out=mix[:, b], in0=row[:, b, 0:W], scalar=consts["cols"][:, bass.ds(c + prev, 1)],
                                                        in1=mix[:, b], op0=ALU.mult, op1=ALU.add))
                    nc.vector.scalar_tensor_tensor(out=mix[:, b], in0=row[:, b, 2:2 + W], scalar=consts["cols"][:, bass.ds(c + nxt, 1)],
                                                   in1=mix[:, b], op0=ALU.mult, op1=ALU.add).then_inc(mixed[b], 1)
                step.end()
            with dve.Fori(HS, HS + HG) as i:
                for b in range(2):
                    for n in range(NT):
                        dve.wait_ge(copied[b][n], i + 1)
                    dve.wait_ge(stored[b], 16 * i + 16 * HS)
                    nc.vector.tensor_scalar(mix[:, b, 0:TOK], row[:, b, 0:TOK], 0.5, 0.5, ALU.mult, ALU.add).then_inc(mixed[b], 1)


CH = 64
RF = 4
RT, KT_, VT, WD, AD, GD = 0, 4, 8, 12, 13, 14
PB = 256
DECAY = float(np.exp(-0.5))


def rwkv_operands(nc, dram, consts):
    with ExitStack() as ctx:
        s = Scope(nc, ctx)
        up_w = s.sb("decay_up", [P, RF * P])
        up_a = s.sb("iclr_up", [P, RF * P])
        reset = s.sb("chunk_reset", [P, RF * PB])
        head_ones = s.sb("head_ones", [P, P])
        half_w0 = s.sb("half_w0", [P, 8])
        half_a0 = s.sb("half_a0", [P, 8])
        pin = s.sb("prep_in", [P, 2, 14, PB])
        W = [P, RF, PB]
        t_wd = s.sb("tanh_wd", [P, PB])
        kk_raw, sq, norm, kk, kka, k1 = (s.sb(n, W) for n in ("kk_raw", "kk_square", "kk_norm", "kk", "k_times_ka", "k_rest"))
        th_w, th_a, cum, e_in, e_ex = (s.sb(n, W) for n in ("tanh_w", "tanh_a", "cum_decay", "e_in", "e_ex"))
        p_in, p_ex, p_inv, kd, ba = (s.sb(n, W) for n in ("p_in", "p_ex", "p_inv", "k_d", "kk_a"))
        outs = s.sb("wkv_out", [P, 2, 4, RF, PB])
        ps_n = s.ps("ps_norm", [P, RF, PB])
        ps_w = s.ps("ps_w", [P, RF, PB])
        ps_a = s.ps("ps_a", [P, RF, PB])
        names = ("consts_in", "halves", "kk_raw_ready", "twd_ready", "sq_ready", "norm_summed", "sqrt_ready", "kk_ready",
                 "w_full", "a_full", "thw_ready", "tha_ready", "lw_used", "e_ready", "exp_ready", "pool_out", "dve_out",
                 "own", "pool_own", "kd_parts", "tha_used", "ends_ready", "norm_used")
        m = {n: s.sem("prep_" + n) for n in names}
        loaded = [s.sem(f"prep_loaded{b}") for b in range(2)]
        in_used = [s.sem(f"prep_in_used{b}") for b in range(2)]
        stored = s.sem("prep_stored")
        block = ctx.enter_context(nc.Block())
        NI = TOK // PB // 2

        def bc(name, k=0):
            return col(consts, name, k, RF).unsqueeze(2).to_broadcast(W)

        @block.sync
        def _(sp):
            sp.dma_start(up_w[:], dram["decay_up"][:, :]).then_inc(m["consts_in"], 16)
            sp.dma_start(up_a[:], dram["iclr_up"][:, :]).then_inc(m["consts_in"], 16)
            sp.dma_start(reset[:], dram["chunk_reset"][:, :]).then_inc(m["consts_in"], 16)
            sp.dma_start(head_ones[:], dram["head_ones"][:, :]).then_inc(m["consts_in"], 16)

            def load(t, b):
                sp.dma_start(pin[:, b], dram["p_t"][0:14, :, bass.ds(t * PB, PB)].rearrange("m p t -> p m t")).then_inc(loaded[b], 16)

            def store(t):
                for d in range(2):
                    sp.wait_ge(m["pool_out"], 2 * t + d + 1)
                    sp.wait_ge(m["dve_out"], 2 * t + d + 1)
                    for j in range(PB // P):
                        sp.dma_start(dram["wkv_in"][d, bass.ds(t * (PB // P) + j, 1)].rearrange("a p x t -> p (a x) t"),
                                     outs[:, d, :, :, P * j:P * j + P].rearrange("p q f t -> p (q f) t")).then_inc(stored, 16)

            for b in range(2):
                load(b, b)
            with sp.Fori(0, NI - 1) as i:
                for b in range(2):
                    store(2 * i + b)
                    sp.wait_ge(in_used[b], i + 1)
                    load(2 * i + (b + 2), b)
            for b in range(2):
                store(2 * NI - 2 + b)
            sp.wait_ge(stored, 64 * 2 * NI)

        @block.tensor
        def _(pe):
            pe.wait_ge(m["consts_in"], 64)
            with pe.Fori(0, NI) as i:
                for b in range(2):
                    t = 2 * i + b
                    pe.wait_ge(m["sq_ready"], t + 1)
                    pe.wait_ge(m["norm_used"], t)
                    for f in range(RF):
                        mm = nc.tensor.matmul(ps_n[:, f], head_ones[:], sq[:, f], start=True, stop=True)
                    mm.then_inc(m["norm_summed"], 1)
                    pe.wait_ge(m["twd_ready"], t + 1)
                    for d in range(2):
                        h = slice(64 * d, 64 * d + 64)
                        pe.wait_ge(m["thw_ready"], 2 * t + d)
                        for f in range(RF):
                            mm = nc.tensor.matmul(ps_w[:, f], up_w[h, P * f:P * f + P], t_wd[h], start=True, stop=True)
                        mm.then_inc(m["w_full"], 1)
                        pe.wait_ge(m["tha_ready"], 2 * t + d)
                        for f in range(RF):
                            mm = nc.tensor.matmul(ps_a[:, f], up_a[h, P * f:P * f + P], pin[h, b, AD], start=True, stop=True)
                        mm.then_inc(m["a_full"], 1)

        @block.scalar
        def _(act):
            act.wait_ge(m["halves"], 2)
            with act.Fori(0, NI) as i:
                for b in range(2):
                    t = 2 * i + b
                    act.wait_ge(m["kk_raw_ready"], t + 1)
                    act.wait_ge(m["norm_summed"], t)
                    nc.scalar.activation(sq[:], kk_raw[:], ACT.Square).then_inc(m["sq_ready"], 1)
                    act.wait_ge(m["norm_summed"], t + 1)
                    act.wait_ge(m["kk_ready"], t)
                    for h in range(2):
                        ins = nc.scalar.activation(norm[:, 2 * h:2 * h + 2], ps_n[:, 2 * h:2 * h + 2], ACT.Sqrt)
                    ins.then_inc(m["sqrt_ready"], 1)
                    act.wait_ge(loaded[b], 16 * i + 16)
                    act.wait_ge(m["w_full"], 2 * t)
                    nc.scalar.activation(t_wd[:], pin[:, b, WD], ACT.Tanh).then_inc(m["twd_ready"], 1)
                    for d in range(2):
                        act.wait_ge(m["w_full"], 2 * t + d + 1)
                        act.wait_ge(m["lw_used"], 2 * t + d)
                        for f in range(RF):
                            ins = nc.scalar.activation(th_w[:, f], ps_w[:, f], ACT.Tanh, bias=half_w0[:, RF * d + f:RF * d + f + 1], scale=0.5)
                        ins.then_inc(m["thw_ready"], 1)
                        act.wait_ge(m["a_full"], 2 * t + d + 1)
                        act.wait_ge(m["tha_used"], 2 * t + d)
                        for f in range(RF):
                            ins = nc.scalar.activation(th_a[:, f], ps_a[:, f], ACT.Tanh, bias=half_a0[:, RF * d + f:RF * d + f + 1], scale=0.5)
                        ins.then_inc(m["tha_ready"], 1)
                        act.wait_ge(m["e_ready"], 2 * t + d + 1)
                        act.wait_ge(m["pool_out"], 2 * t + d)
                        act.wait_ge(m["dve_out"], 2 * t + d)
                        act.wait_ge(m["ends_ready"], 2 * t + d)
                        nc.scalar.activation(p_in[:], e_in[:], ACT.Exp).then_inc(m["exp_ready"], 1)
                        nc.scalar.activation(p_ex[:], e_ex[:], ACT.Exp).then_inc(m["exp_ready"], 1)
                        nc.scalar.activation(p_inv[:], e_in[:], ACT.Exp, scale=-1.0).then_inc(m["exp_ready"], 1)

        @block.gpsimd
        def _(pool):
            with pool.Fori(0, NI) as i:
                step = Chain(pool, m["pool_own"], 0, i, 2)
                for b in range(2):
                    t = 2 * i + b
                    r, k = pin[:, b, RT:RT + 4], pin[:, b, KT_:KT_ + 4]
                    pool.wait_ge(loaded[b], 16 * i + 16)
                    pool.wait_ge(m["kk_ready"], t)
                    nc.gpsimd.tensor_tensor(kk_raw[:], k, bc("k_k"), ALU.mult).then_inc(m["kk_raw_ready"], 1)
                    pool.wait_ge(m["dve_out"], 2 * t)
                    step(nc.gpsimd.tensor_tensor(kka[:], k, bc("k_a"), ALU.mult))
                    nc.gpsimd.tensor_tensor(k1[:], k, kka[:], ALU.subtract).then_inc(m["kd_parts"], 1)
                    pool.wait_ge(m["kk_ready"], t + 1)
                    for d in range(2):
                        pool.wait_ge(m["exp_ready"], 6 * t + 3 * d + 3)
                        pool.wait_ge(stored, 64 * t)
                        nc.gpsimd.tensor_tensor(outs[:, d, 1], r, p_in[:], ALU.mult)
                        nc.gpsimd.tensor_tensor(outs[:, d, 0], kk[:], p_ex[:], ALU.mult).then_inc(m["pool_out"], 1)
                step.end()

        @block.vector
        def _(dve):
            dve.wait_ge(m["consts_in"], 64)
            nc.vector.tensor_scalar(half_w0[:], col(consts, "w0"), 0.5, None, ALU.mult).then_inc(m["halves"], 1)
            nc.vector.tensor_scalar(half_a0[:], col(consts, "a0"), 0.5, None, ALU.mult).then_inc(m["halves"], 1)
            with dve.Fori(0, NI) as i:
                step = Chain(dve, m["own"], 0, i, 2 * 16)
                for b in range(2):
                    t = 2 * i + b
                    dve.wait_ge(m["sqrt_ready"], t + 1)
                    dve.sem_inc(m["norm_used"], 1)
                    step(nc.vector.tensor_scalar(norm[:], norm[:], 1e-12, None, ALU.max))
                    step(nc.vector.reciprocal(norm[:], norm[:]))
                    dve.wait_ge(m["pool_out"], 2 * t)
                    step(nc.vector.tensor_tensor(kk[:], kk_raw[:], norm[:], ALU.mult))
                    dve.sem_inc(m["kk_ready"], 1)
                    dve.wait_ge(m["kd_parts"], t + 1)
                    for d in range(2):
                        dve.wait_ge(m["thw_ready"], 2 * t + d + 1)
                        step(nc.vector.tensor_scalar(th_w[:], th_w[:], -0.5 * DECAY, -0.5 * DECAY, ALU.mult, ALU.add))
                        flat = lambda x: x[:].rearrange("p f t -> p (f t)")
                        chunks = lambda x: x[:].rearrange("p f (c t) -> p (f c) t", t=CH)
                        dve.wait_ge(m["exp_ready"], 6 * t + 3 * d)
                        if d == 0:
                            step(nc.vector.tensor_tensor_scan(flat(e_in), reset[:], flat(th_w), 0.0, ALU.mult, ALU.add))
                            step(nc.vector.tensor_tensor(e_ex[:], e_in[:], th_w[:], ALU.subtract))
                        else:
                            step(nc.vector.tensor_tensor_scan(flat(cum), reset[:], flat(th_w), 0.0, ALU.mult, ALU.add))
                            total = chunks(cum)[:, :, CH - 1:CH].to_broadcast([P, RF * PB // CH, CH])
                            step(nc.vector.tensor_tensor(chunks(e_ex), total, chunks(cum), ALU.subtract))
                            step(nc.vector.tensor_tensor(e_in[:], e_ex[:], th_w[:], ALU.add))
                        dve.sem_inc(m["e_ready"], 1)
                        dve.sem_inc(m["lw_used"], 1)
                        dve.wait_ge(m["tha_ready"], 2 * t + d + 1)
                        dve.wait_ge(m["kk_ready"], t + 1)
                        step(nc.vector.tensor_scalar(th_a[:], th_a[:], 0.5, 0.5, ALU.mult, ALU.add))
                        nc.vector.tensor_tensor(ba[:], kk[:], th_a[:], ALU.mult)
                        step(nc.vector.tensor_tensor(kd[:], kka[:], th_a[:], ALU.mult))
                        dve.sem_inc(m["tha_used"], 1)
                        step(nc.vector.tensor_tensor(kd[:], kd[:], k1[:], ALU.add))
                        dve.wait_ge(m["exp_ready"], 6 * t + 3 * d + 3)
                        dve.wait_ge(stored, 64 * t)
                        end = (CH - 1) if d == 0 else 0
                        nc.vector.tensor_copy(consts["p_end"][:, d, :, bass.ds(t * (PB // CH), PB // CH)],
                                              p_in[:].rearrange("p f (c t) -> p f c t", t=CH)[:, :, :, end]).then_inc(m["ends_ready"], 1)
                        nc.vector.tensor_tensor(outs[:, d, 2], ba[:], p_inv[:], ALU.mult)
                        nc.vector.tensor_tensor(outs[:, d, 3], kd[:], p_inv[:], ALU.mult).then_inc(m["dve_out"], 1)
                    dve.wait_ge(m["pool_out"], 2 * t + 2)
                    dve.sem_inc(in_used[b], 1)
                step.end()


HEADS = 8
LEVELS = 6


def wkv_scan(nc, dram, consts):
    with ExitStack() as ctx:
        s = Scope(nc, ctx)
        H = HEADS
        mask = s.sb("tri_mask", [P, 2, 2, P])
        lmask = s.sb("level_mask", [P, LEVELS, P])
        ident2 = s.sb("ident_halves", [P, CH])
        pair = lambda name, shape: s.sb("sb_" + name, [P, 2] + shape)
        ops = pair("wkv_ops", [4, RF, P])
        v = pair("wkv_v", [RF, P])
        hats = pair("wkv_hats", [2, RF, P])
        rho = pair("wkv_rho", [RF, P])
        lb = pair("wkv_lb", [H, 2, P])
        mk = pair("wkv_mk", [H, 2, P])
        lev = pair("wkv_levels", [LEVELS, H, P])
        x, xt, z = (pair("wkv_" + n, [H, P]) for n in ("x", "xt", "z"))
        v_tok = pair("wkv_v_tok", [RF, P])
        hat_tok = pair("wkv_hat_tok", [2, RF, P])
        am = pair("wkv_am", [H, 2, CH])
        wg = pair("wkv_wg", [H, 2, CH])
        diag = pair("wkv_diag", [2, RF, CH])
        phi = pair("wkv_phi", [2, RF, CH])
        psi = pair("wkv_psi", [2, RF, CH])
        r = pair("wkv_r", [RF, P])
        y0 = pair("wkv_y0", [RF, P])
        y = pair("wkv_y", [RF, P])
        state = pair("wkv_state", [RF, CH])
        ps = [s.ps(f"ps_wkv{d}", [P, 4, 512]) for d in range(2)]
        names = ("in_loaded", "hat_ready", "ops_used", "turned", "tok_copied", "beta_full", "beta_masked", "kappa_full", "kappa_masked",
                 "lev_ready", "xt1_ready", "x1_turned", "x1_ready", "z_full", "z_ready", "xz_full", "x_ready", "xt_full",
                 "xt_ready", "last_full", "inv_ready", "mv_full", "mv_ready", "wg_full", "wg_ready", "trans_full", "diag_ready",
                 "phi_ready", "psi_ready", "bw_full", "r_ready", "y0_full", "y0_ready", "ys_full", "s_full", "s_ready", "y_ready",
                 "y_stored", "s_half")
        m = {n: [s.sem(f"wkv_{n}{d}") for d in range(2)] for n in names}
        consts_in = s.sem("wkv_consts_in")
        unread = s.sem("wkv_unread_pool")
        unread_pe = s.sem("wkv_unread_pe")
        zeroed = s.sem("wkv_zeroed")
        block = ctx.enter_context(nc.Block())
        tiles = (SEQS[0] // P, SEQS[1] // P)
        runs = ((0, tiles[0]), (tiles[0], tiles[0] + tiles[1]))

        def where(i, d, run):
            return i if d == 0 else i * -1 + (run[0] + run[1] - 1)

        def hh(g, f):
            return g * RF + f

        def half(g):
            return slice(64 * g, 64 * g + 64)

        @block.sync
        def _(sp):
            sp.dma_start(mask[:], dram["tri_mask"][:, :, :, :]).then_inc(consts_in, 16)
            sp.dma_start(lmask[:], dram["level_mask"][:, :, :]).then_inc(consts_in, 16)
            sp.dma_start(ident2[:], dram["ident_halves"][:, :]).then_inc(consts_in, 16)
            for run in runs:
                with sp.Fori(*run) as i:
                    for d in range(2):
                        n = where(i, d, run)
                        sp.wait_ge(m["ops_used"][d], i)
                        sp.wait_ge(m["kappa_full"][d], i)
                        sp.dma_start(ops[:, d].rearrange("p q f t -> p (q f) t"),
                                     dram["wkv_in"][d, bass.ds(n, 1)].rearrange("a p x t -> p (a x) t")).then_inc(m["in_loaded"][d], 16)
                        sp.dma_start(v[:, d], dram["p_t"][VT:VT + 4, :, bass.ds(n * P, P)].rearrange("f p t -> p f t")).then_inc(m["in_loaded"][d], 16)

        @block.gpsimd
        def _(pool):
            pool.wait_ge(consts_in, 48)
            for run in runs:
                with pool.Fori(*run) as i:
                    for d in range(2):
                        n = where(i, d, run)
                        end = consts["p_end"][:, d, :, bass.ds(n * 2, 2)]
                        pool.wait_ge(m["in_loaded"][d], 32 * i + 32)
                        pool.wait_ge(m["turned"][d], 4 * i)
                        for q in range(2):
                            for c in range(2):
                                ins = nc.gpsimd.tensor_tensor(hats[:, d, q, :, CH * c:CH * c + CH], ops[:, d, 2 + q, :, CH * c:CH * c + CH],
                                                              end[:, :, c:c + 1].to_broadcast([P, RF, CH]), ALU.mult)
                        ins.then_inc(m["hat_ready"][d], 1)
                        pool.wait_ge(m["r_ready"][d], i)
                        alone(pool, unread)
                        nc.gpsimd.tensor_copy(rho[:, d], ops[:, d, 1]).then_inc(m["ops_used"][d], 1)
                        pool.wait_ge(m["phi_ready"][d], i)
                        alone(pool, unread)
                        for c in range(2):
                            ins = nc.gpsimd.tensor_tensor(diag[:, d, c], ident2[:].unsqueeze(1).to_broadcast([P, RF, CH]),
                                                          end[:, :, c:c + 1].to_broadcast([P, RF, CH]), ALU.mult)
                        ins.then_inc(m["diag_ready"][d], 1)
                    for l in range(LEVELS):
                        for d in range(2):
                            if l == 0:
                                pool.wait_ge(m["beta_masked"][d], i + 1)
                                pool.wait_ge(m["z_full"][d], 5 * i)
                            nc.gpsimd.tensor_tensor(lev[:, d, l], lb[:, d, :, 0], lmask[:, l].unsqueeze(1).to_broadcast([P, H, P]),
                                                    ALU.mult).then_inc(m["lev_ready"][d], 1)

        @block.tensor
        def _(pe):
            ident = consts["ident"][:]
            for run in runs:
                pe.wait_ge(zeroed, 1 + (run[0] > 0))
                with pe.Fori(*run) as i:
                    for d in range(2):
                        pe.wait_ge(m["in_loaded"][d], 32 * i + 32)
                        pe.wait_ge(m["hat_ready"][d], i + 1)
                        pe.wait_ge(m["y_ready"][d], i)
                        pe.wait_ge(m["s_ready"][d], 4 * i)
                        for q, src in enumerate((ops[:, d, 0], v[:, d], hats[:, d, 0], hats[:, d, 1])):
                            for f in range(RF):
                                mm = nc.tensor.transpose(ps[d][:, q, P * f:P * f + P], src[:, f], ident)
                            mm.then_inc(m["turned"][d], 1)
                    for q, (full, free, count) in enumerate((("beta_full", "tok_copied", 4), ("kappa_full", "beta_masked", 1))):
                        for d in range(2):
                            pe.wait_ge(m[free][d], count * i + count)
                            for f in range(RF):
                                for g in range(2):
                                    out = ps[d][:, 2 * g + f // 2, 256 * (f % 2):256 * (f % 2) + 256].rearrange("p (a t) -> p a t", a=2)
                                    mm = nc.tensor.matmul(out, ops[half(g), d, 2 + q, f], ops[half(g), d, 0:2, f], start=True, stop=True)
                            mm.then_inc(m[full][d], 1)
                    for d in range(2):
                        pe.wait_ge(m["kappa_masked"][d], i + 1)
                        for g in range(2):
                            for f in range(RF):
                                mm = nc.tensor.matmul(ps[d][:, 2, CH * hh(g, f):CH * hh(g, f) + CH], mk[:, d, hh(g, f), 0],
                                                      v_tok[:, d, f, half(g)], start=True, stop=True)
                        mm.then_inc(m["mv_full"][d], 1)
                    def over_heads(out, lhs, rhs):
                        for h in range(H):
                            mm = nc.tensor.matmul(out[:, h // 4, P * (h % 4):P * (h % 4) + P], lhs[:, h], rhs[:, h], start=True, stop=True)
                        return mm

                    for d in range(2):
                        pe.wait_ge(m["xt1_ready"][d], i + 1)
                        for h in range(H):
                            mm = nc.tensor.transpose(ps[d][:, h // 4, P * (h % 4):P * (h % 4) + P], xt[:, d, h], ident)
                        mm.then_inc(m["x1_turned"][d], 1)
                    for l in range(1, LEVELS):
                        last = l == LEVELS - 1
                        for d in range(2):
                            pe.wait_ge(m["lev_ready"][d], LEVELS * i + l + 1)
                            if l == 1:
                                pe.wait_ge(m["x1_ready"][d], i + 1)
                            else:
                                pe.wait_ge(m["xt_ready"][d], 4 * i + l - 1)
                            over_heads(ps[d], lev[:, d, l], x[:, d]).then_inc(m["z_full"][d], 1)
                        for d in range(2):
                            pe.wait_ge(m["z_ready"][d], 5 * i + l)
                            if l == 1:
                                pe.wait_ge(m["mv_ready"][d], i + 1)
                            if not last:
                                over_heads(ps[d][:, 2:4], xt[:, d], z[:, d]).then_inc(m["xz_full"][d], 1)
                            else:
                                over_heads(ps[d][:, 2:4], z[:, d], xt[:, d]).then_inc(m["last_full"][d], 1)
                        if not last:
                            for d in range(2):
                                pe.wait_ge(m["x_ready"][d], 4 * i + l)
                                for h in range(H):
                                    mm = nc.tensor.transpose(ps[d][:, h // 4, P * (h % 4):P * (h % 4) + P], x[:, d, h], ident)
                                mm.then_inc(m["xt_full"][d], 1)
                    for d in range(2):
                        pe.wait_ge(m["inv_ready"][d], i + 1)
                        over_heads(ps[d], xt[:, d], am[:, d].rearrange("p h a k -> p h (a k)")).then_inc(m["wg_full"][d], 1)
                    for d in range(2):
                        pe.wait_ge(m["wg_ready"][d], i + 1)
                        alone(pe, unread_pe)
                        for g in range(2):
                            for f in range(RF):
                                for c in range(2):
                                    t = half(c)
                                    at = lambda a: ps[d][half(g), 2 + c, P * f + CH * a:P * f + CH * a + CH]
                                    nc.tensor.matmul(at(0), wg[t, d, hh(g, f), 0], hat_tok[t, d, 0, f, half(g)], start=True, stop=True)
                                for c in range(2):
                                    t = half(c)
                                    at = lambda a: ps[d][half(g), 2 + c, P * f + CH * a:P * f + CH * a + CH]
                                    nc.tensor.matmul(at(1), hat_tok[t, d, 0, f, half(g)], wg[t, d, hh(g, f), 1], start=True, stop=False)
                                    mm = nc.tensor.matmul(at(1), hat_tok[t, d, 1, f, half(g)], v_tok[t, d, f, half(g)], start=False, stop=True)
                        mm.then_inc(m["trans_full"][d], 1)
                    for d in range(2):
                        for f in range(RF):
                            for g in range(2):
                                mm = nc.tensor.matmul(ps[d][half(g), 0, P * f:P * f + P], wg[:, d, hh(g, f), 0], lb[:, d, hh(g, f), 1],
                                                      start=True, stop=True)
                        mm.then_inc(m["bw_full"][d], 1)
                        for f in range(RF):
                            for g in range(2):
                                out = ps[d][half(g), 1, P * f:P * f + P]
                                nc.tensor.matmul(out, wg[:, d, hh(g, f), 1], lb[:, d, hh(g, f), 1], start=True, stop=False)
                                mm = nc.tensor.matmul(out, v_tok[:, d, f, half(g)], mk[:, d, hh(g, f), 1], start=False, stop=True)
                        mm.then_inc(m["y0_full"][d], 1)
                    for k in range(2):
                        for d in range(2):
                            c = k if d == 0 else 1 - k
                            if k == 0:
                                pe.wait_ge(m["r_ready"][d], i + 1)
                                pe.wait_ge(m["y0_ready"][d], i + 1)
                                pe.wait_ge(m["phi_ready"][d], i + 1)
                                pe.wait_ge(m["psi_ready"][d], i + 1)
                            else:
                                pe.wait_ge(m["s_ready"][d], 4 * i + 2)
                            alone(pe, unread_pe)
                            for f in range(RF):
                                for g in range(2):
                                    nc.tensor.matmul(ps[d][half(g), g, P * f + CH * c:P * f + CH * c + CH], state[half(g), d, f],
                                                     r[half(g), d, f, CH * c:CH * c + CH], start=True, stop=True)
                            for f in range(RF):
                                for g in range(2):
                                    mm = nc.tensor.matmul(ps[d][half(g), 2 + g, CH * f:CH * f + CH], phi[half(g), d, c, f], state[half(g), d, f],
                                                          start=True, stop=True)
                            mm.then_inc(m["s_full"][d], 1)

        @block.scalar
        def _(act):
            for run in runs:
                with act.Fori(*run) as i:
                    for d in range(2):
                        by_pair = lambda x: x.rearrange("p (f g k) -> p g f k", g=2, k=CH)
                        dsts = (am[:, d, :, 0].rearrange("p (g f) k -> p g f k", g=2), by_pair(v_tok[:, d].rearrange("p f t -> p (f t)")),
                                by_pair(hat_tok[:, d, 0].rearrange("p f t -> p (f t)")), by_pair(hat_tok[:, d, 1].rearrange("p f t -> p (f t)")))
                        for q, dst in enumerate(dsts):
                            act.wait_ge(m["turned"][d], 4 * i + q + 1)
                            for g in range(2):
                                ins = nc.scalar.copy(dst[:, g], by_pair(ps[d][:, q])[:, g])
                            ins.then_inc(m["tok_copied"][d], 1)
                    for d in range(2):
                        act.wait_ge(m["mv_full"][d], i + 1)
                        nc.scalar.copy(am[:, d, :, 1], ps[d][:, 2].rearrange("p (h k) -> p h k", h=H)).then_inc(m["mv_ready"][d], 1)
                    bank2 = lambda x: x.rearrange("p (b h) t -> p b (h t)", b=2)
                    for d in range(2):
                        act.wait_ge(m["x1_turned"][d], i + 1)
                        nc.scalar.copy(bank2(x[:, d]), ps[d][:, 0:2]).then_inc(m["x1_ready"][d], 1)
                    for l in range(1, LEVELS):
                        for d in range(2):
                            act.wait_ge(m["z_full"][d], 5 * i + l)
                            nc.scalar.copy(bank2(z[:, d]), ps[d][:, 0:2]).then_inc(m["z_ready"][d], 1)
                        if l < LEVELS - 1:
                            for d in range(2):
                                act.wait_ge(m["xt_full"][d], 4 * i + l)
                                nc.scalar.copy(bank2(xt[:, d]), ps[d][:, 0:2]).then_inc(m["xt_ready"][d], 1)
                    for d in range(2):
                        act.wait_ge(m["wg_full"][d], i + 1)
                        nc.scalar.mul(wg[:, d].rearrange("p (b h) a k -> p b (h a k)", b=2), ps[d][:, 0:2], -1.0).then_inc(m["wg_ready"][d], 1)
                    for d in range(2):
                        act.wait_ge(m["phi_ready"][d], i + 1)
                        nc.scalar.copy(psi[:, d], ps[d][:, 2:4].rearrange("p c (f a k) -> p c f a k", f=RF, a=2)[:, :, :, 1]).then_inc(m["psi_ready"][d], 1)
                        act.wait_ge(m["y0_full"][d], i + 1)
                        nc.scalar.copy(y0[:, d].rearrange("p f t -> p (f t)"), ps[d][:, 1]).then_inc(m["y0_ready"][d], 1)
                    for d in range(2):
                        act.wait_ge(m["y_ready"][d], i + 1)
                        n = where(i, d, run)
                        act.dma_start(dram["wkv_y"][d, bass.ds(n, 1)].rearrange("a p f t -> p (a f t)"), y[:, d].rearrange("p f t -> p (f t)")).then_inc(m["y_stored"][d], 16)
            for d in range(2):
                act.wait_ge(m["y_stored"][d], 16 * runs[1][1])

        @block.vector
        def _(dve):
            dve.wait_ge(consts_in, 48)
            for run in runs:
                if run[0]:
                    for d in range(2):
                        dve.wait_ge(m["s_full"][d], 2 * run[0])
                        dve.wait_ge(m["s_ready"][d], 4 * run[0])
                nc.vector.memset(state[:], 0.0).then_inc(zeroed, 1)
                dve.wait_ge(zeroed, 1 + (run[0] > 0))
                with dve.Fori(*run) as i:
                    for q, (dst, full, done) in enumerate(((lb, "beta_full", "beta_masked"), (mk, "kappa_full", "kappa_masked"))):
                        for d in range(2):
                            dve.wait_ge(m[full][d], i + 1)
                            if q == 0:
                                dve.wait_ge(m["lev_ready"][d], LEVELS * i)
                            nc.vector.tensor_tensor(dst[:, d].rearrange("p h a t -> p h (a t)"), ps[d][:].rearrange("p b (h x) -> p (b h) x", h=2),
                                                    mask[:, d].rearrange("p a t -> p (a t)").unsqueeze(1).to_broadcast([P, H, 2 * P]),
                                                    ALU.mult).then_inc(m[done][d], 1)
                    for d in range(2):
                        dve.wait_ge(m["lev_ready"][d], LEVELS * i + 1)
                        dve.wait_ge(m["wg_full"][d], i)
                        nc.vector.tensor_tensor(xt[:, d], consts["ident"][:].unsqueeze(1).to_broadcast([P, H, P]), lev[:, d, 0],
                                                ALU.subtract).then_inc(m["xt1_ready"][d], 1)
                    bank2 = lambda x: x.rearrange("p (b h) t -> p b (h t)", b=2)
                    for l in range(1, LEVELS - 1):
                        for d in range(2):
                            dve.wait_ge(m["xz_full"][d], 4 * i + l)
                            nc.vector.tensor_tensor(bank2(x[:, d]), bank2(x[:, d]), ps[d][:, 2:4], ALU.subtract).then_inc(m["x_ready"][d], 1)
                    for d in range(2):
                        dve.wait_ge(m["last_full"][d], i + 1)
                        nc.vector.tensor_tensor(bank2(xt[:, d]), bank2(xt[:, d]), ps[d][:, 2:4], ALU.subtract).then_inc(m["inv_ready"][d], 1)
                    for d in range(2):
                        dve.wait_ge(m["trans_full"][d], i + 1)
                        dve.wait_ge(m["diag_ready"][d], i + 1)
                        nc.vector.tensor_tensor(phi[:, d], ps[d][:, 2:4].rearrange("p c (f a k) -> p c f a k", f=RF, a=2)[:, :, :, 0], diag[:, d],
                                                ALU.add).then_inc(m["phi_ready"][d], 1)
                        dve.wait_ge(m["bw_full"][d], i + 1)
                        nc.vector.tensor_tensor(r[:, d].rearrange("p f t -> p (f t)"), ps[d][:, 0], rho[:, d].rearrange("p f t -> p (f t)"),
                                                ALU.add).then_inc(m["r_ready"][d], 1)
                    for k in range(2):
                        for d in range(2):
                            c = k if d == 0 else 1 - k
                            dve.wait_ge(m["s_full"][d], 2 * i + k + 1)
                            dve.wait_ge(m["psi_ready"][d], i + 1)
                            if k == 1:
                                dve.wait_ge(m["s_ready"][d], 4 * i + 2)
                            for g in range(2):
                                nc.vector.tensor_tensor(state[half(g), d], ps[d][half(g), 2 + g, 0:RF * CH].rearrange("p (f k) -> p f k", f=RF),
                                                        psi[half(g), d, c], ALU.add).then_inc(m["s_ready"][d], 1)
                    for d in range(2):
                        dve.wait_ge(m["y_stored"][d], 16 * i)
                        dve.wait_ge(m["y0_ready"][d], i + 1)
                        for g in range(2):
                            ins = nc.vector.tensor_tensor(y[half(g), d].rearrange("p f t -> p (f t)"), ps[d][half(g), g],
                                                          y0[half(g), d].rearrange("p f t -> p (f t)"), ALU.add)
                        ins.then_inc(m["y_ready"][d], 1)


GN_EPS = 64e-5


def rwkv_finish(nc, dram, consts, oa_t):
    with ExitStack() as ctx:
        s = Scope(nc, ctx)
        W = [P, RF, PB]
        J = PB // P
        up = s.sb("gate_up", [P, RF * P])
        head_ones = s.sb("head_ones2", [P, P])
        yin = s.sb("fin_y", [P, 2, J, RF, P])
        rkv = s.sb("fin_rkv", [P, 12, PB])
        gd = s.sb("fin_gd", [P, PB])
        y, yc, sq, var, lnv, rstd, rk, rkk, bonus = (s.sb("fin_" + n, W) for n in ("sum", "centred", "square", "var", "ln_var", "rstd", "rk", "rkk", "bonus"))
        yn = s.sb("fin_yn", W)
        ya = s.sb("fin_affine", W)
        sg = s.sb("fin_sg", [P, PB])
        ps_m, ps_v, ps_b, ps_g = (s.ps("ps_fin" + n, W) for n in "mvbg")
        m = {n: s.sem("fin_" + n + "_s") for n in (
            "consts", "loaded", "summed", "mean_full", "centred", "squared", "var_full", "var_ready", "rstd_ready", "normed", "affine", "ln_own",
            "rk_own", "rkk_ready", "bonus_full", "tanh", "sig_ready", "gate_full", "own", "done", "bonus_ready")}
        block = ctx.enter_context(nc.Block())
        N = TOK // PB

        @block.sync
        def _(sp):
            sp.dma_start(up[:], dram["gate_up"][:, :]).then_inc(m["consts"], 16)
            sp.dma_start(head_ones[:], dram["head_ones"][:, :]).then_inc(m["consts"], 16)
            with sp.Fori(0, N) as i:
                sp.wait_ge(m["summed"], i)
                sp.wait_ge(m["tanh"], i)
                sp.wait_ge(m["rkk_ready"], i)
                sp.wait_ge(m["bonus_ready"], i)
                for d in range(2):
                    sp.dma_start(yin[:, d].rearrange("p j f t -> p j (f t)"),
                                 dram["wkv_y"][d, bass.ds(i * J, J)].rearrange("j p f t -> p j (f t)")).then_inc(m["loaded"], 16)
                sp.dma_start(rkv[:], dram["p_t"][0:12, :, bass.ds(i * PB, PB)].rearrange("f p t -> p f t")).then_inc(m["loaded"], 16)
                sp.dma_start(gd[:], dram["p_t"][GD, :, bass.ds(i * PB, PB)]).then_inc(m["loaded"], 16)

        @block.gpsimd
        def _(pool):
            with pool.Fori(0, N) as i:
                pool.wait_ge(m["loaded"], 64 * i + 64)
                pool.wait_ge(m["centred"], i)
                order = "p j f t -> p f j t"
                nc.gpsimd.tensor_tensor(y[:].rearrange("p f (j t) -> p f j t", j=J), yin[:, 0].rearrange(order), yin[:, 1].rearrange(order),
                                        ALU.add).then_inc(m["summed"], 1)
                nc.gpsimd.tensor_tensor(rk[:], rkv[:, 0:4], rkv[:, 4:8], ALU.mult).then_inc(m["rk_own"], 1)
                pool.wait_ge(m["rk_own"], i + 1)
                pool.wait_ge(m["bonus_full"], i)
                nc.gpsimd.tensor_tensor(rkk[:], rk[:], col(consts, "r_k").unsqueeze(2).to_broadcast(W), ALU.mult).then_inc(m["rkk_ready"], 1)

        @block.tensor
        def _(pe):
            pe.wait_ge(m["consts"], 32)
            with pe.Fori(0, N) as i:
                def sums(out, src):
                    for f in range(RF):
                        mm = nc.tensor.matmul(out[:, f], head_ones[:], src[:, f], start=True, stop=True)
                    return mm
                pe.wait_ge(m["summed"], i + 1)
                pe.wait_ge(m["centred"], i)
                sums(ps_m, y).then_inc(m["mean_full"], 1)
                pe.wait_ge(m["rkk_ready"], i + 1)
                pe.wait_ge(m["bonus_ready"], i)
                sums(ps_b, rkk).then_inc(m["bonus_full"], 1)
                pe.wait_ge(m["sig_ready"], i + 1)
                pe.wait_ge(m["done"], i)
                for f in range(RF):
                    mm = nc.tensor.matmul(ps_g[:, f], up[:, P * f:P * f + P], sg[:], start=True, stop=True)
                mm.then_inc(m["gate_full"], 1)
                pe.wait_ge(m["squared"], i + 1)
                pe.wait_ge(m["var_ready"], i)
                sums(ps_v, sq).then_inc(m["var_full"], 1)

        @block.scalar
        def _(act):
            with act.Fori(0, N) as i:
                act.wait_ge(m["loaded"], 64 * i + 64)
                act.wait_ge(m["gate_full"], i)
                nc.scalar.activation(sg[:], gd[:], ACT.Tanh, scale=0.5).then_inc(m["tanh"], 1)
                act.wait_ge(m["centred"], i + 1)
                act.wait_ge(m["var_full"], i)
                nc.scalar.activation(sq[:], yc[:], ACT.Square).then_inc(m["squared"], 1)
                act.wait_ge(m["var_ready"], i + 1)
                nc.scalar.activation(lnv[:], var[:], ACT.Ln).then_inc(m["ln_own"], 1)
                act.wait_ge(m["ln_own"], i + 1)
                nc.scalar.activation(rstd[:], lnv[:], ACT.Exp, scale=-0.5).then_inc(m["rstd_ready"], 1)
                act.wait_ge(m["normed"], i + 1)
                act.wait_ge(m["done"], i)
                for f in range(RF):
                    ins = nc.scalar.activation(ya[:, f], yn[:, f], ACT.Identity, bias=col(consts, "gn_b", f, 1), scale=col(consts, "gn_w", f, 1))
                ins.then_inc(m["affine"], 1)

        @block.vector
        def _(dve):
            with dve.Fori(0, N) as i:
                step = Chain(dve, m["own"], 0, i, 1)
                dve.wait_ge(m["tanh"], i + 1)
                nc.vector.tensor_scalar(sg[:], sg[:], 0.5, 0.5, ALU.mult, ALU.add).then_inc(m["sig_ready"], 1)
                for h in range(2):
                    q = slice(2 * h, 2 * h + 2)
                    if h == 0:
                        dve.wait_ge(m["mean_full"], i + 1)
                        dve.wait_ge(m["squared"], i)
                    ins = nc.vector.scalar_tensor_tensor(out=yc[:, q], in0=ps_m[:, q], scalar=-1.0 / CH, in1=y[:, q], op0=ALU.mult, op1=ALU.add)
                ins.then_inc(m["centred"], 1)
                dve.wait_ge(m["bonus_full"], i + 1)
                nc.vector.tensor_tensor(bonus[:], ps_b[:], rkv[:, 8:12], ALU.mult).then_inc(m["bonus_ready"], 1)
                dve.wait_ge(m["var_full"], i + 1)
                nc.vector.tensor_scalar(var[:], ps_v[:], 1.0 / CH, GN_EPS, ALU.mult, ALU.add).then_inc(m["var_ready"], 1)
                dve.wait_ge(m["rstd_ready"], i + 1)
                nc.vector.tensor_tensor(yn[:], yc[:], rstd[:], ALU.mult).then_inc(m["normed"], 1)
                dve.wait_ge(m["affine"], i + 1)
                dve.wait_ge(m["bonus_ready"], i + 1)
                step(nc.vector.tensor_tensor(ya[:], ya[:], bonus[:], ALU.add))
                dve.wait_ge(m["gate_full"], i + 1)
                nc.vector.tensor_tensor(oa_t[:, :, bass.ds(i * PB, PB)], ya[:], ps_g[:], ALU.mult).then_inc(m["done"], 1)
                step.end()


NOPE, ROPE = 64, 32
HD = NOPE + ROPE
QF, KVF = 6, 2
KPE_TILE, Q_TILE, KV_TILE = 15, 16, 22
SCALE = float(HD) ** -0.5


def mla_project(nc, dram, consts):
    with ExitStack() as ctx:
        s = Scope(nc, ctx)
        w_uq = s.sb("w_uq", [P, QF, HEADS, HD])
        w_uk = s.sb("w_uk", [P, KVF, HEADS, HD])
        w_uv = s.sb("w_uv", [P, KVF, 512])
        part_ones = s.sb("part_means", [HD, HD])
        rotate = s.sb("rotate", [HD, HD])
        rope = s.sb("rope", [HD, 2, NB])
        q_gain = s.sb("scaled_q_gain", [P, 1])
        lat = s.sb("latent", [P, QF + KVF, NB])
        kpe = s.sb("k_pe", [P, NB])
        kpe_now = s.sb("k_pe_now", [P, NB])
        lat_sq = s.sb("latent_square", [P, QF + KVF, NB])
        lat_n = s.sb("latent_normed", [P, QF + KVF, NB])
        var = s.sb("latent_var", [P, 2, NB])
        ln_l = s.sb("latent_ln", [P, 2, NB])
        rms = s.sb("latent_rstd", [P, 2, NB])
        raw, sq, ssb, ln_h, rstd, normed, t_cos, t_sin, outq = (s.sb("head_" + n, [HD, 2, NB]) for n in
                                                         ("raw", "square", "mean", "ln", "rstd", "normed", "cos", "sin", "out"))
        v_out = s.sb("v_out", [P, 2, 512])
        ps_raw = [s.ps(f"ps_raw{b}", [HD, NB]) for b in range(2)]
        ps_sum = [s.ps(f"ps_sum{b}", [HD, NB]) for b in range(2)]
        ps_rot = [s.ps(f"ps_rot{b}", [HD, NB]) for b in range(2)]
        ps_l = [s.ps(f"ps_lat{b}", [P, NB]) for b in range(2)]
        m = {n: s.sem("mla_" + n) for n in (
            "consts", "own", "loaded", "lat_squared", "lat_full", "lat_var", "lat_rstd", "lat_normed", "kpe_kept", "v_full", "v_copied",
            "ln_own", "raw_full", "raw_copied", "sum_full", "mean_ready", "rstd_ready", "normed", "rot_full", "cos_ready", "sin_ready",
            "out_ready")}
        v_stored = [s.sem(f"mla_v_stored{b}") for b in range(2)]
        stored = [s.sem(f"mla_stored{b}") for b in range(2)]
        unread = s.sem("mla_unread")
        block = ctx.enter_context(nc.Block())
        U = 2 * HEADS

        @block.sync
        def _(sp):
            for dst, name in ((w_uq, "w_uq"), (w_uk, "w_uk"), (w_uv, "w_uv"), (part_ones, "part_means"), (rotate, "rotate")):
                sp.dma_start(dst[:], dram[name][tuple([slice(None)] * len(dst.shape))]).then_inc(m["consts"], 16)
            with sp.Fori(0, NT) as i:
                sp.wait_ge(m["lat_normed"], (QF + KVF) * i)
                sp.wait_ge(m["kpe_kept"], i)
                sp.wait_ge(m["lat_squared"], i)
                sp.dma_start(lat[:], dram["p_t"][Q_TILE:Q_TILE + QF + KVF, :, bass.ds(i * NB, NB)].rearrange("f p t -> p f t")).then_inc(m["loaded"], 16)
                sp.dma_start(kpe[:], dram["p_t"][KPE_TILE, :, bass.ds(i * NB, NB)]).then_inc(m["loaded"], 16)
                sp.wait_ge(m["out_ready"], U * i)
                alone(sp, unread)
                sp.dma_start(rope[:], dram["rope"][:, :, bass.ds(i * NB, NB)]).then_inc(m["loaded"], 16)
                for t in range(4):
                    sp.wait_ge(m["v_copied"], 4 * i + t + 1)
                    sp.dma_start(dram["v_mla"][bass.ds(4 * i + t, 1)].rearrange("a p v -> p (a v)"), v_out[:, t % 2]).then_inc(v_stored[t % 2], 16)
                for u in range(U):
                    sp.wait_ge(m["out_ready"], U * i + u + 1)
                    sp.dma_start(dram["qk_t"][u, :, bass.ds(i * NB, NB)], outq[:, u % 2]).then_inc(stored[u % 2], 16)
            for b in range(2):
                sp.wait_ge(stored[b], 16 * U // 2 * NT)
                sp.wait_ge(v_stored[b], 16 * 2 * NT)

        @block.tensor
        def _(pe):
            pe.wait_ge(m["consts"], 80)
            with pe.Fori(0, NT) as i:
                pe.wait_ge(m["lat_squared"], i + 1)
                pe.wait_ge(m["v_copied"], 4 * i)
                for b, (first, n) in enumerate(((0, QF), (QF, KVF))):
                    for k in range(n):
                        mm = nc.tensor.matmul(ps_l[b][:], consts["ones"][:], lat_sq[:, first + k], start=(k == 0), stop=(k == n - 1))
                mm.then_inc(m["lat_full"], 1)
                pe.wait_ge(m["lat_var"], i + 1)
                pe.wait_ge(m["lat_normed"], (QF + KVF) * (i + 1))
                for t in range(4):
                    if t >= 2:
                        pe.wait_ge(m["v_copied"], 4 * i + t - 1)
                    for k in range(KVF):
                        mm = nc.tensor.matmul(ps_l[t % 2][:], lat_n[:, QF + k, P * t:P * t + P], w_uv[:, k], start=(k == 0), stop=(k == KVF - 1))
                    mm.then_inc(m["v_full"], 1)
                pe.wait_ge(m["kpe_kept"], i + 1)
                for u in range(U + 2):
                    if u < U:
                        h, b = u % HEADS, u % 2
                        if u < 2:
                            pe.wait_ge(m["raw_copied"], U * i)
                        else:
                            pe.wait_ge(m["raw_copied"], U * i + u - 1)
                        if u < HEADS:
                            for k in range(QF):
                                mm = nc.tensor.matmul(ps_raw[b][:], w_uq[:, k, h], lat_n[:, k], start=(k == 0), stop=(k == QF - 1))
                        else:
                            nc.tensor.matmul(ps_raw[b][:], consts["ident"][:, 0:HD], kpe_now[:], start=True, stop=False)
                            for k in range(KVF):
                                mm = nc.tensor.matmul(ps_raw[b][:], w_uk[:, k, h], lat_n[:, QF + k], start=False, stop=(k == KVF - 1))
                        mm.then_inc(m["raw_full"], 1)
                    if 0 <= u - 1 < U:
                        pe.wait_ge(m["raw_copied"], U * i + u)
                        if u >= 3:
                            pe.wait_ge(m["mean_ready"], U * i + u - 2)
                        else:
                            pe.wait_ge(m["mean_ready"], U * i)
                        nc.tensor.matmul(ps_sum[(u - 1) % 2][:], part_ones[:], sq[:, (u - 1) % 2], start=True, stop=True).then_inc(m["sum_full"], 1)
                    if 0 <= u - 2 < U:
                        pe.wait_ge(m["normed"], U * i + u - 1)
                        if u >= 4:
                            pe.wait_ge(m["sin_ready"], U * i + u - 3)
                        else:
                            pe.wait_ge(m["sin_ready"], U * i)
                        nc.tensor.matmul(ps_rot[u % 2][:], rotate[:], normed[:, u % 2], start=True, stop=True).then_inc(m["rot_full"], 1)

        @block.scalar
        def _(act):
            with act.Fori(0, NT) as i:
                act.wait_ge(m["loaded"], 48 * i + 48)
                act.wait_ge(m["lat_full"], i)
                nc.scalar.activation(lat_sq[:], lat[:], ACT.Square).then_inc(m["lat_squared"], 1)
                act.wait_ge(m["lat_var"], i + 1)
                nc.scalar.activation(ln_l[:], var[:], ACT.Ln).then_inc(m["ln_own"], 1)
                act.wait_ge(m["ln_own"], (U + 1) * i + 1)
                nc.scalar.activation(rms[:], ln_l[:], ACT.Exp, scale=-0.5).then_inc(m["lat_rstd"], 1)
                for t in range(4):
                    act.wait_ge(m["v_full"], 4 * i + t + 1)
                    act.wait_ge(v_stored[t % 2], 32 * i + 16 * (t // 2))
                    nc.scalar.copy(v_out[:, t % 2], ps_l[t % 2][:]).then_inc(m["v_copied"], 1)
                for u in range(U + 1):
                    b = u % 2
                    if u < U:
                        act.wait_ge(m["raw_full"], U * i + u + 1)
                        if u >= 2:
                            act.wait_ge(m["sum_full"], U * i + u - 1)
                            act.wait_ge(m["normed"], U * i + u - 1)
                        else:
                            act.wait_ge(m["sum_full"], U * i)
                            act.wait_ge(m["normed"], U * i)
                        nc.scalar.activation(sq[:, b], ps_raw[b][:], ACT.Square)
                        nc.scalar.copy(raw[:, b], ps_raw[b][:]).then_inc(m["raw_copied"], 1)
                    if u >= 1:
                        c = (u - 1) % 2
                        act.wait_ge(m["mean_ready"], U * i + u)
                        nc.scalar.activation(ln_h[:, c], ssb[:, c], ACT.Ln).then_inc(m["ln_own"], 1)
                        act.wait_ge(m["ln_own"], (U + 1) * i + u + 1)
                        nc.scalar.activation(rstd[:, c], ln_h[:, c], ACT.Exp, scale=-0.5).then_inc(m["rstd_ready"], 1)

        @block.gpsimd
        def _(pool):
            with pool.Fori(0, NT) as i:
                pool.wait_ge(m["loaded"], 48 * i + 48)
                pool.wait_ge(m["raw_full"], U * i)
                nc.gpsimd.tensor_tensor(kpe_now[:], kpe[:], consts["ones"][:, 0:1].to_broadcast([P, NB]), ALU.mult).then_inc(m["kpe_kept"], 1)
                for u in range(U):
                    b = u % 2
                    pool.wait_ge(m["normed"], U * i + u + 1)
                    if u >= 2:
                        pool.wait_ge(m["out_ready"], U * i + u - 1)
                    else:
                        pool.wait_ge(m["out_ready"], U * i)
                    nc.gpsimd.tensor_tensor(t_cos[:, b], normed[:, b], rope[:, 0], ALU.mult).then_inc(m["cos_ready"], 1)

        @block.vector
        def _(dve):
            nc.vector.tensor_scalar(q_gain[:], col(consts, "q_gain"), SCALE, None, ALU.mult).then_inc(m["own"], 1)
            dve.wait_ge(m["own"], 1)
            with dve.Fori(0, NT) as i:
                dve.wait_ge(m["lat_full"], i + 1)
                dve.wait_ge(m["lat_rstd"], i)
                for b, n in enumerate((QF, KVF)):
                    ins = nc.vector.tensor_scalar(var[:, b], ps_l[b][:], 1.0 / (n * P), EPS, ALU.mult, ALU.add)
                ins.then_inc(m["lat_var"], 1)
                dve.wait_ge(m["lat_rstd"], i + 1)
                dve.wait_ge(m["raw_full"], U * i)
                for k in range(QF + KVF):
                    gain = col(consts, "qa_norm", k, 1) if k < QF else col(consts, "kva_norm", k - QF, 1)
                    nc.vector.scalar_tensor_tensor(out=lat_n[:, k], in0=lat[:, k], scalar=gain, in1=rms[:, int(k >= QF)],
                                                   op0=ALU.mult, op1=ALU.mult).then_inc(m["lat_normed"], 1)
                for u in range(U + 1):
                    b = u % 2
                    if u < U:
                        dve.wait_ge(m["sum_full"], U * i + u + 1)
                        if u >= 2:
                            dve.wait_ge(m["rstd_ready"], U * i + u - 1)
                        else:
                            dve.wait_ge(m["rstd_ready"], U * i)
                        nc.vector.tensor_scalar(ssb[:, b], ps_sum[b][:], EPS, None, ALU.add).then_inc(m["mean_ready"], 1)
                    if u >= 1:
                        c = (u - 1) % 2
                        dve.wait_ge(m["rot_full"], U * i + u)
                        nc.vector.tensor_tensor(t_sin[:, c], ps_rot[c][:], rope[:, 1], ALU.mult).then_inc(m["sin_ready"], 1)
                        dve.wait_ge(m["sin_ready"], U * i + u)
                        dve.wait_ge(m["cos_ready"], U * i + u)
                        dve.wait_ge(stored[c], 8 * U * i + 16 * ((u - 1) // 2))
                        nc.vector.tensor_tensor(outq[:, c], t_sin[:, c], t_cos[:, c], ALU.add).then_inc(m["out_ready"], 1)
                    if u < U:
                        dve.wait_ge(m["rstd_ready"], U * i + u + 1)
                        if u >= 2:
                            dve.wait_ge(m["rot_full"], U * i + u - 1)
                        gain = q_gain[0:HD] if u < HEADS else col(consts, "k_gain")[0:HD]
                        nc.vector.scalar_tensor_tensor(out=normed[:, b], in0=raw[:, b], scalar=gain, in1=rstd[:, b],
                                                       op0=ALU.mult, op1=ALU.mult).then_inc(m["normed"], 1)


def attention(nc, dram, consts, o_all):
    with ExitStack() as ctx:
        s = Scope(nc, ctx)
        q = s.sb("att_q", [HD, 2, TOK])
        k = s.sb("att_k", [HD, 2, TOK])
        v = s.sb("att_v", [P, 2, TT, 64])
        prob = s.sb("att_prob", [P, 2, SEQS[0]])
        prob_t = s.sb("att_prob_t", [P, 2, 2, 512])
        stat = s.sb("att_stat", [P, 2, 3])
        ps_s = [s.ps(f"ps_scores{b}", [P, 2, 512]) for b in range(2)]
        ps_t = s.ps("ps_prob_t", [P, 2, 512])
        ps_o = [s.ps(f"ps_o{b}", [P, 64]) for b in range(2)]
        zeros = s.sb("att_zeros", [P, D])
        zeroed, zeros_stored = s.sem("att_zeroed"), s.sem("att_zeros_stored")
        loaded = [s.sem(f"att_loaded{b}") for b in range(2)]
        m = {n: s.sem("att_" + n) for n in ("s_full", "max_ready", "p_ready", "t_full", "t_copied_act", "t_copied_dve", "o_full",
                                            "inv_ready", "o_ready")}
        block = ctx.enter_context(nc.Block())
        units = [(0, t, SEQS[0] // P) for t in range(SEQS[0] // P)] + [(SEQS[0], SEQS[0] // P + t, SEQS[1] // P) for t in range(SEQS[1] // P)]
        U = len(units)
        todo = [(hb, u) + unit for hb in range(2) for u, unit in enumerate(units)]
        n_turn = 2 * U

        @block.sync
        def _(sp):
            def load(h, b):
                sp.dma_start(q[:, b], dram["qk_t"][bass.ds(h, 1)].rearrange("a d t -> d (a t)")).then_inc(loaded[b], 16)
                sp.dma_start(k[:, b], dram["qk_t"][bass.ds(h + HEADS, 1)].rearrange("a d t -> d (a t)")).then_inc(loaded[b], 16)
                sp.dma_start(v[:, b], dram["v_mla"][:, :, bass.ds(h * 64, 64)].rearrange("t p v -> p t v")).then_inc(loaded[b], 16)

            for b in range(2):
                load(b, b)
            with sp.Fori(0, HEADS // 2 - 1) as i:
                for b in range(2):
                    sp.wait_ge(m["o_full"], n_turn * i + U * (b + 1))
                    load(2 * i + (b + 2), b)

        @block.gpsimd
        def _(pool):
            nc.gpsimd.memset(zeros[:], 0.0).then_inc(zeroed, 1)
            pool.wait_ge(zeroed, 1)
            for n in range(TOK * TOP // MB, BLOCKS):
                pool.dma_start(dram["yb"][n], zeros[:]).then_inc(zeros_stored, 16)
            pool.wait_ge(zeros_stored, 16 * (BLOCKS - TOK * TOP // MB))

        @block.tensor
        def _(pe):
            with pe.Fori(0, HEADS // 2) as i:
                base = n_turn * i
                for n in range(n_turn + 2):
                    if n < n_turn:
                        hb, u, t0, t, nk = todo[n]
                        if u == 0:
                            pe.wait_ge(loaded[hb], 48 * i + 48)
                        pe.wait_ge(m["p_ready"], base + max(0, n - 1))
                        for c in range(nk // 4):
                            mm = nc.tensor.matmul(ps_s[n % 2][:, c], q[:, hb, P * t:P * t + P], k[:, hb, t0 + 512 * c:t0 + 512 * c + 512],
                                                  start=True, stop=True)
                        mm.then_inc(m["s_full"], 1)
                    if 0 <= n - 1 < n_turn:
                        nk = todo[n - 1][4]
                        pe.wait_ge(m["p_ready"], base + n)
                        pe.wait_ge(m["t_copied_act"], base + n - 1)
                        pe.wait_ge(m["t_copied_dve"], base + n - 1)
                        for j in range(nk):
                            mm = nc.tensor.transpose(ps_t[:, j // (nk // 2), P * (j % (nk // 2)):P * (j % (nk // 2)) + P],
                                                     prob[:, (n - 1) % 2, P * j:P * j + P], consts["ident"][:])
                        mm.then_inc(m["t_full"], 1)
                    if 0 <= n - 2 < n_turn:
                        hb, u, t0, t, nk = todo[n - 2]
                        pe.wait_ge(m["t_copied_act"], base + n - 1)
                        pe.wait_ge(m["t_copied_dve"], base + n - 1)
                        pe.wait_ge(m["o_ready"], base + max(0, n - 3))
                        for j in range(nk):
                            mm = nc.tensor.matmul(ps_o[n % 2][:], prob_t[:, n % 2, j // (nk // 2), P * (j % (nk // 2)):P * (j % (nk // 2)) + P],
                                                  v[:, hb, t0 // P + j], start=(j == 0), stop=(j == nk - 1))
                        mm.then_inc(m["o_full"], 1)

        @block.scalar
        def _(act):
            with act.Fori(0, HEADS // 2) as i:
                base = n_turn * i
                for n in range(n_turn + 1):
                    if n < n_turn:
                        nk = todo[n][4]
                        act.wait_ge(m["max_ready"], base + n + 1)
                        act.wait_ge(m["t_full"], base + max(0, n - 1))
                        act.wait_ge(m["inv_ready"], base + max(0, n - 1))
                        nc.scalar.activation(prob[:, n % 2, 0:P * nk].rearrange("p (c x) -> p c x", x=512), ps_s[n % 2][:, 0:nk // 4], ACT.Exp,
                                             bias=stat[:, n % 2, 0:1], accum_out=stat[:, n % 2, 1:2]).then_inc(m["p_ready"], 1)
                    if n >= 1:
                        nk = todo[n - 1][4]
                        act.wait_ge(m["t_full"], base + n)
                        act.wait_ge(m["o_full"], base + max(0, n - 2))
                        nc.scalar.copy(prob_t[:, (n - 1) % 2, 0, 0:P * nk // 2], ps_t[:, 0, 0:P * nk // 2]).then_inc(m["t_copied_act"], 1)

        @block.vector
        def _(dve):
            with dve.Fori(0, HEADS // 2) as i:
                base = n_turn * i
                for n in range(n_turn + 2):
                    if n < n_turn:
                        nk = todo[n][4]
                        dve.wait_ge(m["s_full"], base + n + 1)
                        dve.wait_ge(m["p_ready"], base + max(0, n - 1))
                        nc.vector.tensor_reduce(stat[:, n % 2, 0:1], ps_s[n % 2][:, 0:nk // 4], AX.XY, ALU.max, negate=True).then_inc(m["max_ready"], 1)
                    if 0 <= n - 1 < n_turn:
                        nk = todo[n - 1][4]
                        dve.wait_ge(m["t_full"], base + n)
                        dve.wait_ge(m["o_full"], base + max(0, n - 2))
                        nc.vector.tensor_copy(prob_t[:, (n - 1) % 2, 1, 0:P * nk // 2], ps_t[:, 1, 0:P * nk // 2]).then_inc(m["t_copied_dve"], 1)
                        dve.wait_ge(m["o_ready"], base + max(0, n - 2))
                        nc.vector.reciprocal(stat[:, (n - 1) % 2, 2:3], stat[:, (n - 1) % 2, 1:2]).then_inc(m["inv_ready"], 1)
                    if 0 <= n - 2 < n_turn:
                        hb, u, t0, t, nk = todo[n - 2]
                        dve.wait_ge(m["o_full"], base + n - 1)
                        dve.wait_ge(m["inv_ready"], base + n - 1)
                        nc.vector.tensor_scalar(o_all[:, t, bass.ds(i * 128 + hb * 64, 64)], ps_o[n % 2][:], stat[:, n % 2, 2:3], None,
                                                ALU.mult).then_inc(m["o_ready"], 1)


EXPERTS, GROUPS, PER_GROUP = 32, 4, 8
ROUTER = GROUPS + EXPERTS


def turn_o(nc, dram, consts, o_all, om_t):
    with ExitStack() as ctx:
        s = Scope(nc, ctx)
        ps = s.ps("ps_turn_o", [P, 2, 512])
        full = [s.sem(f"o_turned{b}") for b in range(2)]
        copied = [s.sem(f"o_copied{b}") for b in range(2)]
        block = ctx.enter_context(nc.Block())

        @block.tensor
        def _(pe):
            for t in range(TT):
                pe.wait_ge(copied[t % 2], t // 2)
                for f in range(RF):
                    mm = nc.tensor.transpose(ps[:, t % 2, P * f:P * f + P], o_all[:, t, P * f:P * f + P], consts["ident"][:])
                mm.then_inc(full[t % 2], 1)

        def copies(b, eng, copy):
            for t in range(b, TT, 2):
                eng.wait_ge(full[b], t // 2 + 1)
                copy(om_t[:, :, P * t:P * t + P], ps[:, b].rearrange("p (f t) -> p f t", f=RF)).then_inc(copied[b], 1)

        @block.scalar
        def _(act):
            copies(0, act, nc.scalar.copy)

        @block.vector
        def _(dve):
            copies(1, dve, nc.vector.tensor_copy)


def merge_branches(nc, dram, consts, oa_t, om_t, merged):
    with ExitStack() as ctx:
        s = Scope(nc, ctx)
        w = s.sb("w_o_tile", [P, 2, 2, RF, P])
        g = s.sb("gate_tile", [P, 2, 2, TOK])
        part = s.sb("branch_part", [P, 2, 2, NB])
        ps = s.ps("ps_branch", [P, 2, 2, NB])
        loaded = [s.sem(f"merge_loaded{b}") for b in range(2)]
        full = [s.sem(f"branch_full{b}") for b in range(2)]
        scaled = s.sem("branch_scaled")
        done = [s.sem(f"merged{b}") for b in range(2)]
        block = ctx.enter_context(nc.Block())
        units = [(b, n) for b in range(2) for n in range(NT)]

        @block.sync
        def _(sp):
            with sp.Fori(0, DF // 2) as i:
                for b in range(2):
                    sp.wait_ge(done[0], 3 * i)
                    sp.wait_ge(done[1], 3 * i)
                    for a in range(2):
                        sp.dma_start(w[:, b, a], dram["w_o"][a, bass.ds(2 * i + b, 1)].rearrange("a p f m -> p (a f) m")).then_inc(loaded[b], 16)
                        sp.dma_start(g[:, b, a], dram["gates"][bass.ds(2 * i + (b + a * DF), 1)].rearrange("a p t -> p (a t)")).then_inc(loaded[b], 16)

        @block.tensor
        def _(pe):
            with pe.Fori(0, DF // 2) as i:
                for u, (b, n) in enumerate(units):
                    if n == 0:
                        pe.wait_ge(loaded[b], 64 * i + 64)
                    pe.wait_ge(done[u % 2], 3 * i + u // 2)
                    for a, src in enumerate((oa_t, om_t)):
                        for f in range(RF):
                            mm = nc.tensor.matmul(ps[:, u % 2, a], w[:, b, a, f], src[:, f, NB * n:NB * n + NB], start=(f == 0), stop=(f == RF - 1))
                    mm.then_inc(full[u % 2], 1)

        @block.vector
        def _(dve):
            with dve.Fori(0, DF // 2) as i:
                for u, (b, n) in enumerate(units):
                    dve.wait_ge(full[u % 2], 3 * i + u // 2 + 1)
                    nc.vector.tensor_tensor(part[:, u % 2], ps[:, u % 2], g[:, b, :, NB * n:NB * n + NB], ALU.mult).then_inc(scaled, 1)
                    dve.wait_ge(scaled, 6 * i + u + 1)
                    nc.vector.tensor_tensor(merged[:, bass.ds(2 * i + b, 1), NB * n:NB * n + NB].rearrange("p a t -> p (a t)"),
                                            part[:, u % 2, 0], part[:, u % 2, 1], ALU.add).then_inc(done[u % 2], 1)


def output_and_router(nc, dram, consts, merged, logits):
    with ExitStack() as ctx:
        s = Scope(nc, ctx)
        w = s.sb("w_out", [P, DF, D])
        w_r = s.sb("w_router", [P, DF, ROUTER])
        b_r = s.sb("b_router", [P, ROUTER])
        rows = s.sb("mod_broadcast", [P, 2, 3, D])
        norm2 = s.sb("norm2_broadcast", [P, D])
        stage = s.sb("merged_tile", [P, 2, DF, P])
        x = s.sb("x_again", [P, 2, D])
        x1 = s.sb("x1_tile", [P, 2, D])
        sq = s.sb("x1_square", [P, D])
        h2 = s.sb("h2_tile", [P, 2, D])
        h2_t = s.sb("h2_turned", [P, DF, P])
        st = s.sb("x1_stat", [P, 2, 3])
        ps = [s.ps(f"ps_out{b}", [P, 2, 512]) for b in range(2)]
        ps_t = s.ps("ps_h2_t", [P, 2, 512])
        ps_r = s.ps("ps_router", [P, 512])
        m = {n: s.sem("out_" + n) for n in ("consts", "consts_b", "own", "staged", "full", "squared", "sqrt_in", "sqrt", "h2_ready", "t_full",
                                            "t_copied", "r_full", "r_done", "x1_ready", "unread")}
        x_loaded = [s.sem(f"out_x_loaded{b}") for b in range(2)]
        x1_stored = [s.sem(f"x1_stored{b}") for b in range(2)]
        h2_stored = [s.sem(f"h2_stored{b}") for b in range(2)]
        block = ctx.enter_context(nc.Block())
        runs = ((0, 0, SEQS[0] // P // 2), (1, SEQS[0] // P // 2, TT // 2))

        @block.sync
        def _(sp):
            for q in range(2):
                for j, part in enumerate((GATE1, SHIFT2, SCALE2)):
                    row = (part * 2 + q) * DF
                    sp.dma_start(rows[:, q, j], dram["mod_rows"][row:row + DF, :].rearrange("f p -> (f p)").partition_broadcast(P)).then_inc(m["consts"], 16)
            sp.dma_start(norm2[:], dram["norm2"][:].partition_broadcast(P)).then_inc(m["consts"], 16)
            sp.dma_start(b_r[:], dram["b_router"][:].partition_broadcast(P)).then_inc(m["consts"], 16)
            sp.dma_start(w[:], dram["w_out"][:, :, :]).then_inc(m["consts_b"], 16)
            sp.dma_start(w_r[:], dram["w_router"][:, :, :]).then_inc(m["consts_b"], 16)
            with sp.Fori(0, TT // 2) as i:
                for b in range(2):
                    sp.wait_ge(m["x1_ready"], 2 * i)
                    sp.dma_start(x[:, b], dram["x"][bass.ds(i * 2 * P + b * P, P), :]).then_inc(x_loaded[b], 16)
                for b in range(2):
                    sp.wait_ge(m["x1_ready"], 2 * i + b + 1)
                    sp.dma_start(dram["x1"][bass.ds(i * 2 * P + b * P, P), :], x1[:, b]).then_inc(x1_stored[b], 16)
                    sp.wait_ge(m["h2_ready"], 2 * i + b + 1)
                    sp.dma_start(dram["h2"][bass.ds(i * 2 * P + b * P, P), :], h2[:, b]).then_inc(h2_stored[b], 16)
            for b in range(2):
                sp.wait_ge(x1_stored[b], 16 * (TT // 2))
                sp.wait_ge(h2_stored[b], 16 * (TT // 2))

        @block.tensor
        def _(pe):
            pe.wait_ge(m["consts_b"], 32)

            def turn_and_route(b, count):
                pe.wait_ge(m["h2_ready"], count)
                pe.wait_ge(m["t_copied"], count - 1)
                for k in range(DF):
                    mm = nc.tensor.transpose(ps_t[:, k // 4, P * (k % 4):P * (k % 4) + P], h2[:, b, P * k:P * k + P], consts["ident"][:])
                mm.then_inc(m["t_full"], 1)
                pe.wait_ge(m["t_copied"], count)
                pe.wait_ge(m["r_done"], count - 1)
                for k in range(DF):
                    mm = nc.tensor.matmul(ps_r[:, 0:ROUTER], h2_t[:, k], w_r[:, k], start=(k == 0), stop=(k == DF - 1))
                mm.then_inc(m["r_full"], 1)

            with pe.Fori(0, TT // 2) as i:
                for b in range(2):
                    pe.wait_ge(m["staged"], 2 * i + b + 1)
                    pe.wait_ge(m["x1_ready"], 2 * i)
                    for n in range(2):
                        for k in range(DF):
                            mm = nc.tensor.matmul(ps[b][:, n], stage[:, b, k], w[:, k, 512 * n:512 * n + 512], start=(k == 0), stop=(k == DF - 1))
                    mm.then_inc(m["full"], 1)
                for b in range(2):
                    turn_and_route(b, 2 * i + b + 1)

        @block.scalar
        def _(act):
            with act.Fori(0, TT // 2) as i:
                for b in range(2):
                    act.wait_ge(m["full"], 2 * i)
                    alone(act, m["unread"])
                    nc.scalar.copy(stage[:, b], merged[:, :, bass.ds(i * 2 * P + b * P, P)]).then_inc(m["staged"], 1)
                for b in range(2):
                    act.wait_ge(m["x1_ready"], 2 * i + b + 1)
                    act.wait_ge(m["sqrt"], 2 * i + b)
                    nc.scalar.activation(sq[:], x1[:, b], ACT.Square, accum_out=st[:, b, 0:1]).then_inc(m["squared"], 1)
                    act.wait_ge(m["sqrt_in"], 2 * i + b + 1)
                    nc.scalar.activation(st[:, b, 2:3], st[:, b, 1:2], ACT.Sqrt).then_inc(m["sqrt"], 1)
                for b in range(2):
                    act.wait_ge(m["t_full"], 2 * i + b + 1)
                    act.wait_ge(m["r_full"], 2 * i + b)
                    nc.scalar.copy(h2_t[:].rearrange("p (a k) t -> p a (k t)", a=2), ps_t[:]).then_inc(m["t_copied"], 1)

        @block.vector
        def _(dve):
            start = Chain(dve, m["own"])
            dve.wait_ge(m["consts"], 16 * 8)
            for q in range(2):
                start(nc.vector.tensor_tensor(rows[:, q, 2], rows[:, q, 2], norm2[:], ALU.mult))
            for q, first, end in runs:
                with dve.Fori(first, end) as i:
                    step = Chain(dve, m["own"], start.n, i, 2 * 4)
                    for b in range(2):
                        dve.wait_ge(m["full"], 2 * i + b + 1)
                        dve.wait_ge(x1_stored[b], 16 * i)
                        dve.wait_ge(m["squared"], 2 * i)
                        step(nc.vector.tensor_tensor(x1[:, b].rearrange("p (a x) -> p a x", a=2), ps[b][:],
                                                     rows[:, q, 0].rearrange("p (a x) -> p a x", a=2), ALU.mult))
                        dve.wait_ge(x_loaded[b], 16 * i + 16)
                        nc.vector.tensor_tensor(x1[:, b], x1[:, b], x[:, b], ALU.add).then_inc(m["x1_ready"], 1)
                    for b in range(2):
                        dve.wait_ge(m["squared"], 2 * i + b + 1)
                        nc.vector.tensor_scalar(st[:, b, 1:2], st[:, b, 0:1], 1.0 / D, EPS, ALU.mult, ALU.add).then_inc(m["sqrt_in"], 1)
                        dve.wait_ge(m["sqrt"], 2 * i + b + 1)
                        step(nc.vector.reciprocal(st[:, b, 2:3], st[:, b, 2:3]))
                        dve.wait_ge(h2_stored[b], 16 * i)
                        dve.wait_ge(m["t_full"], 2 * i)
                        step(nc.vector.scalar_tensor_tensor(out=h2[:, b], in0=x1[:, b], scalar=st[:, b, 2:3], in1=rows[:, q, 2],
                                                            op0=ALU.mult, op1=ALU.mult))
                        step(nc.vector.tensor_tensor(h2[:, b], h2[:, b], rows[:, q, 1], ALU.add))
                        dve.sem_inc(m["h2_ready"], 1)
                    for b in range(2):
                        dve.wait_ge(m["r_full"], 2 * i + b + 1)
                        nc.vector.tensor_tensor(logits[:, bass.ds(2 * i + b, 1)].rearrange("p a e -> p (a e)"), ps_r[:, 0:ROUTER], b_r[:],
                                                ALU.add).then_inc(m["r_done"], 1)
                    step.end()


TOP = 2
D_EXPERT = 256
MB = P
BLOCKS = -(-(TOK * TOP + EXPERTS * (MB - 1)) // MB // 2) * 2
FAR = 1e30


def route(nc, dram, consts, logits, weight, slot):
    with ExitStack() as ctx:
        s = Scope(nc, ctx)
        G, E, T = GROUPS, EXPERTS, TT
        rank_g = s.sb("rank_groups", [P, G])
        rank_e = s.sb("rank_experts", [P, E])
        before = s.sb("tokens_before", [P, P])
        full_at = s.sb("full_at", [P, TT])
        block_no = s.sb("block_no", [P, BLOCKS])
        token = s.sb("token_ids", [P, T])
        zero = s.sb("zero_ids", [P, BLOCKS])
        t = lambda name, shape: s.sb("route_" + name, [P] + shape)
        g_max, g_sum, p_grp, e_max, e_max2, ratio, part = (t(n, [T]) for n in ("gmax", "gsum", "pgrp", "emax", "emax2", "ratio", "part"))
        g_exp, g_hot, g_far = (t(n, [T, G]) for n in ("gexp", "ghot", "gfar"))
        e_in, hot1, hot2, hots, value, prod = (t(n, [T, E]) for n in ("ein", "hot1", "hot2", "hots", "value", "prod"))
        total = t("total", [T + 1, E])
        n_blocks, ends, row0 = (t(n, [E]) for n in ("nblocks", "ends", "row0"))
        over = t("over", [E, TT])
        ended = t("ended", [BLOCKS, E])
        block_e = t("block_e", [BLOCKS + 1])
        block_i = s.sb("route_block_i", [P, BLOCKS + 1], I32)
        dest = t("dest", [TOP, T])
        ps_pref = s.ps("ps_prefix", [P, 512])
        ps_tot = s.ps("ps_total", [P, 512])
        m = {n: s.sem("route_" + n) for n in ("consts", "own", "g_in", "g_exp", "r_in", "ratio", "hots", "counted", "zeroed", "zero_stored",
                                              "slots", "scattered", "blocks", "blocks_stored")}
        block = ctx.enter_context(nc.Block())

        @block.sync
        def _(sp):
            for dst, name in ((rank_g, "rank_groups"), (rank_e, "rank_experts"), (full_at, "full_at"), (block_no, "block_no")):
                sp.dma_start(dst[:], dram[name][:].partition_broadcast(P)).then_inc(m["consts"], 16)
            sp.dma_start(before[:], dram["tokens_before"][:, :]).then_inc(m["consts"], 16)
            sp.dma_start(token[:], dram["token_ids"][:, :]).then_inc(m["consts"], 16)
            sp.wait_ge(m["zeroed"], 1)
            sp.dma_start(dram["row_token"].rearrange("(p b) a -> p (b a)", p=P), zero[:]).then_inc(m["zero_stored"], 16)
            sp.wait_ge(m["blocks"], 1)
            sp.dma_start(dram["block_expert"][:, :], block_i[0:1, :]).then_inc(m["blocks_stored"], 16)
            sp.wait_ge(m["blocks_stored"], 16)

        @block.scalar
        def _(act):
            act.wait_ge(m["g_in"], 1)
            nc.scalar.activation(g_exp[:], g_exp[:], ACT.Exp).then_inc(m["g_exp"], 1)
            act.wait_ge(m["r_in"], 1)
            nc.scalar.activation(ratio[:], ratio[:], ACT.Exp).then_inc(m["ratio"], 1)

        @block.tensor
        def _(pe):
            pe.wait_ge(m["hots"], 1)
            flat = hots[:].rearrange("p t e -> p (t e)")
            nc.tensor.matmul(ps_pref[:, 0:T * E], before[:], flat, start=True, stop=True)
            nc.tensor.matmul(ps_tot[:, 0:T * E], consts["ones"][:], flat, start=True, stop=True).then_inc(m["counted"], 1)

        @block.gpsimd
        def _(pool):
            pool.wait_ge(m["slots"], 1)
            pool.wait_ge(m["zero_stored"], 16)
            pool.wait_ge(m["consts"], 96)
            for k in range(TOP):
                for j in range(T):
                    pool.indirect_dma_start(out=dram["row_token"], out_offset=bass.IndirectOffsetOnAxis(ap=slot[:, k, j:j + 1], axis=0),
                                            in_=token[:, j:j + 1], in_offset=None).then_inc(m["scattered"], 16)
            pool.wait_ge(m["scattered"], 16 * TOP * T)

        @block.vector
        def _(dve):
            V = nc.vector
            nc.vector.memset(zero[:], 0).then_inc(m["zeroed"], 1)
            do = Chain(dve, m["own"])
            groups, experts = logits[:, :, 0:G], logits[:, :, G:G + E]
            wide = lambda x, n: x.unsqueeze(2).to_broadcast([P, T, n])
            dve.wait_ge(m["consts"], 96)
            do(V.tensor_reduce(g_max[:], groups, AX.X, ALU.max))
            V.tensor_tensor(g_exp[:], groups, wide(g_max[:], G), ALU.subtract).then_inc(m["g_in"], 1)

            def first_of(hot, values, best, rank, n):
                do(V.tensor_tensor(hot, values, wide(best, n), ALU.is_equal))
                do(V.tensor_tensor(hot, hot, rank[:].unsqueeze(1).to_broadcast([P, T, n]), ALU.mult))
                do(V.tensor_reduce(part[:], hot, AX.X, ALU.max))
                do(V.tensor_tensor(hot, hot, wide(part[:], n), ALU.is_equal))

            first_of(g_hot[:], groups, g_max[:], rank_g, G)
            do(V.tensor_scalar(g_far[:], g_hot[:], FAR, -FAR, ALU.mult, ALU.add))
            by_group = lambda x: x.rearrange("p t (g e) -> p t g e", g=G)
            over_group = lambda x: x.unsqueeze(3).to_broadcast([P, T, G, PER_GROUP])
            for g in range(G):
                part_e = slice(g * PER_GROUP, (g + 1) * PER_GROUP)
                V.tensor_tensor(e_in[:, :, part_e], experts[:, :, part_e], g_hot[:, :, g:g + 1].to_broadcast([P, T, PER_GROUP]), ALU.mult).then_inc(m["own"], 1)
                do.n += 1
            dve.wait_ge(m["own"], do.n)
            for g in range(G):
                part_e = slice(g * PER_GROUP, (g + 1) * PER_GROUP)
                V.tensor_tensor(e_in[:, :, part_e], e_in[:, :, part_e], g_far[:, :, g:g + 1].to_broadcast([P, T, PER_GROUP]), ALU.add).then_inc(m["own"], 1)
                do.n += 1
            dve.wait_ge(m["own"], do.n)
            do(V.tensor_reduce(e_max[:], e_in[:], AX.X, ALU.max))
            first_of(hot1[:], e_in[:], e_max[:], rank_e, E)
            do(V.tensor_scalar(value[:], hot1[:], -3 * FAR, None, ALU.mult))
            do(V.tensor_tensor(e_in[:], e_in[:], value[:], ALU.add))
            do(V.tensor_reduce(e_max2[:], e_in[:], AX.X, ALU.max))
            first_of(hot2[:], e_in[:], e_max2[:], rank_e, E)
            do(V.tensor_tensor(hots[:], hot1[:], hot2[:], ALU.add))
            dve.sem_inc(m["hots"], 1)
            V.tensor_tensor(ratio[:], e_max2[:], e_max[:], ALU.subtract).then_inc(m["r_in"], 1)
            dve.wait_ge(m["g_exp"], 1)
            do(V.tensor_reduce(g_sum[:], g_exp[:], AX.X, ALU.add))
            do(V.reciprocal(p_grp[:], g_sum[:]))
            dve.wait_ge(m["ratio"], 1)
            do(V.tensor_scalar(part[:], ratio[:], 1.0, None, ALU.add))
            do(V.reciprocal(part[:], part[:]))
            do(V.tensor_tensor(weight[:, 0], p_grp[:], part[:], ALU.mult))
            do(V.tensor_tensor(weight[:, 1], weight[:, 0], ratio[:], ALU.mult))
            dve.wait_ge(m["counted"], 1)
            do(V.memset(total[:, 0], 0.0))
            for j in range(T):
                do(V.tensor_tensor(total[:, j + 1], total[:, j], ps_tot[:, E * j:E * j + E], ALU.add))
            do(V.tensor_tensor(over[:], total[:, T].unsqueeze(2).to_broadcast([P, E, TT]), full_at[:].unsqueeze(1).to_broadcast([P, E, TT]), ALU.is_gt))
            do(V.tensor_reduce(n_blocks[:], over[:], AX.X, ALU.add))
            do(V.tensor_tensor_scan(ends[:], consts["ones"][:, 0:E], n_blocks[:], 0.0, ALU.mult, ALU.add))
            do(V.tensor_tensor(row0[:], ends[:], n_blocks[:], ALU.subtract))
            do(V.tensor_scalar(row0[:], row0[:], float(MB), None, ALU.mult))
            do(V.tensor_tensor(value[:], total[:, 0:T], ps_pref[:, 0:T * E].rearrange("p (t e) -> p t e", t=T), ALU.add))
            do(V.tensor_tensor(value[:], value[:], row0[:].unsqueeze(1).to_broadcast([P, T, E]), ALU.add))
            for k, hot in enumerate((hot1, hot2)):
                do(V.tensor_tensor(prod[:], value[:], hot[:], ALU.mult))
                do(V.tensor_reduce(dest[:, k], prod[:], AX.X, ALU.add))
            V.tensor_copy(slot[:], dest[:]).then_inc(m["slots"], 1)
            do(V.tensor_tensor(ended[:], block_no[:].unsqueeze(2).to_broadcast([P, BLOCKS, E]), ends[:].unsqueeze(1).to_broadcast([P, BLOCKS, E]), ALU.is_ge))
            do(V.tensor_reduce(block_e[:, 0:BLOCKS], ended[:], AX.X, ALU.add))
            do(V.tensor_scalar(block_e[:, 0:BLOCKS], block_e[:, 0:BLOCKS], float(E - 1), None, ALU.min))
            do(V.tensor_copy(block_e[:, BLOCKS:BLOCKS + 1], ends[:, E - 1:E]))
            V.tensor_copy(block_i[:], block_e[:]).then_inc(m["blocks"], 1)
            dve.wait_ge(m["slots"], 1)


def experts(nc, dram, consts):
    with ExitStack() as ctx:
        s = Scope(nc, ctx)
        F2 = D_EXPERT // P
        w13 = s.sb("w13_tile", [P, 2, DF, 2 * D_EXPERT])
        w2 = s.sb("w2_tile", [P, 2, F2, D])
        which = s.sb("block_experts", [1, BLOCKS + 1], I32)
        id_rows = s.sb("row_ids_by_block", [BLOCKS, P])
        ids = s.sb("row_ids", [P, BLOCKS], I32)
        ids_now = s.sb("row_ids_now", [P, 2], I32)
        xb = s.sb("xb", [P, 2, D])
        xt = s.sb("xb_turned", [P, 2, DF, P])
        th = s.sb("gate_tanh", [P, 2, F2, P])
        act_in = s.sb("gate_in", [P, 2, F2, P])
        hid = s.sb("hidden", [P, 2, F2, P])
        yb = s.sb("yb_tile", [P, 2, D])
        ps_ids = s.ps("ps_ids", [P, 512])
        ps_h = [s.ps(f"ps_hidden{b}", [P, 2 * F2, P]) for b in range(2)]
        ps_xy = [s.ps(f"ps_xy{b}", [P, 2, 512]) for b in range(2)]
        loaded, ids_turned, unread = s.sem("moe_consts"), s.sem("moe_ids_turned"), s.sem("moe_unread")
        pair = lambda n: [s.sem(f"moe_{n}{b}") for b in range(2)]
        w13_loaded, w2_loaded, x_loaded, ids_ready, stored = (pair(n) for n in ("w13_loaded", "w2_loaded", "x_loaded", "ids_ready", "stored"))
        turned, x_act, x_dve, h_full, tanh = (pair(n) for n in ("turned", "x_act", "x_dve", "h_full", "tanh"))
        gated, hidden, y_full, y_act, y_dve = (pair(n) for n in ("gated", "hidden", "y_full", "y_act", "y_dve"))
        block = ctx.enter_context(nc.Block())

        def used_blocks(eng):
            eng.wait_ge(loaded, 32)
            return eng.value_load(which[0:1, BLOCKS:BLOCKS + 1], min_val=1, max_val=BLOCKS)

        @block.sync
        def _(sp):
            sp.dma_start(which[:], dram["block_expert"][:, :]).then_inc(loaded, 16)
            sp.dma_start(id_rows[:], dram["row_token"].rearrange("(b p) a -> b (p a)", p=P)).then_inc(loaded, 16)
            used = used_blocks(sp)
            with sp.Fori(0, BLOCKS // 2) as i:
                with sp.If(2 * i < used):
                    e = [sp.value_load(which[0:1, bass.ds(2 * i + b, 1)], min_val=0, max_val=EXPERTS - 1) for b in range(2)]
                    for b in range(2):
                        sp.wait_ge(h_full[b], i)
                        alone(sp, unread)
                        sp.dma_start(w13[:, b], dram["w13"][bass.ds(e[b], 1)].rearrange("a p k f -> p (a k) f")).then_inc(w13_loaded[b], 16)
                    for b in range(2):
                        sp.wait_ge(y_full[b], i)
                        alone(sp, unread)
                        sp.dma_start(w2[:, b], dram["w2"][bass.ds(e[b], 1)].rearrange("a p k f -> p (a k) f")).then_inc(w2_loaded[b], 16)

        @block.gpsimd
        def _(pool):
            used = used_blocks(pool)
            pool.wait_ge(ids_turned, 2)
            with pool.Fori(0, BLOCKS // 2) as i:
                with pool.If(2 * i < used):
                    for b in range(2):
                        pool.wait_ge(x_loaded[b], 16 * i)
                        alone(pool, unread)
                        nc.gpsimd.tensor_copy(ids_now[:, b:b + 1], ids[:, bass.ds(2 * i + b, 1)]).then_inc(ids_ready[b], 1)
                        pool.wait_ge(ids_ready[b], i + 1)
                        pool.wait_ge(turned[b], i)
                        alone(pool, unread)
                        pool.indirect_dma_start(out=xb[:, b], out_offset=None, in_=dram["h2"],
                                                in_offset=bass.IndirectOffsetOnAxis(ap=ids_now[:, b:b + 1].bitcast(U32), axis=0)).then_inc(x_loaded[b], 16)

        @block.tensor
        def _(pe):
            used = used_blocks(pe)
            nc.tensor.transpose(ps_ids[:, 0:BLOCKS], id_rows[:], consts["ident"][0:BLOCKS, 0:BLOCKS]).then_inc(ids_turned, 1)
            with pe.Fori(0, BLOCKS // 2) as i:
                with pe.If(2 * i < used):
                    for b in range(2):
                        pe.wait_ge(x_loaded[b], 16 * i + 16)
                        pe.wait_ge(y_act[b], i)
                        pe.wait_ge(y_dve[b], i)
                        for k in range(DF):
                            mm = nc.tensor.transpose(ps_xy[b][:, k // 4, P * (k % 4):P * (k % 4) + P], xb[:, b, P * k:P * k + P], consts["ident"][:])
                        mm.then_inc(turned[b], 1)
                    for b in range(2):
                        pe.wait_ge(w13_loaded[b], 16 * i + 16)
                        pe.wait_ge(x_act[b], i + 1)
                        pe.wait_ge(x_dve[b], i + 1)
                        pe.wait_ge(hidden[b], i)
                        for f in range(2 * F2):
                            for k in range(DF):
                                mm = nc.tensor.matmul(ps_h[b][:, f], w13[:, b, k, P * f:P * f + P], xt[:, b, k], start=(k == 0), stop=(k == DF - 1))
                        mm.then_inc(h_full[b], 1)
                    for b in range(2):
                        pe.wait_ge(w2_loaded[b], 16 * i + 16)
                        pe.wait_ge(hidden[b], i + 1)
                        for c in range(2):
                            for k in range(F2):
                                mm = nc.tensor.matmul(ps_xy[b][:, c], hid[:, b, k], w2[:, b, k, 512 * c:512 * c + 512], start=(k == 0), stop=(k == F2 - 1))
                        mm.then_inc(y_full[b], 1)

        @block.scalar
        def _(act):
            used = used_blocks(act)
            with act.Fori(0, BLOCKS // 2) as i:
                with act.If(2 * i < used):
                    for b in range(2):
                        act.wait_ge(turned[b], i + 1)
                        act.wait_ge(h_full[b], i)
                        nc.scalar.copy(xt[:, b, 0:4].rearrange("p k t -> p (k t)"), ps_xy[b][:, 0]).then_inc(x_act[b], 1)
                    for b in range(2):
                        act.wait_ge(h_full[b], i + 1)
                        act.wait_ge(gated[b], i)
                        nc.scalar.activation(th[:, b], ps_h[b][:, 0:F2], ACT.Tanh, scale=0.5).then_inc(tanh[b], 1)
                    for b in range(2):
                        act.wait_ge(y_full[b], i + 1)
                        act.wait_ge(stored[b], 16 * i)
                        nc.scalar.copy(yb[:, b, 0:512], ps_xy[b][:, 0]).then_inc(y_act[b], 1)
                        act.wait_ge(y_act[b], i + 1)
                        act.wait_ge(y_dve[b], i + 1)
                        act.dma_start(dram["yb"][bass.ds(2 * i + b, 1)].rearrange("a p d -> p (a d)"), yb[:, b]).then_inc(stored[b], 16)
            pairs = used + 1 >> 1
            for b in range(2):
                act.wait_ge(stored[b], 16 * pairs)
                alone(act, unread)

        @block.vector
        def _(dve):
            used = used_blocks(dve)
            dve.wait_ge(ids_turned, 1)
            nc.vector.tensor_copy(ids[:], ps_ids[:, 0:BLOCKS]).then_inc(ids_turned, 1)
            with dve.Fori(0, BLOCKS // 2) as i:
                with dve.If(2 * i < used):
                    for b in range(2):
                        dve.wait_ge(turned[b], i + 1)
                        dve.wait_ge(h_full[b], i)
                        nc.vector.tensor_copy(xt[:, b, 4:8].rearrange("p k t -> p (k t)"), ps_xy[b][:, 1]).then_inc(x_dve[b], 1)
                    for b in range(2):
                        dve.wait_ge(tanh[b], i + 1)
                        dve.wait_ge(hidden[b], i)
                        nc.vector.scalar_tensor_tensor(out=act_in[:, b], in0=th[:, b], scalar=1.0, in1=ps_h[b][:, 0:F2], op0=ALU.add,
                                                       op1=ALU.mult).then_inc(gated[b], 1)
                        dve.wait_ge(gated[b], i + 1)
                        dve.wait_ge(y_full[b], i)
                        nc.vector.scalar_tensor_tensor(out=hid[:, b], in0=act_in[:, b], scalar=0.5, in1=ps_h[b][:, F2:2 * F2], op0=ALU.mult,
                                                       op1=ALU.mult).then_inc(hidden[b], 1)
                    for b in range(2):
                        dve.wait_ge(y_full[b], i + 1)
                        dve.wait_ge(stored[b], 16 * i)
                        nc.vector.tensor_copy(yb[:, b, 512:1024], ps_xy[b][:, 1]).then_inc(y_dve[b], 1)


def combine(nc, dram, consts, weight, slot):
    with ExitStack() as ctx:
        s = Scope(nc, ctx)
        gate2 = s.sb("gate2_broadcast", [P, 2, D])
        x1 = s.sb("x1_again", [P, 2, D])
        picked = s.sb("picked", [P, 2, TOP, D])
        mix = s.sb("mixed", [P, 2, D])
        out = s.sb("out_tile", [P, 2, D])
        pair = lambda n: [s.sem(f"comb_{n}{b}") for b in range(2)]
        loaded, gathered, stored, done = pair("loaded"), pair("gathered"), pair("stored"), pair("done")
        consts_in, own = s.sem("comb_consts"), s.sem("comb_own")
        block = ctx.enter_context(nc.Block())
        yb = dram["yb"].rearrange("b p d -> (b p) d")

        @block.sync
        def _(sp):
            for q in range(2):
                row = (GATE2 * 2 + q) * DF
                sp.dma_start(gate2[:, q], dram["mod_rows"][row:row + DF, :].rearrange("f p -> (f p)").partition_broadcast(P)).then_inc(consts_in, 16)
            for t in range(TT + 1):
                b = t % 2
                if t < TT:
                    if t >= 2:
                        sp.wait_ge(done[b], t // 2)
                    sp.dma_start(x1[:, b], dram["x1"][P * t:P * t + P, :]).then_inc(loaded[b], 16)
                if t >= 1:
                    c = (t - 1) % 2
                    sp.wait_ge(done[c], (t - 1) // 2 + 1)
                    sp.dma_start(dram["y"][P * (t - 1):P * t, :], out[:, c]).then_inc(stored[c], 16)
            for b in range(2):
                sp.wait_ge(stored[b], 16 * (TT // 2))

        @block.gpsimd
        def _(pool):
            for t in range(TT):
                b = t % 2
                if t >= 2:
                    pool.wait_ge(done[b], t // 2)
                for k in range(TOP):
                    pool.indirect_dma_start(out=picked[:, b, k], out_offset=None, in_=yb,
                                            in_offset=bass.IndirectOffsetOnAxis(ap=slot[:, k, t:t + 1], axis=0)).then_inc(gathered[b], 16)

        @block.vector
        def _(dve):
            dve.wait_ge(consts_in, 32)
            do = Chain(dve, own)
            for t in range(TT):
                b, q = t % 2, int(t >= SEQS[0] // P)
                dve.wait_ge(gathered[b], 32 * (t // 2) + 32)
                do(nc.vector.tensor_scalar(mix[:, b], picked[:, b, 0], weight[:, 0, t:t + 1], None, ALU.mult))
                do(nc.vector.scalar_tensor_tensor(out=mix[:, b], in0=picked[:, b, 1], scalar=weight[:, 1, t:t + 1], in1=mix[:, b],
                                                  op0=ALU.mult, op1=ALU.add))
                do(nc.vector.tensor_tensor(mix[:, b], mix[:, b], gate2[:, q], ALU.mult))
                dve.wait_ge(loaded[b], 16 * (t // 2) + 16)
                if t >= 2:
                    dve.wait_ge(stored[b], 16 * (t // 2))
                nc.vector.tensor_tensor(out[:, b], mix[:, b], x1[:, b], ALU.add).then_inc(done[b], 1)


def encoder(nc, dram):
    with ExitStack() as ctx:
        s = Scope(nc, ctx)
        consts = {
            "cols": s.sb("cols", [P, NCOLS]),
            "ident": s.sb("ident", [P, P]),
            "ones": s.sb("ones", [P, P]),
            "mod": s.sb("mod", [P, 6, 2, DF]),
            "scale1": s.sb("scale1", [P, 2, DF]),
            "half_merge": s.sb("half_merge", [P, N_GATES]),
            "p_end": s.sb("p_end", [P, 2, RF, TOK // CH]),
        }
        load_constants(nc, dram, consts)
        modulation(nc, dram, consts)
        with ExitStack() as inner:
            h_t = Scope(nc, inner).sb("h_t", [P, DF, TOK])
            norm_and_turn(nc, dram, consts, h_t)
            project_in(nc, dram, consts, h_t)
        rwkv_operands(nc, dram, consts)
        wkv_scan(nc, dram, consts)
        mla_project(nc, dram, consts)
        logits = s.sb("logits", [P, TT, ROUTER])
        with ExitStack() as outer:
            merged = Scope(nc, outer).sb("merged_t", [P, DF, TOK])
            with ExitStack() as inner:
                i = Scope(nc, inner)
                om_t = i.sb("om_t", [P, RF, TOK])
                with ExitStack() as deep:
                    o_all = Scope(nc, deep).sb("o_all", [P, TT, 512])
                    attention(nc, dram, consts, o_all)
                    turn_o(nc, dram, consts, o_all, om_t)
                oa_t = i.sb("oa_t", [P, RF, TOK])
                rwkv_finish(nc, dram, consts, oa_t)
                merge_branches(nc, dram, consts, oa_t, om_t, merged)
            output_and_router(nc, dram, consts, merged, logits)
        weight = s.sb("weight", [P, TOP, TT])
        slot = s.sb("slot", [P, TOP, TT], U32)
        route(nc, dram, consts, logits, weight, slot)
        experts(nc, dram, consts)
        combine(nc, dram, consts, weight, slot)


INTERNAL = {
    "mod_rows": (96, P),
    "p_t": (N_SHIFTED, P, TOK),
    "gates": (N_GATES, P, TOK),
    "wkv_in": (2, TT, P, 16, P),
    "wkv_y": (2, TT, P, RF, P),
    "qk_t": (2 * HEADS, HD, TOK),
    "v_mla": (TT, P, 512),
    "x1": (TOK, D),
    "h2": (TOK, D),
    "row_token": (BLOCKS * MB, 1),
    "block_expert": (1, BLOCKS + 1),
    "yb": (BLOCKS, MB, D),
}


INTERNAL_TYPES = {"block_expert": I32}


def _tiles(w, width):
    K, M = w.shape
    return np.ascontiguousarray(w.reshape(K // P, P, M // width, width).transpose(2, 1, 0, 3))


def _lay_out(inputs):
    a = {k: np.asarray(v) for k, v in inputs.items()}
    one = {k: v[0] for k, v in a.items() if k not in ("x_prompt", "x_sample", "c_prompt", "c_sample")}
    out = {"x": np.concatenate([a["x_prompt"][0], a["x_sample"][0]])}
    out["c"] = np.concatenate([a["c_prompt"], a["c_sample"]]).reshape(2 * DF, P)
    out["w_ada"] = _tiles(one["w_ada"], 512).reshape(6, 2, P, DF, 512)
    w_in = one["w_in"]
    rw, q, kv, rope = 1920, 768, 256, 32
    wide = np.zeros((D, P), w_in.dtype)
    wide[:, 64:96] = w_in[:, rw + q + kv:rw + q + kv + rope]
    out["w_in"] = _tiles(np.concatenate([w_in[:, :rw], wide, w_in[:, rw:rw + q + kv], w_in[:, rw + q + kv + rope:]], 1), P)

    def columns(v, width):
        v = v.reshape(-1)
        full = np.zeros((width, P), np.float32)
        full.reshape(-1)[:v.size] = v
        return full.T

    gain = lambda a, b: np.concatenate([one[a], one[b]])
    parts = {
        "b_ada": one["b_ada"], "norm1": one["norm1"], "mu_prev": one["shift_mu"][0], "mu_next": one["shift_mu"][1],
        "b_merge": one["b_merge"], "w0": one["decay_w0"], "a0": one["iclr_a0"], "k_k": one["k_k"], "k_a": one["k_a"],
        "r_k": one["r_k"], "gn_w": one["gn_w"], "gn_b": one["gn_b"], "qa_norm": one["q_a_norm"], "kva_norm": one["kv_a_norm"],
        "q_gain": gain("q_nope_norm", "q_rope_norm"), "k_gain": gain("k_nope_norm", "k_rope_norm"),
    }
    out["cols"] = np.ascontiguousarray(np.concatenate([columns(parts[k], w) for k, (_, w) in COLS.items()], 1))
    out["ident"] = np.eye(P, dtype=np.float32)
    out["ones"] = np.ones((P, P), np.float32)
    more_layouts(out, one)
    return out


def more_layouts(out, one):
    out["decay_up"] = one["decay_up"].reshape(P, -1)
    out["iclr_up"] = one["iclr_up"].reshape(P, -1)
    out["chunk_reset"] = np.tile((np.arange(RF * PB) % CH != 0).astype(np.float32), (P, 1))
    out["gate_up"] = one["gate_up"]
    out["w_o"] = np.stack([_tiles(one["w_o_rwkv"], P), _tiles(one["w_o_mla"], P)])
    rows = lambda w: np.ascontiguousarray(w.reshape(-1, P, w.shape[-1]).transpose(1, 0, 2))
    out["w_out"] = rows(one["w_out"])
    out["w_router"] = rows(np.concatenate([one["w_rg"], one["w_re"]], 1))
    out["b_router"] = np.concatenate([one["b_rg"], one["b_re"]])
    out["norm2"] = one["norm2"]
    out["w13"] = np.ascontiguousarray(one["w13"].reshape(EXPERTS, DF, P, -1).transpose(0, 2, 1, 3))
    out["w2"] = np.ascontiguousarray(one["w2"].reshape(EXPERTS, D_EXPERT // P, P, D).transpose(0, 2, 1, 3))
    out["rank_groups"] = np.arange(GROUPS, 0, -1, dtype=np.float32)
    out["rank_experts"] = np.arange(EXPERTS, 0, -1, dtype=np.float32)
    out["full_at"] = MB * np.arange(TT, dtype=np.float32)
    out["block_no"] = np.arange(BLOCKS, dtype=np.float32)
    out["tokens_before"] = np.triu(np.ones((P, P), np.float32), 1)
    out["token_ids"] = np.ascontiguousarray(np.arange(TOK, dtype=np.float32).reshape(TT, P).T)
    by_head = lambda w, n: w.reshape(n, P, HEADS, -1).transpose(1, 0, 2, 3)
    out["w_uq"] = np.ascontiguousarray(by_head(one["w_uq"], QF))
    out["w_uk"] = np.zeros((P, KVF, HEADS, HD), np.float32)
    out["w_uk"][..., :NOPE] = by_head(one["w_uk"], KVF)
    out["w_uv"] = np.ascontiguousarray(one["w_uv"].reshape(KVF, P, 512).transpose(1, 0, 2))
    out["part_means"] = np.zeros((HD, HD), np.float32)
    out["part_means"][:NOPE, :NOPE] = 1.0 / NOPE
    out["part_means"][NOPE:, NOPE:] = 1.0 / ROPE
    out["rotate"] = np.zeros((HD, HD), np.float32)
    for k in range(ROPE // 2):
        out["rotate"][NOPE + ROPE // 2 + k, NOPE + k] = -1.0
        out["rotate"][NOPE + k, NOPE + ROPE // 2 + k] = 1.0
    inv = np.float32(1.0) / (np.float32(10000.0) ** (np.arange(0, ROPE, 2, dtype=np.float32) / np.float32(ROPE)))
    ang = np.concatenate([np.arange(n, dtype=np.float32)[:, None] * inv[None] for n in SEQS]).T
    out["rope"] = np.zeros((HD, 2, TOK), np.float32)
    out["rope"][:NOPE, 0] = 1.0
    out["rope"][NOPE:, 0] = np.tile(np.cos(ang), (2, 1))
    out["rope"][NOPE:, 1] = np.tile(np.sin(ang), (2, 1))
    head = np.arange(P) // CH
    t = np.arange(P)
    same = head[:, None] == head[None]
    before = (t[:, None] < t[None]) & same
    after = (t[:, None] > t[None]) & same
    eye = t[:, None] == t[None]
    out["tri_mask"] = np.ascontiguousarray(np.array([[before, before | eye], [after, after | eye]], np.float32).transpose(2, 0, 1, 3))
    level = [((t[:, None] >> l) ^ (t[None] >> l)) == 1 for l in range(LEVELS)]
    out["level_mask"] = np.ascontiguousarray(np.array(level, np.float32).transpose(1, 0, 2))
    out["ident_halves"] = np.tile(np.eye(CH, dtype=np.float32), (2, 1))
    out["head_ones"] = (head[:, None] == head[None]).astype(np.float32)


def kernel(**inputs):
    import concourse.bacc as bacc
    from concourse.bass_utils import run_bass_kernel_spmd

    nc = bacc.Bacc("TRN2", target_bir_lowering=False, num_devices=1)
    arrays = _lay_out(inputs)
    dram = {k: nc.dram_tensor(f"in_{k}", v.shape, mybir.dt.from_np(v.dtype), kind="ExternalInput").ap() for k, v in arrays.items()}
    for k, shape in INTERNAL.items():
        dram[k] = nc.dram_tensor(k, shape, INTERNAL_TYPES.get(k, F32), kind="Internal").ap()
    dram["y"] = nc.dram_tensor("y", (TOK, D), F32, kind="ExternalOutput").ap()
    encoder(nc, dram)
    r = run_bass_kernel_spmd(nc, [{f"in_{k}": v for k, v in arrays.items()}], core_ids=[0])
    y = r.results[0]["y"]
    return y[None, :SEQS[0]], y[None, SEQS[0]:]
```

```python
from contextlib import ExitStack

import numpy as np

import concourse.bass as bass
from concourse import mybir

ALU = mybir.AluOpType
ACT = mybir.ActivationFunctionType
AX = mybir.AxisListType
F32 = mybir.dt.float32
I32 = mybir.dt.int32
U32 = mybir.dt.uint32
F32R = mybir.dt.float32r

P = 128
D = 1024
DF = D // P
SEQS = (1024, 512)
TOK = sum(SEQS)
TT = TOK // P
NB = 512
NT = TOK // NB
EPS = 1e-6

COLS = {}
_n = 0
for _name, _w in (("norm1", 8), ("mu_prev", 24), ("mu_next", 24), ("b_merge", 16),
                  ("w0", 8), ("a0", 8), ("k_k", 4), ("k_a", 4), ("r_k", 4), ("gn_w", 4), ("gn_b", 4),
                  ("qa_norm", 6), ("kva_norm", 2), ("q_gain", 1), ("k_gain", 1)):
    COLS[_name] = (_n, _w)
    _n += _w
NCOLS = _n

SHIFT1, SCALE1, GATE1, SHIFT2, SCALE2, GATE2 = range(6)
N_SHIFTED = 24
N_GATES = 16


class Chain:

    def __init__(self, eng, sem, base=0, i=None, per=0):
        self.eng, self.sem, self.base, self.i, self.per, self.n = eng, sem, base, i, per, 0

    def value(self):
        v = self.base + self.n
        return v if self.i is None else self.i * self.per + v

    def __call__(self, ins):
        self.n += 1
        ins.then_inc(self.sem, 1)
        self.eng.wait_ge(self.sem, self.value())

    def end(self):
        assert self.i is None or self.n == self.per, (self.n, self.per)


def alone(eng, sem):
    eng.sem_inc(sem, 1)


class Scope:

    def __init__(self, nc, ctx):
        self.nc, self.ctx, self.sems = nc, ctx, []
        ctx.callback(self.clear)

    def clear(self):
        if self.sems:
            self.nc.clear_and_free_semaphores(self.sems)
            self.nc.all_engine_barrier()

    def sb(self, name, shape, dt=F32):
        return self.ctx.enter_context(self.nc.sbuf_tensor(name, shape, dt))

    def ps(self, name, shape, dt=F32):
        return self.ctx.enter_context(self.nc.psum_tensor(name, shape, dt))

    def sem(self, name):
        self.sems.append(self.nc.alloc_semaphore(name))
        return self.sems[-1]


def col(consts, name, k=0, n=None):
    first, width = COLS[name]
    return consts["cols"][:, first + k:first + (width if n is None else k + n)]


def split_product(nc, out, w, x, start, stop):
    nc.tensor.matmul(out, w[0], x[1], start=start, stop=False)
    nc.tensor.matmul(out, w[1], x[0], start=False, stop=False)
    return nc.tensor.matmul(out, w[0], x[0], start=False, stop=stop)


def load_constants(nc, dram, consts):
    with ExitStack() as ctx:
        s = Scope(nc, ctx)
        loaded = s.sem("constants_loaded")
        block = ctx.enter_context(nc.Block())

        @block.sync
        def _(sp):
            sp.dma_start(consts["cols"][:], dram["cols"][:, :]).then_inc(loaded, 16)
            sp.dma_start(consts["ident"][:], dram["ident"][:, :]).then_inc(loaded, 16)
            sp.dma_start(consts["ones"][:], dram["ones"][:, :]).then_inc(loaded, 16)
            sp.wait_ge(loaded, 48)


def modulation(nc, dram, consts):
    mod = consts["mod"]
    BUF = 4
    with ExitStack() as ctx:
        s = Scope(nc, ctx)
        c_rows = s.sb("c_rows", [2 * DF, P])
        c_col = s.sb("c_col", [P, 2 * DF])
        c_tanh = s.sb("c_tanh", [P, 2 * DF])
        c_silu = s.sb("c_silu", [P, DF, 2])
        w = s.sb("w_ada_tile", [P, BUF, DF, 512])
        b_ada = s.sb("b_ada_rows", [2, 6 * D])
        rows = s.sb("mod_rows_sb", [2, 6 * D])
        turned_in = s.sb("mod_rows_turned_in", [96, P])
        ps_c = s.ps("ps_c", [P, 512])
        ps_mod = s.ps("ps_mod", [2, BUF, 512])
        c_loaded, c_turned, tanh_done, silu_done, bias_loaded = (s.sem(n) for n in ("c_loaded", "c_turned", "tanh_done", "silu_done", "b_ada_loaded"))
        w_loaded = [s.sem(f"w_ada_loaded{b}") for b in range(BUF)]
        ps_full = [s.sem(f"mod_ps_full{b}") for b in range(BUF)]
        ps_free = [s.sem(f"mod_ps_free{b}") for b in range(BUF)]
        own, rows_ready, rows_turned = (s.sem(n) for n in ("mod_own", "mod_rows_ready", "mod_rows_turned"))
        stored, reloaded = s.sem("mod_stored"), s.sem("mod_reloaded")
        block = ctx.enter_context(nc.Block())
        N = 12

        @block.sync
        def _(sp):
            sp.dma_start(c_rows[:], dram["c"][:, :]).then_inc(c_loaded, 16)
            with sp.Fori(0, N // BUF) as j:
                for b in range(BUF):
                    sp.wait_ge(ps_full[b], j)
                    sp.dma_start(w[:, b], dram["w_ada"][bass.ds(j * BUF + b, 1)].rearrange("a p k m -> p (a k) m")).then_inc(w_loaded[b], 16)
            sp.wait_ge(rows_ready, 1)
            sp.dma_start(dram["mod_rows"].rearrange("(j q f) p -> q j (f p)", j=6, q=2), rows[:].rearrange("q (j x) -> q j x", j=6)).then_inc(stored, 16)
            sp.wait_ge(stored, 16)
            sp.dma_start(turned_in[:], dram["mod_rows"][:, :]).then_inc(reloaded, 16)

        @block.tensor
        def _(pe):
            pe.wait_ge(c_loaded, 16)
            nc.tensor.transpose(ps_c[:, 0:2 * DF], c_rows[:], consts["ident"][0:2 * DF, 0:2 * DF]).then_inc(c_turned, 1)
            pe.wait_ge(silu_done, 2)
            with pe.Fori(0, N // BUF) as j:
                for b in range(BUF):
                    pe.wait_ge(w_loaded[b], 16 * j + 16)
                    pe.wait_ge(ps_free[b], j)
                    for k in range(DF):
                        mm = nc.tensor.matmul(ps_mod[:, b], c_silu[:, k], w[:, b, k], start=(k == 0), stop=(k == DF - 1))
                    mm.then_inc(ps_full[b], 1)
            pe.wait_ge(reloaded, 16)
            nc.tensor.transpose(ps_c[:, 0:96], turned_in[:], consts["ident"][0:96, 0:96]).then_inc(rows_turned, 1)

        @block.scalar
        def _(act):
            for q in range(2):
                act.dma_start(b_ada[q:q + 1, :], dram["b_ada"][:, :]).then_inc(bias_loaded, 16)
            act.wait_ge(c_turned, 1)
            nc.scalar.activation(c_tanh[:], ps_c[:, 0:2 * DF], ACT.Tanh, scale=0.5).then_inc(tanh_done, 1)

        @block.vector
        def _(dve):
            dve.wait_ge(tanh_done, 1)
            nc.vector.tensor_scalar(c_col[:], ps_c[:, 0:2 * DF], 0.5, None, ALU.mult).then_inc(silu_done, 1)
            dve.wait_ge(silu_done, 1)
            nc.vector.scalar_tensor_tensor(out=c_silu[:].rearrange("p k q -> p q k"), in0=c_tanh[:].rearrange("p (q k) -> p q k", q=2), scalar=1.0,
                                           in1=c_col[:].rearrange("p (q k) -> p q k", q=2), op0=ALU.add, op1=ALU.mult).then_inc(silu_done, 1)
            dve.wait_ge(bias_loaded, 32)
            with dve.Fori(0, N // BUF) as j:
                for b in range(BUF):
                    dve.wait_ge(ps_full[b], j + 1)
                    at = bass.ds(j * (512 * BUF) + 512 * b, 512)
                    nc.vector.tensor_tensor(rows[:, at], ps_mod[:, b], b_ada[:, at], ALU.add).then_inc(ps_free[b], 1)
            for b in range(BUF):
                dve.wait_ge(ps_free[b], N // BUF)
            for part in (SCALE1, SCALE2):
                ins = nc.vector.tensor_scalar(rows[:, D * part:D * part + D], rows[:, D * part:D * part + D], 1.0, None, ALU.add)
            ins.then_inc(rows_ready, 1)
            dve.wait_ge(rows_turned, 1)
            nc.vector.tensor_copy(mod[:].rearrange("p j q f -> p (j q f)"), ps_c[:, 0:96]).then_inc(own, 1)
            dve.wait_ge(own, 1)
            for q in range(2):
                ins = nc.vector.tensor_tensor(consts["scale1"][:, q], mod[:, SCALE1, q], col(consts, "norm1"), ALU.mult)
            ins.then_inc(own, 1)
            dve.wait_ge(own, 2)


def norm_and_turn(nc, dram, consts, h_hi, h_lo):
    with ExitStack() as ctx:
        s = Scope(nc, ctx)
        x = s.sb("x_tile", [P, 2, D])
        sq = s.sb("x_square", [P, 2, D])
        ss = s.sb("x_ss", [P, 2, 2])
        xn = s.sb("x_normed", [P, 2, D])
        ps = s.ps("ps_turn", [P, 2, 2, 512])
        loaded = [s.sem(f"x_loaded{b}") for b in range(2)]
        summed = [s.sem(f"x_summed{b}") for b in range(2)]
        normed = [s.sem(f"x_normed{b}") for b in range(2)]
        turned = [s.sem(f"x_turned{b}") for b in range(2)]
        act_out = [s.sem(f"h_act{b}") for b in range(2)]
        dve_out = [s.sem(f"h_dve{b}") for b in range(2)]
        h = s.sb("h_tile", [P, 2, DF, P])
        hi_ready = [s.sem(f"h_hi{b}") for b in range(2)]
        lo_ready = [s.sem(f"h_lo{b}") for b in range(2)]
        own = s.sem("norm_own")
        unread = s.sem("norm_unread")
        rms_in = [s.sem(f"rms_in{b}") for b in range(2)]
        rms_ready = [s.sem(f"rms_ready{b}") for b in range(2)]
        block = ctx.enter_context(nc.Block())
        runs = ((0, 0, SEQS[0] // P), (1, SEQS[0] // P, SEQS[1] // P))

        @block.sync
        def _(sp):
            with sp.Fori(0, TT // 2) as i:
                for b in range(2):
                    sp.wait_ge(normed[b], i)
                    sp.dma_start(x[:, b], dram["x"][bass.ds(i * 2 * P + b * P, P), :]).then_inc(loaded[b], 16)

        @block.scalar
        def _(act):
            for q, t0, n in runs:
                with act.Fori(t0 // 2, (t0 + n) // 2) as i:
                    for b in range(2):
                        act.wait_ge(loaded[b], 16 * i + 16)
                        nc.scalar.activation(sq[:, b], x[:, b], ACT.Square, accum_out=ss[:, b, 0:1]).then_inc(summed[b], 1)
                    for b in range(2):
                        act.wait_ge(rms_in[b], i + 1)
                        nc.scalar.activation(ss[:, b, 1:2], ss[:, b, 0:1], ACT.Sqrt).then_inc(rms_ready[b], 1)
                    for b in range(2):
                        act.wait_ge(turned[b], i + 1)
                        act.wait_ge(lo_ready[b], i)
                        for f in range(4):
                            ins = nc.scalar.activation(h[:, b, f], ps[:, b, 0, P * f:P * f + P],
                                                       ACT.Identity, bias=consts["mod"][:, SHIFT1, q, f:f + 1],
                                                       scale=consts["scale1"][:, q, f:f + 1])
                        ins.then_inc(act_out[b], 1)
                    for b in range(2):
                        act.wait_ge(act_out[b], i + 1)
                        act.wait_ge(dve_out[b], i + 1)
                        alone(act, unread)
                        nc.scalar.copy(h_hi[:, :, bass.ds(i * 2 * P + b * P, P)], h[:, b]).then_inc(hi_ready[b], 1)

        @block.vector
        def _(dve):
            for q, t0, n in runs:
                with dve.Fori(t0 // 2, (t0 + n) // 2) as i:
                    step = Chain(dve, own, 0, i, 2)
                    for b in range(2):
                        dve.wait_ge(summed[b], i + 1)
                        nc.vector.tensor_scalar(ss[:, b, 0:1], ss[:, b, 0:1], 1.0 / D, EPS, ALU.mult, ALU.add).then_inc(rms_in[b], 1)
                    for b in range(2):
                        dve.wait_ge(rms_ready[b], i + 1)
                        step(nc.vector.reciprocal(ss[:, b, 1:2], ss[:, b, 1:2]))
                        dve.wait_ge(turned[b], i)
                        nc.vector.tensor_scalar(xn[:, b], x[:, b], ss[:, b, 1:2], None, ALU.mult).then_inc(normed[b], 1)
                    step.end()
                    for b in range(2):
                        dve.wait_ge(turned[b], i + 1)
                        dve.wait_ge(lo_ready[b], i)
                        for f in range(4, 8):
                            ins = nc.vector.tensor_scalar(h[:, b, f], ps[:, b, 1, P * (f - 4):P * (f - 3)],
                                                          consts["scale1"][:, q, f:f + 1], consts["mod"][:, SHIFT1, q, f:f + 1],
                                                          ALU.mult, ALU.add)
                        ins.then_inc(dve_out[b], 1)
                    for b in range(2):
                        dve.wait_ge(hi_ready[b], i + 1)
                        at = bass.ds(i * 2 * P + b * P, P)
                        nc.vector.tensor_tensor(h_lo[:, :, at], h[:, b], h_hi[:, :, at].bitcast(F32), ALU.subtract).then_inc(lo_ready[b], 1)

        @block.tensor
        def _(pe):
            with pe.Fori(0, TT // 2) as i:
                for b in range(2):
                    pe.wait_ge(normed[b], i + 1)
                    pe.wait_ge(act_out[b], i)
                    pe.wait_ge(dve_out[b], i)
                    for f in range(DF):
                        mm = nc.tensor.transpose(ps[:, b, f // 4, P * (f % 4):P * (f % 4) + P], xn[:, b, P * f:P * f + P], consts["ident"][:])
                    mm.then_inc(turned[b], 1)


def project_in(nc, dram, consts, h_hi, h_lo):
    L, R = SEQS
    W = TOK + 1
    starts = (1, 513, L + 2)
    with ExitStack() as ctx:
        s = Scope(nc, ctx)
        w = s.sb("w_in_tile", [P, 2, DF, P])
        w_hi = s.sb("w_in_high", [P, 2, DF, P], F32R)
        w_lo = s.sb("w_in_low", [P, 2, DF, P], F32R)
        hi_ready = [s.sem(f"w_in_hi{b}") for b in range(2)]
        w_split = [s.sem(f"w_in_split{b}") for b in range(2)]
        row = s.sb("p_row", [P, 2, TOK + 3])
        mix = s.sb("p_mixed", [P, 2, W])
        mu_c = s.sb("mu_centre", [P, N_SHIFTED])
        ps = s.ps("ps_in", [P, 2, NT, NB])
        w_loaded = [s.sem(f"w_in_loaded{b}") for b in range(2)]
        full = [[s.sem(f"in_full{b}{n}") for n in range(NT)] for b in range(2)]
        copied = [[s.sem(f"in_copied{b}{n}") for n in range(NT)] for b in range(2)]
        mixed = [s.sem(f"in_mixed{b}") for b in range(2)]
        stored = [s.sem(f"in_stored{b}") for b in range(2)]
        ready = s.sem("in_ready")
        bias_now = s.sb("bias_now", [P, 2])
        bias_ready = s.sem("bias_ready")
        own = s.sem("in_own")
        unread, unread_pool = s.sem("in_unread"), s.sem("in_unread_pool")
        block = ctx.enter_context(nc.Block())
        HS, HG = N_SHIFTED // 2, N_GATES // 2

        @block.sync
        def _(sp):
            with sp.Fori(0, HS + HG) as i:
                for b in range(2):
                    sp.wait_ge(w_split[b], i)
                    sp.dma_start(w[:, b], dram["w_in"][bass.ds(2 * i + b, 1)].rearrange("a p k m -> p (a k) m")).then_inc(w_loaded[b], 16)

        @block.gpsimd
        def _(pool):
            with pool.Fori(0, HS + HG) as i:
                for b in range(2):
                    pool.wait_ge(w_loaded[b], 16 * i + 16)
                    pool.wait_ge(full[b][NT - 1], i)
                    alone(pool, unread_pool)
                    nc.gpsimd.tensor_copy(w_hi[:, b], w[:, b]).then_inc(hi_ready[b], 1)
                    pool.wait_ge(hi_ready[b], i + 1)
                    nc.gpsimd.tensor_tensor(w_lo[:, b], w[:, b], w_hi[:, b].bitcast(F32), ALU.subtract).then_inc(w_split[b], 1)

        @block.tensor
        def _(pe):
            with pe.Fori(0, HS + HG) as i:
                for b in range(2):
                    pe.wait_ge(w_split[b], i + 1)
                    for n in range(NT):
                        pe.wait_ge(copied[b][n], i)
                        for k in range(DF):
                            at = slice(NB * n, NB * n + NB)
                            mm = split_product(nc, ps[:, b, n], (w_hi[:, b, k], w_lo[:, b, k]), (h_hi[:, k, at], h_lo[:, k, at]),
                                               start=(k == 0), stop=(k == DF - 1))
                        mm.then_inc(full[b][n], 1)

        @block.scalar
        def _(act):
            act.wait_ge(ready, 1)
            with act.Fori(0, HS) as i:
                for b in range(2):
                    act.wait_ge(mixed[b], i)
                    for n in range(NT):
                        act.wait_ge(full[b][n], i + 1)
                        nc.scalar.copy(row[:, b, starts[n]:starts[n] + NB], ps[:, b, n]).then_inc(copied[b][n], 1)
                    act.wait_ge(mixed[b], i + 1)
                    act.dma_start(dram["p_t"][bass.ds(2 * i + b, 1), :, 0:L].rearrange("a p t -> (a p) t"), mix[:, b, 0:L]).then_inc(stored[b], 16)
                    act.dma_start(dram["p_t"][bass.ds(2 * i + b, 1), :, L:TOK].rearrange("a p t -> (a p) t"), mix[:, b, L + 1:W]).then_inc(stored[b], 16)
            with act.Fori(HS, HS + HG) as i:
                for b in range(2):
                    act.wait_ge(mixed[b], i)
                    alone(act, unread)
                    nc.scalar.copy(bias_now[:, b:b + 1], consts["half_merge"][:, bass.ds(2 * i + (b - N_SHIFTED), 1)]).then_inc(bias_ready, 1)
                    act.wait_ge(bias_ready, 2 * i + (b + 1 - 2 * HS))
                    for n in range(NT):
                        act.wait_ge(full[b][n], i + 1)
                        nc.scalar.activation(row[:, b, NB * n:NB * n + NB], ps[:, b, n], ACT.Tanh, bias=bias_now[:, b:b + 1], scale=0.5).then_inc(copied[b][n], 1)
                    act.wait_ge(mixed[b], i + 1)
                    act.dma_start(dram["gates"][bass.ds(2 * i + (b - N_SHIFTED), 1)].rearrange("a p t -> (a p) t"), mix[:, b, 0:TOK]).then_inc(stored[b], 16)
            for b in range(2):
                act.wait_ge(stored[b], 16 * (2 * HS + HG))

        @block.vector
        def _(dve):
            prev, nxt = COLS["mu_prev"][0], COLS["mu_next"][0]
            start = Chain(dve, own)
            start(nc.vector.tensor_tensor(mu_c[:], col(consts, "mu_prev"), col(consts, "mu_next"), ALU.add))
            start(nc.vector.tensor_scalar(mu_c[:], mu_c[:], -1.0, 1.0, ALU.mult, ALU.add))
            start(nc.vector.tensor_scalar(consts["half_merge"][:], col(consts, "b_merge"), 0.5, None, ALU.mult))
            start(nc.vector.memset(row[:], 0.0))
            start(nc.vector.memset(mix[:], 0.0))
            dve.sem_inc(ready, 1)
            with dve.Fori(0, HS) as i:
                step = Chain(dve, own, start.n, i, 4)
                for b in range(2):
                    c = 2 * i + b
                    for n in range(NT):
                        dve.wait_ge(copied[b][n], i + 1)
                    dve.wait_ge(stored[b], 32 * i)
                    step(nc.vector.tensor_scalar(mix[:, b], row[:, b, 1:1 + W], mu_c[:, bass.ds(c, 1)], None, ALU.mult))
                    step(nc.vector.scalar_tensor_tensor(out=mix[:, b], in0=row[:, b, 0:W], scalar=consts["cols"][:, bass.ds(c + prev, 1)],
                                                        in1=mix[:, b], op0=ALU.mult, op1=ALU.add))
                    nc.vector.scalar_tensor_tensor(out=mix[:, b], in0=row[:, b, 2:2 + W], scalar=consts["cols"][:, bass.ds(c + nxt, 1)],
                                                   in1=mix[:, b], op0=ALU.mult, op1=ALU.add).then_inc(mixed[b], 1)
                step.end()
            with dve.Fori(HS, HS + HG) as i:
                for b in range(2):
                    for n in range(NT):
                        dve.wait_ge(copied[b][n], i + 1)
                    dve.wait_ge(stored[b], 16 * i + 16 * HS)
                    nc.vector.tensor_scalar(mix[:, b, 0:TOK], row[:, b, 0:TOK], 0.5, 0.5, ALU.mult, ALU.add).then_inc(mixed[b], 1)


CH = 64
RF = 4
RT, KT_, VT, WD, AD, GD = 0, 4, 8, 12, 13, 14
PB = 256
DECAY = float(np.exp(-0.5))


def rwkv_operands(nc, dram, consts):
    with ExitStack() as ctx:
        s = Scope(nc, ctx)
        up_w = s.sb("decay_up", [P, RF * P])
        up_a = s.sb("iclr_up", [P, RF * P])
        reset = s.sb("chunk_reset", [P, RF * PB])
        head_ones = s.sb("head_ones", [P, P])
        half_w0 = s.sb("half_w0", [P, 8])
        half_a0 = s.sb("half_a0", [P, 8])
        pin = s.sb("prep_in", [P, 2, 14, PB])
        W = [P, RF, PB]
        t_wd = s.sb("tanh_wd", [P, PB])
        kk_raw, sq, norm, kk, kka, k1 = (s.sb(n, W) for n in ("kk_raw", "kk_square", "kk_norm", "kk", "k_times_ka", "k_rest"))
        th_w, th_a, cum, e_in, e_ex = (s.sb(n, W) for n in ("tanh_w", "tanh_a", "cum_decay", "e_in", "e_ex"))
        p_in, p_ex, p_inv, kd, ba = (s.sb(n, W) for n in ("p_in", "p_ex", "p_inv", "k_d", "kk_a"))
        outs = s.sb("wkv_out", [P, 2, 4, RF, PB])
        ps_n = s.ps("ps_norm", [P, RF, PB])
        ps_w = s.ps("ps_w", [P, RF, PB])
        ps_a = s.ps("ps_a", [P, RF, PB])
        names = ("consts_in", "halves", "kk_raw_ready", "twd_ready", "sq_ready", "norm_summed", "sqrt_ready", "kk_ready",
                 "w_full", "a_full", "thw_ready", "tha_ready", "lw_used", "e_ready", "exp_ready", "pool_out", "dve_out",
                 "own", "pool_own", "kd_parts", "tha_used", "ends_ready", "norm_used")
        m = {n: s.sem("prep_" + n) for n in names}
        loaded = [s.sem(f"prep_loaded{b}") for b in range(2)]
        in_used = [s.sem(f"prep_in_used{b}") for b in range(2)]
        stored = s.sem("prep_stored")
        block = ctx.enter_context(nc.Block())
        NI = TOK // PB // 2

        def bc(name, k=0):
            return col(consts, name, k, RF).unsqueeze(2).to_broadcast(W)

        @block.sync
        def _(sp):
            sp.dma_start(up_w[:], dram["decay_up"][:, :]).then_inc(m["consts_in"], 16)
            sp.dma_start(up_a[:], dram["iclr_up"][:, :]).then_inc(m["consts_in"], 16)
            sp.dma_start(reset[:], dram["chunk_reset"][:, :]).then_inc(m["consts_in"], 16)
            sp.dma_start(head_ones[:], dram["head_ones"][:, :]).then_inc(m["consts_in"], 16)

            def load(t, b):
                sp.dma_start(pin[:, b], dram["p_t"][0:14, :, bass.ds(t * PB, PB)].rearrange("m p t -> p m t")).then_inc(loaded[b], 16)

            def store(t):
                for d in range(2):
                    sp.wait_ge(m["pool_out"], 2 * t + d + 1)
                    sp.wait_ge(m["dve_out"], 2 * t + d + 1)
                    for j in range(PB // P):
                        sp.dma_start(dram["wkv_in"][d, bass.ds(t * (PB // P) + j, 1)].rearrange("a p x t -> p (a x) t"),
                                     outs[:, d, :, :, P * j:P * j + P].rearrange("p q f t -> p (q f) t")).then_inc(stored, 16)

            for b in range(2):
                load(b, b)
            with sp.Fori(0, NI - 1) as i:
                for b in range(2):
                    store(2 * i + b)
                    sp.wait_ge(in_used[b], i + 1)
                    load(2 * i + (b + 2), b)
            for b in range(2):
                store(2 * NI - 2 + b)
            sp.wait_ge(stored, 64 * 2 * NI)

        @block.tensor
        def _(pe):
            pe.wait_ge(m["consts_in"], 64)
            with pe.Fori(0, NI) as i:
                for b in range(2):
                    t = 2 * i + b
                    pe.wait_ge(m["sq_ready"], t + 1)
                    pe.wait_ge(m["norm_used"], t)
                    for f in range(RF):
                        mm = nc.tensor.matmul(ps_n[:, f], head_ones[:], sq[:, f], start=True, stop=True)
                    mm.then_inc(m["norm_summed"], 1)
                    pe.wait_ge(m["twd_ready"], t + 1)
                    for d in range(2):
                        h = slice(64 * d, 64 * d + 64)
                        pe.wait_ge(m["thw_ready"], 2 * t + d)
                        for f in range(RF):
                            mm = nc.tensor.matmul(ps_w[:, f], up_w[h, P * f:P * f + P], t_wd[h], start=True, stop=True)
                        mm.then_inc(m["w_full"], 1)
                        pe.wait_ge(m["tha_ready"], 2 * t + d)
                        for f in range(RF):
                            mm = nc.tensor.matmul(ps_a[:, f], up_a[h, P * f:P * f + P], pin[h, b, AD], start=True, stop=True)
                        mm.then_inc(m["a_full"], 1)

        @block.scalar
        def _(act):
            act.wait_ge(m["halves"], 2)
            with act.Fori(0, NI) as i:
                for b in range(2):
                    t = 2 * i + b
                    act.wait_ge(m["kk_raw_ready"], t + 1)
                    act.wait_ge(m["norm_summed"], t)
                    nc.scalar.activation(sq[:], kk_raw[:], ACT.Square).then_inc(m["sq_ready"], 1)
                    act.wait_ge(m["norm_summed"], t + 1)
                    act.wait_ge(m["kk_ready"], t)
                    for h in range(2):
                        ins = nc.scalar.activation(norm[:, 2 * h:2 * h + 2], ps_n[:, 2 * h:2 * h + 2], ACT.Sqrt)
                    ins.then_inc(m["sqrt_ready"], 1)
                    act.wait_ge(loaded[b], 16 * i + 16)
                    act.wait_ge(m["w_full"], 2 * t)
                    nc.scalar.activation(t_wd[:], pin[:, b, WD], ACT.Tanh).then_inc(m["twd_ready"], 1)
                    for d in range(2):
                        act.wait_ge(m["w_full"], 2 * t + d + 1)
                        act.wait_ge(m["lw_used"], 2 * t + d)
                        for f in range(RF):
                            ins = nc.scalar.activation(th_w[:, f], ps_w[:, f], ACT.Tanh, bias=half_w0[:, RF * d + f:RF * d + f + 1], scale=0.5)
                        ins.then_inc(m["thw_ready"], 1)
                        act.wait_ge(m["a_full"], 2 * t + d + 1)
                        act.wait_ge(m["tha_used"], 2 * t + d)
                        for f in range(RF):
                            ins = nc.scalar.activation(th_a[:, f], ps_a[:, f], ACT.Tanh, bias=half_a0[:, RF * d + f:RF * d + f + 1], scale=0.5)
                        ins.then_inc(m["tha_ready"], 1)
                        act.wait_ge(m["e_ready"], 2 * t + d + 1)
                        act.wait_ge(m["pool_out"], 2 * t + d)
                        act.wait_ge(m["dve_out"], 2 * t + d)
                        act.wait_ge(m["ends_ready"], 2 * t + d)
                        nc.scalar.activation(p_in[:], e_in[:], ACT.Exp).then_inc(m["exp_ready"], 1)
                        nc.scalar.activation(p_ex[:], e_ex[:], ACT.Exp).then_inc(m["exp_ready"], 1)
                        nc.scalar.activation(p_inv[:], e_in[:], ACT.Exp, scale=-1.0).then_inc(m["exp_ready"], 1)

        @block.gpsimd
        def _(pool):
            with pool.Fori(0, NI) as i:
                step = Chain(pool, m["pool_own"], 0, i, 2)
                for b in range(2):
                    t = 2 * i + b
                    r, k = pin[:, b, RT:RT + 4], pin[:, b, KT_:KT_ + 4]
                    pool.wait_ge(loaded[b], 16 * i + 16)
                    pool.wait_ge(m["kk_ready"], t)
                    nc.gpsimd.tensor_tensor(kk_raw[:], k, bc("k_k"), ALU.mult).then_inc(m["kk_raw_ready"], 1)
                    pool.wait_ge(m["dve_out"], 2 * t)
                    step(nc.gpsimd.tensor_tensor(kka[:], k, bc("k_a"), ALU.mult))
                    nc.gpsimd.tensor_tensor(k1[:], k, kka[:], ALU.subtract).then_inc(m["kd_parts"], 1)
                    pool.wait_ge(m["kk_ready"], t + 1)
                    for d in range(2):
                        pool.wait_ge(m["exp_ready"], 6 * t + 3 * d + 3)
                        pool.wait_ge(stored, 64 * t)
                        nc.gpsimd.tensor_tensor(outs[:, d, 1], r, p_in[:], ALU.mult)
                        nc.gpsimd.tensor_tensor(outs[:, d, 0], kk[:], p_ex[:], ALU.mult).then_inc(m["pool_out"], 1)
                step.end()

        @block.vector
        def _(dve):
            dve.wait_ge(m["consts_in"], 64)
            nc.vector.tensor_scalar(half_w0[:], col(consts, "w0"), 0.5, None, ALU.mult).then_inc(m["halves"], 1)
            nc.vector.tensor_scalar(half_a0[:], col(consts, "a0"), 0.5, None, ALU.mult).then_inc(m["halves"], 1)
            with dve.Fori(0, NI) as i:
                step = Chain(dve, m["own"], 0, i, 2 * 16)
                for b in range(2):
                    t = 2 * i + b
                    dve.wait_ge(m["sqrt_ready"], t + 1)
                    dve.sem_inc(m["norm_used"], 1)
                    step(nc.vector.tensor_scalar(norm[:], norm[:], 1e-12, None, ALU.max))
                    step(nc.vector.reciprocal(norm[:], norm[:]))
                    dve.wait_ge(m["pool_out"], 2 * t)
                    step(nc.vector.tensor_tensor(kk[:], kk_raw[:], norm[:], ALU.mult))
                    dve.sem_inc(m["kk_ready"], 1)
                    dve.wait_ge(m["kd_parts"], t + 1)
                    for d in range(2):
                        dve.wait_ge(m["thw_ready"], 2 * t + d + 1)
                        step(nc.vector.tensor_scalar(th_w[:], th_w[:], -0.5 * DECAY, -0.5 * DECAY, ALU.mult, ALU.add))
                        flat = lambda x: x[:].rearrange("p f t -> p (f t)")
                        chunks = lambda x: x[:].rearrange("p f (c t) -> p (f c) t", t=CH)
                        dve.wait_ge(m["exp_ready"], 6 * t + 3 * d)
                        if d == 0:
                            step(nc.vector.tensor_tensor_scan(flat(e_in), reset[:], flat(th_w), 0.0, ALU.mult, ALU.add))
                            step(nc.vector.tensor_tensor(e_ex[:], e_in[:], th_w[:], ALU.subtract))
                        else:
                            step(nc.vector.tensor_tensor_scan(flat(cum), reset[:], flat(th_w), 0.0, ALU.mult, ALU.add))
                            total = chunks(cum)[:, :, CH - 1:CH].to_broadcast([P, RF * PB // CH, CH])
                            step(nc.vector.tensor_tensor(chunks(e_ex), total, chunks(cum), ALU.subtract))
                            step(nc.vector.tensor_tensor(e_in[:], e_ex[:], th_w[:], ALU.add))
                        dve.sem_inc(m["e_ready"], 1)
                        dve.sem_inc(m["lw_used"], 1)
                        dve.wait_ge(m["tha_ready"], 2 * t + d + 1)
                        dve.wait_ge(m["kk_ready"], t + 1)
                        step(nc.vector.tensor_scalar(th_a[:], th_a[:], 0.5, 0.5, ALU.mult, ALU.add))
                        nc.vector.tensor_tensor(ba[:], kk[:], th_a[:], ALU.mult)
                        step(nc.vector.tensor_tensor(kd[:], kka[:], th_a[:], ALU.mult))
                        dve.sem_inc(m["tha_used"], 1)
                        step(nc.vector.tensor_tensor(kd[:], kd[:], k1[:], ALU.add))
                        dve.wait_ge(m["exp_ready"], 6 * t + 3 * d + 3)
                        dve.wait_ge(stored, 64 * t)
                        end = (CH - 1) if d == 0 else 0
                        nc.vector.tensor_copy(consts["p_end"][:, d, :, bass.ds(t * (PB // CH), PB // CH)],
                                              p_in[:].rearrange("p f (c t) -> p f c t", t=CH)[:, :, :, end]).then_inc(m["ends_ready"], 1)
                        nc.vector.tensor_tensor(outs[:, d, 2], ba[:], p_inv[:], ALU.mult)
                        nc.vector.tensor_tensor(outs[:, d, 3], kd[:], p_inv[:], ALU.mult).then_inc(m["dve_out"], 1)
                    dve.wait_ge(m["pool_out"], 2 * t + 2)
                    dve.sem_inc(in_used[b], 1)
                step.end()


HEADS = 8
LEVELS = 6
RING = 3


def wkv_scan(nc, dram, consts):
    with ExitStack() as ctx:
        s = Scope(nc, ctx)
        H = HEADS
        mask = s.sb("tri_mask", [P, 2, 2, CH])
        lmask = s.sb("level_mask", [P, LEVELS, P])
        ident2 = s.sb("ident_halves", [P, CH])
        pair = lambda name, shape: s.sb("sb_" + name, [P, 2] + shape)
        ops = pair("wkv_ops", [4, RF, P])
        by_head = pair("wkv_by_head", [2, 2, RF, P])
        v = pair("wkv_v", [RF, P])
        hats = pair("wkv_hats", [2, RF, P])
        rho = pair("wkv_rho", [RF, P])
        lb = pair("wkv_lb", [H, 2, P])
        mk = pair("wkv_mk", [H, 2, P])
        lev = pair("wkv_levels", [RING, H, P])
        x, xt, z = (pair("wkv_" + n, [H, P]) for n in ("x", "xt", "z"))
        v_tok = pair("wkv_v_tok", [RF, P])
        hat_tok = pair("wkv_hat_tok", [2, RF, P])
        am = pair("wkv_am", [H, 2, CH])
        wg = pair("wkv_wg", [H, 2, CH])
        diag = pair("wkv_diag", [2, RF, CH])
        phi = pair("wkv_phi", [2, RF, CH])
        psi = pair("wkv_psi", [2, RF, CH])
        r = pair("wkv_r", [RF, P])
        y0 = pair("wkv_y0", [RF, P])
        y = pair("wkv_y", [RF, P])
        state = pair("wkv_state", [RF, CH])
        ps = [s.ps(f"ps_wkv{d}", [P, 4, 512]) for d in range(2)]
        names = ("in_loaded", "hat_ready", "ops_used", "turned", "tok_copied", "beta_full", "beta_masked", "kappa_full", "kappa_masked",
                 "lev_ready", "xt1_ready", "x1_ready", "z_full", "z_ready", "xz_full", "x_ready",
                 "xt_ready", "last_full", "inv_ready", "mv_full", "mv_ready", "wg_full", "wg_ready", "trans_full", "diag_ready",
                 "phi_ready", "psi_ready", "bw_full", "r_ready", "y0_full", "y0_ready", "ys_full", "s_full", "s_ready", "y_ready",
                 "y_stored")
        m = {n: [s.sem(f"wkv_{n}{d}") for d in range(2)] for n in names}
        consts_in = s.sem("wkv_consts_in")
        unread = s.sem("wkv_unread_pool")
        unread_pe = s.sem("wkv_unread_pe")
        zeroed = s.sem("wkv_zeroed")
        padded = s.sem("wkv_padded")
        block = ctx.enter_context(nc.Block())
        tiles = (SEQS[0] // P, SEQS[1] // P)
        runs = ((0, tiles[0]), (tiles[0], tiles[0] + tiles[1]))

        def where(i, d, run):
            return i if d == 0 else i * -1 + (run[0] + run[1] - 1)

        def hh(g, f):
            return g * RF + f

        def half(g):
            return slice(64 * g, 64 * g + 64)

        @block.sync
        def _(sp):
            sp.dma_start(mask[:], dram["tri_mask"][:, :, :, :]).then_inc(consts_in, 16)
            sp.dma_start(lmask[:], dram["level_mask"][:, :, :]).then_inc(consts_in, 16)
            sp.dma_start(ident2[:], dram["ident_halves"][:, :]).then_inc(consts_in, 16)
            sp.wait_ge(padded, 3)
            for run in runs:
                with sp.Fori(*run) as i:
                    for d in range(2):
                        n = where(i, d, run)
                        sp.wait_ge(m["ops_used"][d], i)
                        sp.wait_ge(m["kappa_full"][d], i)
                        sp.dma_start(ops[:, d].rearrange("p q f t -> p (q f) t"),
                                     dram["wkv_in"][d, bass.ds(n, 1)].rearrange("a p x t -> p (a x) t")).then_inc(m["in_loaded"][d], 16)
                        for g in range(2):
                            sp.dma_start(by_head[half(g), d, g].rearrange("p q f t -> p (q f) t"),
                                         dram["wkv_in"][d, bass.ds(n, 1), half(g), 0:2 * RF].rearrange("a p x t -> p (a x) t")).then_inc(m["in_loaded"][d], 16)
                        sp.dma_start(v[:, d], dram["p_t"][VT:VT + 4, :, bass.ds(n * P, P)].rearrange("f p t -> p f t")).then_inc(m["in_loaded"][d], 16)

        @block.gpsimd
        def _(pool):
            for part in (by_head, lb, mk):
                nc.gpsimd.memset(part[:], 0.0).then_inc(padded, 1)
            pool.wait_ge(consts_in, 48)
            for run in runs:
                with pool.Fori(*run) as i:
                    for d in range(2):
                        n = where(i, d, run)
                        end = consts["p_end"][:, d, :, bass.ds(n * 2, 2)]
                        pool.wait_ge(m["in_loaded"][d], 64 * i + 64)
                        pool.wait_ge(m["turned"][d], 4 * i)
                        for q in range(2):
                            for c in range(2):
                                ins = nc.gpsimd.tensor_tensor(hats[:, d, q, :, CH * c:CH * c + CH], ops[:, d, 2 + q, :, CH * c:CH * c + CH],
                                                              end[:, :, c:c + 1].to_broadcast([P, RF, CH]), ALU.mult)
                        ins.then_inc(m["hat_ready"][d], 1)
                        pool.wait_ge(m["r_ready"][d], i)
                        alone(pool, unread)
                        nc.gpsimd.tensor_copy(rho[:, d], ops[:, d, 1]).then_inc(m["ops_used"][d], 1)
                        pool.wait_ge(m["phi_ready"][d], i)
                        alone(pool, unread)
                        for c in range(2):
                            ins = nc.gpsimd.tensor_tensor(diag[:, d, c], ident2[:].unsqueeze(1).to_broadcast([P, RF, CH]),
                                                          end[:, :, c:c + 1].to_broadcast([P, RF, CH]), ALU.mult)
                        ins.then_inc(m["diag_ready"][d], 1)
                    for l in range(LEVELS):
                        for d in range(2):
                            if l == 0:
                                pool.wait_ge(m["beta_masked"][d], i + 1)
                                pool.wait_ge(m["z_full"][d], 5 * i)
                            elif l == RING:
                                pool.wait_ge(m["xt1_ready"][d], i + 1)
                            elif l > RING:
                                pool.wait_ge(m["z_full"][d], 5 * i + l - RING)
                            nc.gpsimd.tensor_tensor(lev[:, d, l % RING], lb[:, d, :, 0], lmask[:, l].unsqueeze(1).to_broadcast([P, H, P]),
                                                    ALU.mult).then_inc(m["lev_ready"][d], 1)

        @block.tensor
        def _(pe):
            ident = consts["ident"][:]
            for run in runs:
                pe.wait_ge(zeroed, 1 + (run[0] > 0))
                with pe.Fori(*run) as i:
                    for d in range(2):
                        pe.wait_ge(m["in_loaded"][d], 64 * i + 64)
                        pe.wait_ge(m["hat_ready"][d], i + 1)
                        pe.wait_ge(m["y_ready"][d], i)
                        pe.wait_ge(m["s_ready"][d], 4 * i)
                        for q, src in enumerate((ops[:, d, 0], v[:, d], hats[:, d, 0], hats[:, d, 1])):
                            for f in range(RF):
                                mm = nc.tensor.transpose(ps[d][:, q, P * f:P * f + P], src[:, f], ident)
                            mm.then_inc(m["turned"][d], 1)
                    for q, (full, copied) in enumerate((("beta_full", 2), ("kappa_full", 4))):
                        for d in range(2):
                            pe.wait_ge(m["tok_copied"][d], 4 * i + copied)
                            alone(pe, unread_pe)
                            for f in range(RF):
                                for g in range(2):
                                    for c in range(2):
                                        out = ps[d][half(c), 2 * q + g, P * f:P * f + P].rearrange("p (a t) -> p a t", a=2)
                                        mm = nc.tensor.matmul(out, ops[:, d, 2 + q, f, half(c)], by_head[:, d, g, :, f, half(c)], start=True, stop=True)
                            mm.then_inc(m[full][d], 1)
                    for d in range(2):
                        pe.wait_ge(m["kappa_masked"][d], i + 1)
                        for g in range(2):
                            for f in range(RF):
                                mm = nc.tensor.matmul(ps[d][:, 2, CH * hh(g, f):CH * hh(g, f) + CH], mk[:, d, hh(g, f), 0],
                                                      v_tok[:, d, f, half(g)], start=True, stop=True)
                        mm.then_inc(m["mv_full"][d], 1)
                    def over_heads(out, lhs, rhs):
                        for h in range(H):
                            mm = nc.tensor.matmul(out[:, h // 4, P * (h % 4):P * (h % 4) + P], lhs[:, h], rhs[:, h], start=True, stop=True)
                        return mm

                    for l in range(1, LEVELS):
                        last = l == LEVELS - 1
                        for d in range(2):
                            pe.wait_ge(m["lev_ready"][d], LEVELS * i + l + 1)
                            if l == 1:
                                pe.wait_ge(m["x1_ready"][d], i + 1)
                            else:
                                pe.wait_ge(m["x_ready"][d], 4 * i + l - 1)
                            over_heads(ps[d], lev[:, d, l % RING], x[:, d]).then_inc(m["z_full"][d], 1)
                        for d in range(2):
                            pe.wait_ge(m["z_ready"][d], 5 * i + l)
                            if l == 1:
                                pe.wait_ge(m["mv_ready"][d], i + 1)
                            else:
                                pe.wait_ge(m["xt_ready"][d], 4 * i + l - 1)
                            if not last:
                                over_heads(ps[d][:, 2:4], xt[:, d], z[:, d]).then_inc(m["xz_full"][d], 1)
                            else:
                                over_heads(ps[d][:, 2:4], z[:, d], xt[:, d]).then_inc(m["last_full"][d], 1)
                    for d in range(2):
                        pe.wait_ge(m["inv_ready"][d], i + 1)
                        over_heads(ps[d], xt[:, d], am[:, d].rearrange("p h a k -> p h (a k)")).then_inc(m["wg_full"][d], 1)
                    for d in range(2):
                        pe.wait_ge(m["wg_ready"][d], i + 1)
                        alone(pe, unread_pe)
                        for g in range(2):
                            for f in range(RF):
                                for c in range(2):
                                    t = half(c)
                                    at = lambda a: ps[d][half(g), 2 + c, P * f + CH * a:P * f + CH * a + CH]
                                    nc.tensor.matmul(at(0), wg[t, d, hh(g, f), 0], hat_tok[t, d, 0, f, half(g)], start=True, stop=True)
                                for c in range(2):
                                    t = half(c)
                                    at = lambda a: ps[d][half(g), 2 + c, P * f + CH * a:P * f + CH * a + CH]
                                    nc.tensor.matmul(at(1), hat_tok[t, d, 0, f, half(g)], wg[t, d, hh(g, f), 1], start=True, stop=False)
                                    mm = nc.tensor.matmul(at(1), hat_tok[t, d, 1, f, half(g)], v_tok[t, d, f, half(g)], start=False, stop=True)
                        mm.then_inc(m["trans_full"][d], 1)
                    for d in range(2):
                        for f in range(RF):
                            for g in range(2):
                                mm = nc.tensor.matmul(ps[d][half(g), 0, P * f:P * f + P], wg[:, d, hh(g, f), 0], lb[:, d, hh(g, f), 1],
                                                      start=True, stop=True)
                        mm.then_inc(m["bw_full"][d], 1)
                        for f in range(RF):
                            for g in range(2):
                                out = ps[d][half(g), 1, P * f:P * f + P]
                                nc.tensor.matmul(out, wg[:, d, hh(g, f), 1], lb[:, d, hh(g, f), 1], start=True, stop=False)
                                mm = nc.tensor.matmul(out, v_tok[:, d, f, half(g)], mk[:, d, hh(g, f), 1], start=False, stop=True)
                        mm.then_inc(m["y0_full"][d], 1)
                    for k in range(2):
                        for d in range(2):
                            c = k if d == 0 else 1 - k
                            if k == 0:
                                pe.wait_ge(m["r_ready"][d], i + 1)
                                pe.wait_ge(m["y0_ready"][d], i + 1)
                                pe.wait_ge(m["phi_ready"][d], i + 1)
                                pe.wait_ge(m["psi_ready"][d], i + 1)
                            else:
                                pe.wait_ge(m["s_ready"][d], 4 * i + 2)
                            alone(pe, unread_pe)
                            for f in range(RF):
                                for g in range(2):
                                    nc.tensor.matmul(ps[d][half(g), g, P * f + CH * c:P * f + CH * c + CH], state[half(g), d, f],
                                                     r[half(g), d, f, CH * c:CH * c + CH], start=True, stop=True)
                            for f in range(RF):
                                for g in range(2):
                                    mm = nc.tensor.matmul(ps[d][half(g), 2 + g, CH * f:CH * f + CH], phi[half(g), d, c, f], state[half(g), d, f],
                                                          start=True, stop=True)
                            mm.then_inc(m["s_full"][d], 1)

        @block.scalar
        def _(act):
            for run in runs:
                with act.Fori(*run) as i:
                    for d in range(2):
                        by_pair = lambda x: x.rearrange("p (f g k) -> p g f k", g=2, k=CH)
                        dsts = (am[:, d, :, 0].rearrange("p (g f) k -> p g f k", g=2), by_pair(v_tok[:, d].rearrange("p f t -> p (f t)")),
                                by_pair(hat_tok[:, d, 0].rearrange("p f t -> p (f t)")), by_pair(hat_tok[:, d, 1].rearrange("p f t -> p (f t)")))
                        for q, dst in enumerate(dsts):
                            act.wait_ge(m["turned"][d], 4 * i + q + 1)
                            for g in range(2):
                                ins = nc.scalar.copy(dst[:, g], by_pair(ps[d][:, q])[:, g])
                            ins.then_inc(m["tok_copied"][d], 1)
                    for d in range(2):
                        act.wait_ge(m["mv_full"][d], i + 1)
                        nc.scalar.copy(am[:, d, :, 1], ps[d][:, 2].rearrange("p (h k) -> p h k", h=H)).then_inc(m["mv_ready"][d], 1)
                    bank2 = lambda x: x.rearrange("p (b h) t -> p b (h t)", b=2)
                    for l in range(1, LEVELS):
                        for d in range(2):
                            act.wait_ge(m["z_full"][d], 5 * i + l)
                            nc.scalar.copy(bank2(z[:, d]), ps[d][:, 0:2]).then_inc(m["z_ready"][d], 1)
                    for d in range(2):
                        act.wait_ge(m["wg_full"][d], i + 1)
                        nc.scalar.mul(wg[:, d].rearrange("p (b h) a k -> p b (h a k)", b=2), ps[d][:, 0:2], -1.0).then_inc(m["wg_ready"][d], 1)
                    for d in range(2):
                        act.wait_ge(m["phi_ready"][d], i + 1)
                        nc.scalar.copy(psi[:, d], ps[d][:, 2:4].rearrange("p c (f a k) -> p c f a k", f=RF, a=2)[:, :, :, 1]).then_inc(m["psi_ready"][d], 1)
                        act.wait_ge(m["y0_full"][d], i + 1)
                        nc.scalar.copy(y0[:, d].rearrange("p f t -> p (f t)"), ps[d][:, 1]).then_inc(m["y0_ready"][d], 1)
                    for d in range(2):
                        act.wait_ge(m["y_ready"][d], i + 1)
                        n = where(i, d, run)
                        act.dma_start(dram["wkv_y"][d, bass.ds(n, 1)].rearrange("a p f t -> p (a f t)"), y[:, d].rearrange("p f t -> p (f t)")).then_inc(m["y_stored"][d], 16)
            for d in range(2):
                act.wait_ge(m["y_stored"][d], 16 * runs[1][1])

        @block.vector
        def _(dve):
            dve.wait_ge(consts_in, 48)
            dve.wait_ge(padded, 3)
            for run in runs:
                if run[0]:
                    for d in range(2):
                        dve.wait_ge(m["s_full"][d], 2 * run[0])
                        dve.wait_ge(m["s_ready"][d], 4 * run[0])
                nc.vector.memset(state[:], 0.0).then_inc(zeroed, 1)
                dve.wait_ge(zeroed, 1 + (run[0] > 0))
                with dve.Fori(*run) as i:
                    def masked(q, d, dst, done):
                        for c in range(2):
                            ins = nc.vector.tensor_tensor(dst[half(c), d, :, :, half(c)], ps[d][half(c), 2 * q:2 * q + 2].rearrange("p b (f a t) -> p (b f) a t", f=RF, a=2),
                                                          mask[half(c), d].unsqueeze(1).to_broadcast([CH, H, 2, CH]), ALU.mult)
                        ins.then_inc(m[done][d], 1)

                    for d in range(2):
                        dve.wait_ge(m["beta_full"][d], i + 1)
                        dve.wait_ge(m["lev_ready"][d], LEVELS * i)
                        masked(0, d, lb, "beta_masked")
                    for d in range(2):
                        dve.wait_ge(m["kappa_full"][d], i + 1)
                        masked(1, d, mk, "kappa_masked")
                    for d in range(2):
                        dve.wait_ge(m["lev_ready"][d], LEVELS * i + 1)
                        dve.wait_ge(m["wg_full"][d], i)
                        nc.vector.tensor_tensor(xt[:, d], consts["ident"][:].unsqueeze(1).to_broadcast([P, H, P]), lev[:, d, 0],
                                                ALU.subtract).then_inc(m["xt1_ready"][d], 1)
                    flat = lambda a: a.rearrange("p h t -> p (h t)")
                    for d in range(2):
                        dve.wait_ge(m["xt1_ready"][d], i + 1)
                        nc.vector.transpose(flat(x[:, d]), flat(xt[:, d])).then_inc(m["x1_ready"][d], 1)
                    bank2 = lambda x: x.rearrange("p (b h) t -> p b (h t)", b=2)
                    for l in range(1, LEVELS - 1):
                        for d in range(2):
                            dve.wait_ge(m["xz_full"][d], 4 * i + l)
                            nc.vector.tensor_tensor(bank2(x[:, d]), bank2(x[:, d]), ps[d][:, 2:4], ALU.subtract).then_inc(m["x_ready"][d], 1)
                            dve.wait_ge(m["x_ready"][d], 4 * i + l)
                            nc.vector.transpose(flat(xt[:, d]), flat(x[:, d])).then_inc(m["xt_ready"][d], 1)
                    for d in range(2):
                        dve.wait_ge(m["last_full"][d], i + 1)
                        nc.vector.tensor_tensor(bank2(xt[:, d]), bank2(xt[:, d]), ps[d][:, 2:4], ALU.subtract).then_inc(m["inv_ready"][d], 1)
                    for d in range(2):
                        dve.wait_ge(m["trans_full"][d], i + 1)
                        dve.wait_ge(m["diag_ready"][d], i + 1)
                        nc.vector.tensor_tensor(phi[:, d], ps[d][:, 2:4].rearrange("p c (f a k) -> p c f a k", f=RF, a=2)[:, :, :, 0], diag[:, d],
                                                ALU.add).then_inc(m["phi_ready"][d], 1)
                        dve.wait_ge(m["bw_full"][d], i + 1)
                        nc.vector.tensor_tensor(r[:, d].rearrange("p f t -> p (f t)"), ps[d][:, 0], rho[:, d].rearrange("p f t -> p (f t)"),
                                                ALU.add).then_inc(m["r_ready"][d], 1)
                    for k in range(2):
                        for d in range(2):
                            c = k if d == 0 else 1 - k
                            dve.wait_ge(m["s_full"][d], 2 * i + k + 1)
                            dve.wait_ge(m["psi_ready"][d], i + 1)
                            if k == 1:
                                dve.wait_ge(m["s_ready"][d], 4 * i + 2)
                            for g in range(2):
                                nc.vector.tensor_tensor(state[half(g), d], ps[d][half(g), 2 + g, 0:RF * CH].rearrange("p (f k) -> p f k", f=RF),
                                                        psi[half(g), d, c], ALU.add).then_inc(m["s_ready"][d], 1)
                    for d in range(2):
                        dve.wait_ge(m["y_stored"][d], 16 * i)
                        dve.wait_ge(m["y0_ready"][d], i + 1)
                        for g in range(2):
                            ins = nc.vector.tensor_tensor(y[half(g), d].rearrange("p f t -> p (f t)"), ps[d][half(g), g],
                                                          y0[half(g), d].rearrange("p f t -> p (f t)"), ALU.add)
                        ins.then_inc(m["y_ready"][d], 1)


GN_EPS = 64e-5


def rwkv_finish(nc, dram, consts, oa_t):
    with ExitStack() as ctx:
        s = Scope(nc, ctx)
        W = [P, RF, PB]
        J = PB // P
        up = s.sb("gate_up", [P, RF * P])
        head_ones = s.sb("head_ones2", [P, P])
        yin = s.sb("fin_y", [P, 2, J, RF, P])
        rkv = s.sb("fin_rkv", [P, 12, PB])
        gd = s.sb("fin_gd", [P, PB])
        y, yc, sq, var, lnv, rstd, rk, rkk, bonus = (s.sb("fin_" + n, W) for n in ("sum", "centred", "square", "var", "ln_var", "rstd", "rk", "rkk", "bonus"))
        yn = s.sb("fin_yn", W)
        ya = s.sb("fin_affine", W)
        sg = s.sb("fin_sg", [P, PB])
        ps_m, ps_v, ps_b, ps_g = (s.ps("ps_fin" + n, W) for n in "mvbg")
        m = {n: s.sem("fin_" + n + "_s") for n in (
            "consts", "loaded", "summed", "mean_full", "centred", "squared", "var_full", "var_ready", "rstd_ready", "normed", "affine", "ln_own",
            "rk_own", "rkk_ready", "bonus_full", "tanh", "sig_ready", "gate_full", "own", "done", "bonus_ready")}
        block = ctx.enter_context(nc.Block())
        N = TOK // PB

        @block.sync
        def _(sp):
            sp.dma_start(up[:], dram["gate_up"][:, :]).then_inc(m["consts"], 16)
            sp.dma_start(head_ones[:], dram["head_ones"][:, :]).then_inc(m["consts"], 16)
            with sp.Fori(0, N) as i:
                sp.wait_ge(m["summed"], i)
                sp.wait_ge(m["tanh"], i)
                sp.wait_ge(m["rkk_ready"], i)
                sp.wait_ge(m["bonus_ready"], i)
                for d in range(2):
                    sp.dma_start(yin[:, d].rearrange("p j f t -> p j (f t)"),
                                 dram["wkv_y"][d, bass.ds(i * J, J)].rearrange("j p f t -> p j (f t)")).then_inc(m["loaded"], 16)
                sp.dma_start(rkv[:], dram["p_t"][0:12, :, bass.ds(i * PB, PB)].rearrange("f p t -> p f t")).then_inc(m["loaded"], 16)
                sp.dma_start(gd[:], dram["p_t"][GD, :, bass.ds(i * PB, PB)]).then_inc(m["loaded"], 16)

        @block.gpsimd
        def _(pool):
            with pool.Fori(0, N) as i:
                pool.wait_ge(m["loaded"], 64 * i + 64)
                pool.wait_ge(m["centred"], i)
                order = "p j f t -> p f j t"
                nc.gpsimd.tensor_tensor(y[:].rearrange("p f (j t) -> p f j t", j=J), yin[:, 0].rearrange(order), yin[:, 1].rearrange(order),
                                        ALU.add).then_inc(m["summed"], 1)
                nc.gpsimd.tensor_tensor(rk[:], rkv[:, 0:4], rkv[:, 4:8], ALU.mult).then_inc(m["rk_own"], 1)
                pool.wait_ge(m["rk_own"], i + 1)
                pool.wait_ge(m["bonus_full"], i)
                nc.gpsimd.tensor_tensor(rkk[:], rk[:], col(consts, "r_k").unsqueeze(2).to_broadcast(W), ALU.mult).then_inc(m["rkk_ready"], 1)

        @block.tensor
        def _(pe):
            pe.wait_ge(m["consts"], 32)
            with pe.Fori(0, N) as i:
                def sums(out, src):
                    for f in range(RF):
                        mm = nc.tensor.matmul(out[:, f], head_ones[:], src[:, f], start=True, stop=True)
                    return mm
                pe.wait_ge(m["summed"], i + 1)
                pe.wait_ge(m["centred"], i)
                sums(ps_m, y).then_inc(m["mean_full"], 1)
                pe.wait_ge(m["rkk_ready"], i + 1)
                pe.wait_ge(m["bonus_ready"], i)
                sums(ps_b, rkk).then_inc(m["bonus_full"], 1)
                pe.wait_ge(m["sig_ready"], i + 1)
                pe.wait_ge(m["done"], i)
                for f in range(RF):
                    mm = nc.tensor.matmul(ps_g[:, f], up[:, P * f:P * f + P], sg[:], start=True, stop=True)
                mm.then_inc(m["gate_full"], 1)
                pe.wait_ge(m["squared"], i + 1)
                pe.wait_ge(m["var_ready"], i)
                sums(ps_v, sq).then_inc(m["var_full"], 1)

        @block.scalar
        def _(act):
            with act.Fori(0, N) as i:
                act.wait_ge(m["loaded"], 64 * i + 64)
                act.wait_ge(m["gate_full"], i)
                nc.scalar.activation(sg[:], gd[:], ACT.Tanh, scale=0.5).then_inc(m["tanh"], 1)
                act.wait_ge(m["centred"], i + 1)
                act.wait_ge(m["var_full"], i)
                nc.scalar.activation(sq[:], yc[:], ACT.Square).then_inc(m["squared"], 1)
                act.wait_ge(m["var_ready"], i + 1)
                nc.scalar.activation(lnv[:], var[:], ACT.Ln).then_inc(m["ln_own"], 1)
                act.wait_ge(m["ln_own"], i + 1)
                nc.scalar.activation(rstd[:], lnv[:], ACT.Exp, scale=-0.5).then_inc(m["rstd_ready"], 1)
                act.wait_ge(m["normed"], i + 1)
                act.wait_ge(m["done"], i)
                for f in range(RF):
                    ins = nc.scalar.activation(ya[:, f], yn[:, f], ACT.Identity, bias=col(consts, "gn_b", f, 1), scale=col(consts, "gn_w", f, 1))
                ins.then_inc(m["affine"], 1)

        @block.vector
        def _(dve):
            with dve.Fori(0, N) as i:
                step = Chain(dve, m["own"], 0, i, 1)
                dve.wait_ge(m["tanh"], i + 1)
                nc.vector.tensor_scalar(sg[:], sg[:], 0.5, 0.5, ALU.mult, ALU.add).then_inc(m["sig_ready"], 1)
                for h in range(2):
                    q = slice(2 * h, 2 * h + 2)
                    if h == 0:
                        dve.wait_ge(m["mean_full"], i + 1)
                        dve.wait_ge(m["squared"], i)
                    ins = nc.vector.scalar_tensor_tensor(out=yc[:, q], in0=ps_m[:, q], scalar=-1.0 / CH, in1=y[:, q], op0=ALU.mult, op1=ALU.add)
                ins.then_inc(m["centred"], 1)
                dve.wait_ge(m["bonus_full"], i + 1)
                nc.vector.tensor_tensor(bonus[:], ps_b[:], rkv[:, 8:12], ALU.mult).then_inc(m["bonus_ready"], 1)
                dve.wait_ge(m["var_full"], i + 1)
                nc.vector.tensor_scalar(var[:], ps_v[:], 1.0 / CH, GN_EPS, ALU.mult, ALU.add).then_inc(m["var_ready"], 1)
                dve.wait_ge(m["rstd_ready"], i + 1)
                nc.vector.tensor_tensor(yn[:], yc[:], rstd[:], ALU.mult).then_inc(m["normed"], 1)
                dve.wait_ge(m["affine"], i + 1)
                dve.wait_ge(m["bonus_ready"], i + 1)
                step(nc.vector.tensor_tensor(ya[:], ya[:], bonus[:], ALU.add))
                dve.wait_ge(m["gate_full"], i + 1)
                nc.vector.tensor_tensor(oa_t[:, :, bass.ds(i * PB, PB)], ya[:], ps_g[:], ALU.mult).then_inc(m["done"], 1)
                step.end()


NOPE, ROPE = 64, 32
HD = NOPE + ROPE
QF, KVF = 6, 2
KPE_TILE, Q_TILE, KV_TILE = 15, 16, 22
SCALE = float(HD) ** -0.5


def mla_project(nc, dram, consts):
    with ExitStack() as ctx:
        s = Scope(nc, ctx)
        U = 2 * HEADS
        L = QF + KVF
        w_uq = s.sb("w_uq", [P, QF, HEADS, HD])
        w_uk = s.sb("w_uk", [P, KVF, HEADS, HD])
        w_uv = s.sb("w_uv", [P, KVF, 512])
        gather = s.sb("gather_means", [HD, U, 2 * U])
        spread = s.sb("spread_rstd", [P, U, HD])
        rotate = s.sb("rotate", [HD, HD])
        rope = s.sb("rope", [HD, 2, NB])
        q_gain = s.sb("scaled_q_gain", [P, 1])
        lat = s.sb("latent", [P, L, NB])
        kpe = s.sb("k_pe", [P, NB])
        lat_sq = s.sb("latent_square", [P, L, NB])
        lat_n = s.sb("latent_normed", [P, L, NB])
        var = s.sb("latent_var", [P, 2, NB])
        rms = s.sb("latent_rms", [P, 2, NB])
        rstd_l = s.sb("latent_rstd", [P, 2, NB])
        raw = s.sb("heads_raw", [HD, U, NB])
        sq, normed, t_cos, t_sin, outq = (s.sb("head_" + n, [HD, 2, NB]) for n in ("square", "normed", "cos", "sin", "out"))
        var_h, rms_h = s.sb("heads_var", [2 * U, NB]), s.sb("heads_rms", [2 * U, NB])
        rstd_h = s.sb("heads_rstd", [P, NB])
        v_out = s.sb("v_out", [P, 2, 512])
        ps_raw = [s.ps(f"ps_raw{b}", [HD, NB]) for b in range(2)]
        ps_rot = [s.ps(f"ps_rot{b}", [HD, NB]) for b in range(2)]
        ps_l = [s.ps(f"ps_lat{b}", [P, NB]) for b in range(2)]
        ps_stat = s.ps("ps_heads_mean", [2 * U, NB])
        m = {n: s.sem("mla_" + n) for n in (
            "consts", "own", "lat_squared", "lat_full", "lat_var", "lat_rms", "lat_rstd", "lat_normed", "v_full", "v_copied",
            "raw_full", "raw_copied", "sum_full", "stat_var", "stat_rms", "stat_ready", "spread_full", "normed", "rot_full", "cos_ready",
            "sin_ready", "out_ready", "lat_loaded", "kpe_loaded", "rope_loaded")}
        v_stored = [s.sem(f"mla_v_stored{b}") for b in range(2)]
        stored = [s.sem(f"mla_stored{b}") for b in range(2)]
        unread = s.sem("mla_unread")
        block = ctx.enter_context(nc.Block())

        def blocks(eng, body):
            with eng.Fori(0, NT - 1) as i:
                body(i, True)
            body(NT - 1, False)

        @block.sync
        def _(sp):
            def load_latents(i):
                sp.dma_start(lat[:], dram["p_t"][Q_TILE:Q_TILE + L, :, bass.ds(i * NB, NB)].rearrange("f p t -> p f t")).then_inc(m["lat_loaded"], 16)

            def load_kpe(i):
                sp.dma_start(kpe[:], dram["p_t"][KPE_TILE, :, bass.ds(i * NB, NB)]).then_inc(m["kpe_loaded"], 16)

            def load_rope(i):
                sp.dma_start(rope[:], dram["rope"][:, :, bass.ds(i * NB, NB)]).then_inc(m["rope_loaded"], 16)

            load_latents(0)
            load_kpe(0)
            load_rope(0)
            for dst, name in ((w_uv, "w_uv"), (w_uq, "w_uq"), (w_uk, "w_uk"), (gather, "gather_means"), (spread, "spread_rstd"), (rotate, "rotate")):
                sp.dma_start(dst[:], dram[name][tuple([slice(None)] * len(dst.shape))]).then_inc(m["consts"], 16)

            def body(i, more):
                if more:
                    sp.wait_ge(m["lat_normed"], L * i + L)
                    alone(sp, unread)
                    load_latents(i + 1)
                for t in range(4):
                    sp.wait_ge(m["v_copied"], 4 * i + (t + 1))
                    sp.dma_start(dram["v_mla"][bass.ds(4 * i + t, 1)].rearrange("a p v -> p (a v)"), v_out[:, t % 2]).then_inc(v_stored[t % 2], 16)
                if more:
                    sp.wait_ge(m["raw_full"], U * i + U)
                    alone(sp, unread)
                    load_kpe(i + 1)
                for u in range(U):
                    sp.wait_ge(m["out_ready"], U * i + (u + 1))
                    sp.dma_start(dram["qk_t"][u, :, bass.ds(i * NB, NB)], outq[:, u % 2]).then_inc(stored[u % 2], 16)
                if more:
                    alone(sp, unread)
                    load_rope(i + 1)

            blocks(sp, body)
            for b in range(2):
                sp.wait_ge(stored[b], 16 * U // 2 * NT)
                sp.wait_ge(v_stored[b], 16 * 2 * NT)

        @block.tensor
        def _(pe):
            def latent_sums(i):
                pe.wait_ge(m["lat_squared"], i + 1)
                pe.wait_ge(m["v_copied"], 4 * i)
                for b, (first, n) in enumerate(((0, QF), (QF, KVF))):
                    for k in range(n):
                        mm = nc.tensor.matmul(ps_l[b][:], consts["ones"][:], lat_sq[:, first + k], start=(k == 0), stop=(k == n - 1))
                mm.then_inc(m["lat_full"], 1)

            def body(i, more):
                pe.wait_ge(m["lat_normed"], L * i + L)
                for t in range(4):
                    if t >= 2:
                        pe.wait_ge(m["v_copied"], 4 * i + (t - 1))
                    for k in range(KVF):
                        mm = nc.tensor.matmul(ps_l[t % 2][:], lat_n[:, QF + k, P * t:P * t + P], w_uv[:, k], start=(k == 0), stop=(k == KVF - 1))
                    mm.then_inc(m["v_full"], 1)
                pe.wait_ge(m["kpe_loaded"], 16 * i + 16)
                pe.wait_ge(m["normed"], U * i)
                for u in range(U + 1):
                    if u < U:
                        h, b = u % HEADS, u % 2
                        if u >= 2:
                            pe.wait_ge(m["raw_copied"], U * i + (u - 1))
                        if u < HEADS:
                            for k in range(QF):
                                mm = nc.tensor.matmul(ps_raw[b][:], w_uq[:, k, h], lat_n[:, k], start=(k == 0), stop=(k == QF - 1))
                        else:
                            nc.tensor.matmul(ps_raw[b][:], consts["ident"][:, 0:HD], kpe[:], start=True, stop=False)
                            for k in range(KVF):
                                mm = nc.tensor.matmul(ps_raw[b][:], w_uk[:, k, h], lat_n[:, QF + k], start=False, stop=(k == KVF - 1))
                        mm.then_inc(m["raw_full"], 1)
                    if u >= 1:
                        pe.wait_ge(m["raw_copied"], U * i + u)
                        if u == 1:
                            pe.wait_ge(m["stat_var"], i)
                        nc.tensor.matmul(ps_stat[:], gather[:, u - 1], sq[:, (u - 1) % 2], start=(u == 1), stop=(u == U)).then_inc(m["sum_full"], 1)
                    if more and u == U - 4:
                        latent_sums(i + 1)
                pe.wait_ge(m["stat_ready"], i + 1)
                for u in range(U + 1):
                    if u < U:
                        if u >= 2:
                            pe.wait_ge(m["normed"], U * i + (u - 1))
                        nc.tensor.matmul(ps_raw[u % 2][:], spread[:, u], rstd_h[:], start=True, stop=True).then_inc(m["spread_full"], 1)
                    if u >= 1:
                        c = (u - 1) % 2
                        pe.wait_ge(m["normed"], U * i + u)
                        if u >= 3:
                            pe.wait_ge(m["sin_ready"], U * i + (u - 2))
                        else:
                            pe.wait_ge(m["sin_ready"], U * i)
                        nc.tensor.matmul(ps_rot[c][:], rotate[:], normed[:, c], start=True, stop=True).then_inc(m["rot_full"], 1)

            pe.wait_ge(m["consts"], 96)
            latent_sums(0)
            blocks(pe, body)

        @block.scalar
        def _(act):
            def square_latents(i):
                act.wait_ge(m["lat_loaded"], 16 * i + 16)
                act.wait_ge(m["lat_full"], i)
                nc.scalar.activation(lat_sq[:], lat[:], ACT.Square).then_inc(m["lat_squared"], 1)

            def latent_roots(i):
                act.wait_ge(m["lat_var"], i + 1)
                act.wait_ge(m["lat_rstd"], i)
                nc.scalar.activation(rms[:], var[:], ACT.Sqrt).then_inc(m["lat_rms"], 1)

            def body(i, more):
                for t in range(4):
                    act.wait_ge(m["v_full"], 4 * i + (t + 1))
                    act.wait_ge(v_stored[t % 2], 32 * i + 16 * (t // 2))
                    nc.scalar.copy(v_out[:, t % 2], ps_l[t % 2][:]).then_inc(m["v_copied"], 1)
                for u in range(U):
                    act.wait_ge(m["raw_full"], U * i + (u + 1))
                    if u >= 2:
                        act.wait_ge(m["sum_full"], U * i + (u - 1))
                    nc.scalar.activation(sq[:, u % 2], ps_raw[u % 2][:], ACT.Square)
                    nc.scalar.copy(raw[:, u], ps_raw[u % 2][:]).then_inc(m["raw_copied"], 1)
                    if more and u == HEADS:
                        square_latents(i + 1)
                    if more and u == U - 2:
                        latent_roots(i + 1)
                act.wait_ge(m["stat_var"], i + 1)
                act.wait_ge(m["stat_ready"], i)
                nc.scalar.activation(rms_h[:], var_h[:], ACT.Sqrt).then_inc(m["stat_rms"], 1)

            square_latents(0)
            latent_roots(0)
            blocks(act, body)

        @block.gpsimd
        def _(pool):
            def body(i, more):
                pool.wait_ge(m["rope_loaded"], 16 * i + 16)
                for u in range(U):
                    b = u % 2
                    pool.wait_ge(m["normed"], U * i + (u + 1))
                    if u >= 2:
                        pool.wait_ge(m["out_ready"], U * i + (u - 1))
                    else:
                        pool.wait_ge(m["out_ready"], U * i)
                    nc.gpsimd.tensor_tensor(t_cos[:, b], normed[:, b], rope[:, 0], ALU.mult).then_inc(m["cos_ready"], 1)

            blocks(pool, body)

        @block.vector
        def _(dve):
            nc.vector.memset(rstd_h[:], 0.0).then_inc(m["own"], 1)
            nc.vector.tensor_scalar(q_gain[:], col(consts, "q_gain"), SCALE, None, ALU.mult).then_inc(m["own"], 1)
            dve.wait_ge(m["own"], 2)

            def latent_rstd(i):
                dve.wait_ge(m["lat_full"], i + 1)
                dve.wait_ge(m["lat_rms"], i)
                for b, n in enumerate((QF, KVF)):
                    ins = nc.vector.tensor_scalar(var[:, b], ps_l[b][:], 1.0 / (n * P), EPS, ALU.mult, ALU.add)
                ins.then_inc(m["lat_var"], 1)
                dve.wait_ge(m["lat_rms"], i + 1)
                dve.wait_ge(m["lat_normed"], L * i)
                nc.vector.reciprocal(rstd_l[:], rms[:]).then_inc(m["lat_rstd"], 1)

            def norm_latents(i):
                dve.wait_ge(m["lat_rstd"], i + 1)
                dve.wait_ge(m["raw_full"], U * i)
                for k in range(L):
                    gain = col(consts, "qa_norm", k, 1) if k < QF else col(consts, "kva_norm", k - QF, 1)
                    nc.vector.scalar_tensor_tensor(out=lat_n[:, k], in0=lat[:, k], scalar=gain, in1=rstd_l[:, int(k >= QF)],
                                                   op0=ALU.mult, op1=ALU.mult).then_inc(m["lat_normed"], 1)

            def body(i, more):
                if more:
                    latent_rstd(i + 1)
                dve.wait_ge(m["sum_full"], U * i + U)
                dve.wait_ge(m["stat_rms"], i)
                nc.vector.tensor_scalar(var_h[:], ps_stat[:], EPS, None, ALU.add).then_inc(m["stat_var"], 1)
                dve.wait_ge(m["stat_rms"], i + 1)
                dve.wait_ge(m["spread_full"], U * i)
                nc.vector.reciprocal(rstd_h[0:2 * U], rms_h[:]).then_inc(m["stat_ready"], 1)
                if more:
                    norm_latents(i + 1)
                dve.wait_ge(m["rope_loaded"], 16 * i + 16)
                for u in range(U + 1):
                    b = u % 2
                    if u < U:
                        dve.wait_ge(m["spread_full"], U * i + (u + 1))
                        if u >= 2:
                            dve.wait_ge(m["rot_full"], U * i + (u - 1))
                            dve.wait_ge(m["cos_ready"], U * i + (u - 1))
                        gain = q_gain[0:HD] if u < HEADS else col(consts, "k_gain")[0:HD]
                        nc.vector.scalar_tensor_tensor(out=normed[:, b], in0=raw[:, u], scalar=gain, in1=ps_raw[b][:],
                                                       op0=ALU.mult, op1=ALU.mult).then_inc(m["normed"], 1)
                    if u >= 1:
                        c = (u - 1) % 2
                        dve.wait_ge(m["rot_full"], U * i + u)
                        nc.vector.tensor_tensor(t_sin[:, c], ps_rot[c][:], rope[:, 1], ALU.mult).then_inc(m["sin_ready"], 1)
                        dve.wait_ge(m["sin_ready"], U * i + u)
                        dve.wait_ge(m["cos_ready"], U * i + u)
                        dve.wait_ge(stored[c], 8 * U * i + 16 * ((u - 1) // 2))
                        nc.vector.tensor_tensor(outq[:, c], t_sin[:, c], t_cos[:, c], ALU.add).then_inc(m["out_ready"], 1)

            latent_rstd(0)
            norm_latents(0)
            blocks(dve, body)




def attention(nc, dram, consts, o_all):
    with ExitStack() as ctx:
        s = Scope(nc, ctx)
        q = s.sb("att_q", [HD, 2, TOK])
        k = s.sb("att_k", [HD, 2, TOK])
        v = s.sb("att_v", [P, 2, TT, 64])
        prob = s.sb("att_prob", [P, 2, SEQS[0]])
        prob_t = s.sb("att_prob_t", [P, 2, 2, 512])
        stat = s.sb("att_stat", [P, 2, 3])
        ps_s = [s.ps(f"ps_scores{b}", [P, 2, 512]) for b in range(2)]
        ps_t = s.ps("ps_prob_t", [P, 2, 512])
        ps_o = [s.ps(f"ps_o{b}", [P, 64]) for b in range(2)]
        zeros = s.sb("att_zeros", [P, D])
        zeroed, zeros_stored = s.sem("att_zeroed"), s.sem("att_zeros_stored")
        loaded = [s.sem(f"att_loaded{b}") for b in range(2)]
        m = {n: s.sem("att_" + n) for n in ("s_full", "max_ready", "p_ready", "t_full", "t_copied_act", "t_copied_dve", "o_full",
                                            "inv_ready", "o_ready")}
        block = ctx.enter_context(nc.Block())
        units = [(0, t, SEQS[0] // P) for t in range(SEQS[0] // P)] + [(SEQS[0], SEQS[0] // P + t, SEQS[1] // P) for t in range(SEQS[1] // P)]
        U = len(units)
        todo = [(hb, u) + unit for hb in range(2) for u, unit in enumerate(units)]
        n_turn = 2 * U

        @block.sync
        def _(sp):
            def load(h, b):
                sp.dma_start(q[:, b], dram["qk_t"][bass.ds(h, 1)].rearrange("a d t -> d (a t)")).then_inc(loaded[b], 16)
                sp.dma_start(k[:, b], dram["qk_t"][bass.ds(h + HEADS, 1)].rearrange("a d t -> d (a t)")).then_inc(loaded[b], 16)
                sp.dma_start(v[:, b], dram["v_mla"][:, :, bass.ds(h * 64, 64)].rearrange("t p v -> p t v")).then_inc(loaded[b], 16)

            for b in range(2):
                load(b, b)
            with sp.Fori(0, HEADS // 2 - 1) as i:
                for b in range(2):
                    sp.wait_ge(m["o_full"], n_turn * i + U * (b + 1))
                    load(2 * i + (b + 2), b)

        @block.gpsimd
        def _(pool):
            nc.gpsimd.memset(zeros[:], 0.0).then_inc(zeroed, 1)
            pool.wait_ge(zeroed, 1)
            for n in range(TOK * TOP // MB, BLOCKS):
                pool.dma_start(dram["yb"][n], zeros[:]).then_inc(zeros_stored, 16)
            pool.wait_ge(zeros_stored, 16 * (BLOCKS - TOK * TOP // MB))

        @block.tensor
        def _(pe):
            with pe.Fori(0, HEADS // 2) as i:
                base = n_turn * i
                for n in range(n_turn + 2):
                    if n < n_turn:
                        hb, u, t0, t, nk = todo[n]
                        if u == 0:
                            pe.wait_ge(loaded[hb], 48 * i + 48)
                        pe.wait_ge(m["p_ready"], base + max(0, n - 1))
                        for c in range(nk // 4):
                            mm = nc.tensor.matmul(ps_s[n % 2][:, c], q[:, hb, P * t:P * t + P], k[:, hb, t0 + 512 * c:t0 + 512 * c + 512],
                                                  start=True, stop=True)
                        mm.then_inc(m["s_full"], 1)
                    if 0 <= n - 1 < n_turn:
                        nk = todo[n - 1][4]
                        pe.wait_ge(m["p_ready"], base + n)
                        pe.wait_ge(m["t_copied_act"], base + n - 1)
                        pe.wait_ge(m["t_copied_dve"], base + n - 1)
                        for j in range(nk):
                            mm = nc.tensor.transpose(ps_t[:, j // (nk // 2), P * (j % (nk // 2)):P * (j % (nk // 2)) + P],
                                                     prob[:, (n - 1) % 2, P * j:P * j + P], consts["ident"][:])
                        mm.then_inc(m["t_full"], 1)
                    if 0 <= n - 2 < n_turn:
                        hb, u, t0, t, nk = todo[n - 2]
                        pe.wait_ge(m["t_copied_act"], base + n - 1)
                        pe.wait_ge(m["t_copied_dve"], base + n - 1)
                        pe.wait_ge(m["o_ready"], base + max(0, n - 3))
                        for j in range(nk):
                            mm = nc.tensor.matmul(ps_o[n % 2][:], prob_t[:, n % 2, j // (nk // 2), P * (j % (nk // 2)):P * (j % (nk // 2)) + P],
                                                  v[:, hb, t0 // P + j], start=(j == 0), stop=(j == nk - 1))
                        mm.then_inc(m["o_full"], 1)

        @block.scalar
        def _(act):
            with act.Fori(0, HEADS // 2) as i:
                base = n_turn * i
                for n in range(n_turn + 1):
                    if n < n_turn:
                        nk = todo[n][4]
                        act.wait_ge(m["max_ready"], base + n + 1)
                        act.wait_ge(m["t_full"], base + max(0, n - 1))
                        act.wait_ge(m["inv_ready"], base + max(0, n - 1))
                        nc.scalar.activation(prob[:, n % 2, 0:P * nk].rearrange("p (c x) -> p c x", x=512), ps_s[n % 2][:, 0:nk // 4], ACT.Exp,
                                             bias=stat[:, n % 2, 0:1], accum_out=stat[:, n % 2, 1:2]).then_inc(m["p_ready"], 1)
                    if n >= 1:
                        nk = todo[n - 1][4]
                        act.wait_ge(m["t_full"], base + n)
                        act.wait_ge(m["o_full"], base + max(0, n - 2))
                        nc.scalar.copy(prob_t[:, (n - 1) % 2, 0, 0:P * nk // 2], ps_t[:, 0, 0:P * nk // 2]).then_inc(m["t_copied_act"], 1)

        @block.vector
        def _(dve):
            with dve.Fori(0, HEADS // 2) as i:
                base = n_turn * i
                for n in range(n_turn + 2):
                    if n < n_turn:
                        nk = todo[n][4]
                        dve.wait_ge(m["s_full"], base + n + 1)
                        dve.wait_ge(m["p_ready"], base + max(0, n - 1))
                        nc.vector.tensor_reduce(stat[:, n % 2, 0:1], ps_s[n % 2][:, 0:nk // 4], AX.XY, ALU.max, negate=True).then_inc(m["max_ready"], 1)
                    if 0 <= n - 1 < n_turn:
                        nk = todo[n - 1][4]
                        dve.wait_ge(m["t_full"], base + n)
                        dve.wait_ge(m["o_full"], base + max(0, n - 2))
                        nc.vector.tensor_copy(prob_t[:, (n - 1) % 2, 1, 0:P * nk // 2], ps_t[:, 1, 0:P * nk // 2]).then_inc(m["t_copied_dve"], 1)
                        dve.wait_ge(m["o_ready"], base + max(0, n - 2))
                        nc.vector.reciprocal(stat[:, (n - 1) % 2, 2:3], stat[:, (n - 1) % 2, 1:2]).then_inc(m["inv_ready"], 1)
                    if 0 <= n - 2 < n_turn:
                        hb, u, t0, t, nk = todo[n - 2]
                        dve.wait_ge(m["o_full"], base + n - 1)
                        dve.wait_ge(m["inv_ready"], base + n - 1)
                        nc.vector.tensor_scalar(o_all[:, t, bass.ds(i * 128 + hb * 64, 64)], ps_o[n % 2][:], stat[:, n % 2, 2:3], None,
                                                ALU.mult).then_inc(m["o_ready"], 1)


EXPERTS, GROUPS, PER_GROUP = 32, 4, 8
ROUTER = GROUPS + EXPERTS


def turn_o(nc, dram, consts, o_all, om_t):
    with ExitStack() as ctx:
        s = Scope(nc, ctx)
        ps = s.ps("ps_turn_o", [P, 2, 512])
        full = [s.sem(f"o_turned{b}") for b in range(2)]
        copied = [s.sem(f"o_copied{b}") for b in range(2)]
        block = ctx.enter_context(nc.Block())

        @block.tensor
        def _(pe):
            for t in range(TT):
                pe.wait_ge(copied[t % 2], t // 2)
                for f in range(RF):
                    mm = nc.tensor.transpose(ps[:, t % 2, P * f:P * f + P], o_all[:, t, P * f:P * f + P], consts["ident"][:])
                mm.then_inc(full[t % 2], 1)

        def copies(b, eng, copy):
            for t in range(b, TT, 2):
                eng.wait_ge(full[b], t // 2 + 1)
                copy(om_t[:, :, P * t:P * t + P], ps[:, b].rearrange("p (f t) -> p f t", f=RF)).then_inc(copied[b], 1)

        @block.scalar
        def _(act):
            copies(0, act, nc.scalar.copy)

        @block.vector
        def _(dve):
            copies(1, dve, nc.vector.tensor_copy)


def merge_branches(nc, dram, consts, oa_t, om_t, merged):
    with ExitStack() as ctx:
        s = Scope(nc, ctx)
        w = s.sb("w_o_tile", [P, 2, 2, RF, P])
        g = s.sb("gate_tile", [P, 2, 2, TOK])
        part = s.sb("branch_part", [P, 2, 2, NB])
        ps = s.ps("ps_branch", [P, 2, 2, NB])
        loaded = [s.sem(f"merge_loaded{b}") for b in range(2)]
        full = [s.sem(f"branch_full{b}") for b in range(2)]
        scaled = s.sem("branch_scaled")
        done = [s.sem(f"merged{b}") for b in range(2)]
        unread = s.sem("merge_unread")
        block = ctx.enter_context(nc.Block())
        units = [(b, n) for b in range(2) for n in range(NT)]

        @block.sync
        def _(sp):
            def load(i, b):
                for a in range(2):
                    sp.dma_start(w[:, b, a], dram["w_o"][a, bass.ds(2 * i + b, 1)].rearrange("a p f m -> p (a f) m")).then_inc(loaded[b], 16)
                    sp.dma_start(g[:, b, a], dram["gates"][bass.ds(2 * i + (b + a * DF), 1)].rearrange("a p t -> p (a t)")).then_inc(loaded[b], 16)

            for b in range(2):
                load(0, b)
            with sp.Fori(0, DF // 2 - 1) as i:
                for b in range(2):
                    sp.wait_ge(done[0], 3 * i + (2 + b))
                    alone(sp, unread)
                    sp.wait_ge(done[1], 3 * i + (1 + 2 * b))
                    alone(sp, unread)
                    load(i + 1, b)

        @block.tensor
        def _(pe):
            with pe.Fori(0, DF // 2) as i:
                for u, (b, n) in enumerate(units):
                    if n == 0:
                        pe.wait_ge(loaded[b], 64 * i + 64)
                    pe.wait_ge(done[u % 2], 3 * i + u // 2)
                    for a, src in enumerate((oa_t, om_t)):
                        for f in range(RF):
                            mm = nc.tensor.matmul(ps[:, u % 2, a], w[:, b, a, f], src[:, f, NB * n:NB * n + NB], start=(f == 0), stop=(f == RF - 1))
                    mm.then_inc(full[u % 2], 1)

        @block.vector
        def _(dve):
            with dve.Fori(0, DF // 2) as i:
                for u, (b, n) in enumerate(units):
                    dve.wait_ge(full[u % 2], 3 * i + u // 2 + 1)
                    nc.vector.tensor_tensor(part[:, u % 2], ps[:, u % 2], g[:, b, :, NB * n:NB * n + NB], ALU.mult).then_inc(scaled, 1)
                    dve.wait_ge(scaled, 6 * i + u + 1)
                    nc.vector.tensor_tensor(merged[:, bass.ds(2 * i + b, 1), NB * n:NB * n + NB].rearrange("p a t -> p (a t)"),
                                            part[:, u % 2, 0], part[:, u % 2, 1], ALU.add).then_inc(done[u % 2], 1)


def output_and_router(nc, dram, consts, merged, logits):
    with ExitStack() as ctx:
        s = Scope(nc, ctx)
        w = s.sb("w_out", [P, DF, D])
        w_r = s.sb("w_router", [P, DF, ROUTER])
        b_r = s.sb("b_router", [P, ROUTER])
        rows = s.sb("mod_broadcast", [P, 2, 3, D])
        norm2 = s.sb("norm2_broadcast", [P, D])
        stage = s.sb("merged_tile", [P, 2, DF, P])
        x = s.sb("x_again", [P, 2, D])
        x1 = s.sb("x1_tile", [P, 2, D])
        sq = s.sb("x1_square", [P, D])
        h2 = s.sb("h2_tile", [P, 2, D])
        h2_t = s.sb("h2_turned", [P, DF, P])
        st = s.sb("x1_stat", [P, 2, 3])
        ps = [s.ps(f"ps_out{b}", [P, 2, 512]) for b in range(2)]
        ps_t = s.ps("ps_h2_t", [P, 2, 512])
        ps_r = s.ps("ps_router", [P, 512])
        m = {n: s.sem("out_" + n) for n in ("consts", "consts_b", "own", "staged", "full", "squared", "sqrt_in", "sqrt", "h2_ready", "t_full",
                                            "t_copied", "r_full", "r_done", "x1_ready", "unread")}
        x_loaded = [s.sem(f"out_x_loaded{b}") for b in range(2)]
        x1_stored = [s.sem(f"x1_stored{b}") for b in range(2)]
        h2_stored = [s.sem(f"h2_stored{b}") for b in range(2)]
        block = ctx.enter_context(nc.Block())
        runs = ((0, 0, SEQS[0] // P // 2), (1, SEQS[0] // P // 2, TT // 2))

        @block.sync
        def _(sp):
            for q in range(2):
                for j, part in enumerate((GATE1, SHIFT2, SCALE2)):
                    row = (part * 2 + q) * DF
                    sp.dma_start(rows[:, q, j], dram["mod_rows"][row:row + DF, :].rearrange("f p -> (f p)").partition_broadcast(P)).then_inc(m["consts"], 16)
            sp.dma_start(norm2[:], dram["norm2"][:].partition_broadcast(P)).then_inc(m["consts"], 16)
            sp.dma_start(b_r[:], dram["b_router"][:].partition_broadcast(P)).then_inc(m["consts"], 16)
            with sp.Fori(0, TT // 2) as i:
                for b in range(2):
                    sp.wait_ge(m["x1_ready"], 2 * i)
                    sp.dma_start(x[:, b], dram["x"][bass.ds(i * 2 * P + b * P, P), :]).then_inc(x_loaded[b], 16)
                for b in range(2):
                    sp.wait_ge(m["x1_ready"], 2 * i + b + 1)
                    sp.dma_start(dram["x1"][bass.ds(i * 2 * P + b * P, P), :], x1[:, b]).then_inc(x1_stored[b], 16)
                    sp.wait_ge(m["h2_ready"], 2 * i + b + 1)
                    sp.dma_start(dram["h2"][bass.ds(i * 2 * P + b * P, P), :], h2[:, b]).then_inc(h2_stored[b], 16)
            for b in range(2):
                sp.wait_ge(x1_stored[b], 16 * (TT // 2))
                sp.wait_ge(h2_stored[b], 16 * (TT // 2))

        @block.tensor
        def _(pe):
            pe.wait_ge(m["consts_b"], 32)

            def project(i):
                for b in range(2):
                    pe.wait_ge(m["staged"], 2 * i + (b + 1))
                    pe.wait_ge(m["x1_ready"], 2 * i)
                    for n in range(2):
                        for k in range(DF):
                            mm = nc.tensor.matmul(ps[b][:, n], stage[:, b, k], w[:, k, 512 * n:512 * n + 512], start=(k == 0), stop=(k == DF - 1))
                    mm.then_inc(m["full"], 1)

            def turn_and_route(i):
                for b in range(2):
                    pe.wait_ge(m["h2_ready"], 2 * i + (b + 1))
                    pe.wait_ge(m["t_copied"], 2 * i + b)
                    for k in range(DF):
                        mm = nc.tensor.transpose(ps_t[:, k // 4, P * (k % 4):P * (k % 4) + P], h2[:, b, P * k:P * k + P], consts["ident"][:])
                    mm.then_inc(m["t_full"], 1)
                    pe.wait_ge(m["t_copied"], 2 * i + (b + 1))
                    pe.wait_ge(m["r_done"], 2 * i + b)
                    for k in range(DF):
                        mm = nc.tensor.matmul(ps_r[:, 0:ROUTER], h2_t[:, k], w_r[:, k], start=(k == 0), stop=(k == DF - 1))
                    mm.then_inc(m["r_full"], 1)

            project(0)
            with pe.Fori(1, TT // 2) as i:
                project(i)
                turn_and_route(i - 1)
            turn_and_route(TT // 2 - 1)

        @block.scalar
        def _(act):
            def stage_tiles(i):
                for b in range(2):
                    act.wait_ge(m["full"], max(0, 2 * i + b - 1) if isinstance(i, int) else 2 * i + (b - 1))
                    alone(act, m["unread"])
                    nc.scalar.copy(stage[:, b], merged[:, :, bass.ds(i * 2 * P + b * P, P)]).then_inc(m["staged"], 1)

            def norms(i):
                for b in range(2):
                    act.wait_ge(m["x1_ready"], 2 * i + (b + 1))
                    act.wait_ge(m["sqrt"], 2 * i + b)
                    nc.scalar.activation(sq[:], x1[:, b], ACT.Square, accum_out=st[:, b, 0:1]).then_inc(m["squared"], 1)
                    act.wait_ge(m["sqrt_in"], 2 * i + (b + 1))
                    nc.scalar.activation(st[:, b, 2:3], st[:, b, 1:2], ACT.Sqrt).then_inc(m["sqrt"], 1)

            def copy_turned(i):
                for b in range(2):
                    act.wait_ge(m["t_full"], 2 * i + (b + 1))
                    act.wait_ge(m["r_full"], 2 * i + b)
                    nc.scalar.copy(h2_t[:].rearrange("p (a k) t -> p a (k t)", a=2), ps_t[:]).then_inc(m["t_copied"], 1)

            act.dma_start(w[:], dram["w_out"][:, :, :]).then_inc(m["consts_b"], 16)
            act.dma_start(w_r[:], dram["w_router"][:, :, :]).then_inc(m["consts_b"], 16)
            stage_tiles(0)
            with act.Fori(1, TT // 2) as i:
                stage_tiles(i)
                norms(i - 1)
                copy_turned(i - 1)
            norms(TT // 2 - 1)
            copy_turned(TT // 2 - 1)

        @block.vector
        def _(dve):
            start = Chain(dve, m["own"])
            dve.wait_ge(m["consts"], 16 * 8)
            for q in range(2):
                start(nc.vector.tensor_tensor(rows[:, q, 2], rows[:, q, 2], norm2[:], ALU.mult))

            def add_residual(step, q, i):
                for b in range(2):
                    dve.wait_ge(m["full"], 2 * i + (b + 1))
                    dve.wait_ge(x1_stored[b], 16 * i)
                    dve.wait_ge(m["squared"], 2 * i)
                    step(nc.vector.tensor_tensor(x1[:, b].rearrange("p (a x) -> p a x", a=2), ps[b][:],
                                                 rows[:, q, 0].rearrange("p (a x) -> p a x", a=2), ALU.mult))
                    dve.wait_ge(x_loaded[b], 16 * i + 16)
                    nc.vector.tensor_tensor(x1[:, b], x1[:, b], x[:, b], ALU.add).then_inc(m["x1_ready"], 1)

            def norm_and_modulate(step, q, i):
                for b in range(2):
                    dve.wait_ge(m["squared"], 2 * i + (b + 1))
                    nc.vector.tensor_scalar(st[:, b, 1:2], st[:, b, 0:1], 1.0 / D, EPS, ALU.mult, ALU.add).then_inc(m["sqrt_in"], 1)
                    dve.wait_ge(m["sqrt"], 2 * i + (b + 1))
                    step(nc.vector.reciprocal(st[:, b, 2:3], st[:, b, 2:3]))
                    dve.wait_ge(h2_stored[b], 16 * i)
                    dve.wait_ge(m["t_full"], 2 * i)
                    step(nc.vector.scalar_tensor_tensor(out=h2[:, b], in0=x1[:, b], scalar=st[:, b, 2:3], in1=rows[:, q, 2],
                                                        op0=ALU.mult, op1=ALU.mult))
                    step(nc.vector.tensor_tensor(h2[:, b], h2[:, b], rows[:, q, 1], ALU.add))
                    dve.sem_inc(m["h2_ready"], 1)

            def keep_logits(i):
                for b in range(2):
                    dve.wait_ge(m["r_full"], 2 * i + (b + 1))
                    nc.vector.tensor_tensor(logits[:, bass.ds(2 * i + b, 1)].rearrange("p a e -> p (a e)"), ps_r[:, 0:ROUTER], b_r[:],
                                            ALU.add).then_inc(m["r_done"], 1)

            add_residual(start, 0, 0)
            norm_and_modulate(start, 0, 0)
            for q, first, end in runs:
                with dve.Fori(max(first, 1), end) as i:
                    step = Chain(dve, m["own"], start.n - 8, i, 2 * 4)
                    add_residual(step, q, i)
                    keep_logits(i - 1)
                    norm_and_modulate(step, q, i)
                    step.end()
            keep_logits(TT // 2 - 1)


TOP = 2
D_EXPERT = 256
MB = P
BLOCKS = -(-(TOK * TOP + EXPERTS * (MB - 1)) // MB // 2) * 2
FAR = 1e30


def route(nc, dram, consts, logits, weight, slot):
    with ExitStack() as ctx:
        s = Scope(nc, ctx)
        G, E, T = GROUPS, EXPERTS, TT
        rank_g = s.sb("rank_groups", [P, G])
        rank_e = s.sb("rank_experts", [P, E])
        before = s.sb("tokens_before", [P, P])
        full_at = s.sb("full_at", [P, TT])
        block_no = s.sb("block_no", [P, BLOCKS])
        token = s.sb("token_ids", [P, T])
        zero = s.sb("zero_ids", [P, BLOCKS])
        t = lambda name, shape: s.sb("route_" + name, [P] + shape)
        g_max, g_sum, p_grp, e_max, e_max2, ratio, part = (t(n, [T]) for n in ("gmax", "gsum", "pgrp", "emax", "emax2", "ratio", "part"))
        g_exp, g_hot, g_far = (t(n, [T, G]) for n in ("gexp", "ghot", "gfar"))
        e_in, hot1, hot2, hots, value, prod = (t(n, [T, E]) for n in ("ein", "hot1", "hot2", "hots", "value", "prod"))
        total = t("total", [T + 1, E])
        n_blocks, ends, row0 = (t(n, [E]) for n in ("nblocks", "ends", "row0"))
        over = t("over", [E, TT])
        ended = t("ended", [BLOCKS, E])
        block_e = t("block_e", [BLOCKS + 1])
        block_i = s.sb("route_block_i", [P, BLOCKS + 1], I32)
        dest = t("dest", [TOP, T])
        ps_pref = s.ps("ps_prefix", [P, 512])
        ps_tot = s.ps("ps_total", [P, 512])
        m = {n: s.sem("route_" + n) for n in ("consts", "own", "g_in", "g_exp", "r_in", "ratio", "hots", "counted", "zeroed", "zero_stored",
                                              "slots", "scattered", "blocks", "blocks_stored")}
        block = ctx.enter_context(nc.Block())

        @block.sync
        def _(sp):
            for dst, name in ((rank_g, "rank_groups"), (rank_e, "rank_experts"), (full_at, "full_at"), (block_no, "block_no")):
                sp.dma_start(dst[:], dram[name][:].partition_broadcast(P)).then_inc(m["consts"], 16)
            sp.dma_start(before[:], dram["tokens_before"][:, :]).then_inc(m["consts"], 16)
            sp.dma_start(token[:], dram["token_ids"][:, :]).then_inc(m["consts"], 16)
            sp.wait_ge(m["zeroed"], 1)
            sp.dma_start(dram["row_token"].rearrange("(p b) a -> p (b a)", p=P), zero[:]).then_inc(m["zero_stored"], 16)
            sp.wait_ge(m["blocks"], 1)
            sp.dma_start(dram["block_expert"][:, :], block_i[0:1, :]).then_inc(m["blocks_stored"], 16)
            sp.wait_ge(m["blocks_stored"], 16)

        @block.scalar
        def _(act):
            act.wait_ge(m["g_in"], 1)
            nc.scalar.activation(g_exp[:], g_exp[:], ACT.Exp).then_inc(m["g_exp"], 1)
            act.wait_ge(m["r_in"], 1)
            nc.scalar.activation(ratio[:], ratio[:], ACT.Exp).then_inc(m["ratio"], 1)

        @block.tensor
        def _(pe):
            pe.wait_ge(m["hots"], 1)
            flat = hots[:].rearrange("p t e -> p (t e)")
            nc.tensor.matmul(ps_pref[:, 0:T * E], before[:], flat, start=True, stop=True)
            nc.tensor.matmul(ps_tot[:, 0:T * E], consts["ones"][:], flat, start=True, stop=True).then_inc(m["counted"], 1)

        @block.gpsimd
        def _(pool):
            pool.wait_ge(m["slots"], 1)
            pool.wait_ge(m["zero_stored"], 16)
            pool.wait_ge(m["consts"], 96)
            for k in range(TOP):
                for j in range(T):
                    pool.indirect_dma_start(out=dram["row_token"], out_offset=bass.IndirectOffsetOnAxis(ap=slot[:, k, j:j + 1], axis=0),
                                            in_=token[:, j:j + 1], in_offset=None).then_inc(m["scattered"], 16)
            pool.wait_ge(m["scattered"], 16 * TOP * T)

        @block.vector
        def _(dve):
            V = nc.vector
            nc.vector.memset(zero[:], 0).then_inc(m["zeroed"], 1)
            do = Chain(dve, m["own"])
            groups, experts = logits[:, :, 0:G], logits[:, :, G:G + E]
            wide = lambda x, n: x.unsqueeze(2).to_broadcast([P, T, n])
            dve.wait_ge(m["consts"], 96)
            do(V.tensor_reduce(g_max[:], groups, AX.X, ALU.max))
            V.tensor_tensor(g_exp[:], groups, wide(g_max[:], G), ALU.subtract).then_inc(m["g_in"], 1)

            def first_of(hot, values, best, rank, n):
                do(V.tensor_tensor(hot, values, wide(best, n), ALU.is_equal))
                do(V.tensor_tensor(hot, hot, rank[:].unsqueeze(1).to_broadcast([P, T, n]), ALU.mult))
                do(V.tensor_reduce(part[:], hot, AX.X, ALU.max))
                do(V.tensor_tensor(hot, hot, wide(part[:], n), ALU.is_equal))

            first_of(g_hot[:], groups, g_max[:], rank_g, G)
            do(V.tensor_scalar(g_far[:], g_hot[:], FAR, -FAR, ALU.mult, ALU.add))
            by_group = lambda x: x.rearrange("p t (g e) -> p t g e", g=G)
            over_group = lambda x: x.unsqueeze(3).to_broadcast([P, T, G, PER_GROUP])
            for g in range(G):
                part_e = slice(g * PER_GROUP, (g + 1) * PER_GROUP)
                V.tensor_tensor(e_in[:, :, part_e], experts[:, :, part_e], g_hot[:, :, g:g + 1].to_broadcast([P, T, PER_GROUP]), ALU.mult).then_inc(m["own"], 1)
                do.n += 1
            dve.wait_ge(m["own"], do.n)
            for g in range(G):
                part_e = slice(g * PER_GROUP, (g + 1) * PER_GROUP)
                V.tensor_tensor(e_in[:, :, part_e], e_in[:, :, part_e], g_far[:, :, g:g + 1].to_broadcast([P, T, PER_GROUP]), ALU.add).then_inc(m["own"], 1)
                do.n += 1
            dve.wait_ge(m["own"], do.n)
            do(V.tensor_reduce(e_max[:], e_in[:], AX.X, ALU.max))
            first_of(hot1[:], e_in[:], e_max[:], rank_e, E)
            do(V.tensor_scalar(value[:], hot1[:], -3 * FAR, None, ALU.mult))
            do(V.tensor_tensor(e_in[:], e_in[:], value[:], ALU.add))
            do(V.tensor_reduce(e_max2[:], e_in[:], AX.X, ALU.max))
            first_of(hot2[:], e_in[:], e_max2[:], rank_e, E)
            do(V.tensor_tensor(hots[:], hot1[:], hot2[:], ALU.add))
            dve.sem_inc(m["hots"], 1)
            V.tensor_tensor(ratio[:], e_max2[:], e_max[:], ALU.subtract).then_inc(m["r_in"], 1)
            dve.wait_ge(m["g_exp"], 1)
            do(V.tensor_reduce(g_sum[:], g_exp[:], AX.X, ALU.add))
            do(V.reciprocal(p_grp[:], g_sum[:]))
            dve.wait_ge(m["ratio"], 1)
            do(V.tensor_scalar(part[:], ratio[:], 1.0, None, ALU.add))
            do(V.reciprocal(part[:], part[:]))
            do(V.tensor_tensor(weight[:, 0], p_grp[:], part[:], ALU.mult))
            do(V.tensor_tensor(weight[:, 1], weight[:, 0], ratio[:], ALU.mult))
            dve.wait_ge(m["counted"], 1)
            do(V.memset(total[:, 0], 0.0))
            for j in range(T):
                do(V.tensor_tensor(total[:, j + 1], total[:, j], ps_tot[:, E * j:E * j + E], ALU.add))
            do(V.tensor_tensor(over[:], total[:, T].unsqueeze(2).to_broadcast([P, E, TT]), full_at[:].unsqueeze(1).to_broadcast([P, E, TT]), ALU.is_gt))
            do(V.tensor_reduce(n_blocks[:], over[:], AX.X, ALU.add))
            do(V.tensor_tensor_scan(ends[:], consts["ones"][:, 0:E], n_blocks[:], 0.0, ALU.mult, ALU.add))
            do(V.tensor_tensor(row0[:], ends[:], n_blocks[:], ALU.subtract))
            do(V.tensor_scalar(row0[:], row0[:], float(MB), None, ALU.mult))
            do(V.tensor_tensor(value[:], total[:, 0:T], ps_pref[:, 0:T * E].rearrange("p (t e) -> p t e", t=T), ALU.add))
            do(V.tensor_tensor(value[:], value[:], row0[:].unsqueeze(1).to_broadcast([P, T, E]), ALU.add))
            for k, hot in enumerate((hot1, hot2)):
                do(V.tensor_tensor(prod[:], value[:], hot[:], ALU.mult))
                do(V.tensor_reduce(dest[:, k], prod[:], AX.X, ALU.add))
            V.tensor_copy(slot[:], dest[:]).then_inc(m["slots"], 1)
            do(V.tensor_tensor(ended[:], block_no[:].unsqueeze(2).to_broadcast([P, BLOCKS, E]), ends[:].unsqueeze(1).to_broadcast([P, BLOCKS, E]), ALU.is_ge))
            do(V.tensor_reduce(block_e[:, 0:BLOCKS], ended[:], AX.X, ALU.add))
            do(V.tensor_scalar(block_e[:, 0:BLOCKS], block_e[:, 0:BLOCKS], float(E - 1), None, ALU.min))
            do(V.tensor_copy(block_e[:, BLOCKS:BLOCKS + 1], ends[:, E - 1:E]))
            V.tensor_copy(block_i[:], block_e[:]).then_inc(m["blocks"], 1)
            dve.wait_ge(m["slots"], 1)


def experts(nc, dram, consts):
    with ExitStack() as ctx:
        s = Scope(nc, ctx)
        F2 = D_EXPERT // P
        w13 = s.sb("w13_tile", [P, 2, DF, 2 * D_EXPERT])
        w2 = s.sb("w2_tile", [P, 2, F2, D])
        which = s.sb("block_experts", [1, BLOCKS + 1], I32)
        id_rows = s.sb("row_ids_by_block", [BLOCKS, P])
        ids = s.sb("row_ids", [P, BLOCKS], I32)
        ids_now = s.sb("row_ids_now", [P, 2], I32)
        xb = s.sb("xb", [P, 2, D])
        xt = s.sb("xb_turned", [P, 2, DF, P])
        th = s.sb("gate_tanh", [P, 2, F2, P])
        act_in = s.sb("gate_in", [P, 2, F2, P])
        hid = s.sb("hidden", [P, 2, F2, P])
        yb = s.sb("yb_tile", [P, 2, D])
        ps_ids = s.ps("ps_ids", [P, 512])
        ps_h = [s.ps(f"ps_hidden{b}", [P, 2 * F2, P]) for b in range(2)]
        ps_xy = [s.ps(f"ps_xy{b}", [P, 2, 512]) for b in range(2)]
        loaded, ids_turned, unread = s.sem("moe_consts"), s.sem("moe_ids_turned"), s.sem("moe_unread")
        pair = lambda n: [s.sem(f"moe_{n}{b}") for b in range(2)]
        w13_loaded, w2_loaded, x_loaded, ids_ready, stored = (pair(n) for n in ("w13_loaded", "w2_loaded", "x_loaded", "ids_ready", "stored"))
        turned, x_act, x_dve, h_full, tanh = (pair(n) for n in ("turned", "x_act", "x_dve", "h_full", "tanh"))
        gated, hidden, y_full, y_act, y_dve = (pair(n) for n in ("gated", "hidden", "y_full", "y_act", "y_dve"))
        block = ctx.enter_context(nc.Block())

        def used_blocks(eng):
            eng.wait_ge(loaded, 32)
            return eng.value_load(which[0:1, BLOCKS:BLOCKS + 1], min_val=1, max_val=BLOCKS)

        @block.sync
        def _(sp):
            sp.dma_start(which[:], dram["block_expert"][:, :]).then_inc(loaded, 16)
            sp.dma_start(id_rows[:], dram["row_token"].rearrange("(b p) a -> b (p a)", p=P)).then_inc(loaded, 16)
            used = used_blocks(sp)
            with sp.Fori(0, BLOCKS // 2) as i:
                with sp.If(2 * i < used):
                    e = [sp.value_load(which[0:1, bass.ds(2 * i + b, 1)], min_val=0, max_val=EXPERTS - 1) for b in range(2)]
                    for b in range(2):
                        sp.wait_ge(h_full[b], i)
                        alone(sp, unread)
                        sp.dma_start(w13[:, b], dram["w13"][bass.ds(e[b], 1)].rearrange("a p k f -> p (a k) f")).then_inc(w13_loaded[b], 16)
                    for b in range(2):
                        sp.wait_ge(y_full[b], i)
                        alone(sp, unread)
                        sp.dma_start(w2[:, b], dram["w2"][bass.ds(e[b], 1)].rearrange("a p k f -> p (a k) f")).then_inc(w2_loaded[b], 16)

        @block.gpsimd
        def _(pool):
            used = used_blocks(pool)
            pool.wait_ge(ids_turned, 2)
            with pool.Fori(0, BLOCKS // 2) as i:
                with pool.If(2 * i < used):
                    for b in range(2):
                        pool.wait_ge(x_loaded[b], 16 * i)
                        alone(pool, unread)
                        nc.gpsimd.tensor_copy(ids_now[:, b:b + 1], ids[:, bass.ds(2 * i + b, 1)]).then_inc(ids_ready[b], 1)
                        pool.wait_ge(ids_ready[b], i + 1)
                        pool.wait_ge(turned[b], i)
                        alone(pool, unread)
                        pool.indirect_dma_start(out=xb[:, b], out_offset=None, in_=dram["h2"],
                                                in_offset=bass.IndirectOffsetOnAxis(ap=ids_now[:, b:b + 1].bitcast(U32), axis=0)).then_inc(x_loaded[b], 16)

        @block.tensor
        def _(pe):
            used = used_blocks(pe)
            nc.tensor.transpose(ps_ids[:, 0:BLOCKS], id_rows[:], consts["ident"][0:BLOCKS, 0:BLOCKS]).then_inc(ids_turned, 1)
            with pe.Fori(0, BLOCKS // 2) as i:
                with pe.If(2 * i < used):
                    for b in range(2):
                        pe.wait_ge(x_loaded[b], 16 * i + 16)
                        pe.wait_ge(y_act[b], i)
                        pe.wait_ge(y_dve[b], i)
                        for k in range(DF):
                            mm = nc.tensor.transpose(ps_xy[b][:, k // 4, P * (k % 4):P * (k % 4) + P], xb[:, b, P * k:P * k + P], consts["ident"][:])
                        mm.then_inc(turned[b], 1)
                    for b in range(2):
                        pe.wait_ge(w13_loaded[b], 16 * i + 16)
                        pe.wait_ge(x_act[b], i + 1)
                        pe.wait_ge(x_dve[b], i + 1)
                        pe.wait_ge(hidden[b], i)
                        for f in range(2 * F2):
                            for k in range(DF):
                                mm = nc.tensor.matmul(ps_h[b][:, f], w13[:, b, k, P * f:P * f + P], xt[:, b, k], start=(k == 0), stop=(k == DF - 1))
                        mm.then_inc(h_full[b], 1)
                    for b in range(2):
                        pe.wait_ge(w2_loaded[b], 16 * i + 16)
                        pe.wait_ge(hidden[b], i + 1)
                        for c in range(2):
                            for k in range(F2):
                                mm = nc.tensor.matmul(ps_xy[b][:, c], hid[:, b, k], w2[:, b, k, 512 * c:512 * c + 512], start=(k == 0), stop=(k == F2 - 1))
                        mm.then_inc(y_full[b], 1)

        @block.scalar
        def _(act):
            used = used_blocks(act)
            with act.Fori(0, BLOCKS // 2) as i:
                with act.If(2 * i < used):
                    for b in range(2):
                        act.wait_ge(turned[b], i + 1)
                        act.wait_ge(h_full[b], i)
                        nc.scalar.copy(xt[:, b, 0:4].rearrange("p k t -> p (k t)"), ps_xy[b][:, 0]).then_inc(x_act[b], 1)
                    for b in range(2):
                        act.wait_ge(h_full[b], i + 1)
                        act.wait_ge(gated[b], i)
                        nc.scalar.activation(th[:, b], ps_h[b][:, 0:F2], ACT.Tanh, scale=0.5).then_inc(tanh[b], 1)
                    for b in range(2):
                        act.wait_ge(y_full[b], i + 1)
                        act.wait_ge(stored[b], 16 * i)
                        nc.scalar.copy(yb[:, b, 0:512], ps_xy[b][:, 0]).then_inc(y_act[b], 1)
                        act.wait_ge(y_act[b], i + 1)
                        act.wait_ge(y_dve[b], i + 1)
                        act.dma_start(dram["yb"][bass.ds(2 * i + b, 1)].rearrange("a p d -> p (a d)"), yb[:, b]).then_inc(stored[b], 16)
            pairs = used + 1 >> 1
            for b in range(2):
                act.wait_ge(stored[b], 16 * pairs)
                alone(act, unread)

        @block.vector
        def _(dve):
            used = used_blocks(dve)
            dve.wait_ge(ids_turned, 1)
            nc.vector.tensor_copy(ids[:], ps_ids[:, 0:BLOCKS]).then_inc(ids_turned, 1)
            with dve.Fori(0, BLOCKS // 2) as i:
                with dve.If(2 * i < used):
                    for b in range(2):
                        dve.wait_ge(turned[b], i + 1)
                        dve.wait_ge(h_full[b], i)
                        nc.vector.tensor_copy(xt[:, b, 4:8].rearrange("p k t -> p (k t)"), ps_xy[b][:, 1]).then_inc(x_dve[b], 1)
                    for b in range(2):
                        dve.wait_ge(tanh[b], i + 1)
                        dve.wait_ge(hidden[b], i)
                        nc.vector.scalar_tensor_tensor(out=act_in[:, b], in0=th[:, b], scalar=1.0, in1=ps_h[b][:, 0:F2], op0=ALU.add,
                                                       op1=ALU.mult).then_inc(gated[b], 1)
                        dve.wait_ge(gated[b], i + 1)
                        dve.wait_ge(y_full[b], i)
                        nc.vector.scalar_tensor_tensor(out=hid[:, b], in0=act_in[:, b], scalar=0.5, in1=ps_h[b][:, F2:2 * F2], op0=ALU.mult,
                                                       op1=ALU.mult).then_inc(hidden[b], 1)
                    for b in range(2):
                        dve.wait_ge(y_full[b], i + 1)
                        dve.wait_ge(stored[b], 16 * i)
                        nc.vector.tensor_copy(yb[:, b, 512:1024], ps_xy[b][:, 1]).then_inc(y_dve[b], 1)


def combine(nc, dram, consts, weight, slot):
    with ExitStack() as ctx:
        s = Scope(nc, ctx)
        gate2 = s.sb("gate2_broadcast", [P, 2, D])
        x1 = s.sb("x1_again", [P, 2, D])
        picked = s.sb("picked", [P, 2, TOP, D])
        mix = s.sb("mixed", [P, 2, D])
        out = s.sb("out_tile", [P, 2, D])
        pair = lambda n: [s.sem(f"comb_{n}{b}") for b in range(2)]
        loaded, gathered, stored, done = pair("loaded"), pair("gathered"), pair("stored"), pair("done")
        consts_in, own = s.sem("comb_consts"), s.sem("comb_own")
        block = ctx.enter_context(nc.Block())
        yb = dram["yb"].rearrange("b p d -> (b p) d")

        @block.sync
        def _(sp):
            for q in range(2):
                row = (GATE2 * 2 + q) * DF
                sp.dma_start(gate2[:, q], dram["mod_rows"][row:row + DF, :].rearrange("f p -> (f p)").partition_broadcast(P)).then_inc(consts_in, 16)
            for t in range(TT + 1):
                b = t % 2
                if t < TT:
                    if t >= 2:
                        sp.wait_ge(done[b], t // 2)
                    sp.dma_start(x1[:, b], dram["x1"][P * t:P * t + P, :]).then_inc(loaded[b], 16)
                if t >= 1:
                    c = (t - 1) % 2
                    sp.wait_ge(done[c], (t - 1) // 2 + 1)
                    sp.dma_start(dram["y"][P * (t - 1):P * t, :], out[:, c]).then_inc(stored[c], 16)
            for b in range(2):
                sp.wait_ge(stored[b], 16 * (TT // 2))

        @block.gpsimd
        def _(pool):
            for t in range(TT):
                b = t % 2
                if t >= 2:
                    pool.wait_ge(done[b], t // 2)
                for k in range(TOP):
                    pool.indirect_dma_start(out=picked[:, b, k], out_offset=None, in_=yb,
                                            in_offset=bass.IndirectOffsetOnAxis(ap=slot[:, k, t:t + 1], axis=0)).then_inc(gathered[b], 16)

        @block.vector
        def _(dve):
            dve.wait_ge(consts_in, 32)
            do = Chain(dve, own)
            for t in range(TT):
                b, q = t % 2, int(t >= SEQS[0] // P)
                dve.wait_ge(gathered[b], 32 * (t // 2) + 32)
                do(nc.vector.tensor_scalar(mix[:, b], picked[:, b, 0], weight[:, 0, t:t + 1], None, ALU.mult))
                do(nc.vector.scalar_tensor_tensor(out=mix[:, b], in0=picked[:, b, 1], scalar=weight[:, 1, t:t + 1], in1=mix[:, b],
                                                  op0=ALU.mult, op1=ALU.add))
                do(nc.vector.tensor_tensor(mix[:, b], mix[:, b], gate2[:, q], ALU.mult))
                dve.wait_ge(loaded[b], 16 * (t // 2) + 16)
                if t >= 2:
                    dve.wait_ge(stored[b], 16 * (t // 2))
                nc.vector.tensor_tensor(out[:, b], mix[:, b], x1[:, b], ALU.add).then_inc(done[b], 1)


def encoder(nc, dram):
    with ExitStack() as ctx:
        s = Scope(nc, ctx)
        consts = {
            "cols": s.sb("cols", [P, NCOLS]),
            "ident": s.sb("ident", [P, P]),
            "ones": s.sb("ones", [P, P]),
            "mod": s.sb("mod", [P, 6, 2, DF]),
            "scale1": s.sb("scale1", [P, 2, DF]),
            "half_merge": s.sb("half_merge", [P, N_GATES]),
            "p_end": s.sb("p_end", [P, 2, RF, TOK // CH]),
        }
        load_constants(nc, dram, consts)
        modulation(nc, dram, consts)
        with ExitStack() as inner:
            hs = Scope(nc, inner)
            h_hi, h_lo = hs.sb("h_t_high", [P, DF, TOK], F32R), hs.sb("h_t_low", [P, DF, TOK], F32R)
            norm_and_turn(nc, dram, consts, h_hi, h_lo)
            project_in(nc, dram, consts, h_hi, h_lo)
        rwkv_operands(nc, dram, consts)
        wkv_scan(nc, dram, consts)
        mla_project(nc, dram, consts)
        logits = s.sb("logits", [P, TT, ROUTER])
        with ExitStack() as outer:
            merged = Scope(nc, outer).sb("merged_t", [P, DF, TOK])
            with ExitStack() as inner:
                i = Scope(nc, inner)
                om_t = i.sb("om_t", [P, RF, TOK])
                with ExitStack() as deep:
                    o_all = Scope(nc, deep).sb("o_all", [P, TT, 512])
                    attention(nc, dram, consts, o_all)
                    turn_o(nc, dram, consts, o_all, om_t)
                oa_t = i.sb("oa_t", [P, RF, TOK])
                rwkv_finish(nc, dram, consts, oa_t)
                merge_branches(nc, dram, consts, oa_t, om_t, merged)
            output_and_router(nc, dram, consts, merged, logits)
        weight = s.sb("weight", [P, TOP, TT])
        slot = s.sb("slot", [P, TOP, TT], U32)
        route(nc, dram, consts, logits, weight, slot)
        experts(nc, dram, consts)
        combine(nc, dram, consts, weight, slot)


INTERNAL = {
    "mod_rows": (96, P),
    "p_t": (N_SHIFTED, P, TOK),
    "gates": (N_GATES, P, TOK),
    "wkv_in": (2, TT, P, 16, P),
    "wkv_y": (2, TT, P, RF, P),
    "qk_t": (2 * HEADS, HD, TOK),
    "v_mla": (TT, P, 512),
    "x1": (TOK, D),
    "h2": (TOK, D),
    "row_token": (BLOCKS * MB, 1),
    "block_expert": (1, BLOCKS + 1),
    "yb": (BLOCKS, MB, D),
}


INTERNAL_TYPES = {"block_expert": I32}


def _tiles(w, width):
    K, M = w.shape
    return np.ascontiguousarray(w.reshape(K // P, P, M // width, width).transpose(2, 1, 0, 3))


def _lay_out(inputs):
    a = {k: np.asarray(v) for k, v in inputs.items()}
    one = {k: v[0] for k, v in a.items() if k not in ("x_prompt", "x_sample", "c_prompt", "c_sample")}
    out = {"x": np.concatenate([a["x_prompt"][0], a["x_sample"][0]])}
    out["c"] = np.concatenate([a["c_prompt"], a["c_sample"]]).reshape(2 * DF, P)
    out["w_ada"] = _tiles(one["w_ada"], 512)
    out["b_ada"] = one["b_ada"].reshape(1, -1)
    w_in = one["w_in"]
    rw, q, kv, rope = 1920, 768, 256, 32
    wide = np.zeros((D, P), w_in.dtype)
    wide[:, 64:96] = w_in[:, rw + q + kv:rw + q + kv + rope]
    out["w_in"] = _tiles(np.concatenate([w_in[:, :rw], wide, w_in[:, rw:rw + q + kv], w_in[:, rw + q + kv + rope:]], 1), P)

    def columns(v, width):
        v = v.reshape(-1)
        full = np.zeros((width, P), np.float32)
        full.reshape(-1)[:v.size] = v
        return full.T

    gain = lambda a, b: np.concatenate([one[a], one[b]])
    parts = {
        "norm1": one["norm1"], "mu_prev": one["shift_mu"][0], "mu_next": one["shift_mu"][1],
        "b_merge": one["b_merge"], "w0": one["decay_w0"], "a0": one["iclr_a0"], "k_k": one["k_k"], "k_a": one["k_a"],
        "r_k": one["r_k"], "gn_w": one["gn_w"], "gn_b": one["gn_b"], "qa_norm": one["q_a_norm"], "kva_norm": one["kv_a_norm"],
        "q_gain": gain("q_nope_norm", "q_rope_norm"), "k_gain": gain("k_nope_norm", "k_rope_norm"),
    }
    out["cols"] = np.ascontiguousarray(np.concatenate([columns(parts[k], w) for k, (_, w) in COLS.items()], 1))
    out["ident"] = np.eye(P, dtype=np.float32)
    out["ones"] = np.ones((P, P), np.float32)
    more_layouts(out, one)
    return out


def more_layouts(out, one):
    out["decay_up"] = one["decay_up"].reshape(P, -1)
    out["iclr_up"] = one["iclr_up"].reshape(P, -1)
    out["chunk_reset"] = np.tile((np.arange(RF * PB) % CH != 0).astype(np.float32), (P, 1))
    out["gate_up"] = one["gate_up"]
    out["w_o"] = np.stack([_tiles(one["w_o_rwkv"], P), _tiles(one["w_o_mla"], P)])
    rows = lambda w: np.ascontiguousarray(w.reshape(-1, P, w.shape[-1]).transpose(1, 0, 2))
    out["w_out"] = rows(one["w_out"])
    out["w_router"] = rows(np.concatenate([one["w_rg"], one["w_re"]], 1))
    out["b_router"] = np.concatenate([one["b_rg"], one["b_re"]])
    out["norm2"] = one["norm2"]
    out["w13"] = np.ascontiguousarray(one["w13"].reshape(EXPERTS, DF, P, -1).transpose(0, 2, 1, 3))
    out["w2"] = np.ascontiguousarray(one["w2"].reshape(EXPERTS, D_EXPERT // P, P, D).transpose(0, 2, 1, 3))
    out["rank_groups"] = np.arange(GROUPS, 0, -1, dtype=np.float32)
    out["rank_experts"] = np.arange(EXPERTS, 0, -1, dtype=np.float32)
    out["full_at"] = MB * np.arange(TT, dtype=np.float32)
    out["block_no"] = np.arange(BLOCKS, dtype=np.float32)
    out["tokens_before"] = np.triu(np.ones((P, P), np.float32), 1)
    out["token_ids"] = np.ascontiguousarray(np.arange(TOK, dtype=np.float32).reshape(TT, P).T)
    by_head = lambda w, n: w.reshape(n, P, HEADS, -1).transpose(1, 0, 2, 3)
    out["w_uq"] = np.ascontiguousarray(by_head(one["w_uq"], QF))
    out["w_uk"] = np.zeros((P, KVF, HEADS, HD), np.float32)
    out["w_uk"][..., :NOPE] = by_head(one["w_uk"], KVF)
    out["w_uv"] = np.ascontiguousarray(one["w_uv"].reshape(KVF, P, 512).transpose(1, 0, 2))
    U = 2 * HEADS
    out["gather_means"] = np.zeros((HD, U, 2 * U), np.float32)
    out["spread_rstd"] = np.zeros((P, U, HD), np.float32)
    for u in range(U):
        for j, part in enumerate((slice(0, NOPE), slice(NOPE, HD))):
            out["gather_means"][part, u, 2 * u + j] = 1.0 / (NOPE, ROPE)[j]
            out["spread_rstd"][2 * u + j, u, part] = 1.0
    out["rotate"] = np.zeros((HD, HD), np.float32)
    for k in range(ROPE // 2):
        out["rotate"][NOPE + ROPE // 2 + k, NOPE + k] = -1.0
        out["rotate"][NOPE + k, NOPE + ROPE // 2 + k] = 1.0
    inv = np.float32(1.0) / (np.float32(10000.0) ** (np.arange(0, ROPE, 2, dtype=np.float32) / np.float32(ROPE)))
    ang = np.concatenate([np.arange(n, dtype=np.float32)[:, None] * inv[None] for n in SEQS]).T
    out["rope"] = np.zeros((HD, 2, TOK), np.float32)
    out["rope"][:NOPE, 0] = 1.0
    out["rope"][NOPE:, 0] = np.tile(np.cos(ang), (2, 1))
    out["rope"][NOPE:, 1] = np.tile(np.sin(ang), (2, 1))
    head = np.arange(P) // CH
    j, t = np.arange(CH)[:, None], np.arange(CH)[None]
    masks = np.array([[j < t, j <= t], [j > t, j >= t]], np.float32).transpose(2, 0, 1, 3)
    out["tri_mask"] = np.concatenate([masks, masks])
    j, t = np.arange(P)[:, None], np.arange(P)[None]
    out["level_mask"] = np.array([((j >> l) ^ (t >> l)) == 1 for l in range(LEVELS)], np.float32).transpose(1, 0, 2).copy()
    out["ident_halves"] = np.tile(np.eye(CH, dtype=np.float32), (2, 1))
    out["head_ones"] = (head[:, None] == head[None]).astype(np.float32)


def kernel(**inputs):
    import concourse.bacc as bacc
    from concourse.bass_utils import run_bass_kernel_spmd

    nc = bacc.Bacc("TRN2", target_bir_lowering=False, num_devices=1)
    arrays = _lay_out(inputs)
    dram = {k: nc.dram_tensor(f"in_{k}", v.shape, mybir.dt.from_np(v.dtype), kind="ExternalInput").ap() for k, v in arrays.items()}
    for k, shape in INTERNAL.items():
        dram[k] = nc.dram_tensor(k, shape, INTERNAL_TYPES.get(k, F32), kind="Internal").ap()
    dram["y"] = nc.dram_tensor("y", (TOK, D), F32, kind="ExternalOutput").ap()
    encoder(nc, dram)
    r = run_bass_kernel_spmd(nc, [{f"in_{k}": v for k, v in arrays.items()}], core_ids=[0])
    y = r.results[0]["y"]
    return y[None, :SEQS[0]], y[None, SEQS[0]:]
```

```python
from contextlib import ExitStack

import numpy as np

import concourse.bass as bass
from concourse import mybir

ALU = mybir.AluOpType
ACT = mybir.ActivationFunctionType
AX = mybir.AxisListType
F32 = mybir.dt.float32
I32 = mybir.dt.int32
U32 = mybir.dt.uint32
F32R = mybir.dt.float32r

P = 128
D = 1024
DF = D // P
SEQS = (1024, 512)
TOK = sum(SEQS)
TT = TOK // P
NB = 512
NT = TOK // NB
EPS = 1e-6

COLS = {}
_n = 0
for _name, _w in (("norm1", 8), ("mu_prev", 24), ("mu_next", 24), ("b_merge", 16),
                  ("w0", 8), ("a0", 8), ("k_k", 4), ("k_a", 4), ("r_k", 4), ("gn_w", 4), ("gn_b", 4),
                  ("qa_norm", 6), ("kva_norm", 2), ("q_gain", 1), ("k_gain", 1)):
    COLS[_name] = (_n, _w)
    _n += _w
NCOLS = _n

SHIFT1, SCALE1, GATE1, SHIFT2, SCALE2, GATE2 = range(6)
N_SHIFTED = 24
N_GATES = 16


class Chain:

    def __init__(self, eng, sem, base=0, i=None, per=0):
        self.eng, self.sem, self.base, self.i, self.per, self.n = eng, sem, base, i, per, 0

    def value(self):
        v = self.base + self.n
        return v if self.i is None else self.i * self.per + v

    def __call__(self, ins):
        self.n += 1
        ins.then_inc(self.sem, 1)
        self.eng.wait_ge(self.sem, self.value())

    def end(self):
        assert self.i is None or self.n == self.per, (self.n, self.per)


def alone(eng, sem):
    eng.sem_inc(sem, 1)


class Scope:

    def __init__(self, nc, ctx):
        self.nc, self.ctx, self.sems = nc, ctx, []
        ctx.callback(self.clear)

    def clear(self):
        if self.sems:
            self.nc.clear_and_free_semaphores(self.sems)
            self.nc.all_engine_barrier()

    def sb(self, name, shape, dt=F32):
        return self.ctx.enter_context(self.nc.sbuf_tensor(name, shape, dt))

    def ps(self, name, shape, dt=F32):
        return self.ctx.enter_context(self.nc.psum_tensor(name, shape, dt))

    def sem(self, name):
        self.sems.append(self.nc.alloc_semaphore(name))
        return self.sems[-1]


def col(consts, name, k=0, n=None):
    first, width = COLS[name]
    return consts["cols"][:, first + k:first + (width if n is None else k + n)]


def split_product(nc, out, w, x, start, stop):
    nc.tensor.matmul(out, w[0], x[1], start=start, stop=False)
    nc.tensor.matmul(out, w[1], x[0], start=False, stop=False)
    return nc.tensor.matmul(out, w[0], x[0], start=False, stop=stop)


def load_constants(nc, dram, consts):
    with ExitStack() as ctx:
        s = Scope(nc, ctx)
        loaded = s.sem("constants_loaded")
        block = ctx.enter_context(nc.Block())

        @block.sync
        def _(sp):
            sp.dma_start(consts["cols"][:], dram["cols"][:, :]).then_inc(loaded, 16)
            sp.dma_start(consts["ident"][:], dram["ident"][:, :]).then_inc(loaded, 16)
            sp.dma_start(consts["ones"][:], dram["ones"][:, :]).then_inc(loaded, 16)
            sp.wait_ge(loaded, 48)


def modulation_and_norm(nc, dram, consts, xn_t):
    mod = consts["mod"]
    BUF = 4
    with ExitStack() as ctx:
        s = Scope(nc, ctx)
        c_rows = s.sb("c_rows", [2 * DF, P])
        c_col = s.sb("c_col", [P, 2 * DF])
        c_tanh = s.sb("c_tanh", [P, 2 * DF])
        c_silu = s.sb("c_silu", [P, DF, 2])
        w = s.sb("w_ada_tile", [P, BUF, DF, 512])
        b_ada = s.sb("b_ada_rows", [2, BUF, 512])
        x = s.sb("x_tile", [P, 2, D])
        sq = s.sb("x_square", [P, D])
        ss = s.sb("x_ss", [P, 2, 2])
        xn = s.sb("x_normed", [P, 2, D])
        rows = s.sb("mod_rows_sb", [2, 6 * D])
        turned_in = s.sb("mod_rows_turned_in", [96, P])
        ps_c = s.ps("ps_c", [P, 512])
        ps_mod = s.ps("ps_mod", [2, BUF, 512])
        ps_x = s.ps("ps_x_turned", [P, 2, 512])
        c_loaded, c_turned, tanh_done, silu_done = (s.sem(n) for n in ("c_loaded", "c_turned", "tanh_done", "silu_done"))
        x_loaded = [s.sem(f"x_loaded{b}") for b in range(2)]
        summed, rms_in, rms_ready, inv_ready, normed, turned, kept_act, kept_dve, unread_act, unread_pool = (
            s.sem("x_" + n) for n in ("summed", "rms_in", "rms_ready", "inv_ready", "normed", "turned", "kept_act", "kept_dve", "unread_act", "unread_pool"))
        w_loaded = [s.sem(f"w_ada_loaded{b}") for b in range(BUF)]
        ps_full = [s.sem(f"mod_ps_full{b}") for b in range(BUF)]
        ps_free = [s.sem(f"mod_ps_free{b}") for b in range(BUF)]
        own, rows_ready, rows_turned = (s.sem(n) for n in ("mod_own", "mod_rows_ready", "mod_rows_turned"))
        stored, reloaded = s.sem("mod_stored"), s.sem("mod_reloaded")
        block = ctx.enter_context(nc.Block())
        N = TT
        assert N * 512 == 6 * D

        @block.sync
        def _(sp):
            sp.dma_start(c_rows[:], dram["c"][:, :]).then_inc(c_loaded, 16)
            with sp.Fori(0, N // BUF) as j:
                for b in range(BUF):
                    sp.wait_ge(ps_free[b], j)
                    sp.dma_start(w[:, b], dram["w_ada"][bass.ds(j * BUF + b, 1)].rearrange("a p k m -> p (a k) m")).then_inc(w_loaded[b], 16)
                    for q in range(2):
                        sp.dma_start(b_ada[q:q + 1, b], dram["b_ada"][bass.ds(j * BUF + b, 1), :]).then_inc(w_loaded[b], 16)
            sp.wait_ge(rows_ready, 1)
            sp.dma_start(dram["mod_rows"].rearrange("(j q f) p -> q j (f p)", j=6, q=2), rows[:].rearrange("q (j x) -> q j x", j=6)).then_inc(stored, 16)
            sp.wait_ge(stored, 16)
            sp.dma_start(turned_in[:], dram["mod_rows"][:, :]).then_inc(reloaded, 16)

        @block.tensor
        def _(pe):
            pe.wait_ge(c_loaded, 16)
            nc.tensor.transpose(ps_c[:, 0:2 * DF], c_rows[:], consts["ident"][0:2 * DF, 0:2 * DF]).then_inc(c_turned, 1)
            pe.wait_ge(silu_done, 2)
            with pe.Fori(0, N // BUF) as j:
                for b in range(BUF):
                    t = BUF * j + b
                    pe.wait_ge(w_loaded[b], 48 * j + 48)
                    pe.wait_ge(ps_free[b], j)
                    for k in range(DF):
                        mm = nc.tensor.matmul(ps_mod[:, b], c_silu[:, k], w[:, b, k], start=(k == 0), stop=(k == DF - 1))
                    mm.then_inc(ps_full[b], 1)
                    pe.wait_ge(normed, t + 1)
                    pe.wait_ge(kept_act, t)
                    pe.wait_ge(kept_dve, t)
                    for f in range(DF):
                        mm = nc.tensor.transpose(ps_x[:, f // 4, P * (f % 4):P * (f % 4) + P], xn[:, b % 2, P * f:P * f + P], consts["ident"][:])
                    mm.then_inc(turned, 1)
            pe.wait_ge(reloaded, 16)
            nc.tensor.transpose(ps_c[:, 0:96], turned_in[:], consts["ident"][0:96, 0:96]).then_inc(rows_turned, 1)

        @block.scalar
        def _(act):
            act.wait_ge(c_turned, 1)
            nc.scalar.activation(c_tanh[:], ps_c[:, 0:2 * DF], ACT.Tanh, scale=0.5).then_inc(tanh_done, 1)
            with act.Fori(0, N // BUF) as j:
                for b in range(BUF):
                    t, c = BUF * j + b, b % 2
                    act.wait_ge(x_loaded[c], 32 * j + (16 * (b // 2) + 16))
                    nc.scalar.activation(sq[:], x[:, c], ACT.Square, accum_out=ss[:, c, 0:1]).then_inc(summed, 1)
                    act.wait_ge(rms_in, t + 1)
                    nc.scalar.activation(ss[:, c, 1:2], ss[:, c, 0:1], ACT.Sqrt).then_inc(rms_ready, 1)
                    act.wait_ge(turned, t + 1)
                    alone(act, unread_act)
                    nc.scalar.copy(xn_t[:, 0:4, bass.ds(t * P, P)], ps_x[:, 0].rearrange("p (f t) -> p f t", f=4)).then_inc(kept_act, 1)

        @block.gpsimd
        def _(pool):
            with pool.Fori(0, N // BUF) as j:
                for b in range(BUF):
                    t = BUF * j + b
                    if b < 2:
                        pool.wait_ge(normed, BUF * j)
                    else:
                        pool.wait_ge(normed, BUF * j + (b - 1))
                    alone(pool, unread_pool)
                    pool.dma_start(x[:, b % 2], dram["x"][bass.ds(t * P, P), :]).then_inc(x_loaded[b % 2], 16)

        @block.vector
        def _(dve):
            dve.wait_ge(tanh_done, 1)
            nc.vector.tensor_scalar(c_col[:], ps_c[:, 0:2 * DF], 0.5, None, ALU.mult).then_inc(silu_done, 1)
            dve.wait_ge(silu_done, 1)
            nc.vector.scalar_tensor_tensor(out=c_silu[:].rearrange("p k q -> p q k"), in0=c_tanh[:].rearrange("p (q k) -> p q k", q=2), scalar=1.0,
                                           in1=c_col[:].rearrange("p (q k) -> p q k", q=2), op0=ALU.add, op1=ALU.mult).then_inc(silu_done, 1)
            with dve.Fori(0, N // BUF) as j:
                for b in range(BUF):
                    t, c = BUF * j + b, b % 2
                    dve.wait_ge(summed, t + 1)
                    nc.vector.tensor_scalar(ss[:, c, 0:1], ss[:, c, 0:1], 1.0 / D, EPS, ALU.mult, ALU.add).then_inc(rms_in, 1)
                    dve.wait_ge(rms_ready, t + 1)
                    nc.vector.reciprocal(ss[:, c, 1:2], ss[:, c, 1:2]).then_inc(inv_ready, 1)
                    dve.wait_ge(inv_ready, t + 1)
                    dve.wait_ge(turned, t)
                    nc.vector.tensor_scalar(xn[:, c], x[:, c], ss[:, c, 1:2], None, ALU.mult).then_inc(normed, 1)
                    dve.wait_ge(ps_full[b], j + 1)
                    at = bass.ds(j * (512 * BUF) + 512 * b, 512)
                    nc.vector.tensor_tensor(rows[:, at], ps_mod[:, b], b_ada[:, b], ALU.add).then_inc(ps_free[b], 1)
                    dve.wait_ge(turned, t + 1)
                    nc.vector.tensor_copy(xn_t[:, 4:8, bass.ds(t * P, P)], ps_x[:, 1].rearrange("p (f t) -> p f t", f=4)).then_inc(kept_dve, 1)
            for b in range(BUF):
                dve.wait_ge(ps_free[b], N // BUF)
            for part in (SCALE1, SCALE2):
                ins = nc.vector.tensor_scalar(rows[:, D * part:D * part + D], rows[:, D * part:D * part + D], 1.0, None, ALU.add)
            ins.then_inc(rows_ready, 1)
            dve.wait_ge(rows_turned, 1)
            nc.vector.tensor_copy(mod[:].rearrange("p j q f -> p (j q f)"), ps_c[:, 0:96]).then_inc(own, 1)
            dve.wait_ge(own, 1)
            for q in range(2):
                ins = nc.vector.tensor_tensor(consts["scale1"][:, q], mod[:, SCALE1, q], col(consts, "norm1"), ALU.mult)
            ins.then_inc(own, 1)
            dve.wait_ge(own, 2)


def modulate_and_split(nc, dram, consts, h_hi, h_lo):
    with ExitStack() as ctx:
        s = Scope(nc, ctx)
        h = s.sb("h_now", [P, NT, NB])
        h_ready, hi_ready, lo_ready, unread = (s.sem("h_" + n) for n in ("ready", "hi_ready", "lo_ready", "unread"))
        block = ctx.enter_context(nc.Block())
        sequence = [int(n * NB >= SEQS[0]) for n in range(NT)]
        part = lambda t, f, n: t[:, bass.ds(f, 1), NB * n:NB * n + NB].rearrange("p a t -> p (a t)")

        @block.vector
        def _(dve):
            with dve.Fori(0, DF) as f:
                dve.wait_ge(lo_ready, NT * f)
                for n, q in enumerate(sequence):
                    nc.vector.tensor_scalar(h[:, n], part(h_hi, f, n).bitcast(F32), consts["scale1"][:, q, bass.ds(f, 1)],
                                            consts["mod"][:, SHIFT1, q, bass.ds(f, 1)], ALU.mult, ALU.add).then_inc(h_ready, 1)
                for n in range(NT):
                    dve.wait_ge(hi_ready, NT * f + (n + 1))
                    nc.vector.tensor_tensor(part(h_lo, f, n), h[:, n], part(h_hi, f, n).bitcast(F32), ALU.subtract).then_inc(lo_ready, 1)

        @block.scalar
        def _(act):
            with act.Fori(0, DF) as f:
                for n in range(NT):
                    act.wait_ge(h_ready, NT * f + (n + 1))
                    alone(act, unread)
                    nc.scalar.copy(part(h_hi, f, n), h[:, n]).then_inc(hi_ready, 1)


def project_in(nc, dram, consts, h_hi, h_lo):
    L, R = SEQS
    W = TOK + 1
    starts = (1, 513, L + 2)
    with ExitStack() as ctx:
        s = Scope(nc, ctx)
        w = s.sb("w_in_tile", [P, 2, DF, P])
        w_hi = s.sb("w_in_high", [P, 2, DF, P], F32R)
        w_lo = s.sb("w_in_low", [P, 2, DF, P], F32R)
        hi_ready = [s.sem(f"w_in_hi{b}") for b in range(2)]
        w_split = [s.sem(f"w_in_split{b}") for b in range(2)]
        row = s.sb("p_row", [P, 2, TOK + 3])
        mix = s.sb("p_mixed", [P, 2, W])
        mu_c = s.sb("mu_centre", [P, N_SHIFTED])
        ps = s.ps("ps_in", [P, 2, NT, NB])
        w_loaded = [s.sem(f"w_in_loaded{b}") for b in range(2)]
        full = [[s.sem(f"in_full{b}{n}") for n in range(NT)] for b in range(2)]
        copied = [[s.sem(f"in_copied{b}{n}") for n in range(NT)] for b in range(2)]
        mixed = [s.sem(f"in_mixed{b}") for b in range(2)]
        stored = [s.sem(f"in_stored{b}") for b in range(2)]
        ready = s.sem("in_ready")
        bias_now = s.sb("bias_now", [P, 2])
        bias_ready = s.sem("bias_ready")
        own = s.sem("in_own")
        unread, unread_pool = s.sem("in_unread"), s.sem("in_unread_pool")
        block = ctx.enter_context(nc.Block())
        HS, HG = N_SHIFTED // 2, N_GATES // 2

        @block.sync
        def _(sp):
            with sp.Fori(0, HS + HG) as i:
                for b in range(2):
                    sp.wait_ge(w_split[b], i)
                    sp.dma_start(w[:, b], dram["w_in"][bass.ds(2 * i + b, 1)].rearrange("a p k m -> p (a k) m")).then_inc(w_loaded[b], 16)

        @block.gpsimd
        def _(pool):
            with pool.Fori(0, HS + HG) as i:
                for b in range(2):
                    pool.wait_ge(w_loaded[b], 16 * i + 16)
                    pool.wait_ge(full[b][NT - 1], i)
                    alone(pool, unread_pool)
                    nc.gpsimd.tensor_copy(w_hi[:, b], w[:, b]).then_inc(hi_ready[b], 1)
                    pool.wait_ge(hi_ready[b], i + 1)
                    nc.gpsimd.tensor_tensor(w_lo[:, b], w[:, b], w_hi[:, b].bitcast(F32), ALU.subtract).then_inc(w_split[b], 1)

        @block.tensor
        def _(pe):
            with pe.Fori(0, HS + HG) as i:
                for b in range(2):
                    pe.wait_ge(w_split[b], i + 1)
                    for n in range(NT):
                        pe.wait_ge(copied[b][n], i)
                        for k in range(DF):
                            at = slice(NB * n, NB * n + NB)
                            mm = split_product(nc, ps[:, b, n], (w_hi[:, b, k], w_lo[:, b, k]), (h_hi[:, k, at], h_lo[:, k, at]),
                                               start=(k == 0), stop=(k == DF - 1))
                        mm.then_inc(full[b][n], 1)

        @block.scalar
        def _(act):
            act.wait_ge(ready, 1)
            with act.Fori(0, HS) as i:
                for b in range(2):
                    act.wait_ge(mixed[b], i)
                    for n in range(NT):
                        act.wait_ge(full[b][n], i + 1)
                        nc.scalar.copy(row[:, b, starts[n]:starts[n] + NB], ps[:, b, n]).then_inc(copied[b][n], 1)
                    act.wait_ge(mixed[b], i + 1)
                    act.dma_start(dram["p_t"][bass.ds(2 * i + b, 1), :, 0:L].rearrange("a p t -> (a p) t"), mix[:, b, 0:L]).then_inc(stored[b], 16)
                    act.dma_start(dram["p_t"][bass.ds(2 * i + b, 1), :, L:TOK].rearrange("a p t -> (a p) t"), mix[:, b, L + 1:W]).then_inc(stored[b], 16)
            with act.Fori(HS, HS + HG) as i:
                for b in range(2):
                    act.wait_ge(mixed[b], i)
                    alone(act, unread)
                    nc.scalar.copy(bias_now[:, b:b + 1], consts["half_merge"][:, bass.ds(2 * i + (b - N_SHIFTED), 1)]).then_inc(bias_ready, 1)
                    act.wait_ge(bias_ready, 2 * i + (b + 1 - 2 * HS))
                    for n in range(NT):
                        act.wait_ge(full[b][n], i + 1)
                        nc.scalar.activation(row[:, b, NB * n:NB * n + NB], ps[:, b, n], ACT.Tanh, bias=bias_now[:, b:b + 1], scale=0.5).then_inc(copied[b][n], 1)
                    act.wait_ge(mixed[b], i + 1)
                    act.dma_start(dram["gates"][bass.ds(2 * i + (b - N_SHIFTED), 1)].rearrange("a p t -> (a p) t"), mix[:, b, 0:TOK]).then_inc(stored[b], 16)
            for b in range(2):
                act.wait_ge(stored[b], 16 * (2 * HS + HG))

        @block.vector
        def _(dve):
            prev, nxt = COLS["mu_prev"][0], COLS["mu_next"][0]
            start = Chain(dve, own)
            start(nc.vector.tensor_tensor(mu_c[:], col(consts, "mu_prev"), col(consts, "mu_next"), ALU.add))
            start(nc.vector.tensor_scalar(mu_c[:], mu_c[:], -1.0, 1.0, ALU.mult, ALU.add))
            start(nc.vector.tensor_scalar(consts["half_merge"][:], col(consts, "b_merge"), 0.5, None, ALU.mult))
            start(nc.vector.memset(row[:], 0.0))
            start(nc.vector.memset(mix[:], 0.0))
            dve.sem_inc(ready, 1)
            with dve.Fori(0, HS) as i:
                step = Chain(dve, own, start.n, i, 4)
                for b in range(2):
                    c = 2 * i + b
                    for n in range(NT):
                        dve.wait_ge(copied[b][n], i + 1)
                    dve.wait_ge(stored[b], 32 * i)
                    step(nc.vector.tensor_scalar(mix[:, b], row[:, b, 1:1 + W], mu_c[:, bass.ds(c, 1)], None, ALU.mult))
                    step(nc.vector.scalar_tensor_tensor(out=mix[:, b], in0=row[:, b, 0:W], scalar=consts["cols"][:, bass.ds(c + prev, 1)],
                                                        in1=mix[:, b], op0=ALU.mult, op1=ALU.add))
                    nc.vector.scalar_tensor_tensor(out=mix[:, b], in0=row[:, b, 2:2 + W], scalar=consts["cols"][:, bass.ds(c + nxt, 1)],
                                                   in1=mix[:, b], op0=ALU.mult, op1=ALU.add).then_inc(mixed[b], 1)
                step.end()
            with dve.Fori(HS, HS + HG) as i:
                for b in range(2):
                    for n in range(NT):
                        dve.wait_ge(copied[b][n], i + 1)
                    dve.wait_ge(stored[b], 16 * i + 16 * HS)
                    nc.vector.tensor_scalar(mix[:, b, 0:TOK], row[:, b, 0:TOK], 0.5, 0.5, ALU.mult, ALU.add).then_inc(mixed[b], 1)


CH = 64
RF = 4
RT, KT_, VT, WD, AD, GD = 0, 4, 8, 12, 13, 14
PB = 256
DECAY = float(np.exp(-0.5))


def rwkv_operands(nc, dram, consts):
    with ExitStack() as ctx:
        s = Scope(nc, ctx)
        up_w = s.sb("decay_up", [P, RF * P])
        up_a = s.sb("iclr_up", [P, RF * P])
        reset = s.sb("chunk_reset", [P, RF * PB])
        gather = s.sb("gather_heads", [P, RF, 2 * RF])
        spread = s.sb("spread_heads", [P, RF, P])
        rms8, inv8 = s.sb("kk_norm", [2 * RF, PB]), s.sb("kk_inverse_norm", [P, PB])
        half_w0 = s.sb("half_w0", [P, 8])
        half_a0 = s.sb("half_a0", [P, 8])
        pin = s.sb("prep_in", [P, 2, 14, PB])
        W = [P, RF, PB]
        t_wd = s.sb("tanh_wd", [P, PB])
        kk_raw, sq, kk, kka, k1 = (s.sb(n, W) for n in ("kk_raw", "kk_square", "kk", "k_times_ka", "k_rest"))
        cum, kd, ba = (s.sb(n, W) for n in ("cum_decay", "k_d", "kk_a"))
        th_w, th_a, e_in, e_ex, p_in, p_ex, p_inv = ([s.sb(f"{n}{d}", W) for d in range(2)] for n in ("tanh_w", "tanh_a", "e_in", "e_ex", "p_in", "p_ex", "p_inv"))
        outs = s.sb("wkv_out", [P, 2, 4, RF, PB])
        ps_8 = s.ps("ps_norm_squares", [2 * RF, PB])
        ps_n = s.ps("ps_norm", [P, RF, PB])
        ps_w = s.ps("ps_w", [P, RF, PB])
        ps_a = s.ps("ps_a", [P, RF, PB])
        names = ("consts_in", "halves", "kk_raw_ready", "twd_ready", "sq_ready", "norm_summed", "sqrt_ready", "kk_ready",
                 "w_full", "a_full", "thw_ready", "tha_ready", "lw_used", "e_ready", "exp_ready", "pool_out", "dve_out",
                 "own", "pool_own", "kd_parts", "tha_used", "ends_ready", "inv_ready", "spread_full")
        m = {n: s.sem("prep_" + n) for n in names}
        loaded = [s.sem(f"prep_loaded{b}") for b in range(2)]
        in_used = [s.sem(f"prep_in_used{b}") for b in range(2)]
        stored = [s.sem(f"prep_stored{d}") for d in range(2)]
        block = ctx.enter_context(nc.Block())
        NI = TOK // PB // 2

        def bc(name, k=0):
            return col(consts, name, k, RF).unsqueeze(2).to_broadcast(W)

        def blocks(eng, body):
            with eng.Fori(0, NI - 1) as i:
                body(i, 0, (i, 1))
                body(i, 1, (i + 1, 0))
            body(NI - 1, 0, (NI - 1, 1))
            body(NI - 1, 1, None)

        @block.sync
        def _(sp):
            sp.dma_start(up_w[:], dram["decay_up"][:, :]).then_inc(m["consts_in"], 16)
            sp.dma_start(up_a[:], dram["iclr_up"][:, :]).then_inc(m["consts_in"], 16)
            sp.dma_start(reset[:], dram["chunk_reset"][:, :]).then_inc(m["consts_in"], 16)
            sp.dma_start(gather[:], dram["gather_heads"][:, :, :]).then_inc(m["consts_in"], 16)
            sp.dma_start(spread[:], dram["spread_heads"][:, :, :]).then_inc(m["consts_in"], 16)

            def load(t, b):
                sp.dma_start(pin[:, b], dram["p_t"][0:14, :, bass.ds(t * PB, PB)].rearrange("m p t -> p m t")).then_inc(loaded[b], 16)

            def store(t):
                for d in range(2):
                    sp.wait_ge(m["pool_out"], 2 * t + d + 1)
                    sp.wait_ge(m["dve_out"], 2 * t + d + 1)
                    for j in range(PB // P):
                        sp.dma_start(dram["wkv_in"][d, bass.ds(t * (PB // P) + j, 1)].rearrange("a p x t -> p (a x) t"),
                                     outs[:, d, :, :, P * j:P * j + P].rearrange("p q f t -> p (q f) t")).then_inc(stored[d], 16)

            for b in range(2):
                load(b, b)
            with sp.Fori(0, NI - 1) as i:
                for b in range(2):
                    store(2 * i + b)
                    sp.wait_ge(in_used[b], i + 1)
                    load(2 * i + (b + 2), b)
            for b in range(2):
                store(2 * NI - 2 + b)
            for d in range(2):
                sp.wait_ge(stored[d], 32 * 2 * NI)

        @block.tensor
        def _(pe):
            def gather_squares(t):
                pe.wait_ge(m["sq_ready"], t + 1)
                pe.wait_ge(m["sqrt_ready"], t)
                for f in range(RF):
                    mm = nc.tensor.matmul(ps_8[:], gather[:, f], sq[:, f], start=(f == 0), stop=(f == RF - 1))
                mm.then_inc(m["norm_summed"], 1)

            def spread_inverse(t):
                pe.wait_ge(m["inv_ready"], t + 1)
                pe.wait_ge(m["kk_ready"], t)
                for f in range(RF):
                    mm = nc.tensor.matmul(ps_n[:, f], spread[:, f], inv8[:], start=True, stop=True)
                mm.then_inc(m["spread_full"], 1)

            def body(i, b, then):
                t = 2 * i + b
                pe.wait_ge(m["twd_ready"], t + 1)
                for d in range(2):
                    h = slice(64 * d, 64 * d + 64)
                    pe.wait_ge(m["thw_ready"], 2 * t + d)
                    for f in range(RF):
                        mm = nc.tensor.matmul(ps_w[:, f], up_w[h, P * f:P * f + P], t_wd[h], start=True, stop=True)
                    mm.then_inc(m["w_full"], 1)
                    pe.wait_ge(m["tha_ready"], 2 * t + d)
                    for f in range(RF):
                        mm = nc.tensor.matmul(ps_a[:, f], up_a[h, P * f:P * f + P], pin[h, b, AD], start=True, stop=True)
                    mm.then_inc(m["a_full"], 1)
                if then:
                    gather_squares(t + 1)
                    spread_inverse(t + 1)

            pe.wait_ge(m["consts_in"], 80)
            gather_squares(0)
            spread_inverse(0)
            blocks(pe, body)

        @block.scalar
        def _(act):
            def square_and_root(t):
                act.wait_ge(m["kk_raw_ready"], t + 1)
                act.wait_ge(m["norm_summed"], t)
                nc.scalar.activation(sq[:], kk_raw[:], ACT.Square).then_inc(m["sq_ready"], 1)
                act.wait_ge(m["norm_summed"], t + 1)
                act.wait_ge(m["inv_ready"], t)
                nc.scalar.activation(rms8[:], ps_8[:], ACT.Sqrt).then_inc(m["sqrt_ready"], 1)

            def body(i, b, then):
                t = 2 * i + b
                act.wait_ge(loaded[b], 16 * i + 16)
                act.wait_ge(m["w_full"], 2 * t)
                nc.scalar.activation(t_wd[:], pin[:, b, WD], ACT.Tanh).then_inc(m["twd_ready"], 1)
                for d in range(2):
                    act.wait_ge(m["w_full"], 2 * t + (d + 1))
                    act.wait_ge(m["lw_used"], 2 * t)
                    for f in range(RF):
                        ins = nc.scalar.activation(th_w[d][:, f], ps_w[:, f], ACT.Tanh, bias=half_w0[:, RF * d + f:RF * d + f + 1], scale=0.5)
                    ins.then_inc(m["thw_ready"], 1)
                    act.wait_ge(m["a_full"], 2 * t + (d + 1))
                    act.wait_ge(m["tha_used"], 2 * t)
                    for f in range(RF):
                        ins = nc.scalar.activation(th_a[d][:, f], ps_a[:, f], ACT.Tanh, bias=half_a0[:, RF * d + f:RF * d + f + 1], scale=0.5)
                    ins.then_inc(m["tha_ready"], 1)
                for d in range(2):
                    act.wait_ge(m["e_ready"], 2 * t + (d + 1))
                    act.wait_ge(m["pool_out"], 2 * t)
                    act.wait_ge(m["dve_out"], 2 * t)
                    act.wait_ge(m["ends_ready"], 2 * t)
                    nc.scalar.activation(p_in[d][:], e_in[d][:], ACT.Exp).then_inc(m["exp_ready"], 1)
                    nc.scalar.activation(p_ex[d][:], e_ex[d][:], ACT.Exp).then_inc(m["exp_ready"], 1)
                    nc.scalar.activation(p_inv[d][:], e_in[d][:], ACT.Exp, scale=-1.0).then_inc(m["exp_ready"], 1)
                if then:
                    square_and_root(t + 1)

            act.wait_ge(m["halves"], 2)
            square_and_root(0)
            blocks(act, body)

        @block.gpsimd
        def _(pool):
            def raw_kk(i, b):
                pool.wait_ge(loaded[b], 16 * i + 16)
                pool.wait_ge(m["kk_ready"], 2 * i + b)
                nc.gpsimd.tensor_tensor(kk_raw[:], pin[:, b, KT_:KT_ + 4], bc("k_k"), ALU.mult).then_inc(m["kk_raw_ready"], 1)

            def body(i, b, then):
                t = 2 * i + b
                r, k = pin[:, b, RT:RT + 4], pin[:, b, KT_:KT_ + 4]
                pool.wait_ge(m["dve_out"], 2 * t)
                nc.gpsimd.tensor_tensor(kka[:], k, bc("k_a"), ALU.mult).then_inc(m["pool_own"], 1)
                pool.wait_ge(m["pool_own"], t + 1)
                nc.gpsimd.tensor_tensor(k1[:], k, kka[:], ALU.subtract).then_inc(m["kd_parts"], 1)
                if then:
                    raw_kk(*then)
                pool.wait_ge(m["kk_ready"], t + 1)
                for d in range(2):
                    pool.wait_ge(m["exp_ready"], 6 * t + (3 * d + 3))
                    pool.wait_ge(stored[d], 32 * t)
                    nc.gpsimd.tensor_tensor(outs[:, d, 1], r, p_in[d][:], ALU.mult)
                    nc.gpsimd.tensor_tensor(outs[:, d, 0], kk[:], p_ex[d][:], ALU.mult).then_inc(m["pool_out"], 1)

            raw_kk(0, 0)
            blocks(pool, body)

        @block.vector
        def _(dve):
            def inverse_norm(step, t):
                dve.wait_ge(m["sqrt_ready"], t + 1)
                step(nc.vector.tensor_scalar(rms8[:], rms8[:], 1e-12, None, ALU.max))
                dve.wait_ge(m["spread_full"], t)
                nc.vector.reciprocal(inv8[0:2 * RF], rms8[:]).then_inc(m["inv_ready"], 1)

            def body(step, i, b, then):
                t = 2 * i + b
                dve.wait_ge(m["spread_full"], t + 1)
                dve.wait_ge(m["kk_raw_ready"], t + 1)
                dve.wait_ge(m["pool_out"], 2 * t)
                for h in range(2):
                    ins = nc.vector.tensor_tensor(kk[:, 2 * h:2 * h + 2], kk_raw[:, 2 * h:2 * h + 2], ps_n[:, 2 * h:2 * h + 2], ALU.mult)
                ins.then_inc(m["kk_ready"], 1)
                dve.wait_ge(m["kd_parts"], t + 1)
                for d in range(2):
                    dve.wait_ge(m["thw_ready"], 2 * t + (d + 1))
                    step(nc.vector.tensor_scalar(th_w[d][:], th_w[d][:], -0.5 * DECAY, -0.5 * DECAY, ALU.mult, ALU.add))
                    flat = lambda x: x[:].rearrange("p f t -> p (f t)")
                    chunks = lambda x: x[:].rearrange("p f (c t) -> p (f c) t", t=CH)
                    dve.wait_ge(m["exp_ready"], 6 * t)
                    if d == 0:
                        step(nc.vector.tensor_tensor_scan(flat(e_in[d]), reset[:], flat(th_w[d]), 0.0, ALU.mult, ALU.add))
                        step(nc.vector.tensor_tensor(e_ex[d][:], e_in[d][:], th_w[d][:], ALU.subtract))
                    else:
                        step(nc.vector.tensor_tensor_scan(flat(cum), reset[:], flat(th_w[d]), 0.0, ALU.mult, ALU.add))
                        total = chunks(cum)[:, :, CH - 1:CH].to_broadcast([P, RF * PB // CH, CH])
                        step(nc.vector.tensor_tensor(chunks(e_ex[d]), total, chunks(cum), ALU.subtract))
                        step(nc.vector.tensor_tensor(e_in[d][:], e_ex[d][:], th_w[d][:], ALU.add))
                    dve.sem_inc(m["e_ready"], 1)
                    dve.sem_inc(m["lw_used"], 1)
                for d in range(2):
                    dve.wait_ge(m["tha_ready"], 2 * t + (d + 1))
                    dve.wait_ge(m["kk_ready"], t + 1)
                    step(nc.vector.tensor_scalar(th_a[d][:], th_a[d][:], 0.5, 0.5, ALU.mult, ALU.add))
                    nc.vector.tensor_tensor(ba[:], kk[:], th_a[d][:], ALU.mult)
                    step(nc.vector.tensor_tensor(kd[:], kka[:], th_a[d][:], ALU.mult))
                    dve.sem_inc(m["tha_used"], 1)
                    step(nc.vector.tensor_tensor(kd[:], kd[:], k1[:], ALU.add))
                    dve.wait_ge(m["exp_ready"], 6 * t + (3 * d + 3))
                    dve.wait_ge(stored[d], 32 * t)
                    end = (CH - 1) if d == 0 else 0
                    nc.vector.tensor_copy(consts["p_end"][:, d, :, bass.ds(t * (PB // CH), PB // CH)],
                                          p_in[d][:].rearrange("p f (c t) -> p f c t", t=CH)[:, :, :, end]).then_inc(m["ends_ready"], 1)
                    nc.vector.tensor_tensor(outs[:, d, 2], ba[:], p_inv[d][:], ALU.mult)
                    nc.vector.tensor_tensor(outs[:, d, 3], kd[:], p_inv[d][:], ALU.mult).then_inc(m["dve_out"], 1)
                if then:
                    inverse_norm(step, t + 1)
                dve.wait_ge(m["pool_out"], 2 * t + 2)
                dve.sem_inc(in_used[b], 1)

            dve.wait_ge(m["consts_in"], 80)
            nc.vector.tensor_scalar(half_w0[:], col(consts, "w0"), 0.5, None, ALU.mult).then_inc(m["halves"], 1)
            nc.vector.tensor_scalar(half_a0[:], col(consts, "a0"), 0.5, None, ALU.mult).then_inc(m["halves"], 1)
            start = Chain(dve, m["own"])
            start(nc.vector.memset(inv8[:], 0.0))
            inverse_norm(start, 0)
            per = 2 * 14
            with dve.Fori(0, NI - 1) as i:
                step = Chain(dve, m["own"], start.n, i, per)
                body(step, i, 0, (i, 1))
                body(step, i, 1, (i + 1, 0))
                step.end()
            step = Chain(dve, m["own"], start.n, NI - 1, per)
            body(step, NI - 1, 0, (NI - 1, 1))
            body(step, NI - 1, 1, None)




HEADS = 8
LEVELS = 6
RING = 3


def wkv_scan(nc, dram, consts):
    with ExitStack() as ctx:
        s = Scope(nc, ctx)
        H = HEADS
        mask = s.sb("tri_mask", [P, 2, 2, CH])
        lmask = s.sb("level_mask", [P, LEVELS, P])
        ident2 = s.sb("ident_halves", [P, CH])
        pair = lambda name, shape: s.sb("sb_" + name, [P, 2] + shape)
        ops = pair("wkv_ops", [4, RF, P])
        by_head = pair("wkv_by_head", [2, 2, RF, P])
        v = pair("wkv_v", [RF, P])
        hats = pair("wkv_hats", [2, RF, P])
        rho = pair("wkv_rho", [RF, P])
        lb = pair("wkv_lb", [H, 2, P])
        mk = pair("wkv_mk", [H, 2, P])
        lev = pair("wkv_levels", [RING, H, P])
        x, xt, z = (pair("wkv_" + n, [H, P]) for n in ("x", "xt", "z"))
        v_tok = pair("wkv_v_tok", [RF, P])
        hat_tok = pair("wkv_hat_tok", [2, RF, P])
        am = pair("wkv_am", [H, 2, CH])
        wg = pair("wkv_wg", [H, 2, CH])
        diag = pair("wkv_diag", [2, RF, CH])
        phi = pair("wkv_phi", [2, RF, CH])
        psi = pair("wkv_psi", [2, RF, CH])
        r = pair("wkv_r", [RF, P])
        y0 = pair("wkv_y0", [RF, P])
        y = pair("wkv_y", [RF, P])
        state = pair("wkv_state", [RF, CH])
        ps = [s.ps(f"ps_wkv{d}", [P, 4, 512]) for d in range(2)]
        names = ("in_loaded", "hat_ready", "ops_used", "turned", "tok_copied", "beta_full", "beta_masked", "kappa_full", "kappa_masked",
                 "lev_ready", "xt1_ready", "x1_ready", "z_full", "z_ready", "xz_full", "x_ready",
                 "xt_ready", "last_full", "inv_ready", "mv_full", "mv_ready", "wg_full", "wg_ready", "trans_full", "diag_ready",
                 "phi_ready", "psi_ready", "bw_full", "r_ready", "y0_full", "y0_ready", "s_full", "s_ready", "y_ready",
                 "y_stored")
        m = {n: [s.sem(f"wkv_{n}{d}") for d in range(2)] for n in names}
        consts_in = s.sem("wkv_consts_in")
        unread = s.sem("wkv_unread_pool")
        unread_pe = s.sem("wkv_unread_pe")
        zeroed = s.sem("wkv_zeroed")
        padded = s.sem("wkv_padded")
        block = ctx.enter_context(nc.Block())
        tiles = (SEQS[0] // P, SEQS[1] // P)
        runs = ((0, tiles[0]), (tiles[0], tiles[0] + tiles[1]))

        def where(i, d, run):
            return i if d == 0 else i * -1 + (run[0] + run[1] - 1)

        def hh(g, f):
            return g * RF + f

        def half(g):
            return slice(64 * g, 64 * g + 64)

        @block.sync
        def _(sp):
            sp.dma_start(mask[:], dram["tri_mask"][:, :, :, :]).then_inc(consts_in, 16)
            sp.dma_start(lmask[:], dram["level_mask"][:, :, :]).then_inc(consts_in, 16)
            sp.dma_start(ident2[:], dram["ident_halves"][:, :]).then_inc(consts_in, 16)
            sp.wait_ge(padded, 3)
            for run in runs:
                with sp.Fori(*run) as i:
                    for d in range(2):
                        n = where(i, d, run)
                        sp.wait_ge(m["ops_used"][d], i)
                        sp.wait_ge(m["kappa_full"][d], i)
                        sp.dma_start(ops[:, d].rearrange("p q f t -> p (q f) t"),
                                     dram["wkv_in"][d, bass.ds(n, 1)].rearrange("a p x t -> p (a x) t")).then_inc(m["in_loaded"][d], 16)
                        for g in range(2):
                            sp.dma_start(by_head[half(g), d, g].rearrange("p q f t -> p (q f) t"),
                                         dram["wkv_in"][d, bass.ds(n, 1), half(g), 0:2 * RF].rearrange("a p x t -> p (a x) t")).then_inc(m["in_loaded"][d], 16)
                        sp.dma_start(v[:, d], dram["p_t"][VT:VT + 4, :, bass.ds(n * P, P)].rearrange("f p t -> p f t")).then_inc(m["in_loaded"][d], 16)

        @block.gpsimd
        def _(pool):
            for part in (by_head, lb, mk):
                nc.gpsimd.memset(part[:], 0.0).then_inc(padded, 1)
            pool.wait_ge(consts_in, 48)
            for run in runs:
                with pool.Fori(*run) as i:
                    for d in range(2):
                        n = where(i, d, run)
                        end = consts["p_end"][:, d, :, bass.ds(n * 2, 2)]
                        pool.wait_ge(m["in_loaded"][d], 64 * i + 64)
                        pool.wait_ge(m["turned"][d], 4 * i)
                        for q in range(2):
                            for c in range(2):
                                ins = nc.gpsimd.tensor_tensor(hats[:, d, q, :, CH * c:CH * c + CH], ops[:, d, 2 + q, :, CH * c:CH * c + CH],
                                                              end[:, :, c:c + 1].to_broadcast([P, RF, CH]), ALU.mult)
                        ins.then_inc(m["hat_ready"][d], 1)
                        pool.wait_ge(m["r_ready"][d], i)
                        alone(pool, unread)
                        nc.gpsimd.tensor_copy(rho[:, d], ops[:, d, 1]).then_inc(m["ops_used"][d], 1)
                        pool.wait_ge(m["phi_ready"][d], i)
                        alone(pool, unread)
                        for c in range(2):
                            ins = nc.gpsimd.tensor_tensor(diag[:, d, c], ident2[:].unsqueeze(1).to_broadcast([P, RF, CH]),
                                                          end[:, :, c:c + 1].to_broadcast([P, RF, CH]), ALU.mult)
                        ins.then_inc(m["diag_ready"][d], 1)
                    for l in range(LEVELS):
                        for d in range(2):
                            if l == 0:
                                pool.wait_ge(m["beta_masked"][d], i + 1)
                                pool.wait_ge(m["z_full"][d], 5 * i)
                            elif l == RING:
                                pool.wait_ge(m["xt1_ready"][d], i + 1)
                            elif l > RING:
                                pool.wait_ge(m["z_full"][d], 5 * i + l - RING)
                            nc.gpsimd.tensor_tensor(lev[:, d, l % RING], lb[:, d, :, 0], lmask[:, l].unsqueeze(1).to_broadcast([P, H, P]),
                                                    ALU.mult).then_inc(m["lev_ready"][d], 1)

        @block.tensor
        def _(pe):
            ident = consts["ident"][:]
            for run in runs:
                pe.wait_ge(zeroed, 1 + (run[0] > 0))
                with pe.Fori(*run) as i:
                    for d in range(2):
                        pe.wait_ge(m["in_loaded"][d], 64 * i + 64)
                        pe.wait_ge(m["hat_ready"][d], i + 1)
                        pe.wait_ge(m["y_ready"][d], i)
                        pe.wait_ge(m["s_ready"][d], 4 * i)
                        for q, src in enumerate((ops[:, d, 0], v[:, d], hats[:, d, 0], hats[:, d, 1])):
                            for f in range(RF):
                                mm = nc.tensor.transpose(ps[d][:, q, P * f:P * f + P], src[:, f], ident)
                            mm.then_inc(m["turned"][d], 1)
                    for q, (full, copied) in enumerate((("beta_full", 2), ("kappa_full", 4))):
                        for d in range(2):
                            pe.wait_ge(m["tok_copied"][d], 4 * i + copied)
                            alone(pe, unread_pe)
                            for f in range(RF):
                                for g in range(2):
                                    for c in range(2):
                                        out = ps[d][half(c), 2 * q + g, P * f:P * f + P].rearrange("p (a t) -> p a t", a=2)
                                        mm = nc.tensor.matmul(out, ops[:, d, 2 + q, f, half(c)], by_head[:, d, g, :, f, half(c)], start=True, stop=True)
                            mm.then_inc(m[full][d], 1)
                    for d in range(2):
                        pe.wait_ge(m["kappa_masked"][d], i + 1)
                        for g in range(2):
                            for f in range(RF):
                                for c in range(2):
                                    mm = nc.tensor.matmul(ps[d][half(c), 2, CH * hh(g, f):CH * hh(g, f) + CH], mk[:, d, hh(g, f), 0, half(c)],
                                                          v_tok[:, d, f, half(g)], start=True, stop=True)
                        mm.then_inc(m["mv_full"][d], 1)
                    def over_heads(out, lhs, rhs):
                        for h in range(H):
                            mm = nc.tensor.matmul(out[:, h // 4, P * (h % 4):P * (h % 4) + P], lhs[:, h], rhs[:, h], start=True, stop=True)
                        return mm

                    for l in range(1, LEVELS):
                        last = l == LEVELS - 1
                        for d in range(2):
                            pe.wait_ge(m["lev_ready"][d], LEVELS * i + l + 1)
                            if l == 1:
                                pe.wait_ge(m["x1_ready"][d], i + 1)
                            else:
                                pe.wait_ge(m["x_ready"][d], 4 * i + l - 1)
                            over_heads(ps[d], lev[:, d, l % RING], x[:, d]).then_inc(m["z_full"][d], 1)
                        for d in range(2):
                            pe.wait_ge(m["z_ready"][d], 5 * i + l)
                            if l == 1:
                                pe.wait_ge(m["mv_ready"][d], i + 1)
                            else:
                                pe.wait_ge(m["xt_ready"][d], 4 * i + l - 1)
                            if not last:
                                over_heads(ps[d][:, 2:4], xt[:, d], z[:, d]).then_inc(m["xz_full"][d], 1)
                            else:
                                over_heads(ps[d][:, 2:4], z[:, d], xt[:, d]).then_inc(m["last_full"][d], 1)
                    for d in range(2):
                        pe.wait_ge(m["inv_ready"][d], i + 1)
                        over_heads(ps[d], xt[:, d], am[:, d].rearrange("p h a k -> p h (a k)")).then_inc(m["wg_full"][d], 1)
                    for d in range(2):
                        pe.wait_ge(m["wg_ready"][d], i + 1)
                        alone(pe, unread_pe)
                        for g in range(2):
                            for f in range(RF):
                                for c in range(2):
                                    t = half(c)
                                    at = lambda a: ps[d][half(g), 2 + c, P * f + CH * a:P * f + CH * a + CH]
                                    nc.tensor.matmul(at(0), wg[t, d, hh(g, f), 0], hat_tok[t, d, 0, f, half(g)], start=True, stop=True)
                                for c in range(2):
                                    t = half(c)
                                    at = lambda a: ps[d][half(g), 2 + c, P * f + CH * a:P * f + CH * a + CH]
                                    nc.tensor.matmul(at(1), hat_tok[t, d, 0, f, half(g)], wg[t, d, hh(g, f), 1], start=True, stop=False)
                                    mm = nc.tensor.matmul(at(1), hat_tok[t, d, 1, f, half(g)], v_tok[t, d, f, half(g)], start=False, stop=True)
                        mm.then_inc(m["trans_full"][d], 1)
                    for d in range(2):
                        for f in range(RF):
                            for g in range(2):
                                mm = nc.tensor.matmul(ps[d][half(g), 0, P * f:P * f + P], wg[:, d, hh(g, f), 0], lb[:, d, hh(g, f), 1],
                                                      start=True, stop=True)
                        mm.then_inc(m["bw_full"][d], 1)
                        for f in range(RF):
                            for g in range(2):
                                out = ps[d][half(g), 1, P * f:P * f + P]
                                nc.tensor.matmul(out, wg[:, d, hh(g, f), 1], lb[:, d, hh(g, f), 1], start=True, stop=False)
                                mm = nc.tensor.matmul(out, v_tok[:, d, f, half(g)], mk[:, d, hh(g, f), 1], start=False, stop=True)
                        mm.then_inc(m["y0_full"][d], 1)
                    for k in range(2):
                        for d in range(2):
                            c = k if d == 0 else 1 - k
                            if k == 0:
                                pe.wait_ge(m["r_ready"][d], i + 1)
                                pe.wait_ge(m["y0_ready"][d], i + 1)
                                pe.wait_ge(m["phi_ready"][d], i + 1)
                                pe.wait_ge(m["psi_ready"][d], i + 1)
                            else:
                                pe.wait_ge(m["s_ready"][d], 4 * i + 2)
                            alone(pe, unread_pe)
                            for f in range(RF):
                                for g in range(2):
                                    nc.tensor.matmul(ps[d][half(g), g, P * f + CH * c:P * f + CH * c + CH], state[half(g), d, f],
                                                     r[half(g), d, f, CH * c:CH * c + CH], start=True, stop=True)
                            for f in range(RF):
                                for g in range(2):
                                    mm = nc.tensor.matmul(ps[d][half(g), 2 + g, CH * f:CH * f + CH], phi[half(g), d, c, f], state[half(g), d, f],
                                                          start=True, stop=True)
                            mm.then_inc(m["s_full"][d], 1)

        @block.scalar
        def _(act):
            for run in runs:
                with act.Fori(*run) as i:
                    for d in range(2):
                        by_pair = lambda x: x.rearrange("p (f g k) -> p g f k", g=2, k=CH)
                        dsts = (am[:, d, :, 0].rearrange("p (g f) k -> p g f k", g=2), by_pair(v_tok[:, d].rearrange("p f t -> p (f t)")),
                                by_pair(hat_tok[:, d, 0].rearrange("p f t -> p (f t)")), by_pair(hat_tok[:, d, 1].rearrange("p f t -> p (f t)")))
                        for q, dst in enumerate(dsts):
                            act.wait_ge(m["turned"][d], 4 * i + q + 1)
                            for g in range(2):
                                ins = nc.scalar.copy(dst[:, g], by_pair(ps[d][:, q])[:, g])
                            ins.then_inc(m["tok_copied"][d], 1)
                    for d in range(2):
                        act.wait_ge(m["mv_full"][d], i + 1)
                        nc.scalar.copy(am[:, d, :, 1], ps[d][:, 2].rearrange("p (h k) -> p h k", h=H)).then_inc(m["mv_ready"][d], 1)
                    bank2 = lambda x: x.rearrange("p (b h) t -> p b (h t)", b=2)
                    for l in range(1, LEVELS):
                        for d in range(2):
                            act.wait_ge(m["z_full"][d], 5 * i + l)
                            nc.scalar.copy(bank2(z[:, d]), ps[d][:, 0:2]).then_inc(m["z_ready"][d], 1)
                    for d in range(2):
                        act.wait_ge(m["wg_full"][d], i + 1)
                        nc.scalar.mul(wg[:, d].rearrange("p (b h) a k -> p b (h a k)", b=2), ps[d][:, 0:2], -1.0).then_inc(m["wg_ready"][d], 1)
                    for d in range(2):
                        act.wait_ge(m["phi_ready"][d], i + 1)
                        nc.scalar.copy(psi[:, d], ps[d][:, 2:4].rearrange("p c (f a k) -> p c f a k", f=RF, a=2)[:, :, :, 1]).then_inc(m["psi_ready"][d], 1)
                        act.wait_ge(m["y0_full"][d], i + 1)
                        nc.scalar.copy(y0[:, d].rearrange("p f t -> p (f t)"), ps[d][:, 1]).then_inc(m["y0_ready"][d], 1)
                    for d in range(2):
                        act.wait_ge(m["y_ready"][d], i + 1)
                        n = where(i, d, run)
                        act.dma_start(dram["wkv_y"][d, bass.ds(n, 1)].rearrange("a p f t -> p (a f t)"), y[:, d].rearrange("p f t -> p (f t)")).then_inc(m["y_stored"][d], 16)
            for d in range(2):
                act.wait_ge(m["y_stored"][d], 16 * runs[1][1])

        @block.vector
        def _(dve):
            dve.wait_ge(consts_in, 48)
            dve.wait_ge(padded, 3)
            for run in runs:
                if run[0]:
                    for d in range(2):
                        dve.wait_ge(m["s_full"][d], 2 * run[0])
                        dve.wait_ge(m["s_ready"][d], 4 * run[0])
                nc.vector.memset(state[:], 0.0).then_inc(zeroed, 1)
                dve.wait_ge(zeroed, 1 + (run[0] > 0))
                with dve.Fori(*run) as i:
                    def masked(q, d, dst, done):
                        for c in range(2):
                            ins = nc.vector.tensor_tensor(dst[half(c), d, :, :, half(c)], ps[d][half(c), 2 * q:2 * q + 2].rearrange("p b (f a t) -> p (b f) a t", f=RF, a=2),
                                                          mask[half(c), d].unsqueeze(1).to_broadcast([CH, H, 2, CH]), ALU.mult)
                        ins.then_inc(m[done][d], 1)

                    for d in range(2):
                        dve.wait_ge(m["beta_full"][d], i + 1)
                        dve.wait_ge(m["lev_ready"][d], LEVELS * i)
                        masked(0, d, lb, "beta_masked")
                    for d in range(2):
                        dve.wait_ge(m["kappa_full"][d], i + 1)
                        masked(1, d, mk, "kappa_masked")
                    for d in range(2):
                        dve.wait_ge(m["lev_ready"][d], LEVELS * i + 1)
                        dve.wait_ge(m["wg_full"][d], i)
                        nc.vector.tensor_tensor(xt[:, d], consts["ident"][:].unsqueeze(1).to_broadcast([P, H, P]), lev[:, d, 0],
                                                ALU.subtract).then_inc(m["xt1_ready"][d], 1)
                    flat = lambda a: a.rearrange("p h t -> p (h t)")
                    for d in range(2):
                        dve.wait_ge(m["xt1_ready"][d], i + 1)
                        nc.vector.transpose(flat(x[:, d]), flat(xt[:, d])).then_inc(m["x1_ready"][d], 1)
                    bank2 = lambda x: x.rearrange("p (b h) t -> p b (h t)", b=2)
                    for l in range(1, LEVELS - 1):
                        for d in range(2):
                            dve.wait_ge(m["xz_full"][d], 4 * i + l)
                            nc.vector.tensor_tensor(bank2(x[:, d]), bank2(x[:, d]), ps[d][:, 2:4], ALU.subtract).then_inc(m["x_ready"][d], 1)
                            dve.wait_ge(m["x_ready"][d], 4 * i + l)
                            nc.vector.transpose(flat(xt[:, d]), flat(x[:, d])).then_inc(m["xt_ready"][d], 1)
                    for d in range(2):
                        dve.wait_ge(m["last_full"][d], i + 1)
                        nc.vector.tensor_tensor(bank2(xt[:, d]), bank2(xt[:, d]), ps[d][:, 2:4], ALU.subtract).then_inc(m["inv_ready"][d], 1)
                    for d in range(2):
                        dve.wait_ge(m["trans_full"][d], i + 1)
                        dve.wait_ge(m["diag_ready"][d], i + 1)
                        nc.vector.tensor_tensor(phi[:, d], ps[d][:, 2:4].rearrange("p c (f a k) -> p c f a k", f=RF, a=2)[:, :, :, 0], diag[:, d],
                                                ALU.add).then_inc(m["phi_ready"][d], 1)
                        dve.wait_ge(m["bw_full"][d], i + 1)
                        nc.vector.tensor_tensor(r[:, d].rearrange("p f t -> p (f t)"), ps[d][:, 0], rho[:, d].rearrange("p f t -> p (f t)"),
                                                ALU.add).then_inc(m["r_ready"][d], 1)
                    for k in range(2):
                        for d in range(2):
                            c = k if d == 0 else 1 - k
                            dve.wait_ge(m["s_full"][d], 2 * i + k + 1)
                            dve.wait_ge(m["psi_ready"][d], i + 1)
                            if k == 1:
                                dve.wait_ge(m["s_ready"][d], 4 * i + 2)
                            for g in range(2):
                                nc.vector.tensor_tensor(state[half(g), d], ps[d][half(g), 2 + g, 0:RF * CH].rearrange("p (f k) -> p f k", f=RF),
                                                        psi[half(g), d, c], ALU.add).then_inc(m["s_ready"][d], 1)
                    for d in range(2):
                        dve.wait_ge(m["y_stored"][d], 16 * i)
                        dve.wait_ge(m["y0_ready"][d], i + 1)
                        for g in range(2):
                            ins = nc.vector.tensor_tensor(y[half(g), d].rearrange("p f t -> p (f t)"), ps[d][half(g), g],
                                                          y0[half(g), d].rearrange("p f t -> p (f t)"), ALU.add)
                        ins.then_inc(m["y_ready"][d], 1)




GN_EPS = 64e-5


def rwkv_finish(nc, dram, consts, oa_t):
    with ExitStack() as ctx:
        s = Scope(nc, ctx)
        W = [P, RF, PB]
        J = PB // P
        up = s.sb("gate_up", [P, RF * P])
        head_ones = s.sb("head_ones2", [P, P])
        yin = s.sb("fin_y", [P, 2, J, RF, P])
        rkv = s.sb("fin_rkv", [P, 12, PB])
        gd = s.sb("fin_gd", [P, PB])
        y, yc, sq, var, lnv, rstd, rk, rkk, bonus = (s.sb("fin_" + n, W) for n in ("sum", "centred", "square", "var", "ln_var", "rstd", "rk", "rkk", "bonus"))
        yn = s.sb("fin_yn", W)
        ya = s.sb("fin_affine", W)
        sg = s.sb("fin_sg", [P, PB])
        ps_m, ps_v, ps_b, ps_g = (s.ps("ps_fin" + n, W) for n in "mvbg")
        m = {n: s.sem("fin_" + n + "_s") for n in (
            "unread", "consts", "y_loaded", "gd_loaded", "rk_loaded", "v_loaded", "summed", "mean_full", "centred", "squared", "var_full", "var_ready", "rstd_ready", "normed", "affine", "ln_own",
            "rk_own", "rkk_ready", "bonus_full", "tanh", "sig_ready", "gate_full", "own", "done", "bonus_ready")}
        block = ctx.enter_context(nc.Block())
        N = TOK // PB

        @block.sync
        def _(sp):
            sp.dma_start(up[:], dram["gate_up"][:, :]).then_inc(m["consts"], 16)
            sp.dma_start(head_ones[:], dram["head_ones"][:, :]).then_inc(m["consts"], 16)
            with sp.Fori(0, N) as i:
                sp.wait_ge(m["summed"], i)
                for d in range(2):
                    sp.dma_start(yin[:, d].rearrange("p j f t -> p j (f t)"),
                                 dram["wkv_y"][d, bass.ds(i * J, J)].rearrange("j p f t -> p j (f t)")).then_inc(m["y_loaded"], 16)
                sp.wait_ge(m["tanh"], i)
                sp.dma_start(gd[:], dram["p_t"][GD, :, bass.ds(i * PB, PB)]).then_inc(m["gd_loaded"], 16)
                sp.wait_ge(m["rk_own"], i)
                alone(sp, m["unread"])
                sp.dma_start(rkv[:, 0:8], dram["p_t"][0:8, :, bass.ds(i * PB, PB)].rearrange("f p t -> p f t")).then_inc(m["rk_loaded"], 16)
                sp.wait_ge(m["bonus_ready"], i)
                alone(sp, m["unread"])
                sp.dma_start(rkv[:, 8:12], dram["p_t"][8:12, :, bass.ds(i * PB, PB)].rearrange("f p t -> p f t")).then_inc(m["v_loaded"], 16)

        @block.gpsimd
        def _(pool):
            with pool.Fori(0, N) as i:
                pool.wait_ge(m["y_loaded"], 32 * i + 32)
                pool.wait_ge(m["centred"], i)
                order = "p j f t -> p f j t"
                nc.gpsimd.tensor_tensor(y[:].rearrange("p f (j t) -> p f j t", j=J), yin[:, 0].rearrange(order), yin[:, 1].rearrange(order),
                                        ALU.add).then_inc(m["summed"], 1)
                pool.wait_ge(m["rk_loaded"], 16 * i + 16)
                pool.wait_ge(m["rkk_ready"], i)
                nc.gpsimd.tensor_tensor(rk[:], rkv[:, 0:4], rkv[:, 4:8], ALU.mult).then_inc(m["rk_own"], 1)
                pool.wait_ge(m["rk_own"], i + 1)
                pool.wait_ge(m["bonus_full"], i)
                nc.gpsimd.tensor_tensor(rkk[:], rk[:], col(consts, "r_k").unsqueeze(2).to_broadcast(W), ALU.mult).then_inc(m["rkk_ready"], 1)

        @block.tensor
        def _(pe):
            pe.wait_ge(m["consts"], 32)
            with pe.Fori(0, N) as i:
                def sums(out, src):
                    for f in range(RF):
                        mm = nc.tensor.matmul(out[:, f], head_ones[:], src[:, f], start=True, stop=True)
                    return mm
                pe.wait_ge(m["summed"], i + 1)
                pe.wait_ge(m["centred"], i)
                sums(ps_m, y).then_inc(m["mean_full"], 1)
                pe.wait_ge(m["rkk_ready"], i + 1)
                pe.wait_ge(m["bonus_ready"], i)
                sums(ps_b, rkk).then_inc(m["bonus_full"], 1)
                pe.wait_ge(m["sig_ready"], i + 1)
                pe.wait_ge(m["done"], i)
                for f in range(RF):
                    mm = nc.tensor.matmul(ps_g[:, f], up[:, P * f:P * f + P], sg[:], start=True, stop=True)
                mm.then_inc(m["gate_full"], 1)
                pe.wait_ge(m["squared"], i + 1)
                pe.wait_ge(m["var_ready"], i)
                sums(ps_v, sq).then_inc(m["var_full"], 1)

        @block.scalar
        def _(act):
            with act.Fori(0, N) as i:
                act.wait_ge(m["gd_loaded"], 16 * i + 16)
                act.wait_ge(m["gate_full"], i)
                nc.scalar.activation(sg[:], gd[:], ACT.Tanh, scale=0.5).then_inc(m["tanh"], 1)
                act.wait_ge(m["centred"], i + 1)
                act.wait_ge(m["var_full"], i)
                nc.scalar.activation(sq[:], yc[:], ACT.Square).then_inc(m["squared"], 1)
                act.wait_ge(m["var_ready"], i + 1)
                nc.scalar.activation(lnv[:], var[:], ACT.Ln).then_inc(m["ln_own"], 1)
                act.wait_ge(m["ln_own"], i + 1)
                nc.scalar.activation(rstd[:], lnv[:], ACT.Exp, scale=-0.5).then_inc(m["rstd_ready"], 1)
                act.wait_ge(m["normed"], i + 1)
                act.wait_ge(m["done"], i)
                for f in range(RF):
                    ins = nc.scalar.activation(ya[:, f], yn[:, f], ACT.Identity, bias=col(consts, "gn_b", f, 1), scale=col(consts, "gn_w", f, 1))
                ins.then_inc(m["affine"], 1)

        @block.vector
        def _(dve):
            with dve.Fori(0, N) as i:
                step = Chain(dve, m["own"], 0, i, 1)
                dve.wait_ge(m["tanh"], i + 1)
                nc.vector.tensor_scalar(sg[:], sg[:], 0.5, 0.5, ALU.mult, ALU.add).then_inc(m["sig_ready"], 1)
                for h in range(2):
                    q = slice(2 * h, 2 * h + 2)
                    if h == 0:
                        dve.wait_ge(m["mean_full"], i + 1)
                        dve.wait_ge(m["squared"], i)
                    ins = nc.vector.scalar_tensor_tensor(out=yc[:, q], in0=ps_m[:, q], scalar=-1.0 / CH, in1=y[:, q], op0=ALU.mult, op1=ALU.add)
                ins.then_inc(m["centred"], 1)
                dve.wait_ge(m["bonus_full"], i + 1)
                dve.wait_ge(m["v_loaded"], 16 * i + 16)
                nc.vector.tensor_tensor(bonus[:], ps_b[:], rkv[:, 8:12], ALU.mult).then_inc(m["bonus_ready"], 1)
                dve.wait_ge(m["var_full"], i + 1)
                nc.vector.tensor_scalar(var[:], ps_v[:], 1.0 / CH, GN_EPS, ALU.mult, ALU.add).then_inc(m["var_ready"], 1)
                dve.wait_ge(m["rstd_ready"], i + 1)
                nc.vector.tensor_tensor(yn[:], yc[:], rstd[:], ALU.mult).then_inc(m["normed"], 1)
                dve.wait_ge(m["affine"], i + 1)
                dve.wait_ge(m["bonus_ready"], i + 1)
                step(nc.vector.tensor_tensor(ya[:], ya[:], bonus[:], ALU.add))
                dve.wait_ge(m["gate_full"], i + 1)
                nc.vector.tensor_tensor(oa_t[:, :, bass.ds(i * PB, PB)], ya[:], ps_g[:], ALU.mult).then_inc(m["done"], 1)
                step.end()


NOPE, ROPE = 64, 32
HD = NOPE + ROPE
QF, KVF = 6, 2
KPE_TILE, Q_TILE, KV_TILE = 15, 16, 22
SCALE = float(HD) ** -0.5


def mla_project(nc, dram, consts):
    with ExitStack() as ctx:
        s = Scope(nc, ctx)
        U = 2 * HEADS
        L = QF + KVF
        w_uq = s.sb("w_uq", [P, QF, HEADS, HD])
        w_uk = s.sb("w_uk", [P, KVF, HEADS, HD])
        w_uv = s.sb("w_uv", [P, KVF, 512])
        gather = s.sb("gather_means", [HD, U, 2 * U])
        spread = s.sb("spread_rstd", [P, U, HD])
        rotate = s.sb("rotate", [HD, HD])
        rope = s.sb("rope", [HD, 2, NB])
        q_gain = s.sb("scaled_q_gain", [P, 1])
        lat = s.sb("latent", [P, L, NB])
        kpe = s.sb("k_pe", [P, NB])
        lat_sq = s.sb("latent_square", [P, L, NB])
        lat_n = s.sb("latent_normed", [P, L, NB])
        var = s.sb("latent_var", [P, 2, NB])
        rms = s.sb("latent_rms", [P, 2, NB])
        rstd_l = s.sb("latent_rstd", [P, 2, NB])
        raw = s.sb("heads_raw", [HD, U, NB])
        sq, normed, t_cos, t_sin, outq = (s.sb("head_" + n, [HD, 2, NB]) for n in ("square", "normed", "cos", "sin", "out"))
        var_h, rms_h = s.sb("heads_var", [2 * U, NB]), s.sb("heads_rms", [2 * U, NB])
        rstd_h = s.sb("heads_rstd", [P, NB])
        v_out = s.sb("v_out", [P, 2, 512])
        ps_raw = [s.ps(f"ps_raw{b}", [HD, NB]) for b in range(2)]
        ps_rot = [s.ps(f"ps_rot{b}", [HD, NB]) for b in range(2)]
        ps_l = [s.ps(f"ps_lat{b}", [P, NB]) for b in range(2)]
        ps_stat = s.ps("ps_heads_mean", [2 * U, NB])
        m = {n: s.sem("mla_" + n) for n in (
            "consts", "own", "lat_squared", "lat_full", "lat_var", "lat_rms", "lat_rstd", "lat_normed", "v_full", "v_copied",
            "raw_full", "raw_copied", "sum_full", "stat_var", "stat_rms", "stat_ready", "spread_full", "normed", "rot_full", "cos_ready",
            "sin_ready", "out_ready", "lat_loaded", "kpe_loaded", "rope_loaded")}
        v_stored = [s.sem(f"mla_v_stored{b}") for b in range(2)]
        stored = [s.sem(f"mla_stored{b}") for b in range(2)]
        unread = s.sem("mla_unread")
        block = ctx.enter_context(nc.Block())

        def blocks(eng, body):
            with eng.Fori(0, NT - 1) as i:
                body(i, True)
            body(NT - 1, False)

        @block.sync
        def _(sp):
            def load_latents(i):
                sp.dma_start(lat[:], dram["p_t"][Q_TILE:Q_TILE + L, :, bass.ds(i * NB, NB)].rearrange("f p t -> p f t")).then_inc(m["lat_loaded"], 16)

            def load_kpe(i):
                sp.dma_start(kpe[:], dram["p_t"][KPE_TILE, :, bass.ds(i * NB, NB)]).then_inc(m["kpe_loaded"], 16)

            def load_rope(i):
                sp.dma_start(rope[:], dram["rope"][:, :, bass.ds(i * NB, NB)]).then_inc(m["rope_loaded"], 16)

            load_latents(0)
            load_kpe(0)
            load_rope(0)
            for dst, name in ((w_uv, "w_uv"), (w_uq, "w_uq"), (w_uk, "w_uk"), (gather, "gather_means"), (spread, "spread_rstd"), (rotate, "rotate")):
                sp.dma_start(dst[:], dram[name][tuple([slice(None)] * len(dst.shape))]).then_inc(m["consts"], 16)

            def body(i, more):
                if more:
                    sp.wait_ge(m["lat_normed"], L * i + L)
                    alone(sp, unread)
                    load_latents(i + 1)
                for t in range(4):
                    sp.wait_ge(m["v_copied"], 4 * i + (t + 1))
                    sp.dma_start(dram["v_mla"][bass.ds(4 * i + t, 1)].rearrange("a p v -> p (a v)"), v_out[:, t % 2]).then_inc(v_stored[t % 2], 16)
                if more:
                    sp.wait_ge(m["raw_full"], U * i + U)
                    alone(sp, unread)
                    load_kpe(i + 1)
                for u in range(U):
                    sp.wait_ge(m["out_ready"], U * i + (u + 1))
                    sp.dma_start(dram["qk_t"][u, :, bass.ds(i * NB, NB)], outq[:, u % 2]).then_inc(stored[u % 2], 16)
                if more:
                    alone(sp, unread)
                    load_rope(i + 1)

            blocks(sp, body)
            for b in range(2):
                sp.wait_ge(stored[b], 16 * U // 2 * NT)
                sp.wait_ge(v_stored[b], 16 * 2 * NT)

        @block.tensor
        def _(pe):
            def latent_sums(i):
                pe.wait_ge(m["lat_squared"], i + 1)
                pe.wait_ge(m["v_copied"], 4 * i)
                for b, (first, n) in enumerate(((0, QF), (QF, KVF))):
                    for k in range(n):
                        mm = nc.tensor.matmul(ps_l[b][:], consts["ones"][:], lat_sq[:, first + k], start=(k == 0), stop=(k == n - 1))
                mm.then_inc(m["lat_full"], 1)

            def body(i, more):
                pe.wait_ge(m["lat_normed"], L * i + L)
                for t in range(4):
                    if t >= 2:
                        pe.wait_ge(m["v_copied"], 4 * i + (t - 1))
                    for k in range(KVF):
                        mm = nc.tensor.matmul(ps_l[t % 2][:], lat_n[:, QF + k, P * t:P * t + P], w_uv[:, k], start=(k == 0), stop=(k == KVF - 1))
                    mm.then_inc(m["v_full"], 1)
                pe.wait_ge(m["kpe_loaded"], 16 * i + 16)
                pe.wait_ge(m["normed"], U * i)
                for u in range(U + 1):
                    if u < U:
                        h, b = u % HEADS, u % 2
                        if u >= 2:
                            pe.wait_ge(m["raw_copied"], U * i + (u - 1))
                        if u < HEADS:
                            for k in range(QF):
                                mm = nc.tensor.matmul(ps_raw[b][:], w_uq[:, k, h], lat_n[:, k], start=(k == 0), stop=(k == QF - 1))
                        else:
                            nc.tensor.matmul(ps_raw[b][:], consts["ident"][:, 0:HD], kpe[:], start=True, stop=False)
                            for k in range(KVF):
                                mm = nc.tensor.matmul(ps_raw[b][:], w_uk[:, k, h], lat_n[:, QF + k], start=False, stop=(k == KVF - 1))
                        mm.then_inc(m["raw_full"], 1)
                    if u >= 1:
                        pe.wait_ge(m["raw_copied"], U * i + u)
                        if u == 1:
                            pe.wait_ge(m["stat_var"], i)
                        nc.tensor.matmul(ps_stat[:], gather[:, u - 1], sq[:, (u - 1) % 2], start=(u == 1), stop=(u == U)).then_inc(m["sum_full"], 1)
                    if more and u == U - 4:
                        latent_sums(i + 1)
                pe.wait_ge(m["stat_ready"], i + 1)
                for u in range(U + 1):
                    if u < U:
                        if u >= 2:
                            pe.wait_ge(m["normed"], U * i + (u - 1))
                        nc.tensor.matmul(ps_raw[u % 2][:], spread[:, u], rstd_h[:], start=True, stop=True).then_inc(m["spread_full"], 1)
                    if u >= 1:
                        c = (u - 1) % 2
                        pe.wait_ge(m["normed"], U * i + u)
                        if u >= 3:
                            pe.wait_ge(m["sin_ready"], U * i + (u - 2))
                        else:
                            pe.wait_ge(m["sin_ready"], U * i)
                        nc.tensor.matmul(ps_rot[c][:], rotate[:], normed[:, c], start=True, stop=True).then_inc(m["rot_full"], 1)

            pe.wait_ge(m["consts"], 96)
            latent_sums(0)
            blocks(pe, body)

        @block.scalar
        def _(act):
            def square_latents(i):
                act.wait_ge(m["lat_loaded"], 16 * i + 16)
                act.wait_ge(m["lat_full"], i)
                nc.scalar.activation(lat_sq[:], lat[:], ACT.Square).then_inc(m["lat_squared"], 1)

            def latent_roots(i):
                act.wait_ge(m["lat_var"], i + 1)
                act.wait_ge(m["lat_rstd"], i)
                nc.scalar.activation(rms[:], var[:], ACT.Sqrt).then_inc(m["lat_rms"], 1)

            def body(i, more):
                for t in range(4):
                    act.wait_ge(m["v_full"], 4 * i + (t + 1))
                    act.wait_ge(v_stored[t % 2], 32 * i + 16 * (t // 2))
                    nc.scalar.copy(v_out[:, t % 2], ps_l[t % 2][:]).then_inc(m["v_copied"], 1)
                for u in range(U):
                    act.wait_ge(m["raw_full"], U * i + (u + 1))
                    if u >= 2:
                        act.wait_ge(m["sum_full"], U * i + (u - 1))
                    nc.scalar.activation(sq[:, u % 2], ps_raw[u % 2][:], ACT.Square)
                    nc.scalar.copy(raw[:, u], ps_raw[u % 2][:]).then_inc(m["raw_copied"], 1)
                    if more and u == HEADS:
                        square_latents(i + 1)
                    if more and u == U - 2:
                        latent_roots(i + 1)
                act.wait_ge(m["stat_var"], i + 1)
                act.wait_ge(m["stat_ready"], i)
                nc.scalar.activation(rms_h[:], var_h[:], ACT.Sqrt).then_inc(m["stat_rms"], 1)

            square_latents(0)
            latent_roots(0)
            blocks(act, body)

        @block.gpsimd
        def _(pool):
            def body(i, more):
                pool.wait_ge(m["rope_loaded"], 16 * i + 16)
                for u in range(U):
                    b = u % 2
                    pool.wait_ge(m["normed"], U * i + (u + 1))
                    if u >= 2:
                        pool.wait_ge(m["out_ready"], U * i + (u - 1))
                    else:
                        pool.wait_ge(m["out_ready"], U * i)
                    nc.gpsimd.tensor_tensor(t_cos[:, b], normed[:, b], rope[:, 0], ALU.mult).then_inc(m["cos_ready"], 1)

            blocks(pool, body)

        @block.vector
        def _(dve):
            nc.vector.memset(rstd_h[:], 0.0).then_inc(m["own"], 1)
            nc.vector.tensor_scalar(q_gain[:], col(consts, "q_gain"), SCALE, None, ALU.mult).then_inc(m["own"], 1)
            dve.wait_ge(m["own"], 2)

            def latent_rstd(i):
                dve.wait_ge(m["lat_full"], i + 1)
                dve.wait_ge(m["lat_rms"], i)
                for b, n in enumerate((QF, KVF)):
                    ins = nc.vector.tensor_scalar(var[:, b], ps_l[b][:], 1.0 / (n * P), EPS, ALU.mult, ALU.add)
                ins.then_inc(m["lat_var"], 1)
                dve.wait_ge(m["lat_rms"], i + 1)
                dve.wait_ge(m["lat_normed"], L * i)
                nc.vector.reciprocal(rstd_l[:], rms[:]).then_inc(m["lat_rstd"], 1)

            def norm_latents(i):
                dve.wait_ge(m["lat_rstd"], i + 1)
                dve.wait_ge(m["raw_full"], U * i)
                for k in range(L):
                    gain = col(consts, "qa_norm", k, 1) if k < QF else col(consts, "kva_norm", k - QF, 1)
                    nc.vector.scalar_tensor_tensor(out=lat_n[:, k], in0=lat[:, k], scalar=gain, in1=rstd_l[:, int(k >= QF)],
                                                   op0=ALU.mult, op1=ALU.mult).then_inc(m["lat_normed"], 1)

            def body(i, more):
                if more:
                    latent_rstd(i + 1)
                dve.wait_ge(m["sum_full"], U * i + U)
                dve.wait_ge(m["stat_rms"], i)
                nc.vector.tensor_scalar(var_h[:], ps_stat[:], EPS, None, ALU.add).then_inc(m["stat_var"], 1)
                dve.wait_ge(m["stat_rms"], i + 1)
                dve.wait_ge(m["spread_full"], U * i)
                nc.vector.reciprocal(rstd_h[0:2 * U], rms_h[:]).then_inc(m["stat_ready"], 1)
                if more:
                    norm_latents(i + 1)
                dve.wait_ge(m["rope_loaded"], 16 * i + 16)
                for u in range(U + 1):
                    b = u % 2
                    if u < U:
                        dve.wait_ge(m["spread_full"], U * i + (u + 1))
                        if u >= 2:
                            dve.wait_ge(m["rot_full"], U * i + (u - 1))
                            dve.wait_ge(m["cos_ready"], U * i + (u - 1))
                        gain = q_gain[0:HD] if u < HEADS else col(consts, "k_gain")[0:HD]
                        nc.vector.scalar_tensor_tensor(out=normed[:, b], in0=raw[:, u], scalar=gain, in1=ps_raw[b][:],
                                                       op0=ALU.mult, op1=ALU.mult).then_inc(m["normed"], 1)
                    if u >= 1:
                        c = (u - 1) % 2
                        dve.wait_ge(m["rot_full"], U * i + u)
                        nc.vector.tensor_tensor(t_sin[:, c], ps_rot[c][:], rope[:, 1], ALU.mult).then_inc(m["sin_ready"], 1)
                        dve.wait_ge(m["sin_ready"], U * i + u)
                        dve.wait_ge(m["cos_ready"], U * i + u)
                        dve.wait_ge(stored[c], 8 * U * i + 16 * ((u - 1) // 2))
                        nc.vector.tensor_tensor(outq[:, c], t_sin[:, c], t_cos[:, c], ALU.add).then_inc(m["out_ready"], 1)

            latent_rstd(0)
            norm_latents(0)
            blocks(dve, body)




def attention(nc, dram, consts, o_all):
    with ExitStack() as ctx:
        s = Scope(nc, ctx)
        q = s.sb("att_q", [HD, 2, TOK])
        k = s.sb("att_k", [HD, 2, TOK])
        v = s.sb("att_v", [P, 2, TT, 64])
        prob = s.sb("att_prob", [P, 2, SEQS[0]])
        prob_t = s.sb("att_prob_t", [P, 2, 2, 512])
        stat = s.sb("att_stat", [P, 2, 3])
        ps_s = [s.ps(f"ps_scores{b}", [P, 2, 512]) for b in range(2)]
        ps_t = s.ps("ps_prob_t", [P, 2, 512])
        ps_o = [s.ps(f"ps_o{b}", [P, 64]) for b in range(2)]
        zeros = s.sb("att_zeros", [P, D])
        zeroed, zeros_stored = s.sem("att_zeroed"), s.sem("att_zeros_stored")
        loaded = [s.sem(f"att_loaded{b}") for b in range(2)]
        m = {n: s.sem("att_" + n) for n in ("s_full", "max_ready", "p_ready", "t_full", "t_copied_act", "t_copied_dve", "o_full",
                                            "inv_ready", "o_ready")}
        block = ctx.enter_context(nc.Block())
        units = [(0, t, SEQS[0] // P) for t in range(SEQS[0] // P)] + [(SEQS[0], SEQS[0] // P + t, SEQS[1] // P) for t in range(SEQS[1] // P)]
        U = len(units)
        todo = [(hb, u) + unit for hb in range(2) for u, unit in enumerate(units)]
        n_turn = 2 * U

        @block.sync
        def _(sp):
            def load(h, b):
                sp.dma_start(q[:, b], dram["qk_t"][bass.ds(h, 1)].rearrange("a d t -> d (a t)")).then_inc(loaded[b], 16)
                sp.dma_start(k[:, b], dram["qk_t"][bass.ds(h + HEADS, 1)].rearrange("a d t -> d (a t)")).then_inc(loaded[b], 16)
                sp.dma_start(v[:, b], dram["v_mla"][:, :, bass.ds(h * 64, 64)].rearrange("t p v -> p t v")).then_inc(loaded[b], 16)

            for b in range(2):
                load(b, b)
            with sp.Fori(0, HEADS // 2 - 1) as i:
                for b in range(2):
                    sp.wait_ge(m["o_full"], n_turn * i + U * (b + 1))
                    load(2 * i + (b + 2), b)

        @block.gpsimd
        def _(pool):
            nc.gpsimd.memset(zeros[:], 0.0).then_inc(zeroed, 1)
            pool.wait_ge(zeroed, 1)
            for n in range(TOK * TOP // MB, BLOCKS):
                pool.dma_start(dram["yb"][n], zeros[:]).then_inc(zeros_stored, 16)
            pool.wait_ge(zeros_stored, 16 * (BLOCKS - TOK * TOP // MB))

        @block.tensor
        def _(pe):
            with pe.Fori(0, HEADS // 2) as i:
                base = n_turn * i
                for n in range(n_turn + 2):
                    if n < n_turn:
                        hb, u, t0, t, nk = todo[n]
                        if u == 0:
                            pe.wait_ge(loaded[hb], 48 * i + 48)
                        pe.wait_ge(m["p_ready"], base + max(0, n - 1))
                        for c in range(nk // 4):
                            mm = nc.tensor.matmul(ps_s[n % 2][:, c], q[:, hb, P * t:P * t + P], k[:, hb, t0 + 512 * c:t0 + 512 * c + 512],
                                                  start=True, stop=True)
                        mm.then_inc(m["s_full"], 1)
                    if 0 <= n - 1 < n_turn:
                        nk = todo[n - 1][4]
                        pe.wait_ge(m["p_ready"], base + n)
                        pe.wait_ge(m["t_copied_act"], base + n - 1)
                        pe.wait_ge(m["t_copied_dve"], base + n - 1)
                        for j in range(nk):
                            mm = nc.tensor.transpose(ps_t[:, j // (nk // 2), P * (j % (nk // 2)):P * (j % (nk // 2)) + P],
                                                     prob[:, (n - 1) % 2, P * j:P * j + P], consts["ident"][:])
                        mm.then_inc(m["t_full"], 1)
                    if 0 <= n - 2 < n_turn:
                        hb, u, t0, t, nk = todo[n - 2]
                        pe.wait_ge(m["t_copied_act"], base + n - 1)
                        pe.wait_ge(m["t_copied_dve"], base + n - 1)
                        pe.wait_ge(m["o_ready"], base + max(0, n - 3))
                        for j in range(nk):
                            mm = nc.tensor.matmul(ps_o[n % 2][:], prob_t[:, n % 2, j // (nk // 2), P * (j % (nk // 2)):P * (j % (nk // 2)) + P],
                                                  v[:, hb, t0 // P + j], start=(j == 0), stop=(j == nk - 1))
                        mm.then_inc(m["o_full"], 1)

        @block.scalar
        def _(act):
            with act.Fori(0, HEADS // 2) as i:
                base = n_turn * i
                for n in range(n_turn + 1):
                    if n < n_turn:
                        nk = todo[n][4]
                        act.wait_ge(m["max_ready"], base + n + 1)
                        act.wait_ge(m["t_full"], base + max(0, n - 1))
                        act.wait_ge(m["inv_ready"], base + max(0, n - 1))
                        nc.scalar.activation(prob[:, n % 2, 0:P * nk].rearrange("p (c x) -> p c x", x=512), ps_s[n % 2][:, 0:nk // 4], ACT.Exp,
                                             bias=stat[:, n % 2, 0:1], accum_out=stat[:, n % 2, 1:2]).then_inc(m["p_ready"], 1)
                    if n >= 1:
                        nk = todo[n - 1][4]
                        act.wait_ge(m["t_full"], base + n)
                        act.wait_ge(m["o_full"], base + max(0, n - 2))
                        nc.scalar.copy(prob_t[:, (n - 1) % 2, 0, 0:P * nk // 2], ps_t[:, 0, 0:P * nk // 2]).then_inc(m["t_copied_act"], 1)

        @block.vector
        def _(dve):
            with dve.Fori(0, HEADS // 2) as i:
                base = n_turn * i
                for n in range(n_turn + 2):
                    if n < n_turn:
                        nk = todo[n][4]
                        dve.wait_ge(m["s_full"], base + n + 1)
                        dve.wait_ge(m["p_ready"], base + max(0, n - 1))
                        nc.vector.tensor_reduce(stat[:, n % 2, 0:1], ps_s[n % 2][:, 0:nk // 4], AX.XY, ALU.max, negate=True).then_inc(m["max_ready"], 1)
                    if 0 <= n - 1 < n_turn:
                        nk = todo[n - 1][4]
                        dve.wait_ge(m["t_full"], base + n)
                        dve.wait_ge(m["o_full"], base + max(0, n - 2))
                        nc.vector.tensor_copy(prob_t[:, (n - 1) % 2, 1, 0:P * nk // 2], ps_t[:, 1, 0:P * nk // 2]).then_inc(m["t_copied_dve"], 1)
                        dve.wait_ge(m["o_ready"], base + max(0, n - 2))
                        nc.vector.reciprocal(stat[:, (n - 1) % 2, 2:3], stat[:, (n - 1) % 2, 1:2]).then_inc(m["inv_ready"], 1)
                    if 0 <= n - 2 < n_turn:
                        hb, u, t0, t, nk = todo[n - 2]
                        dve.wait_ge(m["o_full"], base + n - 1)
                        dve.wait_ge(m["inv_ready"], base + n - 1)
                        nc.vector.tensor_scalar(o_all[:, t, bass.ds(i * 128 + hb * 64, 64)], ps_o[n % 2][:], stat[:, n % 2, 2:3], None,
                                                ALU.mult).then_inc(m["o_ready"], 1)


EXPERTS, GROUPS, PER_GROUP = 32, 4, 8
ROUTER = GROUPS + EXPERTS


def turn_o(nc, dram, consts, o_all, om_t):
    with ExitStack() as ctx:
        s = Scope(nc, ctx)
        ps = s.ps("ps_turn_o", [P, 2, 512])
        full = [s.sem(f"o_turned{b}") for b in range(2)]
        copied = [s.sem(f"o_copied{b}") for b in range(2)]
        block = ctx.enter_context(nc.Block())

        @block.tensor
        def _(pe):
            for t in range(TT):
                pe.wait_ge(copied[t % 2], t // 2)
                for f in range(RF):
                    mm = nc.tensor.transpose(ps[:, t % 2, P * f:P * f + P], o_all[:, t, P * f:P * f + P], consts["ident"][:])
                mm.then_inc(full[t % 2], 1)

        def copies(b, eng, copy):
            for t in range(b, TT, 2):
                eng.wait_ge(full[b], t // 2 + 1)
                copy(om_t[:, :, P * t:P * t + P], ps[:, b].rearrange("p (f t) -> p f t", f=RF)).then_inc(copied[b], 1)

        @block.scalar
        def _(act):
            copies(0, act, nc.scalar.copy)

        @block.vector
        def _(dve):
            copies(1, dve, nc.vector.tensor_copy)


def merge_branches(nc, dram, consts, oa_t, om_t, merged):
    with ExitStack() as ctx:
        s = Scope(nc, ctx)
        w = s.sb("w_o_tile", [P, 2, 2, RF, P])
        g = s.sb("gate_tile", [P, 2, 2, TOK])
        part = s.sb("branch_part", [P, 2, 2, NB])
        ps = s.ps("ps_branch", [P, 2, 2, NB])
        loaded = [s.sem(f"merge_loaded{b}") for b in range(2)]
        full = [s.sem(f"branch_full{b}") for b in range(2)]
        scaled = s.sem("branch_scaled")
        done = [s.sem(f"merged{b}") for b in range(2)]
        unread = s.sem("merge_unread")
        block = ctx.enter_context(nc.Block())
        units = [(b, n) for b in range(2) for n in range(NT)]

        @block.sync
        def _(sp):
            def load(i, b):
                for a in range(2):
                    sp.dma_start(w[:, b, a], dram["w_o"][a, bass.ds(2 * i + b, 1)].rearrange("a p f m -> p (a f) m")).then_inc(loaded[b], 16)
                    sp.dma_start(g[:, b, a], dram["gates"][bass.ds(2 * i + (b + a * DF), 1)].rearrange("a p t -> p (a t)")).then_inc(loaded[b], 16)

            for b in range(2):
                load(0, b)
            with sp.Fori(0, DF // 2 - 1) as i:
                for b in range(2):
                    sp.wait_ge(done[0], 3 * i + (2 + b))
                    alone(sp, unread)
                    sp.wait_ge(done[1], 3 * i + (1 + 2 * b))
                    alone(sp, unread)
                    load(i + 1, b)

        @block.tensor
        def _(pe):
            with pe.Fori(0, DF // 2) as i:
                for u, (b, n) in enumerate(units):
                    if n == 0:
                        pe.wait_ge(loaded[b], 64 * i + 64)
                    pe.wait_ge(done[u % 2], 3 * i + u // 2)
                    for a, src in enumerate((oa_t, om_t)):
                        for f in range(RF):
                            mm = nc.tensor.matmul(ps[:, u % 2, a], w[:, b, a, f], src[:, f, NB * n:NB * n + NB], start=(f == 0), stop=(f == RF - 1))
                    mm.then_inc(full[u % 2], 1)

        @block.vector
        def _(dve):
            with dve.Fori(0, DF // 2) as i:
                for u, (b, n) in enumerate(units):
                    dve.wait_ge(full[u % 2], 3 * i + u // 2 + 1)
                    nc.vector.tensor_tensor(part[:, u % 2], ps[:, u % 2], g[:, b, :, NB * n:NB * n + NB], ALU.mult).then_inc(scaled, 1)
                    dve.wait_ge(scaled, 6 * i + u + 1)
                    nc.vector.tensor_tensor(merged[:, bass.ds(2 * i + b, 1), NB * n:NB * n + NB].rearrange("p a t -> p (a t)"),
                                            part[:, u % 2, 0], part[:, u % 2, 1], ALU.add).then_inc(done[u % 2], 1)


def output_and_router(nc, dram, consts, merged, logits):
    with ExitStack() as ctx:
        s = Scope(nc, ctx)
        w_hi, w_lo = s.sb("w_out_high", [P, DF, D], F32R), s.sb("w_out_low", [P, DF, D], F32R)
        w_r = s.sb("w_router", [P, DF, ROUTER])
        b_r = s.sb("b_router", [P, ROUTER])
        rows = s.sb("mod_broadcast", [P, 2, 3, D])
        stage_hi, stage_lo = s.sb("merged_high", [P, 2, DF, P], F32R), s.sb("merged_low", [P, 2, DF, P], F32R)
        x = s.sb("x_again", [P, 2, D])
        x1 = s.sb("x1_tile", [P, 2, D])
        h2 = s.sb("h2_tile", [P, 2, D])
        h2_t = s.sb("h2_turned", [P, DF, P])
        st = s.sb("x1_stat", [P, 2, 3])
        norm2 = h2_t[:].rearrange("p k t -> p (k t)")
        w_now = [x1[:, 0], x1[:, 1], h2[:, 0], h2[:, 1]]
        ps = [s.ps(f"ps_out{b}", [P, 2, 512]) for b in range(2)]
        ps_t = s.ps("ps_h2_t", [P, 2, 512])
        ps_r = s.ps("ps_router", [P, 512])
        m = {n: s.sem("out_" + n) for n in ("consts", "consts_b", "own", "staged", "full", "squared", "sqrt_in", "sqrt", "h2_ready", "t_full",
                                            "t_copied", "r_full", "r_done", "x1_ready", "unread", "hi_ready", "w_hi_ready", "w_split")}
        w_loaded = [s.sem(f"w_out_loaded{b}") for b in range(4)]
        x_loaded = [s.sem(f"out_x_loaded{b}") for b in range(2)]
        x1_kept = [s.sem(f"x1_kept{b}") for b in range(2)]
        unread_pool = s.sem("out_unread_pool")
        h2_stored = [s.sem(f"h2_stored{b}") for b in range(2)]
        block = ctx.enter_context(nc.Block())
        runs = ((0, 0, SEQS[0] // P // 2), (1, SEQS[0] // P // 2, TT // 2))

        @block.sync
        def _(sp):
            def load_weights(k):
                sp.dma_start(w_now[k % 4], dram["w_out"][:, k]).then_inc(w_loaded[k % 4], 16)

            for k in range(4):
                load_weights(k)
            for q in range(2):
                for j, part in enumerate((GATE1, SHIFT2, SCALE2)):
                    row = (part * 2 + q) * DF
                    sp.dma_start(rows[:, q, j], dram["mod_rows"][row:row + DF, :].rearrange("f p -> (f p)").partition_broadcast(P)).then_inc(m["consts"], 16)
            sp.dma_start(norm2, dram["norm2"][:].partition_broadcast(P)).then_inc(m["consts"], 16)
            sp.dma_start(b_r[:], dram["b_router"][:].partition_broadcast(P)).then_inc(m["consts"], 16)
            for k in range(4, DF):
                sp.wait_ge(m["w_split"], k - 3)
                load_weights(k)
            with sp.Fori(0, TT // 2) as i:
                for b in range(2):
                    sp.wait_ge(m["x1_ready"], 2 * i)
                    sp.dma_start(x[:, b], dram["x"][bass.ds(i * 2 * P + b * P, P), :]).then_inc(x_loaded[b], 16)
                for b in range(2):
                    sp.wait_ge(m["h2_ready"], 2 * i + b + 1)
                    sp.dma_start(dram["h2"][bass.ds(i * 2 * P + b * P, P), :], h2[:, b]).then_inc(h2_stored[b], 16)
            for b in range(2):
                sp.wait_ge(h2_stored[b], 16 * (TT // 2))

        @block.gpsimd
        def _(pool):
            with pool.Fori(0, TT // 2) as i:
                for b in range(2):
                    pool.wait_ge(m["x1_ready"], 2 * i + (b + 1))
                    alone(pool, unread_pool)
                    nc.gpsimd.tensor_copy(merged[:, :, bass.ds(i * 2 * P + b * P, P)], x1[:, b].rearrange("p (k c) -> p k c", k=DF)).then_inc(x1_kept[b], 1)

        @block.tensor
        def _(pe):
            pe.wait_ge(m["consts_b"], 16)
            pe.wait_ge(m["w_split"], DF)

            def project(i):
                for b in range(2):
                    pe.wait_ge(m["staged"], 2 * i + (b + 1))
                    pe.wait_ge(m["x1_ready"], 2 * i)
                    for n in range(2):
                        for k in range(DF):
                            at = slice(512 * n, 512 * n + 512)
                            mm = split_product(nc, ps[b][:, n], (stage_hi[:, b, k], stage_lo[:, b, k]), (w_hi[:, k, at], w_lo[:, k, at]),
                                               start=(k == 0), stop=(k == DF - 1))
                    mm.then_inc(m["full"], 1)

            def turn_and_route(i):
                for b in range(2):
                    pe.wait_ge(m["h2_ready"], 2 * i + (b + 1))
                    pe.wait_ge(m["t_copied"], 2 * i + b)
                    for k in range(DF):
                        mm = nc.tensor.transpose(ps_t[:, k // 4, P * (k % 4):P * (k % 4) + P], h2[:, b, P * k:P * k + P], consts["ident"][:])
                    mm.then_inc(m["t_full"], 1)
                    pe.wait_ge(m["t_copied"], 2 * i + (b + 1))
                    pe.wait_ge(m["r_done"], 2 * i + b)
                    for k in range(DF):
                        mm = nc.tensor.matmul(ps_r[:, 0:ROUTER], h2_t[:, k], w_r[:, k], start=(k == 0), stop=(k == DF - 1))
                    mm.then_inc(m["r_full"], 1)

            project(0)
            with pe.Fori(1, TT // 2) as i:
                project(i)
                turn_and_route(i - 1)
            turn_and_route(TT // 2 - 1)

        @block.scalar
        def _(act):
            def stage_tiles(i):
                for b in range(2):
                    act.wait_ge(m["full"], max(0, 2 * i + b - 1) if isinstance(i, int) else 2 * i + (b - 1))
                    alone(act, m["unread"])
                    nc.scalar.copy(stage_hi[:, b], merged[:, :, bass.ds(i * 2 * P + b * P, P)]).then_inc(m["hi_ready"], 1)

            def norms(i):
                for b in range(2):
                    act.wait_ge(m["x1_ready"], 2 * i + (b + 1))
                    act.wait_ge(m["sqrt"], 2 * i + b)
                    act.wait_ge(m["t_full"], 2 * i)
                    act.wait_ge(h2_stored[b], 16 * i)
                    nc.scalar.activation(h2[:, b], x1[:, b], ACT.Square, accum_out=st[:, b, 0:1]).then_inc(m["squared"], 1)
                    act.wait_ge(m["sqrt_in"], 2 * i + (b + 1))
                    nc.scalar.activation(st[:, b, 2:3], st[:, b, 1:2], ACT.Sqrt).then_inc(m["sqrt"], 1)

            def copy_turned(i):
                for b in range(2):
                    act.wait_ge(m["t_full"], 2 * i + (b + 1))
                    act.wait_ge(m["r_full"], 2 * i + b)
                    nc.scalar.copy(h2_t[:].rearrange("p (a k) t -> p a (k t)", a=2), ps_t[:]).then_inc(m["t_copied"], 1)

            act.dma_start(w_r[:], dram["w_router"][:, :, :]).then_inc(m["consts_b"], 16)
            stage_tiles(0)
            for k in range(DF):
                act.wait_ge(w_loaded[k % 4], 16 * (k // 4) + 16)
                nc.scalar.copy(w_hi[:, k], w_now[k % 4]).then_inc(m["w_hi_ready"], 1)
            act.wait_ge(m["w_split"], DF)
            stage_tiles(1)
            last = TT // 2 - 1
            with act.Fori(1, last) as i:
                norms(i - 1)
                stage_tiles(i + 1)
                copy_turned(i - 1)
            for i in (last - 1, last):
                norms(i)
                copy_turned(i)

        @block.vector
        def _(dve):
            def stage_low(i):
                for b in range(2):
                    dve.wait_ge(m["hi_ready"], 2 * i + (b + 1))
                    nc.vector.tensor_tensor(stage_lo[:, b], merged[:, :, bass.ds(i * 2 * P + b * P, P)], stage_hi[:, b].bitcast(F32),
                                            ALU.subtract).then_inc(m["staged"], 1)

            stage_low(0)
            for k in range(DF):
                dve.wait_ge(m["w_hi_ready"], k + 1)
                nc.vector.tensor_tensor(w_lo[:, k], w_now[k % 4], w_hi[:, k].bitcast(F32), ALU.subtract).then_inc(m["w_split"], 1)
            dve.wait_ge(m["w_split"], DF)
            start = Chain(dve, m["own"])
            dve.wait_ge(m["consts"], 16 * 8)
            for q in range(2):
                start(nc.vector.tensor_tensor(rows[:, q, 2], rows[:, q, 2], norm2, ALU.mult))

            def add_residual(step, q, i):
                for b in range(2):
                    dve.wait_ge(m["full"], 2 * i + (b + 1))
                    dve.wait_ge(x1_kept[b], i)
                    dve.wait_ge(m["squared"], 2 * i)
                    step(nc.vector.tensor_tensor(x1[:, b].rearrange("p (a x) -> p a x", a=2), ps[b][:],
                                                 rows[:, q, 0].rearrange("p (a x) -> p a x", a=2), ALU.mult))
                    dve.wait_ge(x_loaded[b], 16 * i + 16)
                    nc.vector.tensor_tensor(x1[:, b], x1[:, b], x[:, b], ALU.add).then_inc(m["x1_ready"], 1)

            def norm_and_modulate(step, q, i):
                for b in range(2):
                    dve.wait_ge(m["squared"], 2 * i + (b + 1))
                    nc.vector.tensor_scalar(st[:, b, 1:2], st[:, b, 0:1], 1.0 / D, EPS, ALU.mult, ALU.add).then_inc(m["sqrt_in"], 1)
                    dve.wait_ge(m["sqrt"], 2 * i + (b + 1))
                    step(nc.vector.reciprocal(st[:, b, 2:3], st[:, b, 2:3]))
                    dve.wait_ge(h2_stored[b], 16 * i)
                    dve.wait_ge(m["t_full"], 2 * i)
                    step(nc.vector.scalar_tensor_tensor(out=h2[:, b], in0=x1[:, b], scalar=st[:, b, 2:3], in1=rows[:, q, 2],
                                                        op0=ALU.mult, op1=ALU.mult))
                    step(nc.vector.tensor_tensor(h2[:, b], h2[:, b], rows[:, q, 1], ALU.add))
                    dve.sem_inc(m["h2_ready"], 1)

            def keep_logits(i):
                for b in range(2):
                    dve.wait_ge(m["r_full"], 2 * i + (b + 1))
                    nc.vector.tensor_tensor(logits[:, bass.ds(2 * i + b, 1)].rearrange("p a e -> p (a e)"), ps_r[:, 0:ROUTER], b_r[:],
                                            ALU.add).then_inc(m["r_done"], 1)

            def body(step, q, i, more):
                add_residual(step, q, i)
                if more:
                    stage_low(i + 1)
                keep_logits(i - 1)
                norm_and_modulate(step, q, i)

            add_residual(start, 0, 0)
            stage_low(1)
            norm_and_modulate(start, 0, 0)
            last = TT // 2 - 1
            for q, first, end in runs:
                with dve.Fori(max(first, 1), min(end, last)) as i:
                    step = Chain(dve, m["own"], start.n - 8, i, 2 * 4)
                    body(step, q, i, True)
                    step.end()
            body(Chain(dve, m["own"], start.n - 8, last, 2 * 4), 1, last, False)
            keep_logits(last)


TOP = 2
D_EXPERT = 256
MB = P
BLOCKS = -(-(TOK * TOP + EXPERTS * (MB - 1)) // MB // 2) * 2
FAR = 1e30


def route(nc, dram, consts, logits, weight, slot):
    with ExitStack() as ctx:
        s = Scope(nc, ctx)
        G, E, T = GROUPS, EXPERTS, TT
        rank_g = s.sb("rank_groups", [P, G])
        rank_e = s.sb("rank_experts", [P, E])
        before = s.sb("tokens_before", [P, P])
        full_at = s.sb("full_at", [P, TT])
        block_no = s.sb("block_no", [P, BLOCKS])
        token = s.sb("token_ids", [P, T])
        zero = s.sb("zero_ids", [P, BLOCKS])
        t = lambda name, shape: s.sb("route_" + name, [P] + shape)
        g_max, g_sum, p_grp, e_max, e_max2, ratio, part = (t(n, [T]) for n in ("gmax", "gsum", "pgrp", "emax", "emax2", "ratio", "part"))
        g_exp, g_hot, g_far = (t(n, [T, G]) for n in ("gexp", "ghot", "gfar"))
        e_in, hot1, hot2, hots, value, prod = (t(n, [T, E]) for n in ("ein", "hot1", "hot2", "hots", "value", "prod"))
        total = t("total", [T + 1, E])
        n_blocks, ends, row0 = (t(n, [E]) for n in ("nblocks", "ends", "row0"))
        over = t("over", [E, TT])
        ended = t("ended", [BLOCKS, E])
        block_e = t("block_e", [BLOCKS + 1])
        block_i = s.sb("route_block_i", [P, BLOCKS + 1], I32)
        dest = t("dest", [TOP, T])
        ps_pref = s.ps("ps_prefix", [P, 512])
        ps_tot = s.ps("ps_total", [P, 512])
        m = {n: s.sem("route_" + n) for n in ("consts", "own", "g_in", "g_exp", "r_in", "ratio", "hots", "counted", "zeroed", "zero_stored",
                                              "slots", "scattered", "blocks", "blocks_stored")}
        block = ctx.enter_context(nc.Block())

        @block.sync
        def _(sp):
            for dst, name in ((rank_g, "rank_groups"), (rank_e, "rank_experts"), (full_at, "full_at"), (block_no, "block_no")):
                sp.dma_start(dst[:], dram[name][:].partition_broadcast(P)).then_inc(m["consts"], 16)
            sp.dma_start(before[:], dram["tokens_before"][:, :]).then_inc(m["consts"], 16)
            sp.dma_start(token[:], dram["token_ids"][:, :]).then_inc(m["consts"], 16)
            sp.wait_ge(m["zeroed"], 1)
            sp.dma_start(dram["row_token"].rearrange("(p b) a -> p (b a)", p=P), zero[:]).then_inc(m["zero_stored"], 16)
            sp.wait_ge(m["blocks"], 1)
            sp.dma_start(dram["block_expert"][:, :], block_i[0:1, :]).then_inc(m["blocks_stored"], 16)
            sp.wait_ge(m["blocks_stored"], 16)

        @block.scalar
        def _(act):
            act.wait_ge(m["g_in"], 1)
            nc.scalar.activation(g_exp[:], g_exp[:], ACT.Exp).then_inc(m["g_exp"], 1)
            act.wait_ge(m["r_in"], 1)
            nc.scalar.activation(ratio[:], ratio[:], ACT.Exp).then_inc(m["ratio"], 1)

        @block.tensor
        def _(pe):
            pe.wait_ge(m["hots"], 1)
            flat = hots[:].rearrange("p t e -> p (t e)")
            nc.tensor.matmul(ps_pref[:, 0:T * E], before[:], flat, start=True, stop=True)
            nc.tensor.matmul(ps_tot[:, 0:T * E], consts["ones"][:], flat, start=True, stop=True).then_inc(m["counted"], 1)

        @block.gpsimd
        def _(pool):
            pool.wait_ge(m["slots"], 1)
            pool.wait_ge(m["zero_stored"], 16)
            pool.wait_ge(m["consts"], 96)
            for k in range(TOP):
                for j in range(T):
                    pool.indirect_dma_start(out=dram["row_token"], out_offset=bass.IndirectOffsetOnAxis(ap=slot[:, k, j:j + 1], axis=0),
                                            in_=token[:, j:j + 1], in_offset=None).then_inc(m["scattered"], 16)
            pool.wait_ge(m["scattered"], 16 * TOP * T)

        @block.vector
        def _(dve):
            V = nc.vector
            nc.vector.memset(zero[:], 0).then_inc(m["zeroed"], 1)
            do = Chain(dve, m["own"])
            groups, experts = logits[:, :, 0:G], logits[:, :, G:G + E]
            wide = lambda x, n: x.unsqueeze(2).to_broadcast([P, T, n])
            dve.wait_ge(m["consts"], 96)
            do(V.tensor_reduce(g_max[:], groups, AX.X, ALU.max))
            V.tensor_tensor(g_exp[:], groups, wide(g_max[:], G), ALU.subtract).then_inc(m["g_in"], 1)

            def first_of(hot, values, best, rank, n):
                do(V.tensor_tensor(hot, values, wide(best, n), ALU.is_equal))
                do(V.tensor_tensor(hot, hot, rank[:].unsqueeze(1).to_broadcast([P, T, n]), ALU.mult))
                do(V.tensor_reduce(part[:], hot, AX.X, ALU.max))
                do(V.tensor_tensor(hot, hot, wide(part[:], n), ALU.is_equal))

            first_of(g_hot[:], groups, g_max[:], rank_g, G)
            do(V.tensor_scalar(g_far[:], g_hot[:], FAR, -FAR, ALU.mult, ALU.add))
            for g in range(G):
                part_e = slice(g * PER_GROUP, (g + 1) * PER_GROUP)
                V.tensor_tensor(e_in[:, :, part_e], experts[:, :, part_e], g_hot[:, :, g:g + 1].to_broadcast([P, T, PER_GROUP]), ALU.mult).then_inc(m["own"], 1)
                do.n += 1
            dve.wait_ge(m["own"], do.n)
            for g in range(G):
                part_e = slice(g * PER_GROUP, (g + 1) * PER_GROUP)
                V.tensor_tensor(e_in[:, :, part_e], e_in[:, :, part_e], g_far[:, :, g:g + 1].to_broadcast([P, T, PER_GROUP]), ALU.add).then_inc(m["own"], 1)
                do.n += 1
            dve.wait_ge(m["own"], do.n)
            do(V.tensor_reduce(e_max[:], e_in[:], AX.X, ALU.max))
            first_of(hot1[:], e_in[:], e_max[:], rank_e, E)
            do(V.tensor_scalar(value[:], hot1[:], -3 * FAR, None, ALU.mult))
            do(V.tensor_tensor(e_in[:], e_in[:], value[:], ALU.add))
            do(V.tensor_reduce(e_max2[:], e_in[:], AX.X, ALU.max))
            first_of(hot2[:], e_in[:], e_max2[:], rank_e, E)
            do(V.tensor_tensor(hots[:], hot1[:], hot2[:], ALU.add))
            dve.sem_inc(m["hots"], 1)
            V.tensor_tensor(ratio[:], e_max2[:], e_max[:], ALU.subtract).then_inc(m["r_in"], 1)
            dve.wait_ge(m["g_exp"], 1)
            do(V.tensor_reduce(g_sum[:], g_exp[:], AX.X, ALU.add))
            do(V.reciprocal(p_grp[:], g_sum[:]))
            dve.wait_ge(m["ratio"], 1)
            do(V.tensor_scalar(part[:], ratio[:], 1.0, None, ALU.add))
            do(V.reciprocal(part[:], part[:]))
            do(V.tensor_tensor(weight[:, 0], p_grp[:], part[:], ALU.mult))
            do(V.tensor_tensor(weight[:, 1], weight[:, 0], ratio[:], ALU.mult))
            dve.wait_ge(m["counted"], 1)
            do(V.memset(total[:, 0], 0.0))
            for j in range(T):
                do(V.tensor_tensor(total[:, j + 1], total[:, j], ps_tot[:, E * j:E * j + E], ALU.add))
            do(V.tensor_tensor(over[:], total[:, T].unsqueeze(2).to_broadcast([P, E, TT]), full_at[:].unsqueeze(1).to_broadcast([P, E, TT]), ALU.is_gt))
            do(V.tensor_reduce(n_blocks[:], over[:], AX.X, ALU.add))
            do(V.tensor_tensor_scan(ends[:], consts["ones"][:, 0:E], n_blocks[:], 0.0, ALU.mult, ALU.add))
            do(V.tensor_tensor(row0[:], ends[:], n_blocks[:], ALU.subtract))
            do(V.tensor_scalar(row0[:], row0[:], float(MB), None, ALU.mult))
            do(V.tensor_tensor(value[:], total[:, 0:T], ps_pref[:, 0:T * E].rearrange("p (t e) -> p t e", t=T), ALU.add))
            do(V.tensor_tensor(value[:], value[:], row0[:].unsqueeze(1).to_broadcast([P, T, E]), ALU.add))
            for k, hot in enumerate((hot1, hot2)):
                do(V.tensor_tensor(prod[:], value[:], hot[:], ALU.mult))
                do(V.tensor_reduce(dest[:, k], prod[:], AX.X, ALU.add))
            V.tensor_copy(slot[:], dest[:]).then_inc(m["slots"], 1)
            do(V.tensor_tensor(ended[:], block_no[:].unsqueeze(2).to_broadcast([P, BLOCKS, E]), ends[:].unsqueeze(1).to_broadcast([P, BLOCKS, E]), ALU.is_ge))
            do(V.tensor_reduce(block_e[:, 0:BLOCKS], ended[:], AX.X, ALU.add))
            do(V.tensor_scalar(block_e[:, 0:BLOCKS], block_e[:, 0:BLOCKS], float(E - 1), None, ALU.min))
            do(V.tensor_copy(block_e[:, BLOCKS:BLOCKS + 1], ends[:, E - 1:E]))
            V.tensor_copy(block_i[:], block_e[:]).then_inc(m["blocks"], 1)
            dve.wait_ge(m["slots"], 1)


def experts(nc, dram, consts):
    with ExitStack() as ctx:
        s = Scope(nc, ctx)
        F2 = D_EXPERT // P
        w13 = s.sb("w13_tile", [P, 2, DF, 2 * D_EXPERT])
        w2 = s.sb("w2_tile", [P, 2, F2, D])
        which = s.sb("block_experts", [1, BLOCKS + 1], I32)
        id_rows = s.sb("row_ids_by_block", [BLOCKS, P])
        ids = s.sb("row_ids", [P, BLOCKS], I32)
        ids_now = s.sb("row_ids_now", [P, 2], I32)
        xb = s.sb("xb", [P, 2, D])
        xt = s.sb("xb_turned", [P, 2, DF, P])
        th = s.sb("gate_tanh", [P, 2, F2, P])
        act_in = s.sb("gate_in", [P, 2, F2, P])
        hid = s.sb("hidden", [P, 2, F2, P])
        yb = s.sb("yb_tile", [P, 2, D])
        ps_ids = s.ps("ps_ids", [P, 512])
        ps_h = [s.ps(f"ps_hidden{b}", [P, 2 * F2, P]) for b in range(2)]
        ps_xy = [s.ps(f"ps_xy{b}", [P, 2, 512]) for b in range(2)]
        loaded, ids_turned, unread = s.sem("moe_consts"), s.sem("moe_ids_turned"), s.sem("moe_unread")
        pair = lambda n: [s.sem(f"moe_{n}{b}") for b in range(2)]
        w13_loaded, w2_loaded, x_loaded, ids_ready, stored = (pair(n) for n in ("w13_loaded", "w2_loaded", "x_loaded", "ids_ready", "stored"))
        turned, x_act, x_dve, h_full, tanh = (pair(n) for n in ("turned", "x_act", "x_dve", "h_full", "tanh"))
        gated, hidden, y_full, y_act, y_dve = (pair(n) for n in ("gated", "hidden", "y_full", "y_act", "y_dve"))
        block = ctx.enter_context(nc.Block())

        def used_blocks(eng):
            eng.wait_ge(loaded, 32)
            return eng.value_load(which[0:1, BLOCKS:BLOCKS + 1], min_val=1, max_val=BLOCKS)

        @block.sync
        def _(sp):
            sp.dma_start(which[:], dram["block_expert"][:, :]).then_inc(loaded, 16)
            sp.dma_start(id_rows[:], dram["row_token"].rearrange("(b p) a -> b (p a)", p=P)).then_inc(loaded, 16)
            used = used_blocks(sp)
            with sp.Fori(0, BLOCKS // 2) as i:
                with sp.If(2 * i < used):
                    e = [sp.value_load(which[0:1, bass.ds(2 * i + b, 1)], min_val=0, max_val=EXPERTS - 1) for b in range(2)]
                    for b in range(2):
                        sp.wait_ge(h_full[b], i)
                        alone(sp, unread)
                        sp.dma_start(w13[:, b], dram["w13"][bass.ds(e[b], 1)].rearrange("a p k f -> p (a k) f")).then_inc(w13_loaded[b], 16)
                    for b in range(2):
                        sp.wait_ge(y_full[b], i)
                        alone(sp, unread)
                        sp.dma_start(w2[:, b], dram["w2"][bass.ds(e[b], 1)].rearrange("a p k f -> p (a k) f")).then_inc(w2_loaded[b], 16)

        @block.gpsimd
        def _(pool):
            used = used_blocks(pool)
            pool.wait_ge(ids_turned, 2)
            with pool.Fori(0, BLOCKS // 2) as i:
                with pool.If(2 * i < used):
                    for b in range(2):
                        pool.wait_ge(x_loaded[b], 16 * i)
                        alone(pool, unread)
                        nc.gpsimd.tensor_copy(ids_now[:, b:b + 1], ids[:, bass.ds(2 * i + b, 1)]).then_inc(ids_ready[b], 1)
                        pool.wait_ge(ids_ready[b], i + 1)
                        pool.wait_ge(turned[b], i)
                        alone(pool, unread)
                        pool.indirect_dma_start(out=xb[:, b], out_offset=None, in_=dram["h2"],
                                                in_offset=bass.IndirectOffsetOnAxis(ap=ids_now[:, b:b + 1].bitcast(U32), axis=0)).then_inc(x_loaded[b], 16)

        @block.tensor
        def _(pe):
            used = used_blocks(pe)
            nc.tensor.transpose(ps_ids[:, 0:BLOCKS], id_rows[:], consts["ident"][0:BLOCKS, 0:BLOCKS]).then_inc(ids_turned, 1)
            with pe.Fori(0, BLOCKS // 2) as i:
                with pe.If(2 * i < used):
                    for b in range(2):
                        pe.wait_ge(x_loaded[b], 16 * i + 16)
                        pe.wait_ge(y_act[b], i)
                        pe.wait_ge(y_dve[b], i)
                        for k in range(DF):
                            mm = nc.tensor.transpose(ps_xy[b][:, k // 4, P * (k % 4):P * (k % 4) + P], xb[:, b, P * k:P * k + P], consts["ident"][:])
                        mm.then_inc(turned[b], 1)
                    for b in range(2):
                        pe.wait_ge(w13_loaded[b], 16 * i + 16)
                        pe.wait_ge(x_act[b], i + 1)
                        pe.wait_ge(x_dve[b], i + 1)
                        pe.wait_ge(hidden[b], i)
                        for f in range(2 * F2):
                            for k in range(DF):
                                mm = nc.tensor.matmul(ps_h[b][:, f], w13[:, b, k, P * f:P * f + P], xt[:, b, k], start=(k == 0), stop=(k == DF - 1))
                        mm.then_inc(h_full[b], 1)
                    for b in range(2):
                        pe.wait_ge(w2_loaded[b], 16 * i + 16)
                        pe.wait_ge(hidden[b], i + 1)
                        for c in range(2):
                            for k in range(F2):
                                mm = nc.tensor.matmul(ps_xy[b][:, c], hid[:, b, k], w2[:, b, k, 512 * c:512 * c + 512], start=(k == 0), stop=(k == F2 - 1))
                        mm.then_inc(y_full[b], 1)

        @block.scalar
        def _(act):
            used = used_blocks(act)
            with act.Fori(0, BLOCKS // 2) as i:
                with act.If(2 * i < used):
                    for b in range(2):
                        act.wait_ge(turned[b], i + 1)
                        act.wait_ge(h_full[b], i)
                        nc.scalar.copy(xt[:, b, 0:4].rearrange("p k t -> p (k t)"), ps_xy[b][:, 0]).then_inc(x_act[b], 1)
                    for b in range(2):
                        act.wait_ge(h_full[b], i + 1)
                        act.wait_ge(gated[b], i)
                        nc.scalar.activation(th[:, b], ps_h[b][:, 0:F2], ACT.Tanh, scale=0.5).then_inc(tanh[b], 1)
                    for b in range(2):
                        act.wait_ge(y_full[b], i + 1)
                        act.wait_ge(stored[b], 16 * i)
                        nc.scalar.copy(yb[:, b, 0:512], ps_xy[b][:, 0]).then_inc(y_act[b], 1)
                        act.wait_ge(y_act[b], i + 1)
                        act.wait_ge(y_dve[b], i + 1)
                        act.dma_start(dram["yb"][bass.ds(2 * i + b, 1)].rearrange("a p d -> p (a d)"), yb[:, b]).then_inc(stored[b], 16)
            pairs = used + 1 >> 1
            for b in range(2):
                act.wait_ge(stored[b], 16 * pairs)
                alone(act, unread)

        @block.vector
        def _(dve):
            used = used_blocks(dve)
            dve.wait_ge(ids_turned, 1)
            nc.vector.tensor_copy(ids[:], ps_ids[:, 0:BLOCKS]).then_inc(ids_turned, 1)
            with dve.Fori(0, BLOCKS // 2) as i:
                with dve.If(2 * i < used):
                    for b in range(2):
                        dve.wait_ge(turned[b], i + 1)
                        dve.wait_ge(h_full[b], i)
                        nc.vector.tensor_copy(xt[:, b, 4:8].rearrange("p k t -> p (k t)"), ps_xy[b][:, 1]).then_inc(x_dve[b], 1)
                    for b in range(2):
                        dve.wait_ge(tanh[b], i + 1)
                        dve.wait_ge(hidden[b], i)
                        nc.vector.scalar_tensor_tensor(out=act_in[:, b], in0=th[:, b], scalar=1.0, in1=ps_h[b][:, 0:F2], op0=ALU.add,
                                                       op1=ALU.mult).then_inc(gated[b], 1)
                        dve.wait_ge(gated[b], i + 1)
                        dve.wait_ge(y_full[b], i)
                        nc.vector.scalar_tensor_tensor(out=hid[:, b], in0=act_in[:, b], scalar=0.5, in1=ps_h[b][:, F2:2 * F2], op0=ALU.mult,
                                                       op1=ALU.mult).then_inc(hidden[b], 1)
                    for b in range(2):
                        dve.wait_ge(y_full[b], i + 1)
                        dve.wait_ge(stored[b], 16 * i)
                        nc.vector.tensor_copy(yb[:, b, 512:1024], ps_xy[b][:, 1]).then_inc(y_dve[b], 1)


def combine(nc, dram, consts, x1, weight, slot):
    BUF = 4
    with ExitStack() as ctx:
        s = Scope(nc, ctx)
        gate2 = s.sb("gate2_broadcast", [P, 2, D])
        picked = s.sb("picked", [P, BUF, TOP, D])
        mix = s.sb("mixed", [P, BUF, D])
        out = s.sb("out_tile", [P, BUF, D])
        pair = lambda n: [s.sem(f"comb_{n}{b}") for b in range(BUF)]
        gathered, stored, done = pair("gathered"), pair("stored"), pair("done")
        consts_in, own = s.sem("comb_consts"), s.sem("comb_own")
        block = ctx.enter_context(nc.Block())
        yb = dram["yb"].rearrange("b p d -> (b p) d")

        @block.sync
        def _(sp):
            for q in range(2):
                row = (GATE2 * 2 + q) * DF
                sp.dma_start(gate2[:, q], dram["mod_rows"][row:row + DF, :].rearrange("f p -> (f p)").partition_broadcast(P)).then_inc(consts_in, 16)
            for t in range(TT):
                b = t % BUF
                sp.wait_ge(done[b], t // BUF + 1)
                sp.dma_start(dram["y"][P * t:P * t + P, :], out[:, b]).then_inc(stored[b], 16)
            for b in range(BUF):
                sp.wait_ge(stored[b], 16 * (TT // BUF))

        @block.gpsimd
        def _(pool):
            for t in range(TT):
                b = t % BUF
                if t >= BUF:
                    pool.wait_ge(done[b], t // BUF)
                for k in range(TOP):
                    pool.indirect_dma_start(out=picked[:, b, k], out_offset=None, in_=yb,
                                            in_offset=bass.IndirectOffsetOnAxis(ap=slot[:, k, t:t + 1], axis=0)).then_inc(gathered[b], 16)

        @block.vector
        def _(dve):
            dve.wait_ge(consts_in, 32)
            do = Chain(dve, own)
            for t in range(TT):
                b, q = t % BUF, int(t >= SEQS[0] // P)
                dve.wait_ge(gathered[b], 32 * (t // BUF) + 32)
                do(nc.vector.tensor_scalar(mix[:, b], picked[:, b, 0], weight[:, 0, t:t + 1], None, ALU.mult))
                do(nc.vector.scalar_tensor_tensor(out=mix[:, b], in0=picked[:, b, 1], scalar=weight[:, 1, t:t + 1], in1=mix[:, b],
                                                  op0=ALU.mult, op1=ALU.add))
                do(nc.vector.tensor_tensor(mix[:, b], mix[:, b], gate2[:, q], ALU.mult))
                if t >= BUF:
                    dve.wait_ge(stored[b], 16 * (t // BUF))
                nc.vector.tensor_tensor(out[:, b].rearrange("p (k c) -> p k c", k=DF), mix[:, b].rearrange("p (k c) -> p k c", k=DF), x1[:, :, P * t:P * t + P], ALU.add).then_inc(done[b], 1)


def encoder(nc, dram):
    with ExitStack() as ctx:
        s = Scope(nc, ctx)
        consts = {
            "cols": s.sb("cols", [P, NCOLS]),
            "ident": s.sb("ident", [P, P]),
            "ones": s.sb("ones", [P, P]),
            "mod": s.sb("mod", [P, 6, 2, DF]),
            "scale1": s.sb("scale1", [P, 2, DF]),
            "half_merge": s.sb("half_merge", [P, N_GATES]),
            "p_end": s.sb("p_end", [P, 2, RF, TOK // CH]),
        }
        load_constants(nc, dram, consts)
        with ExitStack() as inner:
            hs = Scope(nc, inner)
            h_hi = hs.sb("h_t_high", [P, DF, TOK], F32R)
            modulation_and_norm(nc, dram, consts, h_hi[:].bitcast(F32))
            h_lo = hs.sb("h_t_low", [P, DF, TOK], F32R)
            modulate_and_split(nc, dram, consts, h_hi, h_lo)
            project_in(nc, dram, consts, h_hi, h_lo)
        rwkv_operands(nc, dram, consts)
        wkv_scan(nc, dram, consts)
        mla_project(nc, dram, consts)
        logits = s.sb("logits", [P, TT, ROUTER])
        merged = s.sb("merged_t", [P, DF, TOK])
        with ExitStack() as inner:
            i = Scope(nc, inner)
            om_t = i.sb("om_t", [P, RF, TOK])
            with ExitStack() as deep:
                o_all = Scope(nc, deep).sb("o_all", [P, TT, 512])
                attention(nc, dram, consts, o_all)
                turn_o(nc, dram, consts, o_all, om_t)
            oa_t = i.sb("oa_t", [P, RF, TOK])
            rwkv_finish(nc, dram, consts, oa_t)
            merge_branches(nc, dram, consts, oa_t, om_t, merged)
        output_and_router(nc, dram, consts, merged, logits)
        weight = s.sb("weight", [P, TOP, TT])
        slot = s.sb("slot", [P, TOP, TT], U32)
        route(nc, dram, consts, logits, weight, slot)
        experts(nc, dram, consts)
        combine(nc, dram, consts, merged, weight, slot)




INTERNAL = {
    "mod_rows": (96, P),
    "p_t": (N_SHIFTED, P, TOK),
    "gates": (N_GATES, P, TOK),
    "wkv_in": (2, TT, P, 16, P),
    "wkv_y": (2, TT, P, RF, P),
    "qk_t": (2 * HEADS, HD, TOK),
    "v_mla": (TT, P, 512),
    "h2": (TOK, D),
    "row_token": (BLOCKS * MB, 1),
    "block_expert": (1, BLOCKS + 1),
    "yb": (BLOCKS, MB, D),
}


INTERNAL_TYPES = {"block_expert": I32}


def _tiles(w, width):
    K, M = w.shape
    return np.ascontiguousarray(w.reshape(K // P, P, M // width, width).transpose(2, 1, 0, 3))


def _lay_out(inputs):
    a = {k: np.asarray(v) for k, v in inputs.items()}
    one = {k: v[0] for k, v in a.items() if k not in ("x_prompt", "x_sample", "c_prompt", "c_sample")}
    out = {"x": np.concatenate([a["x_prompt"][0], a["x_sample"][0]])}
    out["c"] = np.concatenate([a["c_prompt"], a["c_sample"]]).reshape(2 * DF, P)
    out["w_ada"] = _tiles(one["w_ada"], 512)
    out["b_ada"] = one["b_ada"].reshape(-1, 512)
    w_in = one["w_in"]
    rw, q, kv, rope = 1920, 768, 256, 32
    wide = np.zeros((D, P), w_in.dtype)
    wide[:, 64:96] = w_in[:, rw + q + kv:rw + q + kv + rope]
    out["w_in"] = _tiles(np.concatenate([w_in[:, :rw], wide, w_in[:, rw:rw + q + kv], w_in[:, rw + q + kv + rope:]], 1), P)

    def columns(v, width):
        v = v.reshape(-1)
        full = np.zeros((width, P), np.float32)
        full.reshape(-1)[:v.size] = v
        return full.T

    gain = lambda a, b: np.concatenate([one[a], one[b]])
    parts = {
        "norm1": one["norm1"], "mu_prev": one["shift_mu"][0], "mu_next": one["shift_mu"][1],
        "b_merge": one["b_merge"], "w0": one["decay_w0"], "a0": one["iclr_a0"], "k_k": one["k_k"], "k_a": one["k_a"],
        "r_k": one["r_k"], "gn_w": one["gn_w"], "gn_b": one["gn_b"], "qa_norm": one["q_a_norm"], "kva_norm": one["kv_a_norm"],
        "q_gain": gain("q_nope_norm", "q_rope_norm"), "k_gain": gain("k_nope_norm", "k_rope_norm"),
    }
    out["cols"] = np.ascontiguousarray(np.concatenate([columns(parts[k], w) for k, (_, w) in COLS.items()], 1))
    out["ident"] = np.eye(P, dtype=np.float32)
    out["ones"] = np.ones((P, P), np.float32)
    more_layouts(out, one)
    return out


def more_layouts(out, one):
    out["decay_up"] = one["decay_up"].reshape(P, -1)
    out["iclr_up"] = one["iclr_up"].reshape(P, -1)
    out["chunk_reset"] = np.tile((np.arange(RF * PB) % CH != 0).astype(np.float32), (P, 1))
    out["gate_up"] = one["gate_up"]
    out["w_o"] = np.stack([_tiles(one["w_o_rwkv"], P), _tiles(one["w_o_mla"], P)])
    rows = lambda w: np.ascontiguousarray(w.reshape(-1, P, w.shape[-1]).transpose(1, 0, 2))
    out["w_out"] = rows(one["w_out"])
    out["w_router"] = rows(np.concatenate([one["w_rg"], one["w_re"]], 1))
    out["b_router"] = np.concatenate([one["b_rg"], one["b_re"]])
    out["norm2"] = one["norm2"]
    out["w13"] = np.ascontiguousarray(one["w13"].reshape(EXPERTS, DF, P, -1).transpose(0, 2, 1, 3))
    out["w2"] = np.ascontiguousarray(one["w2"].reshape(EXPERTS, D_EXPERT // P, P, D).transpose(0, 2, 1, 3))
    out["rank_groups"] = np.arange(GROUPS, 0, -1, dtype=np.float32)
    out["rank_experts"] = np.arange(EXPERTS, 0, -1, dtype=np.float32)
    out["full_at"] = MB * np.arange(TT, dtype=np.float32)
    out["block_no"] = np.arange(BLOCKS, dtype=np.float32)
    out["tokens_before"] = np.triu(np.ones((P, P), np.float32), 1)
    out["token_ids"] = np.ascontiguousarray(np.arange(TOK, dtype=np.float32).reshape(TT, P).T)
    by_head = lambda w, n: w.reshape(n, P, HEADS, -1).transpose(1, 0, 2, 3)
    out["w_uq"] = np.ascontiguousarray(by_head(one["w_uq"], QF))
    out["w_uk"] = np.zeros((P, KVF, HEADS, HD), np.float32)
    out["w_uk"][..., :NOPE] = by_head(one["w_uk"], KVF)
    out["w_uv"] = np.ascontiguousarray(one["w_uv"].reshape(KVF, P, 512).transpose(1, 0, 2))
    U = 2 * HEADS
    out["gather_means"] = np.zeros((HD, U, 2 * U), np.float32)
    out["spread_rstd"] = np.zeros((P, U, HD), np.float32)
    for u in range(U):
        for j, part in enumerate((slice(0, NOPE), slice(NOPE, HD))):
            out["gather_means"][part, u, 2 * u + j] = 1.0 / (NOPE, ROPE)[j]
            out["spread_rstd"][2 * u + j, u, part] = 1.0
    out["rotate"] = np.zeros((HD, HD), np.float32)
    for k in range(ROPE // 2):
        out["rotate"][NOPE + ROPE // 2 + k, NOPE + k] = -1.0
        out["rotate"][NOPE + k, NOPE + ROPE // 2 + k] = 1.0
    inv = np.float32(1.0) / (np.float32(10000.0) ** (np.arange(0, ROPE, 2, dtype=np.float32) / np.float32(ROPE)))
    ang = np.concatenate([np.arange(n, dtype=np.float32)[:, None] * inv[None] for n in SEQS]).T
    out["rope"] = np.zeros((HD, 2, TOK), np.float32)
    out["rope"][:NOPE, 0] = 1.0
    out["rope"][NOPE:, 0] = np.tile(np.cos(ang), (2, 1))
    out["rope"][NOPE:, 1] = np.tile(np.sin(ang), (2, 1))
    head = np.arange(P) // CH
    j, t = np.arange(CH)[:, None], np.arange(CH)[None]
    masks = np.array([[j < t, j <= t], [j > t, j >= t]], np.float32).transpose(2, 0, 1, 3)
    out["tri_mask"] = np.concatenate([masks, masks])
    j, t = np.arange(P)[:, None], np.arange(P)[None]
    out["level_mask"] = np.array([((j >> l) ^ (t >> l)) == 1 for l in range(LEVELS)], np.float32).transpose(1, 0, 2).copy()
    out["ident_halves"] = np.tile(np.eye(CH, dtype=np.float32), (2, 1))
    out["gather_heads"] = np.zeros((P, RF, 2 * RF), np.float32)
    out["spread_heads"] = np.zeros((P, RF, P), np.float32)
    for f in range(RF):
        for g in range(2):
            out["gather_heads"][CH * g:CH * g + CH, f, 2 * f + g] = 1.0
            out["spread_heads"][2 * f + g, f, CH * g:CH * g + CH] = 1.0
    out["head_ones"] = (head[:, None] == head[None]).astype(np.float32)


def kernel(**inputs):
    import concourse.bacc as bacc
    from concourse.bass_utils import run_bass_kernel_spmd

    nc = bacc.Bacc("TRN2", target_bir_lowering=False, num_devices=1)
    arrays = _lay_out(inputs)
    dram = {k: nc.dram_tensor(f"in_{k}", v.shape, mybir.dt.from_np(v.dtype), kind="ExternalInput").ap() for k, v in arrays.items()}
    for k, shape in INTERNAL.items():
        dram[k] = nc.dram_tensor(k, shape, INTERNAL_TYPES.get(k, F32), kind="Internal").ap()
    dram["y"] = nc.dram_tensor("y", (TOK, D), F32, kind="ExternalOutput").ap()
    encoder(nc, dram)
    r = run_bass_kernel_spmd(nc, [{f"in_{k}": v for k, v in arrays.items()}], core_ids=[0])
    y = r.results[0]["y"]
    return y[None, :SEQS[0]], y[None, SEQS[0]:]
```
